# Optimizing a Trainium2 kernel written in Bass

```python
import math
import jax
import jax.numpy as jnp
from jax import lax
import numpy as np

D_MODEL = 1024
BATCH = 1
SEQ = 1024
DEPTH = 1
DEC_BATCH = 8
DEC_SEQ = 8
PAST_LEN = 8192
PAGE_SIZE = 128

RW_HEAD = 64
RW_HEADS = D_MODEL // 128
RW_DIM = RW_HEADS * RW_HEAD
RW_DECAY_LORA = 64
RW_A_LORA = 64
RW_GATE_LORA = 128
RW_LN_EPS = 64e-5
RW_COLS = 3 * RW_DIM + RW_DECAY_LORA + RW_A_LORA + RW_GATE_LORA
SSM_DIM = D_MODEL
SSM_HEAD = 64
SSM_HEADS = SSM_DIM // SSM_HEAD
SSM_GROUPS = 2
SSM_STATE = 128
SSM_CONV = 4
SSM_CHUNK = 128
SSM_CONV_DIM = SSM_DIM + 2 * SSM_GROUPS * SSM_STATE
SSM_COLS = SSM_DIM + SSM_CONV_DIM + SSM_HEADS
GATE_COLS = 2 * D_MODEL
IN_COLS = RW_COLS + SSM_COLS + GATE_COLS
PEER_HEADS = 8
PEER_NKEYS = 128
PEER_EXPERTS = PEER_NKEYS * PEER_NKEYS
PEER_TOPK = 16
PEER_DKEY = 256
PEER_BLOCK = 128
NORM_EPS = 1e-6

kernel_name = 'rwkv7_mamba2_peer_hybrid_step'

def _rmsnorm(x, g):
    xf = x.astype(jnp.float32)
    y = xf * lax.rsqrt(jnp.mean(xf * xf, axis=-1, keepdims=True) + NORM_EPS)
    return (y * g.astype(jnp.float32)).astype(x.dtype)

def _seg_decay(a):
    L = a.shape[-1]
    cs = jnp.cumsum(a, axis=-1)
    seg = cs[..., :, None] - cs[..., None, :]
    mask = jnp.tril(jnp.ones((L, L), dtype=bool))
    return jnp.exp(jnp.where(mask, seg, -jnp.inf))

def _rwkv7(p, p_prev, s0, mu, w0, w2, a0, a2, g2, k_k, k_a, r_k, ln_w, ln_b):
    f32 = jnp.float32
    B, T, _ = p.shape
    prev = jnp.concatenate([p_prev[:, None], p[:, :-1]], axis=1)
    q = p + (prev - p) * mu
    o = 0
    r = q[..., o:o + RW_DIM]; o += RW_DIM
    k = q[..., o:o + RW_DIM]; o += RW_DIM
    v = q[..., o:o + RW_DIM]; o += RW_DIM
    lw = q[..., o:o + RW_DECAY_LORA]; o += RW_DECAY_LORA
    la = q[..., o:o + RW_A_LORA]; o += RW_A_LORA
    lg = q[..., o:o + RW_GATE_LORA]
    w = -jax.nn.softplus(-(w0 + jnp.tanh(lw) @ w2).astype(f32)) - 0.5
    decay = jnp.exp(-jnp.exp(w))
    a = jax.nn.sigmoid((a0 + la @ a2).astype(f32))
    g = (jax.nn.sigmoid(lg) @ g2).astype(f32)
    hs = lambda t: t.reshape(B, T, RW_HEADS, RW_HEAD).astype(f32)
    r, k, v, decay, a = hs(r), hs(k), hs(v), hs(decay), hs(a)
    kk = k * k_k.reshape(RW_HEADS, RW_HEAD).astype(f32)
    kk = kk / jnp.maximum(jnp.sqrt(jnp.sum(kk * kk, axis=-1, keepdims=True)), 1e-12)
    k = k * (1.0 + (a - 1.0) * k_a.reshape(RW_HEADS, RW_HEAD).astype(f32))

    def step(S, inp):
        r_t, d_t, k_t, v_t, kk_t, b_t = inp
        sk = jnp.einsum('bhvk,bhk->bhv', S, kk_t)
        S = S * d_t[:, :, None, :] - sk[..., None] * b_t[:, :, None, :] + v_t[..., None] * k_t[:, :, None, :]
        return S, jnp.einsum('bhvk,bhk->bhv', S, r_t)

    tm = lambda t: jnp.moveaxis(t, 1, 0)
    sT, y = lax.scan(step, s0.astype(f32), (tm(r), tm(decay), tm(k), tm(v), tm(kk), tm(kk * a)))
    y = jnp.moveaxis(y, 0, 1)
    mean = jnp.mean(y, axis=-1, keepdims=True)
    var = jnp.mean(jnp.square(y - mean), axis=-1, keepdims=True)
    yn = ((y - mean) * lax.rsqrt(var + RW_LN_EPS)).reshape(B, T, RW_DIM)
    yn = yn * ln_w.astype(f32) + ln_b.astype(f32)
    bonus = (jnp.sum(r * k * r_k.astype(f32), axis=-1, keepdims=True) * v).reshape(B, T, RW_DIM)
    out = ((yn + bonus) * g).astype(p.dtype)
    return out, sT.astype(s0.dtype)

def _ssd(X, dA, Bm, Cm, h0):
    Bsz, T, H, P = X.shape
    G, N = Bm.shape[2], Bm.shape[3]
    J = H // G
    L = math.gcd(T, SSM_CHUNK)
    nc = T // L
    X = X.reshape(Bsz, nc, L, G, J, P)
    a = jnp.transpose(dA.reshape(Bsz, nc, L, G, J), (0, 3, 4, 1, 2))
    Bc = Bm.reshape(Bsz, nc, L, G, N)
    Cc = Cm.reshape(Bsz, nc, L, G, N)
    cs = jnp.cumsum(a, axis=-1)
    cb = jnp.einsum('bclgn,bcsgn->bgcls', Cc, Bc)
    y_diag = jnp.einsum('bgcls,bgjcls,bcsgjp->bclgjp', cb, _seg_decay(a), X)
    decay_states = jnp.exp(cs[..., -1:] - cs)
    states = jnp.einsum('bclgn,bgjcl,bclgjp->bcgjpn', Bc, decay_states, X)
    states = jnp.concatenate([h0.reshape(Bsz, 1, G, J, P, N), states], axis=1)
    chunk_a = jnp.pad(cs[..., -1], ((0, 0), (0, 0), (0, 0), (1, 0)))
    new_states = jnp.einsum('bgjzc,bcgjpn->bzgjpn', _seg_decay(chunk_a), states)
    y_off = jnp.einsum('bclgn,bcgjpn,bgjcl->bclgjp', Cc, new_states[:, :-1], jnp.exp(cs))
    y = (y_diag + y_off).reshape(Bsz, T, H, P)
    return y, new_states[:, -1].reshape(Bsz, H, P, N)

def _mamba2(p, conv_buf, h0, conv_w, conv_b, dt_bias, A_log, D_skip, norm_w):
    f32 = jnp.float32
    B, T, _ = p.shape
    z = p[..., :SSM_DIM]
    xbc = p[..., SSM_DIM:SSM_DIM + SSM_CONV_DIM]
    dt = p[..., SSM_DIM + SSM_CONV_DIM:]
    full = jnp.concatenate([conv_buf.astype(p.dtype), xbc], axis=1)
    new_buf = full[:, -(SSM_CONV - 1):]
    conv = conv_b + full[:, 0:T] * conv_w[0]
    for j in range(1, SSM_CONV):
        conv = conv + full[:, j:j + T] * conv_w[j]
    xbc = jax.nn.silu(conv)
    gn = SSM_GROUPS * SSM_STATE
    xs = xbc[..., :SSM_DIM].reshape(B, T, SSM_HEADS, SSM_HEAD).astype(f32)
    Bm = xbc[..., SSM_DIM:SSM_DIM + gn].reshape(B, T, SSM_GROUPS, SSM_STATE).astype(f32)
    Cm = xbc[..., SSM_DIM + gn:].reshape(B, T, SSM_GROUPS, SSM_STATE).astype(f32)
    dt = jax.nn.softplus((dt + dt_bias).astype(f32))
    A = -jnp.exp(A_log.astype(f32))
    y, hT = _ssd(xs * dt[..., None], dt * A, Bm, Cm, h0.astype(f32))
    y = y + xs * D_skip.astype(f32)[:, None]
    y = y.reshape(B, T, SSM_DIM) * jax.nn.silu(z.astype(f32))
    yg = y.reshape(B, T, SSM_GROUPS, SSM_DIM // SSM_GROUPS)
    yg = yg * lax.rsqrt(jnp.mean(yg * yg, axis=-1, keepdims=True) + NORM_EPS)
    out = (yg.reshape(B, T, SSM_DIM) * norm_w.astype(f32)).astype(p.dtype)
    return out, new_buf.astype(conv_buf.dtype), hT.astype(h0.dtype)

def _peer(xn, wq, keys, u, v):
    B, T, D = xn.shape
    n = B * T
    n_pad = -(-n // PEER_BLOCK) * PEER_BLOCK
    xt = jnp.pad(xn.reshape(n, D), ((0, n_pad - n), (0, 0))).reshape(n_pad // PEER_BLOCK, PEER_BLOCK, D)

    def block(xb):
        q = (xb @ wq).reshape(PEER_BLOCK, PEER_HEADS, 2, PEER_DKEY // 2)
        s = jnp.einsum('thpd,hpkd->thpk', q, keys).astype(jnp.float32)
        s1, i1 = lax.top_k(s[:, :, 0], PEER_TOPK)
        s2, i2 = lax.top_k(s[:, :, 1], PEER_TOPK)
        cand = (s1[..., :, None] + s2[..., None, :]).reshape(PEER_BLOCK, PEER_HEADS, PEER_TOPK * PEER_TOPK)
        sc, ic = lax.top_k(cand, PEER_TOPK)
        e1 = jnp.take_along_axis(i1, ic // PEER_TOPK, axis=-1)
        e2 = jnp.take_along_axis(i2, ic % PEER_TOPK, axis=-1)
        idx = e1 * PEER_NKEYS + e2
        gate = jax.nn.softmax(sc, axis=-1)
        act = jax.nn.gelu(jnp.einsum('td,thkd->thk', xb, u[idx]).astype(jnp.float32), approximate=False)
        return jnp.einsum('thk,thkd->td', (gate * act).astype(xb.dtype), v[idx])

    out = lax.map(block, xt)
    return out.reshape(n_pad, D)[:n].reshape(B, T, D)

def _layer(x, c, shift0, wkv0, conv0, ssm0, lp):
    f32 = jnp.float32
    mod = jax.nn.silu(c) @ lp['w_ada'] + lp['b_ada']
    sh1, sc1, gt1, sh2, sc2, gt2 = jnp.split(mod, 6, axis=-1)
    xn = _rmsnorm(x, lp['norm1_g']) * (1 + sc1[:, None]) + sh1[:, None]
    proj = xn @ lp['w_in']
    p_rw = proj[..., :RW_COLS]
    p_ssm = proj[..., RW_COLS:RW_COLS + SSM_COLS]
    p_gate = proj[..., RW_COLS + SSM_COLS:]
    p_prev = shift0.astype(x.dtype) @ lp['w_in'][:, :RW_COLS]
    o_a, wkvT = _rwkv7(p_rw, p_prev, wkv0, lp['rw_mu'], lp['rw_w0'], lp['rw_w2'], lp['rw_a0'], lp['rw_a2'],
                       lp['rw_g2'], lp['rw_k_k'], lp['rw_k_a'], lp['rw_r_k'], lp['rw_ln_w'], lp['rw_ln_b'])
    o_b, convT, ssmT = _mamba2(p_ssm, conv0, ssm0, lp['ssm_conv_w'], lp['ssm_conv_b'], lp['ssm_dt_bias'],
                               lp['ssm_A_log'], lp['ssm_D'], lp['ssm_norm_w'])
    g = jax.nn.sigmoid(p_gate.astype(f32)).astype(x.dtype)
    merged = g[..., :D_MODEL] * (o_a @ lp['w_pa']) + g[..., D_MODEL:] * (o_b @ lp['w_pb'])
    x = x + gt1[:, None] * (merged @ lp['w_out'])
    xn2 = _rmsnorm(x, lp['norm2_g']) * (1 + sc2[:, None]) + sh2[:, None]
    x = x + gt2[:, None] * _peer(xn2, lp['peer_wq'], lp['peer_keys'], lp['peer_u'], lp['peer_v'])
    return x, xn[:, -1].astype(shift0.dtype), wkvT, convT, ssmT

def _trunk(x, c, shift, wkv, conv, ssm, params, final_g, w_ada_f, b_ada_f):
    n_sh, n_wkv, n_conv, n_ssm = [], [], [], []
    for l in range(DEPTH):
        lp = {name: arr[l] for name, arr in params.items()}
        x, s_sh, s_wkv, s_conv, s_ssm = _layer(x, c, shift[l], wkv[l], conv[l], ssm[l], lp)
        n_sh.append(s_sh); n_wkv.append(s_wkv); n_conv.append(s_conv); n_ssm.append(s_ssm)
    fm = jax.nn.silu(c) @ w_ada_f + b_ada_f
    shf, scf = jnp.split(fm, 2, axis=-1)
    y = _rmsnorm(x, final_g) * (1 + scf[:, None]) + shf[:, None]
    return y, jnp.stack(n_sh), jnp.stack(n_wkv), jnp.stack(n_conv), jnp.stack(n_ssm)

def setup_inputs(seed: int = 0) -> dict:
    key = jax.random.key(seed)
    ks = iter(jax.random.split(key, 48))
    f32 = jnp.float32
    nrm = lambda shape, scale: jax.random.normal(next(ks), shape, f32) * scale
    uni = lambda shape, lo, hi: jax.random.uniform(next(ks), shape, f32, lo, hi)
    L = DEPTH
    dt0 = jnp.exp(uni((L, SSM_HEADS), math.log(1e-3), math.log(1e-1)))
    return {
        'x_prompt': nrm((BATCH, SEQ, D_MODEL), 1.0),
        'x_sample': nrm((DEC_BATCH, DEC_SEQ, D_MODEL), 1.0),
        'c_prompt': nrm((BATCH, D_MODEL), 1.0),
        'c_sample': nrm((DEC_BATCH, D_MODEL), 1.0),
        'state_shift': nrm((L, DEC_BATCH, D_MODEL), 1.0),
        'state_wkv': nrm((L, DEC_BATCH, RW_HEADS, RW_HEAD, RW_HEAD), 0.3),
        'state_conv': nrm((L, DEC_BATCH, SSM_CONV - 1, SSM_CONV_DIM), 1.0),
        'state_ssm': nrm((L, DEC_BATCH, SSM_HEADS, SSM_HEAD, SSM_STATE), 0.1),
        'w_ada': nrm((L, D_MODEL, 6 * D_MODEL), 0.5 * D_MODEL ** -0.5),
        'b_ada': nrm((L, 6 * D_MODEL), 0.01),
        'norm1_g': 1.0 + nrm((L, D_MODEL), 0.02),
        'w_in': nrm((L, D_MODEL, IN_COLS), D_MODEL ** -0.5),
        'rw_mu': uni((L, RW_COLS), 0.0, 1.0),
        'rw_w0': uni((L, RW_DIM), -3.0, 0.0),
        'rw_w2': nrm((L, RW_DECAY_LORA, RW_DIM), 0.5 * RW_DECAY_LORA ** -0.5),
        'rw_a0': nrm((L, RW_DIM), 0.1),
        'rw_a2': nrm((L, RW_A_LORA, RW_DIM), 0.5 * RW_A_LORA ** -0.5),
        'rw_g2': nrm((L, RW_GATE_LORA, RW_DIM), RW_GATE_LORA ** -0.5),
        'rw_k_k': 0.85 + nrm((L, RW_DIM), 0.1),
        'rw_k_a': 1.0 + nrm((L, RW_DIM), 0.1),
        'rw_r_k': nrm((L, RW_HEADS, RW_HEAD), 0.1),
        'rw_ln_w': 1.0 + nrm((L, RW_DIM), 0.02),
        'rw_ln_b': nrm((L, RW_DIM), 0.01),
        'ssm_conv_w': nrm((L, SSM_CONV, SSM_CONV_DIM), 0.5),
        'ssm_conv_b': nrm((L, SSM_CONV_DIM), 0.01),
        'ssm_dt_bias': dt0 + jnp.log(-jnp.expm1(-dt0)),
        'ssm_A_log': jnp.log(uni((L, SSM_HEADS), 1.0, 16.0)),
        'ssm_D': 1.0 + nrm((L, SSM_HEADS), 0.1),
        'ssm_norm_w': 1.0 + nrm((L, SSM_DIM), 0.02),
        'w_pa': nrm((L, RW_DIM, D_MODEL), RW_DIM ** -0.5),
        'w_pb': nrm((L, SSM_DIM, D_MODEL), SSM_DIM ** -0.5),
        'w_out': nrm((L, D_MODEL, D_MODEL), D_MODEL ** -0.5),
        'norm2_g': 1.0 + nrm((L, D_MODEL), 0.02),
        'peer_wq': nrm((L, D_MODEL, PEER_HEADS * PEER_DKEY), D_MODEL ** -0.5),
        'peer_keys': nrm((L, PEER_HEADS, 2, PEER_NKEYS, PEER_DKEY // 2), (PEER_DKEY // 2) ** -0.5),
        'peer_u': nrm((L, PEER_EXPERTS, D_MODEL), D_MODEL ** -0.5),
        'peer_v': nrm((L, PEER_EXPERTS, D_MODEL), PEER_HEADS ** -0.5),
        'final_g': 1.0 + nrm((D_MODEL,), 0.02),
        'w_ada_f': nrm((D_MODEL, 2 * D_MODEL), 0.5 * D_MODEL ** -0.5),
        'b_ada_f': nrm((2 * D_MODEL,), 0.01),
    }

def reference(x_prompt, x_sample, c_prompt, c_sample, state_shift, state_wkv, state_conv, state_ssm,
              w_ada, b_ada, norm1_g, w_in, rw_mu, rw_w0, rw_w2, rw_a0, rw_a2, rw_g2, rw_k_k, rw_k_a, rw_r_k,
              rw_ln_w, rw_ln_b, ssm_conv_w, ssm_conv_b, ssm_dt_bias, ssm_A_log, ssm_D, ssm_norm_w,
              w_pa, w_pb, w_out, norm2_g, peer_wq, peer_keys, peer_u, peer_v, final_g, w_ada_f, b_ada_f):
    params = {
        'w_ada': w_ada, 'b_ada': b_ada, 'norm1_g': norm1_g, 'w_in': w_in,
        'rw_mu': rw_mu, 'rw_w0': rw_w0, 'rw_w2': rw_w2, 'rw_a0': rw_a0, 'rw_a2': rw_a2, 'rw_g2': rw_g2,
        'rw_k_k': rw_k_k, 'rw_k_a': rw_k_a, 'rw_r_k': rw_r_k, 'rw_ln_w': rw_ln_w, 'rw_ln_b': rw_ln_b,
        'ssm_conv_w': ssm_conv_w, 'ssm_conv_b': ssm_conv_b, 'ssm_dt_bias': ssm_dt_bias,
        'ssm_A_log': ssm_A_log, 'ssm_D': ssm_D, 'ssm_norm_w': ssm_norm_w,
        'w_pa': w_pa, 'w_pb': w_pb, 'w_out': w_out, 'norm2_g': norm2_g,
        'peer_wq': peer_wq, 'peer_keys': peer_keys, 'peer_u': peer_u, 'peer_v': peer_v,
    }
    Bp = x_prompt.shape[0]
    dt = x_prompt.dtype
    z_shift = jnp.zeros((DEPTH, Bp, D_MODEL), dt)
    z_wkv = jnp.zeros((DEPTH, Bp, RW_HEADS, RW_HEAD, RW_HEAD), dt)
    z_conv = jnp.zeros((DEPTH, Bp, SSM_CONV - 1, SSM_CONV_DIM), dt)
    z_ssm = jnp.zeros((DEPTH, Bp, SSM_HEADS, SSM_HEAD, SSM_STATE), dt)
    y_prompt, p_shift, p_wkv, p_conv, p_ssm = _trunk(x_prompt, c_prompt, z_shift, z_wkv, z_conv, z_ssm,
                                                     params, final_g, w_ada_f, b_ada_f)
    y_sample, s_shift, s_wkv, s_conv, s_ssm = _trunk(x_sample, c_sample, state_shift, state_wkv, state_conv,
                                                     state_ssm, params, final_g, w_ada_f, b_ada_f)
    return (y_prompt, y_sample, p_shift, p_wkv, p_conv, p_ssm, s_shift, s_wkv, s_conv, s_ssm)


_drawn_inputs = setup_inputs


def setup_inputs(seed=0):
    import zlib

    import numpy as np

    out = dict(_drawn_inputs(seed))
    spreads = {}
    factors = {'rw_ln_w': 8.0,
     'rw_ln_b': 8.0,
     'ssm_conv_b': 3.635,
     'ssm_D': 5.41,
     'ssm_norm_w': 8.0,
     'norm2_g': 7.326,
     'final_g': 2.765,
     'b_ada_f': 4.267}
    for name, (base, spread) in spreads.items():
        noise = np.random.default_rng([zlib.crc32(name.encode()), seed]).standard_normal(out[name].shape)
        drawn = base * np.exp(spread * noise) if base else spread * noise
        out[name] = jnp.asarray(drawn.astype(out[name].dtype))
    for name, factor in factors.items():
        out[name] = (out[name] * factor).astype(out[name].dtype)
    return out
```

```python
from contextlib import ExitStack

import numpy as np
import concourse.bass as bass
from concourse import mybir

F32 = mybir.dt.float32
I32 = mybir.dt.int32
U32 = mybir.dt.uint32
ALU = mybir.AluOpType
ACT = mybir.ActivationFunctionType
AX = mybir.AxisListType

P = 128
D = 1024
KC = D // P
SEQ = 1024
NSEQ, DSEQ = 8, 8
T = SEQ + NSEQ * DSEQ
TX = 1 + SEQ + NSEQ * (DSEQ + 1)
NCOND = 1 + NSEQ
RH, RD = 8, 64
RDIM = RH * RD
NPAIR = RDIM // P
SH, SD, SG, SN = 16, 64, 2, 128
NXBC = 12
CONVK = 4
EXP_NEG_HALF = float(np.exp(-0.5))
RW_TILES = 14
PROJ_TILES = 50
Z0, XBC0, GATE0, DT0 = 14, 22, 34, 50
CL = 64
NCH = SEQ // CL
SL = 128
NSC = SEQ // SL
LEVELS = 6
PH, NK, TOPK = 8, 128, 16
NORM_EPS = 1e-6
LN_EPS = 64e-5
LN_SCALE = 2.0 ** 30

PCOLS = {}
_at = 0
for _name, _n in (("b_ada", 64), ("norm1_g", 8), ("norm2_g", 8), ("final_g", 8), ("mu_lora", 2),
                  ("conv_w", 48), ("conv_b", 12), ("ssm_norm_w", 8), ("ln_w", 4), ("ln_b", 4)):
    PCOLS[_name] = slice(_at, _at + _n)
    _at += _n
NPAR = _at
RWP_MU, RWP_W0, RWP_A0, RWP_KK, RWP_KA, RWP_RK = 0, 3, 4, 5, 6, 7
SH1, SC1, GT1, SH2, SC2, GT2, SHF, SCF = (8 * i for i in range(8))
EXT_CHUNKS = ((0, 512), (512, 1024), (1024, TX))
TOK_CHUNKS = ((0, 364), (364, 728), (728, T))
TOK_CHUNKS_BANKED = ((0, 512), (512, 1024), (1024, T))


class Progress:

    def __init__(self, sem, *steps):
        self.sem, self.steps, self.n = sem, list(steps), len(steps)
        assert len(set(steps)) == len(steps), steps
        self.next = 0

    def inc(self, step):
        assert self.steps[self.next % self.n] == step, (self.steps[self.next % self.n], step)
        self.next += 1
        return self.sem, 1

    def done(self, step, rounds=0):
        return rounds * self.n + self.steps.index(step) + 1

    def credit(self, eng):
        eng.sem_inc(self.sem, self.n)

    def now(self, step, r):
        return r * self.n + (self.n + self.steps.index(step) + 1)

    def before(self, step, r):
        return r * self.n + (self.steps.index(step) + 1)

    def back(self, n, m, r):
        return self.now(self.steps[n - m], r) if n >= m else self.before(self.steps[n - m], r)


def bc(ap, shape):
    return ap.broadcast_to(shape)


def flat(ap):
    return ap.rearrange("p a b -> p (a b)")


class Core:

    def __init__(self, nc, ctx, io):
        self.nc, self.ctx, self.io, self.sems = nc, ctx, io, []

    def sem(self, name):
        self.sems.append(self.nc.alloc_semaphore(name=name))
        return self.sems[-1]

    def recycle_semaphores(self):
        self.nc.all_engine_barrier()
        self.nc.clear_and_free_semaphores(self.sems)
        self.nc.all_engine_barrier()
        self.sems = []

    def lasting(self, name, shape, dt=F32):
        return self.ctx.enter_context(self.nc.sbuf_tensor(name, shape, dt))


def phase_ada(k):
    nc, io = k.nc, k.io
    with ExitStack() as ctx:
        sb = lambda n, s, dt=F32: ctx.enter_context(nc.sbuf_tensor(n, s, dt))
        cT = sb("cT", [P, KC, NCOND])
        ce = sb("ce", [P, KC, NCOND])
        w = [sb(f"ada_w{i}", [P, KC, 512]) for i in range(3)]
        ps = [ctx.enter_context(nc.psum_tensor(f"ada_ps{i}", [P, 512], F32)) for i in range(2)]
        s_c = k.sem("cond_loaded")
        s_par = k.sem("params_loaded")
        s_w = [k.sem(f"ada_w{i}_loaded") for i in range(3)]
        s_exp = k.sem("cond_exp_done")
        s_silu = k.sem("cond_silu_step")
        s_mm = k.sem("ada_matmul_done")
        s_mod = k.sem("ada_mod_done")
        s_const = k.sem("const_step")
        G = 16

        with nc.Block() as block:
            @block.sync
            def _(sp):
                sp.dma_start(cT[:, :, :], io["cT"]).then_inc(s_c, 16)
                sp.dma_start(k.par[:, :], io["params"]).then_inc(s_par, 16)
                for g in range(G):
                    if g >= 3:
                        sp.wait_ge(s_mm, g - 2)
                    sp.dma_start(w[g % 3][:, :, :], io["w_ada"][g]).then_inc(s_w[g % 3], 16)

            @block.scalar
            def _(act):
                act.wait_ge(s_c, 16)
                nc.scalar.activation(ce[:, :, :], cT[:, :, :], ACT.Exp, scale=-1.0).then_inc(s_exp, 1)

            @block.gpsimd
            def _(pool):
                nc.gpsimd.memset(k.ident[:, :], 0.0).then_inc(s_const, 1)
                nc.gpsimd.memset(k.ones[:, :], 1.0).then_inc(s_const, 1)
                nc.gpsimd.memset(k.pairones[:, :], 0.0).then_inc(s_const, 1)
                nc.gpsimd.memset(k.const[:, 0:1], NORM_EPS).then_inc(s_const, 1)
                nc.gpsimd.memset(k.const[:, 1:2], LN_EPS).then_inc(s_const, 1)
                nc.gpsimd.memset(k.const[:, 2:3], 1.0).then_inc(s_const, 1)
                pool.wait_ge(s_const, 6)
                nc.gpsimd.affine_select(out=k.ident[:, :], in_=k.ident[:, :], compare_op=ALU.not_equal, fill=1.0,
                                        base=0, pattern=[[-1, P]], channel_multiplier=1).then_inc(s_const, 1)
                pool.wait_ge(s_const, 7)
                nc.gpsimd.memset(k.pairones[0:64, 0:64], 1.0).then_inc(s_const, 1)
                pool.wait_ge(s_const, 8)
                nc.gpsimd.memset(k.pairones[64:128, 64:128], 1.0).then_inc(s_const, 1)

            @block.tensor
            def _(pe):
                pe.wait_ge(s_silu, 3)
                for g in range(G):
                    pe.wait_ge(s_w[g % 3], 16 * (g // 3 + 1))
                    if g >= 2:
                        pe.wait_ge(s_mod, g - 1)
                    for m in range(4):
                        for kc in range(KC):
                            mm = nc.tensor.matmul(ps[g % 2][:, m * NCOND:(m + 1) * NCOND],
                                                  w[g % 3][:, kc, m * P:(m + 1) * P], cT[:, kc, :],
                                                  start=kc == 0, stop=kc == KC - 1)
                    mm.then_inc(s_mm, 1)

            @block.vector
            def _(dve):
                dve.wait_ge(s_exp, 1)
                nc.vector.tensor_scalar(ce[:, :, :], ce[:, :, :], 1.0, None, ALU.add).then_inc(s_silu, 1)
                dve.wait_ge(s_silu, 1)
                nc.vector.reciprocal(ce[:, :, :], ce[:, :, :]).then_inc(s_silu, 1)
                dve.wait_ge(s_silu, 2)
                nc.vector.tensor_tensor(cT[:, :, :], cT[:, :, :], ce[:, :, :], ALU.mult).then_inc(s_silu, 1)
                dve.wait_ge(s_par, 16)
                for g in range(G):
                    dve.wait_ge(s_mm, g + 1)
                    nc.vector.tensor_tensor(k.mod[:, 4 * g:4 * g + 4, :],
                                            ps[g % 2][:, 0:4 * NCOND].rearrange("p (m c) -> p m c", m=4),
                                            bc(k.par[:, 4 * g:4 * g + 4].unsqueeze(2), [P, 4, NCOND]),
                                            ALU.add).then_inc(s_mod, 1)
                dve.wait_ge(s_mod, G)
                for n, (at, g) in enumerate(((SC1, "norm1_g"), (SC2, "norm2_g"), (SCF, "final_g"))):
                    nc.vector.scalar_tensor_tensor(out=k.mod[:, at:at + 8, :], in0=k.mod[:, at:at + 8, :], scalar=1.0,
                                                   in1=bc(k.par[:, PCOLS[g]].unsqueeze(2), [P, 8, NCOND]),
                                                   op0=ALU.add, op1=ALU.mult).then_inc(s_mod, 1)


def rmsnorm_mod(k, tag, x, out_prompt, out_sample, scale_at, shift_at, load=None, store=None):
    nc = k.nc
    with ExitStack() as ctx:
        sb = lambda n, s, dt=F32: ctx.enter_context(nc.sbuf_tensor(f"{tag}_{n}", s, dt))
        sq = sb("sq", [P, 2, T])
        rstd = sb("rstd", [P, T])
        xr = sb("xr", [P, 2, T])
        ps = ctx.enter_context(nc.psum_tensor(f"{tag}_ps", [P, 3, 512], F32))
        pf = flat(ps[:, :, :])
        s_x = k.sem(f"{tag}_x_loaded")
        s_sq = k.sem(f"{tag}_square_done")
        s_sum = k.sem(f"{tag}_sum_step")
        s_r = k.sem(f"{tag}_rstd_step")
        s_o = k.sem(f"{tag}_out_step")
        s_st = k.sem(f"{tag}_stored")
        need = [0]
        with nc.Block() as block:
            @block.sync
            def _(sp):
                if load:
                    need[0] = load(sp, s_x)
                if store:
                    sp.wait_ge(s_o, 4 * KC)
                    n = store(sp, s_st)
                    sp.wait_ge(s_st, n)

            @block.scalar
            def _(act):
                if need[0]:
                    act.wait_ge(s_x, need[0])
                for kc in range(KC):
                    if kc >= 2:
                        act.wait_ge(s_sum, kc - 1)
                    nc.scalar.activation(sq[:, kc % 2, :], x[:, kc, :], ACT.Square).then_inc(s_sq, 1)
                act.wait_ge(s_sum, KC)
                nc.scalar.activation(rstd[:, :], pf[:, 0:T], ACT.Ln, scale=1.0 / D, bias=k.const[:, 0:1]).then_inc(s_r, 1)
                act.wait_ge(s_r, 1)
                nc.scalar.activation(rstd[:, :], rstd[:, :], ACT.Exp, scale=-0.5).then_inc(s_r, 1)

            @block.tensor
            def _(pe):
                for kc in range(KC):
                    pe.wait_ge(s_sq, kc + 1)
                    for a, b in ((0, 512), (512, 1024), (1024, T)):
                        mm = nc.tensor.matmul(pf[:, a:b], k.ones[:, :], sq[:, kc % 2, a:b], start=kc == 0, stop=kc == KC - 1)
                    mm.then_inc(s_sum, 1)

            @block.vector
            def _(dve):
                if need[0]:
                    dve.wait_ge(s_x, need[0])
                dve.wait_ge(s_r, 2)
                n = 0
                for kc in range(KC):
                    if kc >= 2:
                        dve.wait_ge(s_o, 4 * (kc - 1))
                    nc.vector.tensor_tensor(xr[:, kc % 2, :], x[:, kc, :], rstd[:, :], ALU.mult).then_inc(s_o, 1)
                    n += 1
                    dve.wait_ge(s_o, n)
                    a, b = k.mod[:, scale_at + kc, :], k.mod[:, shift_at + kc, :]
                    nc.vector.tensor_scalar(out_prompt(kc), xr[:, kc % 2, 0:SEQ], a[:, 0:1], b[:, 0:1],
                                            ALU.mult, ALU.add).then_inc(s_o, 1)
                    smp = xr[:, kc % 2, SEQ:T].rearrange("p (s t) -> p s t", s=NSEQ)
                    nc.vector.tensor_tensor(smp, smp, bc(a[:, 1:NCOND].unsqueeze(2), [P, NSEQ, DSEQ]), ALU.mult).then_inc(s_o, 1)
                    n += 2
                    dve.wait_ge(s_o, n)
                    nc.vector.tensor_tensor(out_sample(kc), smp, bc(b[:, 1:NCOND].unsqueeze(2), [P, NSEQ, DSEQ]), ALU.add).then_inc(s_o, 1)
                    n += 1


def phase_norm1(k, xe):
    nc, io = k.nc, k.io
    with nc.sbuf_tensor("x_in", [P, KC, T], F32) as x:
        smp = lambda kc: xe[:, kc, 1 + SEQ:TX].rearrange("p (s t) -> p s t", s=NSEQ)
        s_z = k.sem("xe_pad_done")
        s_sh = k.sem("xe_shift_loaded")

        def load(sp, sem):
            sp.dma_start(x[:, :, :], io["xT"]).then_inc(sem, 16)
            sp.dma_start(k.shift_sb[:, :, :], io["shiftT"]).then_inc(s_sh, 16)
            sp.wait_ge(s_sh, 16)
            return 16

        def store(sp, sem):
            with nc.allow_non_contiguous_dma(reason="last rows"):
                sp.dma_start(io["shift_out"][:, :, 0:1], xe[:, :, SEQ:SEQ + 1]).then_inc(sem, 16)
                for kc in range(KC):
                    sp.dma_start(io["shift_out"][:, kc, 1:NCOND], smp(kc)[:, :, DSEQ]).then_inc(sem, 16)
            return 16 * (KC + 1)

        rmsnorm_mod(k, "norm1", x, lambda kc: xe[:, kc, 1:1 + SEQ], lambda kc: smp(kc)[:, :, 1:1 + DSEQ],
                    SC1, SH1, load, store)
        with nc.Block() as block:
            @block.gpsimd
            def _(pool):
                nc.gpsimd.memset(xe[:, :, 0:1], 0.0).then_inc(s_z, 1)
                for kc in range(KC):
                    nc.gpsimd.tensor_copy(smp(kc)[:, :, 0], k.shift_sb[:, kc, :]).then_inc(s_z, 1)


def phase_proj(k, xe):
    nc, io = k.nc, k.io
    with ExitStack() as ctx:
        sb = lambda n, s, dt=F32: ctx.enter_context(nc.sbuf_tensor(n, s, dt))
        NW = 4
        w = [sb(f"in_w{i}", [P, KC, P]) for i in range(NW)]
        wdt = sb("in_wdt", [P, KC, SH])
        out = [sb(f"in_out{i}", [P, TX]) for i in range(2)]
        ps = [ctx.enter_context(nc.psum_tensor(f"in_ps{i}", [P, 3, 512], F32)) for i in range(2)]
        s_w = [k.sem(f"in_w{i}_loaded") for i in range(NW)]
        s_wdt = k.sem("in_wdt_loaded")
        s_mm = k.sem("in_matmul_done")
        s_ev = [k.sem(f"in_evac{i}_done") for i in range(2)]
        s_st = [k.sem(f"in_stored{i}") for i in range(2)]
        R = PROJ_TILES // NW
        REST = PROJ_TILES - R * NW

        with nc.Block() as block:
            @block.sync
            def _(sp):
                sp.dma_start(wdt[:, :, :], io["w_dt"]).then_inc(s_wdt, 16)
                for j in range(NW):
                    sp.dma_start(w[j][:, :, :], io["w_in"][j]).then_inc(s_w[j], 16)
                with sp.Fori(0, R - 1) as r:
                    for j in range(NW):
                        sp.wait_ge(s_mm, r * NW + j + 1)
                        sp.dma_start(w[j][:, :, :], io["w_in"][r * NW + NW + j]).then_inc(s_w[j], 16)
                for j in range(REST):
                    sp.wait_ge(s_mm, (R - 1) * NW + j + 1)
                    sp.dma_start(w[j][:, :, :], io["w_in"][R * NW + j]).then_inc(s_w[j], 16)

            def tile(pe, wt, cols, parity):
                pf = flat(ps[parity][:, :, :])
                for kc in range(KC):
                    for a, b in EXT_CHUNKS:
                        mm = nc.tensor.matmul(pf[0:cols, a:b], wt[:, kc, :], xe[:, kc, a:b], start=kc == 0, stop=kc == KC - 1)
                mm.then_inc(s_mm, 1)

            @block.tensor
            def _(pe):
                with pe.Fori(0, R) as r:
                    for j in range(NW):
                        pe.wait_ge(s_w[j], 16 * r + 16)
                        if j >= 2:
                            pe.wait_ge(s_ev[j % 2], 2 * r + 1)
                        else:
                            pe.wait_ge(s_ev[j % 2], 2 * r)
                        tile(pe, w[j], P, j % 2)
                for j in range(REST):
                    pe.wait_ge(s_w[j], 16 * R + 16)
                    pe.wait_ge(s_ev[j % 2], 2 * R + j // 2)
                    tile(pe, w[j], P, j % 2)
                pe.wait_ge(s_wdt, 16)
                pe.wait_ge(s_ev[0], PROJ_TILES // 2)
                tile(pe, wdt, SH, 0)

            def evac(eng, parity, copy):
                pf = flat(ps[parity][:, :, :])
                n = PROJ_TILES // 2
                with eng.Fori(0, n) as i:
                    eng.wait_ge(s_mm, 2 * i + parity + 1)
                    eng.wait_ge(s_st[parity], 16 * i)
                    copy(out[parity][:, :], pf[:, 0:TX]).then_inc(s_ev[parity], 1)
                    eng.wait_ge(s_ev[parity], i + 1)
                    eng.dma_start(io["proj"][2 * i + parity], out[parity][:, :]).then_inc(s_st[parity], 16)
                eng.wait_ge(s_st[parity], 16 * n)

            @block.scalar
            def _(act):
                evac(act, 0, lambda o, i: nc.scalar.activation(o, i, ACT.Copy))
                act.wait_ge(s_mm, PROJ_TILES + 1)
                nc.scalar.activation(out[0][0:SH, :], flat(ps[0][:, :, :])[0:SH, 0:TX], ACT.Copy).then_inc(s_ev[0], 1)
                act.wait_ge(s_ev[0], PROJ_TILES // 2 + 1)
                act.dma_start(io["proj"][DT0, 0:SH, :], out[0][0:SH, :]).then_inc(s_st[0], 16)
                act.wait_ge(s_st[0], 16 * (PROJ_TILES // 2 + 1))

            @block.vector
            def _(dve):
                pf = flat(ps[1][:, :, :])
                with dve.Fori(0, PROJ_TILES // 2) as i:
                    dve.wait_ge(s_mm, 2 * i + 2)
                    dve.wait_ge(s_st[1], 16 * i)
                    nc.vector.tensor_copy(out[1][:, :], pf[:, 0:TX]).then_inc(s_ev[1], 1)

            @block.gpsimd
            def _(pool):
                with pool.Fori(0, PROJ_TILES // 2) as i:
                    pool.wait_ge(s_ev[1], i + 1)
                    pool.dma_start(io["proj"][2 * i + 1], out[1][:, :]).then_inc(s_st[1], 16)
                pool.wait_ge(s_st[1], 16 * (PROJ_TILES // 2))


def predecessor_views(ext):
    smp = ext[:, 1 + SEQ:TX].rearrange("p (s t) -> p s t", s=NSEQ)
    return (ext[:, 0:SEQ], ext[:, 1:1 + SEQ]), (smp[:, :, 0:DSEQ], smp[:, :, 1:1 + DSEQ])


def token_views(tok):
    return tok[:, 0:SEQ], tok[:, SEQ:T].rearrange("p (s t) -> p s t", s=NSEQ)


def token_shift(dve, out, ext, mu, sub_done, wait_sub):
    for o, e in zip(out, ext):
        for ov, (prev, cur) in zip(token_views(o), predecessor_views(e)):
            last = dve.tensor_tensor(ov, prev, cur, ALU.subtract)
    last.then_inc(*sub_done)
    wait_sub()
    for o, e, m in zip(out, ext, mu):
        for ov, (_, cur) in zip(token_views(o), predecessor_views(e)):
            last = dve.scalar_tensor_tensor(out=ov, in0=ov, scalar=m, in1=cur, op0=ALU.mult, op1=ALU.add)
    return last


def phase_rw_pre(k):
    nc, io = k.nc, k.io
    with ExitStack() as ctx:
        sb = lambda n, s, dt=F32: ctx.enter_context(nc.sbuf_tensor(f"rwp_{n}", s, dt))
        lora_x = sb("lora_x", [P, 2, TX])
        lora = sb("lora", [P, 2, T])
        x = sb("x", [P, 3, TX])
        q = sb("q", [P, 3, T])
        rp = sb("rp", [P, 8])
        lw = sb("lw", [P, 2, P])
        keep = sb("keep", [P, T])
        sw, a, lam, linv, lprev, cs = (sb(n, [P, T]) for n in ("sw", "a", "lam", "linv", "lprev", "cs"))
        kk, rn, t1, kp, gate, bonus = (sb(n, [P, T]) for n in ("kk", "rn", "t1", "kp", "gate", "bonus"))
        o = sb("o", [P, 4, T])
        ps = [ctx.enter_context(nc.psum_tensor(f"rwp_ps{i}", [P, 3, 512], F32)) for i in range(2)]
        pa, pb = (flat(p_[:, :, :]) for p_ in ps)
        s_lx = k.sem("rwp_lora_loaded")
        s_x = k.sem("rwp_x_loaded")
        s_w = k.sem("rwp_weights_loaded")
        s_st = k.sem("rwp_stored")
        s_keep = k.sem("rwp_keep_step")
        s_lora = k.sem("rwp_lora_step")
        PE = Progress(k.sem("rwp_pe"), "zw", "za", "gate", "norm", "bonus")
        AC = Progress(k.sem("rwp_act"), "sw", "a", "gate", "lam", "linv", "lprev", "ln", "rn")
        DV = Progress(k.sem("rwp_dve"), "sub", "mix", "kkr", "sq", "cs", "csx", "norm_floor", "am", "kp", "kk",
                      "b", "rk", "outs", "bonus")
        NST = 7
        c = EXP_NEG_HALF

        with nc.Block() as block:
            @block.sync
            def _(sp):
                for i in range(2):
                    sp.dma_start(lora_x[:, i, :], io["proj"][12 + i]).then_inc(s_lx, 16)

                def load(r):
                    for i in range(3):
                        sp.dma_start(x[:, i, :], io["proj"][4 * i + r]).then_inc(s_x, 16)
                    sp.dma_start(rp[:, :], io["rw_params"][r]).then_inc(s_w, 16)
                    sp.dma_start(lw[:, :, :], io["lora_w"][r]).then_inc(s_w, 16)

                with sp.Fori(0, NPAIR) as r:
                    sp.wait_ge(DV.sem, DV.before("bonus", r))
                    load(r)
                    sp.wait_ge(DV.sem, DV.now("outs", r))
                    for n in range(4):
                        sp.dma_start(io["rwc"][:, :, n, r, :].rearrange("c p t -> p c t"),
                                     o[:, n, :].rearrange("p (c t) -> p c t", t=CL)).then_inc(s_st, 16)
                    sp.dma_start(io["rwc"][:, :, 4, r, :].rearrange("c p t -> p c t"),
                                 q[:, 2, :].rearrange("p (c t) -> p c t", t=CL)).then_inc(s_st, 16)
                    sp.dma_start(io["rw_gate"][r], gate[:, :]).then_inc(s_st, 16)
                    sp.wait_ge(DV.sem, DV.now("bonus", r))
                    sp.dma_start(io["rw_bonus"][r], bonus[:, :]).then_inc(s_st, 16)
                sp.wait_ge(s_st, 16 * NST * NPAIR)

            @block.gpsimd
            def _(pool):
                nc.gpsimd.memset(keep[:, :], 1.0).then_inc(s_keep, 1)
                pool.wait_ge(s_keep, 1)
                nc.gpsimd.memset(keep[:, 0:SEQ].rearrange("p (c t) -> p c t", t=CL)[:, :, 0:1], 0.0).then_inc(s_keep, 1)
                nc.gpsimd.memset(keep[:, SEQ:T].rearrange("p (c t) -> p c t", t=DSEQ)[:, :, 0:1], 0.0).then_inc(s_keep, 1)

            @block.tensor
            def _(pe):
                PE.credit(pe)
                pe.wait_ge(s_lora, 4)

                def product(out, lhsT, rhs, step):
                    for a0, b0 in TOK_CHUNKS_BANKED:
                        mm = nc.tensor.matmul(out[:, a0:b0], lhsT, rhs[:, a0:b0], start=True, stop=True)
                    mm.then_inc(*PE.inc(step))

                with pe.Fori(0, NPAIR) as r:
                    pe.wait_ge(s_w, 32 * r + 32)
                    pe.wait_ge(DV.sem, DV.before("bonus", r))
                    product(pa, lw[0:64, 0, :], lora[0:64, 0, :], "zw")
                    product(pb, lw[64:128, 0, :], lora[64:128, 0, :], "za")
                    pe.wait_ge(AC.sem, AC.now("sw", r))
                    product(pa, lw[:, 1, :], lora[:, 1, :], "gate")
                    pe.wait_ge(AC.sem, AC.now("a", r))
                    pe.wait_ge(DV.sem, DV.now("sq", r))
                    product(pb, k.pairones[:, :], rn, "norm")
                    pe.wait_ge(AC.sem, AC.now("gate", r))
                    pe.wait_ge(DV.sem, DV.now("rk", r))
                    product(pa, k.pairones[:, :], t1, "bonus")

            @block.scalar
            def _(act):
                AC.credit(act)
                act.wait_ge(s_lora, 2)
                nc.scalar.activation(lora[0:64, 0, :], lora[0:64, 0, :], ACT.Tanh).then_inc(s_lora, 1)
                nc.scalar.activation(lora[:, 1, :], lora[:, 1, :], ACT.Sigmoid).then_inc(s_lora, 1)
                with act.Fori(0, NPAIR) as r:
                    act.wait_ge(DV.sem, DV.before("bonus", r))
                    act.wait_ge(s_w, 32 * r + 32)
                    act.wait_ge(PE.sem, PE.now("zw", r))
                    nc.scalar.activation(sw[:, :], pa[:, 0:T], ACT.Sigmoid, bias=rp[:, RWP_W0:RWP_W0 + 1]).then_inc(*AC.inc("sw"))
                    act.wait_ge(PE.sem, PE.now("za", r))
                    nc.scalar.activation(a[:, :], pb[:, 0:T], ACT.Sigmoid, bias=rp[:, RWP_A0:RWP_A0 + 1]).then_inc(*AC.inc("a"))
                    act.wait_ge(PE.sem, PE.now("gate", r))
                    act.wait_ge(s_st, 16 * NST * r)
                    nc.scalar.activation(gate[:, :], pa[:, 0:T], ACT.Copy).then_inc(*AC.inc("gate"))
                    act.wait_ge(DV.sem, DV.now("cs", r))
                    nc.scalar.activation(lam[:, :], cs[:, :], ACT.Exp, scale=-c).then_inc(*AC.inc("lam"))
                    nc.scalar.activation(linv[:, :], cs[:, :], ACT.Exp, scale=c).then_inc(*AC.inc("linv"))
                    act.wait_ge(DV.sem, DV.now("csx", r))
                    nc.scalar.activation(lprev[:, :], lprev[:, :], ACT.Exp, scale=-c).then_inc(*AC.inc("lprev"))
                    act.wait_ge(DV.sem, DV.now("norm_floor", r))
                    nc.scalar.activation(rn[:, :], rn[:, :], ACT.Ln).then_inc(*AC.inc("ln"))
                    act.wait_ge(AC.sem, AC.now("ln", r))
                    nc.scalar.activation(rn[:, :], rn[:, :], ACT.Exp, scale=-0.5).then_inc(*AC.inc("rn"))

            @block.vector
            def _(dve):
                v = nc.vector
                DV.credit(dve)
                dve.wait_ge(s_lx, 32)
                mu = k.par[:, PCOLS["mu_lora"]]
                token_shift(v, [lora[:, i, :] for i in range(2)], [lora_x[:, i, :] for i in range(2)],
                            [mu[:, i:i + 1] for i in range(2)], (s_lora, 1),
                            lambda: dve.wait_ge(s_lora, 1)).then_inc(s_lora, 1)
                dve.wait_ge(s_keep, 3)
                with dve.Fori(0, NPAIR) as r:
                    now = lambda s: dve.wait_ge(DV.sem, DV.now(s, r))
                    col = lambda n: rp[:, n:n + 1]
                    dve.wait_ge(s_x, 48 * r + 48)
                    dve.wait_ge(s_w, 32 * r + 32)
                    dve.wait_ge(s_st, 16 * NST * r)
                    token_shift(v, [q[:, i, :] for i in range(3)], [x[:, i, :] for i in range(3)],
                                [col(RWP_MU + i) for i in range(3)], DV.inc("sub"),
                                lambda: now("sub")).then_inc(*DV.inc("mix"))
                    now("mix")
                    v.tensor_scalar(kk[:, :], q[:, 1, :], col(RWP_KK), None, ALU.mult).then_inc(*DV.inc("kkr"))
                    now("kkr")
                    v.tensor_tensor(rn[:, :], kk[:, :], kk[:, :], ALU.mult).then_inc(*DV.inc("sq"))
                    dve.wait_ge(AC.sem, AC.now("sw", r))
                    v.tensor_tensor_scan(cs[:, :], keep[:, :], sw[:, :], 0.0, ALU.mult, ALU.add).then_inc(*DV.inc("cs"))
                    now("cs")
                    v.tensor_tensor(lprev[:, :], cs[:, :], sw[:, :], ALU.subtract).then_inc(*DV.inc("csx"))
                    dve.wait_ge(PE.sem, PE.now("norm", r))
                    v.tensor_scalar(rn[:, :], pb[:, 0:T], 1e-24, LN_SCALE, ALU.max, ALU.mult).then_inc(*DV.inc("norm_floor"))
                    dve.wait_ge(AC.sem, AC.now("a", r))
                    v.scalar_tensor_tensor(out=t1[:, :], in0=a[:, :], scalar=-1.0, in1=q[:, 1, :],
                                           op0=ALU.add, op1=ALU.mult).then_inc(*DV.inc("am"))
                    now("am")
                    v.scalar_tensor_tensor(out=kp[:, :], in0=t1[:, :], scalar=col(RWP_KA), in1=q[:, 1, :],
                                           op0=ALU.mult, op1=ALU.add).then_inc(*DV.inc("kp"))
                    dve.wait_ge(AC.sem, AC.now("rn", r))
                    v.scalar_tensor_tensor(out=kk[:, :], in0=kk[:, :], scalar=LN_SCALE ** 0.5, in1=rn[:, :],
                                           op0=ALU.mult, op1=ALU.mult).then_inc(*DV.inc("kk"))
                    now("kk")
                    v.tensor_tensor(rn[:, :], kk[:, :], a[:, :], ALU.mult).then_inc(*DV.inc("b"))
                    v.scalar_tensor_tensor(out=t1[:, :], in0=q[:, 0, :], scalar=col(RWP_RK), in1=kp[:, :],
                                           op0=ALU.mult, op1=ALU.mult).then_inc(*DV.inc("rk"))
                    dve.wait_ge(AC.sem, AC.now("lprev", r))
                    now("b")
                    v.tensor_tensor(o[:, 0, :], kk[:, :], lprev[:, :], ALU.mult)
                    v.tensor_tensor(o[:, 1, :], q[:, 0, :], lam[:, :], ALU.mult)
                    v.tensor_tensor(o[:, 2, :], rn[:, :], linv[:, :], ALU.mult)
                    v.tensor_tensor(o[:, 3, :], kp[:, :], linv[:, :], ALU.mult)
                    v.tensor_copy(k.lam_end[:, r, 0:NCH], lam[:, CL - 1:SEQ:CL])
                    v.tensor_copy(k.lam_end[:, r, NCH:NCH + NSEQ], lam[:, SEQ + DSEQ - 1:T:DSEQ]).then_inc(*DV.inc("outs"))
                    dve.wait_ge(PE.sem, PE.now("bonus", r))
                    v.tensor_tensor(bonus[:, :], pa[:, 0:T], q[:, 2, :], ALU.mult).then_inc(*DV.inc("bonus"))


def halves():
    return slice(0, 64), slice(64, 128)


def phase_masks(k):
    nc = k.nc
    s = k.sem("mask_step")
    with nc.Block() as block:
        @block.gpsimd
        def _(pool):
            g = nc.gpsimd
            n = [0]

            def stage(ops):
                for op in ops:
                    op().then_inc(s, 1)
                    n[0] += 1
                    pool.wait_ge(s, n[0])

            def keep(view, pattern, base, cm):
                return lambda: g.affine_select(out=view, in_=view, compare_op=ALU.is_ge, fill=0.0, base=base,
                                               pattern=pattern, channel_multiplier=cm)

            stage([lambda: g.memset(k.mt_mask[:, :, :, :], 1.0), lambda: g.memset(k.lv_mask[:, :, :, :], 0.0),
                   lambda: g.memset(k.seq_cols[:, :, :], 1.0), lambda: g.memset(k.seq_rows[:, :], 1.0)])
            for rows in halves():
                for kind in range(2):
                    for b in range(4):
                        m = k.mt_mask[rows, kind, b, :]
                        stage([keep(m, [[1, CL]], -1 if b % 2 == 0 else 0, -1)])
                blk = k.mt_mask[rows, 1, :, :].rearrange("p b (s t) -> p b s t", s=NSEQ)
                for b in range(4):
                    stage([keep(blk[:, b], [[-DSEQ, NSEQ], [0, DSEQ]], 0, 1)])
                    stage([keep(blk[:, b], [[DSEQ, NSEQ], [0, DSEQ]], DSEQ - 1, -1)])
                stage([keep(k.seq_rows[rows, :], [[-DSEQ, NSEQ]], 0, 1)])
                stage([keep(k.seq_rows[rows, :], [[DSEQ, NSEQ]], DSEQ - 1, -1)])
                for lv in range(LEVELS):
                    z = 1 << lv
                    nb = CL // (2 * z)
                    xm = k.lv_mask[rows, lv, 0, :].rearrange("p (b h w) -> p b h w", h=2, w=z)[:, :, 0, :]
                    ym = k.lv_mask[rows, lv, 1, :].rearrange("p (b h w) -> p b h w", h=2, w=z)[:, :, 1, :]
                    stage([lambda: g.memset(xm, 1.0), lambda: g.memset(ym, 1.0)])
                    stage([keep(xm, [[-2 * z, nb], [0, z]], -z, 1), keep(ym, [[-2 * z, nb], [0, z]], 0, 1)])
                    stage([keep(xm, [[2 * z, nb], [0, z]], 2 * z - 1, -1), keep(ym, [[2 * z, nb], [0, z]], z - 1, -1)])
                for i in range(2):
                    stage([lambda: g.tensor_copy(k.ident2[rows, i, :], k.ident[rows, rows])])
            stage([lambda: g.memset(k.ssd_mask[:, :], 1.0), lambda: g.memset(k.ssd_mask_smp[:, :], 1.0),
                   lambda: g.memset(k.head_sel[:, :, :], 1.0)])
            stage([keep(k.ssd_mask[:, :], [[1, SL]], 0, -1), keep(k.ssd_mask_smp[:, :], [[1, CL]], 0, -1)])
            blk = k.ssd_mask_smp[:, :].rearrange("p (s t) -> p s t", s=NSEQ)
            stage([keep(blk, [[-DSEQ, NSEQ], [0, DSEQ]], 0, 1)])
            stage([keep(k.head_sel[:, :, :], [[-1, SH], [0, P]], 0, 1)])
            stage([keep(k.head_sel[:, :, :], [[1, SH], [0, P]], 0, -1)])
            stage([keep(k.seq_cols[:, :, :], [[-DSEQ, NSEQ], [1, CL]], 0, 0)])
            stage([keep(k.seq_cols[:, :, :], [[DSEQ, NSEQ], [-1, CL]], DSEQ - 1, 0)])


KA, RB, BT, KT, VV = range(5)
BANK_MT, BANK_M, BANK_TOK, BANK_P, BANK_Q, BANK_U, BANK_Y, BANK_S = 0, 2, 3, 5, 6, 7, 2, 5


def level_steps(name, levels):
    return [f"{name}{lv}" for lv in range(1, levels)]


def rw_matrix_pe(k, b, pe, in5, levels, at):
    nc, PE, AC, DV = k.nc, b.PE, b.AC, b.DV
    ps = b.ps
    heads = [(p_, rows) for p_ in range(NPAIR) for rows in halves()]
    mt = ps[:, BANK_MT:BANK_MT + 2, :].rearrange("p a (b m) -> p (a b) m", m=256)
    tok = ps[:, BANK_TOK:BANK_TOK + 2, :].rearrange("p a b -> p (a b)")[:, 0:768].rearrange("p (q a t) -> p q a t", q=3, a=4)
    four = lambda bank: ps[:, bank, 0:256].rearrange("p (a t) -> p a t", a=4)
    pq = ps[:, BANK_Q, :].rearrange("p (a i t) -> p a i t", a=4, i=2)
    for p_, rows in heads:
        for i, w in enumerate((BT, KT)):
            mm = nc.tensor.matmul(mt[rows, p_, 128 * i:128 * i + 128], in5[rows, w, p_, :], in5[rows, KA:RB + 1, p_, :],
                                  start=True, stop=True)
    mm.then_inc(*PE.inc("mt"))
    for p_, rows in heads:
        mm = nc.tensor.matmul(four(BANK_M)[rows, p_, :], in5[rows, KA, p_, :], in5[rows, BT, p_, :], start=True, stop=True)
    mm.then_inc(*PE.inc("m"))
    for q, w in enumerate((BT, KT, VV)):
        for p_, rows in heads:
            mm = nc.tensor.matmul(tok[rows, q, p_, :], in5[rows, w, p_, :], k.ident[rows, rows], start=True, stop=True)
    mm.then_inc(*PE.inc("tok"))
    for lv in range(1, levels):
        at(DV, f"xy{lv - 1}")
        for p_, rows in heads:
            mm = nc.tensor.matmul(four(BANK_P)[rows, p_, :], b.mt[rows, p_, 0:64], b.xy[rows, p_, 0, :], start=True, stop=True)
        mm.then_inc(*PE.inc(f"mx{lv}"))
        at(AC, f"mx{lv}")
        for p_, rows in heads:
            nc.tensor.matmul(pq[rows, p_, 0, :], b.xy[rows, p_, 1, :], b.mx[rows, p_, :], start=True, stop=True)
            mm = nc.tensor.matmul(pq[rows, p_, 1, :], b.mx[rows, p_, :], b.xy[rows, p_, 1, :], start=True, stop=True)
        mm.then_inc(*PE.inc(f"xmx{lv}"))


def rw_matrix_act(k, b, levels, at):
    nc, PE, AC = k.nc, b.PE, b.AC
    tok = b.ps[:, BANK_TOK:BANK_TOK + 2, :].rearrange("p a b -> p (a b)")[:, 0:768]
    at(PE, "tok")
    nc.scalar.activation(b.tok[:, :, :, :].rearrange("p q a t -> p (q a t)"), tok, ACT.Copy).then_inc(*AC.inc("tok"))
    for lv in range(1, levels):
        at(PE, f"mx{lv}")
        nc.scalar.activation(b.mx[:, :, :].rearrange("p a t -> p (a t)"), b.ps[:, BANK_P, 0:256], ACT.Copy).then_inc(*AC.inc(f"mx{lv}"))


def rw_matrix_dve(k, b, kind, levels, at):
    v, PE, DV = k.nc.vector, b.PE, b.DV
    mt = b.ps[:, BANK_MT:BANK_MT + 2, :].rearrange("p a (b m) -> p (a b) m", m=256)
    m = b.ps[:, BANK_M, 0:256].rearrange("p (a t) -> p a t", a=4)
    mask = k.mt_mask[:, kind, :, :].rearrange("p b t -> p (b t)").unsqueeze(1)
    at(PE, "mt")
    v.tensor_tensor(b.mt[:, :, :], mt, bc(mask, [P, NPAIR, 256]), ALU.mult).then_inc(*DV.inc("mt"))
    at(PE, "m")
    at(DV, "mt")
    v.tensor_tensor(b.tmp[:, :, 0, :], m, bc(k.lv_mask[:, 0, 0:1, :], [P, NPAIR, CL]), ALU.mult)
    v.tensor_tensor(b.tmp[:, :, 1, :], b.mt[:, :, 0:64], bc(k.lv_mask[:, 0, 1:2, :], [P, NPAIR, CL]), ALU.mult).then_inc(*DV.inc("t0"))
    at(DV, "t0")
    xy = b.xy[:, :, :, :].rearrange("p a i t -> p a (i t)")
    tmp = b.tmp[:, :, :, :].rearrange("p a i t -> p a (i t)")
    one = bc(k.ident2[:, :, :].rearrange("p i t -> p (i t)").unsqueeze(1), [P, NPAIR, 128])
    v.tensor_tensor(xy, one, tmp, ALU.subtract).then_inc(*DV.inc("xy0"))
    pq = b.ps[:, BANK_Q, :].rearrange("p (a m) -> p a m", a=4)
    for lv in range(1, levels):
        at(PE, f"xmx{lv}")
        lm = k.lv_mask[:, lv, :, :].rearrange("p i t -> p (i t)").unsqueeze(1)
        v.tensor_tensor(tmp, pq, bc(lm, [P, NPAIR, 128]), ALU.mult).then_inc(*DV.inc(f"t{lv}"))
        at(DV, f"t{lv}")
        v.tensor_tensor(xy, xy, tmp, ALU.subtract).then_inc(*DV.inc(f"xy{lv}"))


class RwBuffers:
    def __init__(self, k, ctx, tag, levels):
        sb = lambda n, s: ctx.enter_context(k.nc.sbuf_tensor(f"{tag}_{n}", s, F32))
        self.mt = sb("mt", [P, NPAIR, 256])
        self.xy = sb("xy", [P, NPAIR, 2, CL])
        self.mx = sb("mx", [P, NPAIR, CL])
        self.tmp = sb("tmp", [P, NPAIR, 2, CL])
        self.tok = sb("tok", [P, 3, NPAIR, CL])
        self.rhs = sb("rhs", [P, NPAIR, CL])
        self.u = sb("u", [P, NPAIR, CL])
        self.ps = ctx.enter_context(k.nc.psum_tensor(f"{tag}_ps", [P, 8, 512], F32))
        self.PE = Progress(k.sem(f"{tag}_pe"), "mt", "m", "tok",
                           *[s for lv in range(1, levels) for s in (f"mx{lv}", f"xmx{lv}")], "rhs", "u", "y", "s")
        self.AC = Progress(k.sem(f"{tag}_act"), "tok", *level_steps("mx", levels), "u", "y")
        self.DV = Progress(k.sem(f"{tag}_dve"), "mt", "t0", "xy0",
                           *[s for lv in range(1, levels) for s in (f"t{lv}", f"xy{lv}")],
                           *(["masked", "rhs", "umask"] if tag == "rws" else ["rhs"]), "s_add", "s")


def phase_rw_prompt(k):
    nc, io = k.nc, k.io
    with ExitStack() as ctx:
        b = RwBuffers(k, ctx, "rwc", LEVELS)
        PE, AC, DV = b.PE, b.AC, b.DV
        in5 = [ctx.enter_context(nc.sbuf_tensor(f"rwc_in{i}", [P, 5, NPAIR, CL], F32)) for i in range(2)]
        S = ctx.enter_context(nc.sbuf_tensor("rwc_state", [P, NPAIR, CL], F32))
        y = [ctx.enter_context(nc.sbuf_tensor(f"rwc_y{i}", [P, NPAIR, CL], F32)) for i in range(2)]
        s_in = [k.sem(f"rwc_in{i}_loaded") for i in range(2)]
        s_y = k.sem("rwc_y_stored")
        s_init = k.sem("rwc_state_zeroed")
        heads = [(p_, rows) for p_ in range(NPAIR) for rows in halves()]
        four = lambda bank: b.ps[:, bank, 0:256].rearrange("p (a t) -> p a t", a=4)

        def at_of(eng, c):
            return lambda S_, step: eng.wait_ge(S_.sem, S_.now(step, c))

        def pe_at_of(pe, c, one):
            def at(S_, step):
                pe.wait_ge(S_.sem, S_.now(step, c))
                pe.reg_alu(one, one, 1, ALU.max)
            return at

        with nc.Block() as block:
            @block.sync
            def _(sp):
                for h in range(2):
                    sp.dma_start(in5[h][:, :, :, :], io["rwc"][h]).then_inc(s_in[h], 16)
                with sp.Fori(0, NCH // 2) as r:
                    for h in range(2):
                        c = 2 * r + h
                        sp.wait_ge(AC.sem, AC.now("y", c))
                        sp.dma_start(io["rw_y"][c], y[h][:, :, :]).then_inc(s_y, 16)
                        sp.wait_ge(PE.sem, PE.now("y", c))
                        sp.dma_start(in5[h][:, :, :, :], io["rwc"][(2 * r + h + 2) % NCH]).then_inc(s_in[h], 16)
                sp.wait_ge(DV.sem, DV.now("s", NCH - 1))
                sp.dma_start(io["wkv_out"][0], S[:, :, :]).then_inc(s_y, 16)
                sp.wait_ge(s_y, 16 * NCH + 16)
                for h in range(2):
                    sp.wait_ge(s_in[h], 16 * (NCH // 2 + 1))

            @block.tensor
            def _(pe):
                PE.credit(pe)
                one = pe.alloc_register("rwc_one")
                pe.reg_mov(one, 1)
                with pe.Fori(0, NCH // 2) as r:
                    for h in range(2):
                        c = 2 * r + h
                        at = pe_at_of(pe, c, one)
                        pe.wait_ge(s_in[h], 16 * r + 16)
                        pe.wait_ge(DV.sem, DV.before("s", c))
                        pe.wait_ge(AC.sem, AC.before("y", c))
                        pe.wait_ge(s_init, one)
                        pe.reg_alu(one, one, 1, ALU.max)
                        rw_matrix_pe(k, b, pe, in5[h], LEVELS, at)
                        at(AC, "tok")
                        for p_, rows in heads:
                            o_ = four(BANK_U)[rows, p_, :]
                            nc.tensor.matmul(o_, in5[h][rows, KA, p_, :], S[rows, p_, :], start=True, stop=False)
                            mm = nc.tensor.matmul(o_, b.mt[rows, p_, 128:192], b.tok[rows, 2, p_, :], start=False, stop=True)
                        mm.then_inc(*PE.inc("rhs"))
                        at(DV, "rhs")
                        for p_, rows in heads:
                            mm = nc.tensor.matmul(four(BANK_U)[rows, p_, :], b.xy[rows, p_, 1, :], b.rhs[rows, p_, :],
                                                  start=True, stop=True)
                        mm.then_inc(*PE.inc("u"))
                        at(AC, "u")
                        for p_, rows in heads:
                            o_ = four(BANK_Y)[rows, p_, :]
                            nc.tensor.matmul(o_, S[rows, p_, :], in5[h][rows, RB, p_, :], start=True, stop=False)
                            nc.tensor.matmul(o_, b.u[rows, p_, :], b.mt[rows, p_, 64:128], start=False, stop=False)
                            mm = nc.tensor.matmul(o_, b.tok[rows, 2, p_, :], b.mt[rows, p_, 192:256], start=False, stop=True)
                        mm.then_inc(*PE.inc("y"))
                        for p_, rows in heads:
                            o_ = four(BANK_S)[rows, p_, :]
                            nc.tensor.matmul(o_, b.tok[rows, 0, p_, :], b.u[rows, p_, :], start=True, stop=False)
                            mm = nc.tensor.matmul(o_, b.tok[rows, 1, p_, :], b.tok[rows, 2, p_, :], start=False, stop=True)
                        mm.then_inc(*PE.inc("s"))

            @block.scalar
            def _(act):
                AC.credit(act)
                with act.Fori(0, NCH // 2) as r:
                    for h in range(2):
                        c = 2 * r + h
                        at = at_of(act, c)
                        rw_matrix_act(k, b, LEVELS, at)
                        at(PE, "u")
                        nc.scalar.activation(b.u[:, :, :].rearrange("p a t -> p (a t)"), b.ps[:, BANK_U, 0:256],
                                             ACT.Copy, scale=-1.0).then_inc(*AC.inc("u"))
                        at(PE, "y")
                        act.wait_ge(s_y, 32 * r)
                        nc.scalar.activation(y[h][:, :, :].rearrange("p a t -> p (a t)"), b.ps[:, BANK_Y, 0:256],
                                             ACT.Copy).then_inc(*AC.inc("y"))

            @block.vector
            def _(dve):
                v = nc.vector
                DV.credit(dve)
                v.memset(S[:, :, :], 0.0).then_inc(s_init, 1)
                with dve.Fori(0, NCH // 2) as r:
                    for h in range(2):
                        c = 2 * r + h
                        at = at_of(dve, c)
                        rw_matrix_dve(k, b, 0, LEVELS, at)
                        at(PE, "rhs")
                        v.tensor_copy(b.rhs[:, :, :], four(BANK_U)).then_inc(*DV.inc("rhs"))
                        at(PE, "s")
                        dve.wait_ge(s_init, 1)
                        dve.wait_ge(DV.sem, DV.before("s", c))
                        v.tensor_tensor(S[:, :, :], four(BANK_S), S[:, :, :], ALU.add).then_inc(*DV.inc("s_add"))
                        at(DV, "s_add")
                        v.tensor_tensor(S[:, :, :], S[:, :, :], bc(k.lam_end[:, :, bass.ds(c, 1)], [P, NPAIR, CL]),
                                        ALU.mult).then_inc(*DV.inc("s"))


def phase_rw_samples(k):
    nc, io = k.nc, k.io
    levels = DSEQ.bit_length() - 1
    with ExitStack() as ctx:
        b = RwBuffers(k, ctx, "rws", levels)
        PE, AC, DV = b.PE, b.AC, b.DV
        sb = lambda n, s: ctx.enter_context(nc.sbuf_tensor(f"rws_{n}", s, F32))
        in5 = sb("in", [P, 5, NPAIR, CL])
        S = sb("state", [P, NSEQ, NPAIR, CL])
        y = sb("y", [P, NPAIR, CL])
        kr = sb("kr", [P, 2 * NPAIR, NSEQ, CL])
        um = sb("um", [P, 2, NPAIR, NSEQ, CL])
        s_in = k.sem("rws_loaded")
        s_out = k.sem("rws_stored")
        heads = [(p_, rows) for p_ in range(NPAIR) for rows in halves()]
        four = lambda bank: b.ps[:, bank, 0:256].rearrange("p (a t) -> p a t", a=4)
        at_of = lambda eng: (lambda S_, step: eng.wait_ge(S_.sem, S_.done(step)))
        SBANK = (0, 1, 3, 4)

        with nc.Block() as block:
            @block.sync
            def _(sp):
                sp.dma_start(in5[:, :, :, :], io["rwc"][NCH]).then_inc(s_in, 16)
                sp.dma_start(S[:, :, :, :], io["wkvT"].rearrange("s p a v -> p s a v")).then_inc(s_in, 16)
                sp.wait_ge(AC.sem, AC.done("y"))
                sp.dma_start(io["rw_y"][NCH], y[:, :, :]).then_inc(s_out, 16)
                sp.wait_ge(DV.sem, DV.done("s"))
                sp.dma_start(io["wkv_out"][1:NCOND].rearrange("s p a v -> p s a v"), S[:, :, :, :]).then_inc(s_out, 16)
                sp.wait_ge(s_out, 32)

            @block.tensor
            def _(pe):
                at = at_of(pe)
                pe.wait_ge(s_in, 32)
                rw_matrix_pe(k, b, pe, in5, levels, at)
                at(AC, "tok")
                at(DV, "masked")
                for p_, rows in heads:
                    o_ = four(BANK_U)[rows, p_, :]
                    for s in range(NSEQ):
                        nc.tensor.matmul(o_, kr[rows, p_, s, :], S[rows, s, p_, :], start=s == 0, stop=False)
                    mm = nc.tensor.matmul(o_, b.mt[rows, p_, 128:192], b.tok[rows, 2, p_, :], start=False, stop=True)
                mm.then_inc(*PE.inc("rhs"))
                at(DV, "rhs")
                for p_, rows in heads:
                    mm = nc.tensor.matmul(four(BANK_U)[rows, p_, :], b.xy[rows, p_, 1, :], b.rhs[rows, p_, :],
                                          start=True, stop=True)
                mm.then_inc(*PE.inc("u"))
                at(AC, "u")
                for p_, rows in heads:
                    o_ = four(BANK_Y)[rows, p_, :]
                    for s in range(NSEQ):
                        nc.tensor.matmul(o_, S[rows, s, p_, :], kr[rows, NPAIR + p_, s, :], start=s == 0, stop=False)
                    nc.tensor.matmul(o_, b.u[rows, p_, :], b.mt[rows, p_, 64:128], start=False, stop=False)
                    mm = nc.tensor.matmul(o_, b.tok[rows, 2, p_, :], b.mt[rows, p_, 192:256], start=False, stop=True)
                mm.then_inc(*PE.inc("y"))
                at(DV, "umask")
                for p_, rows in heads:
                    o_ = b.ps[rows, SBANK[p_], :]
                    nc.tensor.matmul(o_, b.tok[rows, 0, p_, :], um[rows, 0, p_, :, :], start=True, stop=False)
                    mm = nc.tensor.matmul(o_, b.tok[rows, 1, p_, :], um[rows, 1, p_, :, :], start=False, stop=True)
                mm.then_inc(*PE.inc("s"))

            @block.scalar
            def _(act):
                at = at_of(act)
                rw_matrix_act(k, b, levels, at)
                at(PE, "u")
                nc.scalar.activation(b.u[:, :, :].rearrange("p a t -> p (a t)"), b.ps[:, BANK_U, 0:256],
                                     ACT.Copy, scale=-1.0).then_inc(*AC.inc("u"))
                at(PE, "y")
                nc.scalar.activation(y[:, :, :].rearrange("p a t -> p (a t)"), b.ps[:, BANK_Y, 0:256],
                                     ACT.Copy).then_inc(*AC.inc("y"))

            @block.vector
            def _(dve):
                v = nc.vector
                at = at_of(dve)
                rw_matrix_dve(k, b, 1, levels, at)
                dve.wait_ge(s_in, 32)
                src = in5[:, 0:2, :, :].rearrange("p q a t -> p (q a) t").unsqueeze(2)
                v.tensor_tensor(kr[:, :, :, :], bc(src, [P, 2 * NPAIR, NSEQ, CL]),
                                bc(k.seq_cols[:, :, :].unsqueeze(1), [P, 2 * NPAIR, NSEQ, CL]),
                                ALU.mult).then_inc(*DV.inc("masked"))
                at(PE, "rhs")
                v.tensor_copy(b.rhs[:, :, :], four(BANK_U)).then_inc(*DV.inc("rhs"))
                at(AC, "u")
                rows_of = bc(k.seq_rows[:, :].unsqueeze(1).unsqueeze(3), [P, NPAIR, NSEQ, CL])
                v.tensor_tensor(um[:, 0], bc(b.u[:, :, :].unsqueeze(2), [P, NPAIR, NSEQ, CL]), rows_of, ALU.mult)
                v.tensor_tensor(um[:, 1], bc(b.tok[:, 2, :, :].unsqueeze(2), [P, NPAIR, NSEQ, CL]), rows_of,
                                ALU.mult).then_inc(*DV.inc("umask"))
                at(PE, "s")
                for p_ in range(NPAIR):
                    last = v.tensor_tensor(S[:, :, p_, :], b.ps[:, SBANK[p_], :].rearrange("p (s t) -> p s t", s=NSEQ),
                                           S[:, :, p_, :], ALU.add)
                last.then_inc(*DV.inc("s_add"))
                at(DV, "s_add")
                for p_ in range(NPAIR):
                    last = v.tensor_tensor(S[:, :, p_, :], S[:, :, p_, :],
                                           bc(k.lam_end[:, p_, NCH:NCH + NSEQ].unsqueeze(2), [P, NSEQ, CL]), ALU.mult)
                last.then_inc(*DV.inc("s"))


PADP = CONVK - 1
CONV_IN = PADP + SEQ + NSEQ * (PADP + DSEQ)
CONV_OUT = CONV_IN - PADP


def conv_sample_view(tile):
    return tile[:, PADP + SEQ:CONV_IN].rearrange("p (s t) -> p s t", s=NSEQ)


def phase_ssd_pre(k):
    nc, io = k.nc, k.io
    with ExitStack() as ctx:
        sb = lambda n, s: ctx.enter_context(nc.sbuf_tensor(f"cv_{n}", s, F32))
        e = [sb(f"in{i}", [P, CONV_IN]) for i in range(2)]
        acc = [sb(f"acc{i}", [P, CONV_IN]) for i in range(2)]
        sg = [sb(f"sig{i}", [P, CONV_IN]) for i in range(2)]
        out = [sb(f"out{i}", [P, T]) for i in range(2)]
        state = sb("state", [P, NXBC, NSEQ, PADP])
        new = sb("new", [P, NXBC, NCOND, PADP])
        hp = sb("hp", [SH, 2])
        neg_a = sb("neg_a", [SH, 1])
        dx = sb("dx", [SH, TX])
        keep, x, ex, sq, poly, rec = (sb(n, [SH, T]) for n in ("keep", "x", "ex", "sq", "poly", "rec"))
        rows = sb("rows", [SH, 3, T])
        s_in = [k.sem(f"cv_in{i}_loaded") for i in range(2)]
        s_state = k.sem("cv_state_loaded")
        s_dt = k.sem("dt_loaded")
        s_pad = k.sem("cv_pad_zeroed")
        s_out = [k.sem(f"cv_out{i}_stored") for i in range(2)]
        s_fin = k.sem("cv_states_and_dt_stored")
        s_keep = k.sem("dt_keep_step")
        s_dx = k.sem("dt_act_step")
        s_dv = k.sem("dt_dve_step")
        s_rows = k.sem("dt_rows_done")
        PO = Progress(k.sem("cv_pool"), "state", "new")
        AC = Progress(k.sem("cv_act"), "sigmoid")
        DV = Progress(k.sem("cv_dve"), "tap0", "tap1", "tap2", "tap3", "silu")
        cw, cb = k.par[:, PCOLS["conv_w"]], k.par[:, PCOLS["conv_b"]]

        with nc.Block() as block:
            @block.sync
            def _(sp):
                sp.dma_start(dx[:, :], io["proj"][DT0, 0:SH, :]).then_inc(s_dt, 16)
                sp.dma_start(hp[:, :], io["head_params"]).then_inc(s_dt, 16)
                sp.dma_start(state[:, :, :, :], io["convT"]).then_inc(s_state, 16)
                with sp.Fori(0, NXBC // 2) as r:
                    for h in range(2):
                        m = 2 * r + h
                        sp.wait_ge(DV.sem, DV.before("silu", 2 * r))
                        sp.dma_start(e[h][:, PADP:PADP + SEQ], io["proj"][m + XBC0, :, 1:1 + SEQ]).then_inc(s_in[h], 16)
                        src = io["proj"][m + XBC0, :, 1 + SEQ:TX].rearrange("p (s t) -> p s t", s=NSEQ)
                        sp.dma_start(conv_sample_view(e[h])[:, :, PADP:], src[:, :, 1:1 + DSEQ]).then_inc(s_in[h], 16)
                sp.wait_ge(s_rows, 2)
                sp.dma_start(io["ssd_rows"], rows[:, :, :]).then_inc(s_fin, 16)
                sp.wait_ge(PO.sem, PO.now("new", NXBC - 1))
                sp.dma_start(io["conv_out"], new[:, :, :, :]).then_inc(s_fin, 16)
                sp.wait_ge(s_fin, 32)

            @block.gpsimd
            def _(pool):
                g = nc.gpsimd
                PO.credit(pool)
                g.memset(keep[:, :], 1.0).then_inc(s_keep, 1)
                for i in range(2):
                    g.memset(e[i][:, 0:PADP], 0.0).then_inc(s_pad, 1)
                pool.wait_ge(s_keep, 1)
                g.memset(keep[:, 0:SEQ].rearrange("p (c t) -> p c t", t=SL)[:, :, 0:1], 0.0).then_inc(s_keep, 1)
                g.memset(keep[:, SEQ:T].rearrange("p (c t) -> p c t", t=DSEQ)[:, :, 0:1], 0.0).then_inc(s_keep, 1)
                pool.wait_ge(s_state, 16)
                with pool.Fori(0, NXBC // 2) as r:
                    for h in range(2):
                        m = 2 * r + h
                        smp = conv_sample_view(e[h])
                        pool.wait_ge(DV.sem, DV.before("silu", 2 * r))
                        g.tensor_copy(smp[:, :, 0:PADP], state[:, bass.ds(m, 1), :, :].rearrange("p a s t -> p (a s) t")).then_inc(*PO.inc("state"))
                        pool.wait_ge(s_in[h], 32 * r + 32)
                        g.tensor_copy(new[:, bass.ds(m, 1), 0, :].rearrange("p a t -> p (a t)"), e[h][:, SEQ:SEQ + PADP])
                        g.tensor_copy(new[:, bass.ds(m, 1), 1:NCOND, :].rearrange("p a s t -> p (a s) t"), smp[:, :, DSEQ:]).then_inc(*PO.inc("new"))

            @block.scalar
            def _(act):
                a = nc.scalar
                act.wait_ge(s_dt, 32)
                a.activation(neg_a[:, :], hp[:, 1:2], ACT.Exp).then_inc(s_dx, 1)
                act.wait_ge(s_dv, 2)
                a.activation(ex[:, :], x[:, :], ACT.Abs).then_inc(s_dx, 1)
                act.wait_ge(s_dx, 2)
                a.activation(ex[:, :], ex[:, :], ACT.Exp, scale=-1.0).then_inc(s_dx, 1)
                AC.credit(act)
                with act.Fori(0, NXBC // 2) as r:
                    for h in range(2):
                        m = 2 * r + h
                        act.wait_ge(DV.sem, DV.now("tap3", m))
                        a.activation(sg[h][:, 0:CONV_OUT], acc[h][:, 0:CONV_OUT], ACT.Sigmoid).then_inc(*AC.inc("sigmoid"))
                        act.wait_ge(DV.sem, DV.now("silu", m))
                        act.dma_start(io["xbc"][m], out[h][:, :]).then_inc(s_out[h], 16)
                for h in range(2):
                    act.wait_ge(s_out[h], 16 * (NXBC // 2))

            @block.vector
            def _(dve):
                v = nc.vector
                n = [0]

                def step(ins):
                    ins.then_inc(s_dv, 1)
                    n[0] += 1
                    dve.wait_ge(s_dv, n[0])

                dve.wait_ge(s_dt, 32)
                v.tensor_copy(x[:, 0:SEQ], dx[:, 1:1 + SEQ])
                step(v.tensor_copy(token_views(x)[1], predecessor_views(dx)[1][1]))
                step(v.tensor_scalar(x[:, :], x[:, :], hp[:, 0:1], None, ALU.add))
                dve.wait_ge(s_dx, 3)
                step(v.tensor_scalar(rec[:, :], ex[:, :], 2.0, None, ALU.add))
                step(v.reciprocal(rec[:, :], rec[:, :]))
                step(v.tensor_tensor(ex[:, :], ex[:, :], rec[:, :], ALU.mult))
                step(v.tensor_tensor(sq[:, :], ex[:, :], ex[:, :], ALU.mult))
                step(v.tensor_scalar(poly[:, :], sq[:, :], 1.0 / 15, None, ALU.mult))
                for d in (13, 11, 9, 7, 5, 3):
                    step(v.scalar_tensor_tensor(out=poly[:, :], in0=poly[:, :], scalar=1.0 / d, in1=sq[:, :],
                                                op0=ALU.add, op1=ALU.mult))
                step(v.scalar_tensor_tensor(out=poly[:, :], in0=poly[:, :], scalar=1.0, in1=ex[:, :], op0=ALU.add, op1=ALU.mult))
                step(v.tensor_scalar(x[:, :], x[:, :], 0.0, None, ALU.max))
                step(v.scalar_tensor_tensor(out=rows[:, 0, :], in0=poly[:, :], scalar=2.0, in1=x[:, :], op0=ALU.mult, op1=ALU.add))
                dve.wait_ge(s_keep, 3)
                step(v.tensor_scalar(x[:, :], rows[:, 0, :], neg_a[:, 0:1], -1.0, ALU.mult, ALU.mult))
                step(v.tensor_tensor_scan(rows[:, 1, :], keep[:, :], x[:, :], 0.0, ALU.mult, ALU.add))
                for span, lo, hi in ((SL, 0, SEQ), (DSEQ, SEQ, T)):
                    cs = rows[:, 1, lo:hi].rearrange("p (c t) -> p c t", t=span)
                    v.tensor_tensor(rows[:, 2, lo:hi].rearrange("p (c t) -> p c t", t=span),
                                    bc(cs[:, :, span - 1:span], [SH, (hi - lo) // span, span]), cs, ALU.subtract).then_inc(s_rows, 1)
                DV.credit(dve)
                dve.wait_ge(s_pad, 2)
                with dve.Fori(0, NXBC // 2) as r:
                    for h in range(2):
                        m = 2 * r + h
                        now = lambda s_: dve.wait_ge(DV.sem, DV.now(s_, m))
                        dve.wait_ge(s_in[h], 32 * r + 32)
                        dve.wait_ge(PO.sem, PO.now("new", m))
                        wc = lambda j: cw[:, bass.ds(m + j * NXBC, 1)]
                        a_ = acc[h][:, 0:CONV_OUT]
                        v.tensor_scalar(a_, e[h][:, 0:CONV_OUT], wc(0), cb[:, bass.ds(m, 1)], ALU.mult, ALU.add).then_inc(*DV.inc("tap0"))
                        for j in range(1, CONVK):
                            now(f"tap{j - 1}")
                            v.scalar_tensor_tensor(out=a_, in0=e[h][:, j:j + CONV_OUT], scalar=wc(j), in1=a_,
                                                   op0=ALU.mult, op1=ALU.add).then_inc(*DV.inc(f"tap{j}"))
                        dve.wait_ge(AC.sem, AC.now("sigmoid", m))
                        dve.wait_ge(s_out[h], 16 * r)
                        v.tensor_tensor(out[h][:, 0:SEQ], acc[h][:, 0:SEQ], sg[h][:, 0:SEQ], ALU.mult)
                        v.tensor_tensor(token_views(out[h])[1], conv_sample_view(acc[h])[:, :, 0:DSEQ],
                                        conv_sample_view(sg[h])[:, :, 0:DSEQ], ALU.mult).then_inc(*DV.inc("silu"))


def phase_ssd(k):
    for c in ("prompt", "samples"):
        ssd_chunks(k, c)


def ssd_chunks(k, which):
    nc, io = k.nc, k.io
    smp = which == "samples"
    L = NSEQ * DSEQ if smp else SL
    rounds = 1 if smp else NSC // 2
    slots = 1 if smp else 2
    tag = "ss" if smp else "sp"
    with ExitStack() as ctx:
        sb = lambda n, s: ctx.enter_context(nc.sbuf_tensor(f"{tag}_{n}", s, F32))
        inx = [sb(f"in{i}", [P, NXBC, L]) for i in range(slots)]
        rows = [sb(f"rows{i}", [SH, 3, L]) for i in range(slots)]
        y = [sb(f"y{i}", [P, KC, L]) for i in range(slots)]
        S = sb("state", [P, NSEQ if smp else 1, SH, SD])
        col = sb("col", [P, 3, SH])
        cb = sb("cb", [P, SG, L])
        btok = sb("btok", [P, SG, SN])
        xt = sb("xt", [P, SH, SD])
        xd = sb("xd", [P, SH, SD])
        w = sb("w", [P, SH, L])
        ce = sb("ce", [P, SH, L])
        end = sb("end", [P, NSEQ if smp else 1, SH])
        xm = [sb(f"xm{i}", [P, SH, SD]) for i in range(2)] if smp else None
        ps = ctx.enter_context(nc.psum_tensor(f"{tag}_ps", [P, 8, 512], F32))
        s_in = [k.sem(f"{tag}_in{i}_loaded") for i in range(slots)]
        s_S = k.sem(f"{tag}_state_ready")
        s_y = k.sem(f"{tag}_y_stored")
        s_out = k.sem(f"{tag}_state_stored")
        s_xm = k.sem(f"{tag}_masked_x")
        s_sm = k.sem(f"{tag}_state_matmul")
        s_sv = k.sem(f"{tag}_state_step")
        PE = Progress(k.sem(f"{tag}_pe"), "col", "bc", "x", "csb", "y", "s")
        AC = Progress(k.sem(f"{tag}_act"), "col", "btok", "excs", "dec", "y")
        DV = Progress(k.sem(f"{tag}_dve"), "cb", "x", "xd", "diff", "end", "w", "ce", "s_decay", "s")
        cview = ps[:, 0, 0:3 * SH].rearrange("p (q h) -> p q h", q=3)
        bcv = ps[:, 1, :].rearrange("p (i g m) -> p i g m", i=2, g=SG)
        xv = ps[:, 2:4, :].rearrange("p a b -> p (a b)").rearrange("p (h m) -> p h m", h=SH)
        csb = ps[:, 4:8, :].rearrange("p a b -> p (a b)")[:, 0:SH * SL].rearrange("p (h l) -> p h l", h=SH)[:, :, 0:L]
        yv = ps[:, 2:4, :].rearrange("p a b -> p (a b)").rearrange("p (a l) -> p a l", a=KC)[:, :, 0:L]
        tokens = lambda c: slice(SEQ, T) if smp else bass.ds(c * SL, SL)

        def at_of(eng, c):
            if smp:
                return lambda S_, step: eng.wait_ge(S_.sem, S_.done(step))
            return lambda S_, step: eng.wait_ge(S_.sem, S_.now(step, c))

        def chunks(eng):
            if smp:
                yield 0, 0, 0
                return
            with eng.Fori(0, rounds) as r:
                for h in range(2):
                    yield 2 * r + h, h, r

        with nc.Block() as block:
            @block.sync
            def _(sp):
                if smp:
                    sp.dma_start(S[:, :, :, :].rearrange("p s h m -> p s (h m)"), io["ssmT"].rearrange("s n m -> n s m")).then_inc(s_S, 16)
                for c, h, r in chunks(sp):
                    if not smp:
                        sp.wait_ge(PE.sem, PE.before("y", 2 * r))
                        sp.wait_ge(DV.sem, DV.before("ce", 2 * r))
                    sp.dma_start(inx[h][:, :, :], io["xbc"][:, :, tokens(c)].rearrange("a p t -> p a t")).then_inc(s_in[h], 16)
                    sp.dma_start(rows[h][:, :, :], io["ssd_rows"][:, :, tokens(c)]).then_inc(s_in[h], 16)
                if smp:
                    sp.wait_ge(s_sv, 2 * NSEQ * 2)
                    sp.dma_start(io["ssm_out"][1:NCOND].rearrange("s n m -> n s m"), S[:, :, :, :].rearrange("p s h m -> p s (h m)")).then_inc(s_S, 16)
                    sp.wait_ge(s_S, 32)
                else:
                    sp.wait_ge(DV.sem, DV.now("s", NSC - 1))
                    sp.dma_start(io["ssm_out"][0], S[:, 0, :, :].rearrange("p h m -> p (h m)")).then_inc(s_out, 16)
                    sp.wait_ge(s_out, 16)

            @block.gpsimd
            def _(pool):
                for c, h, r in chunks(pool):
                    at_of(pool, c)(AC, "y")
                    pool.dma_start(io["ssd_y"][:, :, tokens(c)].rearrange("a p t -> p a t"), y[h][:, :, :]).then_inc(s_y, 16)
                pool.wait_ge(s_y, 16 if smp else 16 * NSC)

            @block.tensor
            def _(pe):
                if not smp:
                    PE.credit(pe)
                for c, h, r in chunks(pe):
                    at = at_of(pe, c)
                    pe.wait_ge(s_in[h], 32 * r + 32)
                    if not smp:
                        pe.wait_ge(DV.sem, DV.before("s", c))
                        pe.wait_ge(AC.sem, AC.before("y", c))
                        pe.wait_ge(s_S, 1)
                    for i in range(3):
                        mm = nc.tensor.matmul(cview[0:L, i, :], rows[h][:, i, :], k.ident[0:SH, 0:SH], start=True, stop=True)
                    mm.then_inc(*PE.inc("col"))
                    for g in range(SG):
                        nc.tensor.matmul(bcv[0:L, 0, g, 0:L], inx[h][:, 8 + g, :], inx[h][:, 10 + g, :], start=True, stop=True)
                        mm = nc.tensor.transpose(bcv[0:L, 1, g, :], inx[h][:, 8 + g, :], k.ident[:, :])
                    mm.then_inc(*PE.inc("bc"))
                    for i in range(KC):
                        mm = nc.tensor.transpose(xv[0:L, 2 * i:2 * i + 2, :].rearrange("p h m -> p (h m)"), inx[h][:, i, :], k.ident[:, :])
                    mm.then_inc(*PE.inc("x"))
                    for i in range(SH):
                        mm = nc.tensor.matmul(csb[:, i, :], k.head_sel[:, i, :], rows[h][:, 1, :], start=True, stop=True)
                    mm.then_inc(*PE.inc("csb"))
                    if smp:
                        pe.wait_ge(s_S, 16)
                    at(DV, "x")
                    at(DV, "w")
                    at(DV, "ce")
                    for i in range(SH):
                        o_ = yv[64 * (i % 2):64 * (i % 2) + 64, i // 2, :]
                        nc.tensor.matmul(o_, xt[0:L, i, :], w[0:L, i, :], start=True, stop=False)
                        if smp:
                            for s in range(NSEQ):
                                t = slice(DSEQ * s, DSEQ * s + DSEQ)
                                mm = nc.tensor.matmul(o_[:, t], S[:, s, i, :], ce[:, i, t], start=False, stop=s == NSEQ - 1)
                        else:
                            mm = nc.tensor.matmul(o_, S[:, 0, i, :], ce[:, i, :], start=False, stop=True)
                    mm.then_inc(*PE.inc("y"))
                    at(AC, "col")
                    at(AC, "btok")
                    at(DV, "xd")
                    if smp:
                        for s in range(NSEQ):
                            pe.wait_ge(s_xm, s + 1)
                            for g in range(SG):
                                n = 2 * s + g
                                if n >= 2:
                                    pe.wait_ge(s_sv, 2 * (n - 1))
                                nc.tensor.matmul(ps[:, n % 2, :], btok[0:L, g, :],
                                                 xm[s % 2][0:L, 8 * g:8 * g + 8, :].rearrange("p h m -> p (h m)"),
                                                 start=True, stop=True).then_inc(s_sm, 1)
                    else:
                        for g in range(SG):
                            mm = nc.tensor.matmul(ps[:, g, :], btok[:, g, :], xd[:, 8 * g:8 * g + 8, :].rearrange("p h m -> p (h m)"),
                                                  start=True, stop=True)
                        mm.then_inc(*PE.inc("s"))

            @block.scalar
            def _(act):
                a = nc.scalar
                if not smp:
                    AC.credit(act)
                for c, h, r in chunks(act):
                    at = at_of(act, c)
                    at(PE, "col")
                    a.activation(col[0:L, 0:2, :], cview[0:L, 0:2, :], ACT.Copy)
                    a.activation(col[0:L, 2, :], cview[0:L, 2, :], ACT.Exp).then_inc(*AC.inc("col"))
                    at(PE, "bc")
                    a.activation(btok[0:L, :, :], bcv[0:L, 1, :, :], ACT.Copy).then_inc(*AC.inc("btok"))
                    at(PE, "csb")
                    a.activation(ce[:, :, :], csb, ACT.Exp).then_inc(*AC.inc("excs"))
                    at(DV, "diff")
                    a.activation(w[0:L, :, :], w[0:L, :, :], ACT.Exp).then_inc(*AC.inc("dec"))
                    at(PE, "y")
                    if not smp:
                        act.wait_ge(s_y, 32 * r)
                    a.activation(y[h][:, :, :], yv, ACT.Copy).then_inc(*AC.inc("y"))

            @block.vector
            def _(dve):
                v = nc.vector
                if not smp:
                    DV.credit(dve)
                    v.memset(S[:, 0, :, :], 0.0).then_inc(s_S, 1)
                mask = k.ssd_mask_smp if smp else k.ssd_mask
                for c, h, r in chunks(dve):
                    at = at_of(dve, c)
                    at(AC, "btok")
                    v.tensor_tensor(cb[0:L, :, :], bcv[0:L, 0, :, 0:L], bc(mask[0:L, 0:L].unsqueeze(1), [L, SG, L]),
                                    ALU.mult).then_inc(*DV.inc("cb"))
                    at(PE, "x")
                    v.tensor_tensor(xt[0:L, :, :], xv[0:L, :, :], bc(col[0:L, 0, :].unsqueeze(2), [L, SH, SD]), ALU.mult).then_inc(*DV.inc("x"))
                    at(DV, "x")
                    v.tensor_tensor(xd[0:L, :, :], xt[0:L, :, :], bc(col[0:L, 2, :].unsqueeze(2), [L, SH, SD]), ALU.mult).then_inc(*DV.inc("xd"))
                    at(AC, "excs")
                    for i in range(SH):
                        last = v.tensor_scalar(w[0:L, i, :], csb[0:L, i, :], col[0:L, 1, i:i + 1], 0.0, ALU.subtract, ALU.min)
                    last.then_inc(*DV.inc("diff"))
                    if smp:
                        v.tensor_copy(end[:, :, :], ce[:, :, DSEQ - 1:L:DSEQ].rearrange("p h s -> p s h")).then_inc(*DV.inc("end"))
                    else:
                        v.tensor_copy(end[:, 0, :], ce[:, :, L - 1]).then_inc(*DV.inc("end"))
                    at(AC, "dec")
                    for g in range(SG):
                        hh = slice(8 * g, 8 * g + 8)
                        last = v.tensor_tensor(w[0:L, hh, :], w[0:L, hh, :], bc(cb[0:L, g:g + 1, :], [L, 8, L]), ALU.mult)
                    last.then_inc(*DV.inc("w"))
                    at(DV, "end")
                    for g in range(SG):
                        hh = slice(8 * g, 8 * g + 8)
                        last = v.tensor_tensor(ce[:, hh, :], ce[:, hh, :], bc(inx[h][:, 10 + g:11 + g, :], [P, 8, L]), ALU.mult)
                    last.then_inc(*DV.inc("ce"))
                    at(PE, "y")
                    if smp:
                        for s in range(NSEQ):
                            if s >= 2:
                                dve.wait_ge(s_sm, 2 * (s - 1))
                            v.tensor_scalar(xm[s % 2][0:L, :, :], xd[0:L, :, :], k.seq_rows[0:L, s:s + 1], None, ALU.mult).then_inc(s_xm, 1)
                            for g in range(SG):
                                n = 2 * s + g
                                sv = S[:, s, 8 * g:8 * g + 8, :]
                                v.tensor_tensor(sv, sv, bc(end[:, s, 8 * g:8 * g + 8].unsqueeze(2), [P, 8, SD]), ALU.mult).then_inc(s_sv, 1)
                                dve.wait_ge(s_sv, 2 * n + 1)
                                dve.wait_ge(s_sm, n + 1)
                                v.tensor_tensor(sv, sv, ps[:, n % 2, :].rearrange("p (h m) -> p h m", h=8), ALU.add).then_inc(s_sv, 1)
                    else:
                        dve.wait_ge(s_S, 1)
                        v.tensor_tensor(S[:, 0], S[:, 0], bc(end[:, 0, :].unsqueeze(2), [P, SH, SD]), ALU.mult).then_inc(*DV.inc("s_decay"))
                        at(DV, "s_decay")
                        at(PE, "s")
                        for g in range(SG):
                            sv = S[:, 0, 8 * g:8 * g + 8, :]
                            last = v.tensor_tensor(sv, sv, ps[:, g, :].rearrange("p (h m) -> p h m", h=8), ALU.add)
                        last.then_inc(*DV.inc("s"))


def phase_rw_post(k, oa):
    nc, io = k.nc, k.io
    with ExitStack() as ctx:
        sb = lambda n, s: ctx.enter_context(nc.sbuf_tensor(f"ro_{n}", s, F32))
        y, gate, bonus = ([sb(f"{n}{i}", [P, T]) for i in range(2)] for n in ("y", "gate", "bonus"))
        sq, rs = sb("sq", [P, T]), sb("rs", [P, T])
        ps = [ctx.enter_context(nc.psum_tensor(f"ro_ps{i}", [P, 3, 512], F32)) for i in range(2)]
        pm, pv = (flat(p_[:, :, :]) for p_ in ps)
        s_in = [k.sem(f"ro_in{i}_loaded") for i in range(2)]
        PE = Progress(k.sem("ro_pe"), "mean", "var")
        AC = Progress(k.sem("ro_act"), "sq", "ln", "rstd")
        DV = Progress(k.sem("ro_dve"), "center", "norm", "affine", "bonus", "gate")
        with nc.Block() as block:
            @block.sync
            def _(sp):
                for p_ in range(NPAIR):
                    h = p_ % 2
                    if p_ >= 2:
                        sp.wait_ge(DV.sem, DV.done("gate", p_ - 2))
                    sp.dma_start(y[h][:, :].rearrange("p (c t) -> p c t", t=CL),
                                 io["rw_y"][:, :, p_, :].rearrange("c p t -> p c t")).then_inc(s_in[h], 16)
                    sp.dma_start(gate[h][:, :], io["rw_gate"][p_]).then_inc(s_in[h], 16)
                    sp.dma_start(bonus[h][:, :], io["rw_bonus"][p_]).then_inc(s_in[h], 16)

            @block.tensor
            def _(pe):
                for p_ in range(NPAIR):
                    pe.wait_ge(s_in[p_ % 2], 48 * (p_ // 2 + 1))
                    for out, src, step in ((pm, y[p_ % 2], "mean"), (pv, sq, "var")):
                        if step == "var":
                            pe.wait_ge(AC.sem, AC.done("sq", p_))
                        elif p_ >= 1:
                            pe.wait_ge(DV.sem, DV.done("center", p_ - 1))
                        for a, b in TOK_CHUNKS_BANKED:
                            mm = nc.tensor.matmul(out[:, a:b], k.pairones[:, :], src[:, a:b], start=True, stop=True)
                        mm.then_inc(*PE.inc(step))

            @block.scalar
            def _(act):
                for p_ in range(NPAIR):
                    act.wait_ge(DV.sem, DV.done("center", p_))
                    nc.scalar.activation(sq[:, :], y[p_ % 2][:, :], ACT.Square).then_inc(*AC.inc("sq"))
                    act.wait_ge(PE.sem, PE.done("var", p_))
                    nc.scalar.activation(rs[:, :], pv[:, 0:T], ACT.Ln, scale=1.0 / RD, bias=k.const[:, 1:2]).then_inc(*AC.inc("ln"))
                    act.wait_ge(AC.sem, AC.done("ln", p_))
                    nc.scalar.activation(rs[:, :], rs[:, :], ACT.Exp, scale=-0.5).then_inc(*AC.inc("rstd"))

            @block.vector
            def _(dve):
                v = nc.vector
                lnw, lnb = k.par[:, PCOLS["ln_w"]], k.par[:, PCOLS["ln_b"]]
                for p_ in range(NPAIR):
                    h = p_ % 2
                    yt = y[h][:, :]
                    now = lambda s_: dve.wait_ge(DV.sem, DV.done(s_, p_))
                    dve.wait_ge(PE.sem, PE.done("mean", p_))
                    v.scalar_tensor_tensor(out=yt, in0=pm[:, 0:T], scalar=-1.0 / RD, in1=yt, op0=ALU.mult,
                                           op1=ALU.add).then_inc(*DV.inc("center"))
                    dve.wait_ge(AC.sem, AC.done("rstd", p_))
                    v.tensor_tensor(yt, yt, rs[:, :], ALU.mult).then_inc(*DV.inc("norm"))
                    now("norm")
                    v.tensor_scalar(yt, yt, lnw[:, p_:p_ + 1], lnb[:, p_:p_ + 1], ALU.mult, ALU.add).then_inc(*DV.inc("affine"))
                    now("affine")
                    v.tensor_tensor(yt, yt, bonus[h][:, :], ALU.add).then_inc(*DV.inc("bonus"))
                    now("bonus")
                    v.tensor_tensor(oa[:, p_, :], yt, gate[h][:, :], ALU.mult).then_inc(*DV.inc("gate"))


def phase_ssd_post(k, ob):
    nc, io = k.nc, k.io
    GT = KC // SG
    with ExitStack() as ctx:
        sb = lambda n, s: ctx.enter_context(nc.sbuf_tensor(f"so_{n}", s, F32))
        y, x, z = ([sb(f"{n}{i}", [P, T]) for i in range(2)] for n in ("y", "x", "z"))
        sg, sq, rs = sb("sg", [P, T]), sb("sq", [P, T]), sb("rs", [P, T])
        d = sb("d", [P, KC])
        ps = ctx.enter_context(nc.psum_tensor("so_ps", [P, 3, 512], F32))
        pf = flat(ps[:, :, :])
        s_in = [k.sem(f"so_in{i}_loaded") for i in range(2)]
        s_d = k.sem("so_d_loaded")
        s_r = k.sem("so_rstd_step")
        s_n = k.sem("so_scaled")
        PE = Progress(k.sem("so_pe"), "sum")
        AC = Progress(k.sem("so_act"), "sigmoid", "sq")
        DV = Progress(k.sem("so_dve"), "silu", "skip", "gate")
        with nc.Block() as block:
            @block.sync
            def _(sp):
                for h, rows in enumerate(halves()):
                    sp.dma_start(d[rows, :], bc(io["ssm_D"][h:h + 1, :], [64, KC])).then_inc(s_d, 16)
                for i in range(KC):
                    if i >= 2:
                        sp.wait_ge(DV.sem, DV.done("gate", i - 2))
                    for t, src in ((y, io["ssd_y"][i]), (x, io["xbc"][i]), ):
                        sp.dma_start(t[i % 2][:, :], src).then_inc(s_in[i % 2], 16)
                    zsrc = io["proj"][Z0 + i]
                    (_, zp), (_, zs) = predecessor_views(zsrc)
                    op, os = token_views(z[i % 2])
                    sp.dma_start(op, zp).then_inc(s_in[i % 2], 16)
                    sp.dma_start(os, zs).then_inc(s_in[i % 2], 16)

            @block.tensor
            def _(pe):
                for i in range(KC):
                    pe.wait_ge(AC.sem, AC.done("sq", i))
                    if i and i % GT == 0:
                        pe.wait_ge(s_r, 2 * (i // GT))
                    for a, b in TOK_CHUNKS_BANKED:
                        mm = nc.tensor.matmul(pf[:, a:b], k.ones[:, :], sq[:, a:b], start=i % GT == 0, stop=i % GT == GT - 1)
                    mm.then_inc(*PE.inc("sum"))

            @block.scalar
            def _(act):
                for i in range(KC):
                    act.wait_ge(s_in[i % 2], 64 * (i // 2 + 1))
                    if i:
                        act.wait_ge(DV.sem, DV.done("silu", i - 1))
                    nc.scalar.activation(sg[:, :], z[i % 2][:, :], ACT.Sigmoid).then_inc(*AC.inc("sigmoid"))
                    act.wait_ge(DV.sem, DV.done("gate", i))
                    if i:
                        act.wait_ge(PE.sem, PE.done("sum", i - 1))
                    nc.scalar.activation(sq[:, :], ob[:, i, :], ACT.Square).then_inc(*AC.inc("sq"))
                    if i % GT == GT - 1:
                        act.wait_ge(PE.sem, PE.done("sum", i))
                        if i > GT:
                            act.wait_ge(s_n, GT)
                        nc.scalar.activation(rs[:, :], pf[:, 0:T], ACT.Ln, scale=1.0 / (GT * P), bias=k.const[:, 0:1]).then_inc(s_r, 1)
                        act.wait_ge(s_r, 2 * (i // GT) + 1)
                        nc.scalar.activation(rs[:, :], rs[:, :], ACT.Exp, scale=-0.5).then_inc(s_r, 1)

            @block.vector
            def _(dve):
                v = nc.vector
                nw = k.par[:, PCOLS["ssm_norm_w"]]
                dve.wait_ge(s_d, 32)
                for i in range(KC):
                    h = i % 2
                    now = lambda s_: dve.wait_ge(DV.sem, DV.done(s_, i))
                    dve.wait_ge(AC.sem, AC.done("sigmoid", i))
                    v.tensor_tensor(z[h][:, :], z[h][:, :], sg[:, :], ALU.mult).then_inc(*DV.inc("silu"))
                    v.scalar_tensor_tensor(out=y[h][:, :], in0=x[h][:, :], scalar=d[:, i:i + 1], in1=y[h][:, :],
                                           op0=ALU.mult, op1=ALU.add).then_inc(*DV.inc("skip"))
                    now("skip")
                    v.tensor_tensor(ob[:, i, :], y[h][:, :], z[h][:, :], ALU.mult).then_inc(*DV.inc("gate"))
                    if i % GT == GT - 1:
                        dve.wait_ge(s_r, 2 * (i // GT) + 2)
                        now("gate")
                        for j in range(i - GT + 1, i + 1):
                            v.scalar_tensor_tensor(out=ob[:, j, :], in0=ob[:, j, :], scalar=nw[:, j:j + 1], in1=rs[:, :],
                                                   op0=ALU.mult, op1=ALU.mult).then_inc(s_n, 1)


def phase_merge(k, oa, ob, x1):
    nc, io = k.nc, k.io
    with ExitStack() as ctx:
        sb = lambda n, s: ctx.enter_context(nc.sbuf_tensor(f"mg_{n}", s, F32))
        merged = sb("merged", [P, KC, T])
        wa = [sb(f"wa{i}", [P, NPAIR, P]) for i in range(2)]
        wb = [sb(f"wb{i}", [P, KC, P]) for i in range(2)]
        wo = [sb(f"wo{i}", [P, KC, P]) for i in range(2)]
        ga = [sb(f"ga{i}", [P, T]) for i in range(2)]
        gb = [sb(f"gb{i}", [P, T]) for i in range(2)]
        tmp = sb("tmp", [P, T])
        ps = [ctx.enter_context(nc.psum_tensor(f"mg_ps{i}", [P, 3, 512], F32)) for i in range(2)]
        pf = [flat(p_[:, :, :]) for p_ in ps]
        s_w = [k.sem(f"mg_w{i}_loaded") for i in range(2)]
        s_g = [k.sem(f"mg_gates{i}_loaded") for i in range(2)]
        s_wo = [k.sem(f"mg_wo{i}_loaded") for i in range(2)]
        s_x = k.sem("mg_x_loaded")
        s_xs = k.sem("mg_x1_stored")
        PE = Progress(k.sem("mg_pe"), "a", "b")
        AC = Progress(k.sem("mg_act"), "ga", "gb")
        DV = Progress(k.sem("mg_dve"), "a", "b", "sum")
        s_out = k.sem("mg_out_matmul")
        s_res = k.sem("mg_residual_step")

        with nc.Block() as block:
            @block.sync
            def _(sp):
                sp.dma_start(x1[:, :, :], io["xT"]).then_inc(s_x, 16)
                for m in range(KC):
                    h = m % 2
                    if m >= 2:
                        sp.wait_ge(PE.sem, PE.done("b", m - 2))
                    sp.dma_start(wa[h][:, :, :], io["w_pa"][m]).then_inc(s_w[h], 16)
                    sp.dma_start(wb[h][:, :, :], io["w_pb"][m]).then_inc(s_w[h], 16)
                    if m >= 2:
                        sp.wait_ge(DV.sem, DV.done("sum", m - 2))
                    for t, at in ((ga, 0), (gb, KC)):
                        (_, gp), (_, gs) = predecessor_views(io["proj"][GATE0 + at + m])
                        op, os = token_views(t[h])
                        sp.dma_start(op, gp).then_inc(s_g[h], 16)
                        sp.dma_start(os, gs).then_inc(s_g[h], 16)
                for m in range(KC):
                    if m >= 2:
                        sp.wait_ge(s_out, m - 1)
                    sp.dma_start(wo[m % 2][:, :, :], io["w_out"][m]).then_inc(s_wo[m % 2], 16)
                sp.wait_ge(s_res, 3 * KC)
                sp.dma_start(io["x1"], x1[:, :, :]).then_inc(s_xs, 16)
                sp.wait_ge(s_xs, 16)

            @block.tensor
            def _(pe):
                for m in range(KC):
                    h = m % 2
                    pe.wait_ge(s_w[h], 32 * (m // 2 + 1))
                    for out, w, src, n, step in ((pf[0], wa[h], oa, NPAIR, "a"), (pf[1], wb[h], ob, KC, "b")):
                        if m:
                            pe.wait_ge(DV.sem, DV.done(step, m - 1))
                        for kc in range(n):
                            for a, b in TOK_CHUNKS_BANKED:
                                mm = nc.tensor.matmul(out[:, a:b], w[:, kc, :], src[:, kc, a:b], start=kc == 0, stop=kc == n - 1)
                        mm.then_inc(*PE.inc(step))
                pe.wait_ge(DV.sem, DV.done("sum", KC - 1))
                for m in range(KC):
                    pe.wait_ge(s_wo[m % 2], 16 * (m // 2 + 1))
                    if m >= 2:
                        pe.wait_ge(s_res, 3 * (m - 1))
                    for kc in range(KC):
                        for a, b in TOK_CHUNKS_BANKED:
                            mm = nc.tensor.matmul(pf[m % 2][:, a:b], wo[m % 2][:, kc, :], merged[:, kc, a:b], start=kc == 0, stop=kc == KC - 1)
                    mm.then_inc(s_out, 1)

            @block.scalar
            def _(act):
                for m in range(KC):
                    h = m % 2
                    act.wait_ge(s_g[h], 64 * (m // 2 + 1))
                    nc.scalar.activation(ga[h][:, :], ga[h][:, :], ACT.Sigmoid).then_inc(*AC.inc("ga"))
                    nc.scalar.activation(gb[h][:, :], gb[h][:, :], ACT.Sigmoid).then_inc(*AC.inc("gb"))

            @block.vector
            def _(dve):
                v = nc.vector
                for m in range(KC):
                    h = m % 2
                    dve.wait_ge(AC.sem, AC.done("ga", m))
                    dve.wait_ge(PE.sem, PE.done("a", m))
                    v.tensor_tensor(ga[h][:, :], pf[0][:, 0:T], ga[h][:, :], ALU.mult).then_inc(*DV.inc("a"))
                    dve.wait_ge(AC.sem, AC.done("gb", m))
                    dve.wait_ge(PE.sem, PE.done("b", m))
                    v.tensor_tensor(gb[h][:, :], pf[1][:, 0:T], gb[h][:, :], ALU.mult).then_inc(*DV.inc("b"))
                    dve.wait_ge(DV.sem, DV.done("b", m))
                    v.tensor_tensor(merged[:, m, :], ga[h][:, :], gb[h][:, :], ALU.add).then_inc(*DV.inc("sum"))
                dve.wait_ge(s_x, 16)
                for m in range(KC):
                    dve.wait_ge(s_out, m + 1)
                    add_gated(k, dve, x1[:, m, :], pf[m % 2][:, 0:T], tmp, GT1 + m, s_res, 3 * m)


def add_gated(k, dve, x, y, tmp, gate_at, sem, base):
    v = k.nc.vector
    g = k.mod[:, gate_at, :]
    (xp, xs), (yp, ys), (_, ts) = token_views(x), token_views(y), token_views(tmp)
    if base:
        dve.wait_ge(sem, base)
    v.tensor_tensor(ts, ys, bc(g[:, 1:NCOND].unsqueeze(2), [P, NSEQ, DSEQ]), ALU.mult).then_inc(sem, 1)
    v.scalar_tensor_tensor(out=xp, in0=yp, scalar=g[:, 0:1], in1=xp, op0=ALU.mult, op1=ALU.add).then_inc(sem, 1)
    dve.wait_ge(sem, base + 1)
    v.tensor_tensor(xs, xs, ts, ALU.add).then_inc(sem, 1)


def phase_norm2(k, x, load=None):
    rmsnorm_mod(k, "norm2", x, lambda kc: x[:, kc, 0:SEQ], lambda kc: token_views(x[:, kc, :])[1], SC2, SH2, load)


NTILE = -(-T // P)
LAST = T - (NTILE - 1) * P
NEG = -3.0e38


def phase_scores(k, xn2, scores):
    nc, io = k.nc, k.io
    NQ = 2 * PH
    with ExitStack() as ctx:
        sb = lambda n, s: ctx.enter_context(nc.sbuf_tensor(f"sc_{n}", s, F32))
        w = [sb(f"w{i}", [P, KC, P]) for i in range(2)]
        q = [sb(f"q{i}", [P, T]) for i in range(2)]
        keys = sb("keys", [P, NQ, NK])
        psq = ctx.enter_context(nc.psum_tensor("sc_psq", [P, 3, 512], F32))
        pss = ctx.enter_context(nc.psum_tensor("sc_pss", [P, 3, 512], F32))
        pq = flat(psq[:, :, :])
        s_w = [k.sem(f"sc_w{i}_loaded") for i in range(2)]
        s_k = k.sem("sc_keys_loaded")
        s_q = k.sem("sc_query_matmul")
        s_s = k.sem("sc_score_matmul")
        s_qe = k.sem("sc_query_evac")
        s_se = k.sem("sc_score_evac")
        with nc.Block() as block:
            @block.sync
            def _(sp):
                sp.dma_start(keys[:, :, :], io["keysT"]).then_inc(s_k, 16)
                for i in range(NQ):
                    if i >= 2:
                        sp.wait_ge(s_q, i - 1)
                    sp.dma_start(w[i % 2][:, :, :], io["w_q"][i]).then_inc(s_w[i % 2], 16)

            def score(pe, i):
                pe.wait_ge(s_qe, i + 1)
                if i:
                    pe.wait_ge(s_se, i)
                for j in range(NTILE):
                    n = LAST if j == NTILE - 1 else P
                    mm = nc.tensor.matmul(flat(pss[:, :, :])[0:n, j * NK:(j + 1) * NK], q[i % 2][:, j * P:j * P + n],
                                          keys[:, i, :], start=True, stop=True)
                mm.then_inc(s_s, 1)

            @block.tensor
            def _(pe):
                pe.wait_ge(s_k, 16)
                for i in range(NQ):
                    pe.wait_ge(s_w[i % 2], 16 * (i // 2 + 1))
                    if i:
                        pe.wait_ge(s_qe, i)
                    for kc in range(KC):
                        for a, b in TOK_CHUNKS_BANKED:
                            mm = nc.tensor.matmul(pq[:, a:b], w[i % 2][:, kc, :], xn2[:, kc, a:b], start=kc == 0, stop=kc == KC - 1)
                    mm.then_inc(s_q, 1)
                    if i:
                        score(pe, i - 1)
                score(pe, NQ - 1)

            @block.scalar
            def _(act):
                for i in range(NQ):
                    act.wait_ge(s_q, i + 1)
                    if i >= 2:
                        act.wait_ge(s_s, i - 1)
                    nc.scalar.activation(q[i % 2][:, :], pq[:, 0:T], ACT.Copy).then_inc(s_qe, 1)

            @block.vector
            def _(dve):
                v = nc.vector
                full = (NTILE - 1) * NK
                for i in range(NQ):
                    dve.wait_ge(s_s, i + 1)
                    v.tensor_copy(scores[:, 0:NTILE - 1, i, :], flat(pss[:, :, :])[:, 0:full].rearrange("p (j n) -> p j n", n=NK))
                    v.tensor_copy(scores[0:LAST, NTILE - 1, i, :], flat(pss[:, :, :])[0:LAST, full:full + NK]).then_inc(s_se, 1)


def phase_topk(k, scores, selT):
    nc = k.nc
    NQ, K2 = 2 * PH, TOPK * TOPK
    HK = PH * TOPK
    with ExitStack() as ctx:
        sb = lambda n, s, dt=F32: ctx.enter_context(nc.sbuf_tensor(f"tk_{n}", s, dt))
        s1 = [sb(f"s{i}", [P, NQ, NK]) for i in range(2)]
        val = sb("val", [P, NQ, TOPK])
        idx = sb("idx", [P, NQ, TOPK], U32)
        idf = sb("idf", [P, NQ, TOPK])
        cand = sb("cand", [P, PH, K2])
        best = sb("best", [P, PH, TOPK])
        prob = sb("prob", [P, PH, TOPK])
        pos = sb("pos", [P, PH, TOPK], U32)
        ab = sb("ab", [P, 2, HK], U32)
        abf = sb("abf", [P, 2, HK])
        eq = sb("eq", [P, HK, TOPK])
        sel = [sb(f"sel{i}", [P, 3, HK]) for i in range(2)]
        ssum = sb("ssum", [P, PH])
        iota_i = sb("iota_i", [P, TOPK], I32)
        iota = sb("iota", [P, TOPK])
        ps = [ctx.enter_context(nc.psum_tensor(f"tk_ps{i}", [P, 512], F32)) for i in range(2)]
        s_io = k.sem("tk_iota_step")
        AC = Progress(k.sem("tk_act"), "stage", "exp", "sel")
        PE = Progress(k.sem("tk_pe"), "turned")
        DV = Progress(k.sem("tk_dve"), "max1", "idx1", "rep1", "max2", "idx2", "idf", "cand", "cmax1", "cidx1", "crep1",
                      "cmax2", "cidx2", "shift", "abf", "off", "eq0", "pick0", "e0", "eq1", "pick1", "e1", "sum", "rec", "gate")

        def select(dve, v, j, slot, n, done):
            r = slice(0, n)
            sc = s1[slot]
            for i in range(NQ):
                last = v.max(val[r, i, 0:8], sc[r, i, :])
            last.then_inc(*DV.inc("max1"))
            done(DV, "max1")
            for i in range(NQ):
                last = v.max_index(idx[r, i, 0:8], val[r, i, 0:8], sc[r, i, :])
            last.then_inc(*DV.inc("idx1"))
            done(DV, "idx1")
            for i in range(NQ):
                last = v.match_replace(out=sc[r, i, :], in_to_replace=val[r, i, 0:8], in_values=sc[r, i, :], imm_value=NEG)
            last.then_inc(*DV.inc("rep1"))
            done(DV, "rep1")
            for i in range(NQ):
                last = v.max(val[r, i, 8:16], sc[r, i, :])
            last.then_inc(*DV.inc("max2"))
            done(DV, "max2")
            for i in range(NQ):
                last = v.max_index(idx[r, i, 8:16], val[r, i, 8:16], sc[r, i, :])
            last.then_inc(*DV.inc("idx2"))
            done(DV, "idx2")
            v.tensor_copy(idf[r, :, :], idx[r, :, :]).then_inc(*DV.inc("idf"))
            vv = val[r, :, :].rearrange("p (h s) a -> p h s a", s=2)
            v.tensor_tensor(cand[r, :, :].rearrange("p h (a b) -> p h a b", a=TOPK),
                            bc(vv[:, :, 0, :].unsqueeze(3), [n, PH, TOPK, TOPK]),
                            bc(vv[:, :, 1, :].unsqueeze(2), [n, PH, TOPK, TOPK]), ALU.add).then_inc(*DV.inc("cand"))
            done(DV, "cand")
            for h in range(PH):
                last = v.max(best[r, h, 0:8], cand[r, h, :])
            last.then_inc(*DV.inc("cmax1"))
            done(DV, "cmax1")
            for h in range(PH):
                last = v.max_index(pos[r, h, 0:8], best[r, h, 0:8], cand[r, h, :])
            last.then_inc(*DV.inc("cidx1"))
            done(DV, "cidx1")
            for h in range(PH):
                last = v.match_replace(out=cand[r, h, :], in_to_replace=best[r, h, 0:8], in_values=cand[r, h, :], imm_value=NEG)
            last.then_inc(*DV.inc("crep1"))
            done(DV, "crep1")
            for h in range(PH):
                last = v.max(best[r, h, 8:16], cand[r, h, :])
            last.then_inc(*DV.inc("cmax2"))
            done(DV, "cmax2")
            for h in range(PH):
                last = v.max_index(pos[r, h, 8:16], best[r, h, 8:16], cand[r, h, :])
            last.then_inc(*DV.inc("cidx2"))
            done(DV, "cidx2")
            pf = pos[r, :, :].rearrange("p h a -> p (h a)")
            v.tensor_scalar(ab[r, 0, :], pf, 4, None, ALU.logical_shift_right)
            v.tensor_scalar(ab[r, 1, :], pf, TOPK - 1, None, ALU.bitwise_and).then_inc(*DV.inc("shift"))
            done(DV, "shift")
            v.tensor_copy(abf[r, :, :], ab[r, :, :]).then_inc(*DV.inc("abf"))
            v.tensor_tensor(prob[r, :, :], best[r, :, :], bc(best[r, :, 0:1], [n, PH, TOPK]), ALU.subtract).then_inc(*DV.inc("off"))
            done(DV, "abf")
            out = sel[slot]
            idh = idf[r, :, :].rearrange("p (h s) a -> p h s a", s=2)
            for side in range(2):
                v.tensor_tensor(eq[r, :, :], bc(abf[r, side, :].unsqueeze(2), [n, HK, TOPK]),
                                bc(iota[r, :].unsqueeze(1), [n, HK, TOPK]), ALU.is_equal).then_inc(*DV.inc(f"eq{side}"))
                done(DV, f"eq{side}")
                for h in range(PH):
                    e_ = eq[r, TOPK * h:TOPK * h + TOPK, :]
                    last = v.tensor_tensor(e_, e_, bc(idh[:, h, side, :].unsqueeze(1), [n, TOPK, TOPK]), ALU.mult)
                last.then_inc(*DV.inc(f"pick{side}"))
                done(DV, f"pick{side}")
                v.tensor_reduce(out[r, side, :], eq[r, :, :], AX.X, ALU.add).then_inc(*DV.inc(f"e{side}"))
                done(DV, f"e{side}")
            done(AC, "exp")
            v.tensor_reduce(ssum[r, :], prob[r, :, :], AX.X, ALU.add).then_inc(*DV.inc("sum"))
            done(DV, "sum")
            v.reciprocal(ssum[r, :], ssum[r, :]).then_inc(*DV.inc("rec"))
            done(DV, "rec")
            v.tensor_tensor(out[r, 2, :].rearrange("p (h a) -> p h a", h=PH), prob[r, :, :],
                            bc(ssum[r, :].unsqueeze(2), [n, PH, TOPK]), ALU.mult).then_inc(*DV.inc("gate"))

        FULL = NTILE - 1

        def tiles(eng, body):
            with eng.Fori(0, FULL // 2) as r:
                for h in range(2):
                    body(2 * r + h, h, P)
            body(FULL, 0, LAST)

        with nc.Block() as block:
            @block.gpsimd
            def _(pool):
                nc.gpsimd.iota(iota_i[:, :], [[1, TOPK]], base=0, channel_multiplier=0).then_inc(s_io, 1)
                pool.wait_ge(s_io, 1)
                nc.gpsimd.tensor_copy(iota[:, :], iota_i[:, :]).then_inc(s_io, 1)

            @block.scalar
            def _(act):
                AC.credit(act)

                def body(j, slot, n):
                    act.wait_ge(DV.sem, DV.before("idx2", j))
                    src = scores[0:n, bass.ds(j, 1), :, :].rearrange("p a i n -> p (a i) n")
                    nc.scalar.activation(s1[slot][0:n, :, :], src, ACT.Copy).then_inc(*AC.inc("stage"))
                    act.wait_ge(DV.sem, DV.now("off", j))
                    nc.scalar.activation(prob[0:n, :, :], prob[0:n, :, :], ACT.Exp).then_inc(*AC.inc("exp"))
                    act.wait_ge(PE.sem, PE.now("turned", j))
                    at = j * P
                    dst = selT[:, :, at:at + n] if isinstance(j, int) else selT[:, :, bass.ds(at, n)]
                    nc.scalar.activation(dst, ps[slot][:, 0:3 * P].rearrange("p (q t) -> p q t", q=3)[:, :, 0:n],
                                         ACT.Copy).then_inc(*AC.inc("sel"))
                tiles(act, body)

            @block.tensor
            def _(pe):
                PE.credit(pe)

                def body(j, slot, n):
                    pe.wait_ge(DV.sem, DV.now("gate", j))
                    pe.wait_ge(AC.sem, AC.before("sel", j))
                    for i in range(3):
                        mm = nc.tensor.transpose(ps[slot][:, i * P:i * P + n], sel[slot][0:n, i, :], k.ident[0:n, 0:n])
                    mm.then_inc(*PE.inc("turned"))
                tiles(pe, body)

            @block.vector
            def _(dve):
                DV.credit(dve)
                two = dve.alloc_register("tk_two")
                dve.reg_mov(two, 2)

                def body(j, slot, n):
                    dve.wait_ge(AC.sem, AC.now("stage", j))
                    dve.wait_ge(PE.sem, PE.before("turned", j))

                    def done(S_, step):
                        dve.wait_ge(S_.sem, S_.now(step, j))
                        dve.reg_alu(two, two, 2, ALU.max)
                    dve.wait_ge(s_io, two)
                    dve.reg_alu(two, two, 2, ALU.max)
                    select(dve, nc.vector, j, slot, n, done)
                tiles(dve, body)


TB = 64
NTB = T // TB
BATCH = 4


def phase_spread(k, selT):
    nc, io = k.nc, k.io
    RING = 4 * BATCH
    NB = TB // BATCH
    with ExitStack() as ctx:
        sb = lambda n, s, dt=F32: ctx.enter_context(nc.sbuf_tensor(f"wt_{n}", s, dt))
        iota_i = sb("iota_i", [P, NK], I32)
        iota = sb("iota", [P, NK])
        one1 = sb("one1", [P, RING, NK])
        one2 = sb("one2", [P, RING, NK])
        stage = sb("stage", [P, 2, NK, TB])
        here = sb("here", [P, 3, TB])
        ps = ctx.enter_context(nc.psum_tensor("wt_ps", [P, 8, BATCH, NK], F32))
        s_io = k.sem("wt_iota_step")
        s_here = k.sem("wt_columns_staged")
        s_st = [k.sem(f"wt_stored{i}") for i in range(2)]
        batches = [f"batch{n}" for n in range(NB)]
        OH = Progress(k.sem("wt_onehots"), *batches)
        PE = Progress(k.sem("wt_matmul"), *batches)
        EV = Progress(k.sem("wt_evac"), *batches)

        def blocks(eng, body):
            with eng.Fori(0, NTB // 2) as r:
                for h in range(2):
                    body(2 * r + h, h, r)
            body(NTB - 1, 0, NTB // 2)

        with nc.Block() as block:
            @block.gpsimd
            def _(pool):
                nc.gpsimd.iota(iota_i[:, :], [[1, NK]], base=0, channel_multiplier=0).then_inc(s_io, 1)
                pool.wait_ge(s_io, 1)
                nc.gpsimd.tensor_copy(iota[:, :], iota_i[:, :]).then_inc(s_io, 1)

            @block.sync
            def _(sp):
                def body(b, slot, r):
                    sp.wait_ge(EV.sem, EV.now(batches[-1], b))
                    sp.dma_start(io["weights"][b].rearrange("e f t -> e (f t)"),
                                 stage[:, slot, :, :].rearrange("p f t -> p (f t)")).then_inc(s_st[slot], 16)
                blocks(sp, body)
                sp.wait_ge(s_st[0], 16 * (NTB // 2 + 1))
                sp.wait_ge(s_st[1], 16 * (NTB // 2))

            @block.vector
            def _(dve):
                v = nc.vector
                OH.credit(dve)
                dve.wait_ge(s_io, 2)

                def body(b, slot, r):
                    dve.wait_ge(OH.sem, OH.before(batches[-1], b))
                    cols = selT[:, :, b * TB:b * TB + TB] if isinstance(b, int) else selT[:, :, bass.ds(b * TB, TB)]
                    v.tensor_copy(here[:, :, :], cols).then_inc(s_here, 1)
                    dve.wait_ge(s_here, b + 1)
                    for n in range(NB):
                        dve.wait_ge(PE.sem, PE.back(n, 4, b))
                        for t in range(n * BATCH, (n + 1) * BATCH):
                            at = t % RING
                            v.tensor_scalar(one1[:, at, :], iota[:, :], here[:, 0, t:t + 1], None, ALU.is_equal)
                            last = v.tensor_scalar(one2[:, at, :], iota[:, :], here[:, 1, t:t + 1], here[:, 2, t:t + 1],
                                                   ALU.is_equal, ALU.mult)
                        last.then_inc(*OH.inc(batches[n]))
                blocks(dve, body)

            @block.tensor
            def _(pe):
                PE.credit(pe)

                def body(b, slot, r):
                    for n in range(NB):
                        pe.wait_ge(OH.sem, OH.now(batches[n], b))
                        pe.wait_ge(EV.sem, EV.back(n, 8, b))
                        for t in range(n * BATCH, (n + 1) * BATCH):
                            mm = nc.tensor.matmul(ps[:, n % 8, t % BATCH, :], one2[:, t % RING, :], one1[:, t % RING, :],
                                                  start=True, stop=True)
                        mm.then_inc(*PE.inc(batches[n]))
                blocks(pe, body)

            @block.scalar
            def _(act):
                EV.credit(act)

                def body(b, slot, r):
                    act.wait_ge(s_st[slot], 16 * r)
                    for n in range(NB):
                        act.wait_ge(PE.sem, PE.now(batches[n], b))
                        dst = stage[:, slot, :, n * BATCH:(n + 1) * BATCH].rearrange("p f t -> p t f")
                        nc.scalar.activation(dst, ps[:, n % 8, :, :], ACT.Copy).then_inc(*EV.inc(batches[n]))
                blocks(act, body)


EG = 4
NG = NK // EG
NOUT = KC * len(TOK_CHUNKS)


def phase_experts(k, xn2, acc):
    nc, io = k.nc, k.io
    NC = len(TOK_CHUNKS)
    NJ = EG * NC
    with ExitStack() as ctx:
        sb = lambda n, s: ctx.enter_context(nc.sbuf_tensor(f"ex_{n}", s, F32))
        u = [sb(f"u{i}", [P, KC, P]) for i in range(EG)]
        vt = [sb(f"v{i}", [P, EG, D]) for i in range(2)]
        g = [sb(f"g{i}", [P, NTB, EG, TB]) for i in range(2)]
        w = [sb(f"w{i}", [P, EG, T]) for i in range(2)]
        psa = [ctx.enter_context(nc.psum_tensor(f"ex_psa{i}", [P, 512], F32)) for i in range(2)]
        pso = [ctx.enter_context(nc.psum_tensor(f"ex_pso{i}", [P, 512], F32)) for i in range(6)]
        s_u = [k.sem(f"ex_u{i}_loaded") for i in range(EG)]
        s_v = [k.sem(f"ex_v{i}_loaded") for i in range(2)]
        s_g = [k.sem(f"ex_g{i}_loaded") for i in range(2)]
        s_zero = k.sem("ex_acc_zeroed")
        jobs = [f"u{j}" for j in range(NJ)]
        outs = [f"v{n}" for n in range(NOUT)]
        PU = Progress(k.sem("ex_u_products"), *jobs)
        GE = Progress(k.sem("ex_gelu"), *jobs)
        MU = Progress(k.sem("ex_weighted"), *[f"e{i}" for i in range(EG)])
        PV = Progress(k.sem("ex_v_products"), *outs)
        AD = Progress(k.sem("ex_added"), *outs)
        R = NG // 2 - 1

        def schedule(eng, first, both, last):
            first((0, 0, 0))
            with eng.Fori(0, R) as r:
                both((2 * r + 1, 1, r), (2 * r, 0, r))
                both((2 * r + 2, 0, r + 1), (2 * r + 1, 1, r))
            both((NG - 1, 1, R), (NG - 2, 0, R))
            last((NG - 1, 1, R))

        with nc.Block() as block:
            @block.sync
            def _(sp):
                def load(ug, wait=True):
                    grp, _, _ = ug
                    for i in range(EG):
                        if wait:
                            sp.wait_ge(PU.sem, PU.before(jobs[NC * i + NC - 1], grp))
                        sp.dma_start(u[i][:, :, :], io["u"][grp * EG + i]).then_inc(s_u[i], 16)

                schedule(sp, lambda ug: load(ug, False), lambda ug, vg: load(ug), lambda vg: None)

            @block.gpsimd
            def _(pool):
                def load(grp, par, wait):
                    sl = slice(grp * EG, grp * EG + EG) if isinstance(grp, int) else bass.ds(grp * EG, EG)
                    if wait:
                        pool.wait_ge(MU.sem, MU.before(f"e{EG - 1}", grp - 1))
                    pool.dma_start(g[par][:, :, :, :].rearrange("p b e t -> p b (e t)"),
                                   io["weights"][:, :, sl, :].rearrange("b p e t -> p b (e t)")).then_inc(s_g[par], 16)
                    if wait:
                        pool.wait_ge(PV.sem, PV.before(outs[-1], grp - 1))
                    pool.dma_start(vt[par][:, :, :], io["v"][sl].rearrange("e p d -> p e d")).then_inc(s_v[par], 16)

                load(0, 0, False)
                load(1, 1, False)
                with pool.Fori(0, R) as r:
                    load(2 * r + 2, 0, True)
                    load(2 * r + 3, 1, True)

            @block.tensor
            def _(pe):
                def u_job(ug, j):
                    grp, _, _ = ug
                    i, c = divmod(j, NC)
                    if c == 0:
                        pe.wait_ge(s_u[i], 16 * grp + 16)
                    pe.wait_ge(GE.sem, GE.back(j, 2, grp))
                    a, b = TOK_CHUNKS[c]
                    for kc in range(KC):
                        mm = nc.tensor.matmul(psa[j % 2][:, 0:b - a], u[i][:, kc, :], xn2[:, kc, a:b],
                                              start=kc == 0, stop=kc == KC - 1)
                    mm.then_inc(*PU.inc(jobs[j]))

                def v_job(vg, n):
                    grp, par, number = vg
                    dc, c = divmod(n, NC)
                    if n == 0:
                        pe.wait_ge(s_v[par], 16 * number + 16)
                        pe.wait_ge(MU.sem, MU.now(f"e{EG - 1}", grp))
                    pe.wait_ge(AD.sem, AD.back(n, 6, grp))
                    a, b = TOK_CHUNKS[c]
                    for i in range(EG):
                        mm = nc.tensor.matmul(pso[n % 6][:, 0:b - a], vt[par][:, i, dc * P:(dc + 1) * P], w[par][:, i, a:b],
                                              start=i == 0, stop=i == EG - 1)
                    mm.then_inc(*PV.inc(outs[n]))

                def both(ug, vg):
                    for j in range(NJ):
                        u_job(ug, j)
                        v_job(vg, 2 * j)
                        v_job(vg, 2 * j + 1)

                PU.credit(pe)
                PV.credit(pe)
                schedule(pe, lambda ug: [u_job(ug, j) for j in range(NJ)], both, lambda vg: [v_job(vg, n) for n in range(NOUT)])

            @block.scalar
            def _(act):
                def gelus(ug):
                    grp, par, _ = ug
                    for j in range(NJ):
                        i, c = divmod(j, NC)
                        a, b = TOK_CHUNKS[c]
                        act.wait_ge(PU.sem, PU.now(jobs[j], grp))
                        nc.scalar.activation(w[par][:, i, a:b], psa[j % 2][:, 0:b - a], ACT.Gelu).then_inc(*GE.inc(jobs[j]))

                GE.credit(act)
                schedule(act, gelus, lambda ug, vg: gelus(ug), lambda vg: None)

            @block.vector
            def _(dve):
                v = nc.vector

                def weigh(ug, i):
                    grp, par, number = ug
                    if i == 0:
                        dve.wait_ge(s_g[par], 16 * number + 16)
                    dve.wait_ge(GE.sem, GE.now(jobs[NC * i + NC - 1], grp))
                    wv = w[par][:, i, :].rearrange("p (b t) -> p b t", t=TB)
                    v.tensor_tensor(wv, wv, g[par][:, :, i, :], ALU.mult).then_inc(*MU.inc(f"e{i}"))

                def add(vg, n):
                    grp, _, _ = vg
                    dc, c = divmod(n, NC)
                    a, b = TOK_CHUNKS[c]
                    dve.wait_ge(PV.sem, PV.now(outs[n], grp))
                    dve.wait_ge(AD.sem, AD.before(outs[n], grp))
                    v.tensor_tensor(acc[:, dc, a:b], pso[n % 6][:, 0:b - a], acc[:, dc, a:b], ALU.add).then_inc(*AD.inc(outs[n]))

                def both(ug, vg):
                    for j in range(NJ):
                        if j and j % NC == 0:
                            weigh(ug, j // NC - 1)
                        add(vg, 2 * j)
                        add(vg, 2 * j + 1)
                    weigh(ug, EG - 1)

                MU.credit(dve)
                AD.credit(dve)
                v.memset(acc[:, :, :], 0.0).then_inc(s_zero, 1)
                dve.wait_ge(s_zero, 1)
                schedule(dve, lambda ug: [weigh(ug, i) for i in range(EG)], both, lambda vg: [add(vg, n) for n in range(NOUT)])


def phase_final(k, acc):
    nc, io = k.nc, k.io
    with nc.sbuf_tensor("fin_x", [P, KC, T], F32) as x, nc.sbuf_tensor("fin_tmp", [P, T], F32) as tmp:
        s_x = k.sem("fin_x1_loaded")
        s_res = k.sem("fin_residual_step")
        with nc.Block() as block:
            @block.sync
            def _(sp):
                sp.dma_start(x[:, :, :], io["x1"]).then_inc(s_x, 16)

            @block.vector
            def _(dve):
                dve.wait_ge(s_x, 16)
                for m in range(KC):
                    add_gated(k, dve, x[:, m, :], acc[:, m, :], tmp, GT2 + m, s_res, 3 * m)

        def store(sp, sem):
            sp.dma_start(io["y_out"], acc[:, :, :]).then_inc(sem, 16)
            return 16

        rmsnorm_mod(k, "final", x, lambda kc: acc[:, kc, 0:SEQ], lambda kc: token_views(acc[:, kc, :])[1],
                    SCF, SHF, None, store)


def program(nc, io):
    with ExitStack() as ctx:
        k = Core(nc, ctx, io)
        for name, shape in (("proj", (PROJ_TILES + 1, P, TX)), ("rwc", (NCH + 1, P, 5, NPAIR, CL)),
                            ("rw_gate", (NPAIR, P, T)), ("rw_bonus", (NPAIR, P, T)), ("rw_y", (NCH + 1, P, NPAIR, CL)),
                            ("xbc", (NXBC, P, T)), ("ssd_rows", (SH, 3, T)), ("ssd_y", (KC, P, T)), ("x1", (P, KC, T)),
                            ("weights", (NTB, NK, NK, TB))):
            io[name] = nc.dram_tensor(name, shape, F32, kind="Internal").ap()
        k.par = k.lasting("par", [P, NPAR])
        k.mod = k.lasting("mod", [P, 64, NCOND])
        k.ident = k.lasting("ident", [P, P])
        k.ones = k.lasting("ones", [P, P])
        k.pairones = k.lasting("pairones", [P, P])
        k.const = k.lasting("const", [P, 4])
        k.shift_sb = k.lasting("shift_sb", [P, KC, NSEQ])
        k.lam_end = k.lasting("lam_end", [P, NPAIR, NCH + NSEQ])
        k.mt_mask = k.lasting("mt_mask", [P, 2, 4, CL])
        k.lv_mask = k.lasting("lv_mask", [P, LEVELS, 2, CL])
        k.ident2 = k.lasting("ident2", [P, 2, CL])
        k.seq_cols = k.lasting("seq_cols", [P, NSEQ, CL])
        k.seq_rows = k.lasting("seq_rows", [P, NSEQ])
        k.ssd_mask = k.lasting("ssd_mask", [P, SL])
        k.ssd_mask_smp = k.lasting("ssd_mask_smp", [CL, CL])
        k.head_sel = k.lasting("head_sel", [SH, SH, P])
        phase_ada(k)
        with nc.sbuf_tensor("xe", [P, KC, TX], F32) as xe:
            phase_norm1(k, xe)
            phase_proj(k, xe)
        phase_masks(k)
        phase_rw_pre(k)
        phase_rw_prompt(k)
        phase_rw_samples(k)
        phase_ssd_pre(k)
        phase_ssd(k)
        k.recycle_semaphores()
        with nc.sbuf_tensor("x1_sb", [P, KC, T], F32) as xn2:
            with nc.sbuf_tensor("oa", [P, NPAIR, T], F32) as oa, nc.sbuf_tensor("ob", [P, KC, T], F32) as ob:
                phase_rw_post(k, oa)
                phase_ssd_post(k, ob)
                phase_merge(k, oa, ob, xn2)
            phase_norm2(k, xn2)
            with nc.sbuf_tensor("selT", [P, 3, T], F32) as selT:
                with nc.sbuf_tensor("scores", [P, NTILE, 2 * PH, NK], F32) as scores:
                    phase_scores(k, xn2, scores)
                    phase_topk(k, scores, selT)
                phase_spread(k, selT)
            with nc.sbuf_tensor("acc", [P, KC, T], F32) as acc:
                phase_experts(k, xn2, acc)
                phase_final(k, acc)


def _rows(a, tiles):
    return np.ascontiguousarray(a.reshape(tiles, P, -1).transpose(1, 0, 2))


def _cols(v):
    return v.reshape(-1, P).T


def _weight(a):
    kk, m = a.shape
    return np.ascontiguousarray(a.reshape(kk // P, P, m // P, P).transpose(2, 1, 0, 3))


def _arrays(x):
    f = lambda n: np.asarray(x[n])
    out = {}
    toks = np.concatenate([f("x_prompt").reshape(SEQ, D), f("x_sample").reshape(NSEQ * DSEQ, D)])
    out["xT"] = _rows(toks.T, KC)
    out["cT"] = _rows(np.concatenate([f("c_prompt"), f("c_sample")]).T, KC)
    out["shiftT"] = _rows(f("state_shift")[0].T, KC)
    wa = np.concatenate([f("w_ada")[0], f("w_ada_f")], axis=1)
    out["w_ada"] = np.ascontiguousarray(wa.reshape(KC, P, 16, 512).transpose(2, 1, 0, 3))
    cw = f("ssm_conv_w")[0].reshape(CONVK, NXBC, P).transpose(2, 0, 1).reshape(P, CONVK * NXBC)
    mu = f("rw_mu")[0]
    out["params"] = np.ascontiguousarray(np.concatenate(
        [_cols(f("b_ada")[0]), _cols(f("b_ada_f")), _cols(f("norm1_g")[0]), _cols(f("norm2_g")[0]), _cols(f("final_g")),
         _cols(mu[3 * RDIM:]), cw, _cols(f("ssm_conv_b")[0]), _cols(f("ssm_norm_w")[0]),
         _cols(f("rw_ln_w")[0]), _cols(f("rw_ln_b")[0])], axis=1))
    r3 = [mu[0:RDIM], mu[RDIM:2 * RDIM], mu[2 * RDIM:3 * RDIM], f("rw_w0")[0], f("rw_a0")[0], f("rw_k_k")[0],
          f("rw_k_a")[0], f("rw_r_k")[0].reshape(-1)]
    out["rw_params"] = np.ascontiguousarray(np.stack([v.reshape(NPAIR, P) for v in r3], axis=2))
    wi = f("w_in")[0]
    ssm0 = RW_TILES * P
    dt0 = ssm0 + D + NXBC * P
    main = np.concatenate([wi[:, :dt0], wi[:, dt0 + SH:]], axis=1)
    out["w_in"] = _weight(main)
    out["w_dt"] = _rows(wi[:, dt0:dt0 + SH], KC)
    out["lora_w"] = np.ascontiguousarray(np.stack(
        [np.concatenate([f("rw_w2")[0], f("rw_a2")[0]]), f("rw_g2")[0]]).reshape(2, P, NPAIR, P).transpose(2, 1, 0, 3))
    out["head_params"] = np.ascontiguousarray(np.stack([f("ssm_dt_bias")[0], f("ssm_A_log")[0]], axis=1))
    out["ssm_D"] = np.ascontiguousarray(f("ssm_D")[0].reshape(KC, 2).T)
    sw = f("state_wkv")[0].reshape(NSEQ, NPAIR, 2, RD, RD)
    out["wkvT"] = np.ascontiguousarray(sw.transpose(0, 2, 4, 1, 3).reshape(NSEQ, P, NPAIR, RD))
    out["convT"] = _rows(f("state_conv")[0].transpose(2, 0, 1).reshape(NXBC * P, -1), NXBC).reshape(P, NXBC, NSEQ, CONVK - 1)
    out["ssmT"] = np.ascontiguousarray(f("state_ssm")[0].transpose(0, 3, 1, 2).reshape(NSEQ, SN, SH * SD))
    out["w_pa"] = _weight(f("w_pa")[0])
    out["w_pb"] = _weight(f("w_pb")[0])
    out["w_out"] = _weight(f("w_out")[0])
    out["w_q"] = _weight(f("peer_wq")[0])
    out["keysT"] = np.ascontiguousarray(f("peer_keys")[0].reshape(2 * PH, NK, P).transpose(2, 0, 1))
    out["u"] = np.ascontiguousarray(f("peer_u")[0].reshape(NK, NK, KC, P).transpose(0, 3, 2, 1))
    out["v"] = np.ascontiguousarray(f("peer_v")[0].reshape(NK, NK, D))
    return out


_OUTS = {"shift_out": (P, KC, NCOND), "y_out": (P, KC, T), "wkv_out": (NCOND, P, NPAIR, RD),
         "conv_out": (P, NXBC, NCOND, CONVK - 1), "ssm_out": (NCOND, SN, SH * SD)}


def kernel(**inputs):
    import numpy as _np
    import concourse.bacc as _bacc
    from concourse import mybir as _mybir
    from concourse.bass_utils import run_bass_kernel_spmd as _run

    nc = _bacc.Bacc("TRN2", target_bir_lowering=False, num_devices=1)
    arrays, io = {}, {}
    for name, a in _arrays(inputs).items():
        arrays["in_" + name] = a
        io[name] = nc.dram_tensor("in_" + name, a.shape, _mybir.dt.from_np(a.dtype), kind="ExternalInput").ap()
    for name, shape in _OUTS.items():
        io[name] = nc.dram_tensor("out_" + name, shape, F32, kind="ExternalOutput").ap()
    program(nc, io)
    r = _run(nc, [arrays], core_ids=[0])
    got = {n: r.results[0]["out_" + n] for n in _OUTS}

    unrow = lambda a: a.transpose(1, 0, 2).reshape(-1, a.shape[2])
    y = unrow(got["y_out"]).T
    shift = unrow(got["shift_out"]).T
    wkv = got["wkv_out"].reshape(NCOND, 2, RD, NPAIR, RD).transpose(0, 3, 1, 4, 2).reshape(NCOND, RH, RD, RD)
    conv = unrow(got["conv_out"].reshape(P, NXBC, NCOND * (CONVK - 1))).reshape(-1, NCOND, CONVK - 1).transpose(1, 2, 0)
    ssm = got["ssm_out"].reshape(NCOND, SN, SH, SD).transpose(0, 2, 3, 1)
    c = _np.ascontiguousarray
    return (c(y[:SEQ].reshape(1, SEQ, D)), c(y[SEQ:].reshape(NSEQ, DSEQ, D)),
            c(shift[None, 0:1]), c(wkv[None, 0:1]), c(conv[None, 0:1]), c(ssm[None, 0:1]),
            c(shift[None, 1:]), c(wkv[None, 1:]), c(conv[None, 1:]), c(ssm[None, 1:]))
```

```python
from contextlib import ExitStack

import numpy as np
import concourse.bass as bass
from concourse import mybir

F32 = mybir.dt.float32
I32 = mybir.dt.int32
U32 = mybir.dt.uint32
ALU = mybir.AluOpType
ACT = mybir.ActivationFunctionType
AX = mybir.AxisListType

P = 128
D = 1024
KC = D // P
SEQ = 1024
NSEQ, DSEQ = 8, 8
T = SEQ + NSEQ * DSEQ
TX = 1 + SEQ + NSEQ * (DSEQ + 1)
NCOND = 1 + NSEQ
RH, RD = 8, 64
RDIM = RH * RD
NPAIR = RDIM // P
SH, SD, SG, SN = 16, 64, 2, 128
NXBC = 12
CONVK = 4
EXP_NEG_HALF = float(np.exp(-0.5))
RW_TILES = 14
PROJ_TILES = 50
XBC_TILES = 12
XBC0, RW0, Z0, GATE0, DT0 = 0, 12, 26, 34, 50
CL = 64
NCH = SEQ // CL
SL = 128
NSC = SEQ // SL
LEVELS = 6
PH, NK, TOPK = 8, 128, 16
NORM_EPS = 1e-6
LN_EPS = 64e-5
LN_SCALE = 2.0 ** 30

PCOLS = {}
_at = 0
for _name, _n in (("b_ada", 64), ("norm1_g", 8), ("norm2_g", 8), ("final_g", 8), ("mu_lora", 2),
                  ("conv_w", 48), ("conv_b", 12), ("ssm_norm_w", 8), ("ln_w", 4), ("ln_b", 4)):
    PCOLS[_name] = slice(_at, _at + _n)
    _at += _n
NPAR = _at
RWP_MU, RWP_W0, RWP_A0, RWP_KK, RWP_KA, RWP_RK = 0, 3, 4, 5, 6, 7
SH1, SC1, GT1, SH2, SC2, GT2, SHF, SCF = (8 * i for i in range(8))
EXT_CHUNKS = ((0, 512), (512, 1024), (1024, TX))
TOK_CHUNKS = ((0, 364), (364, 728), (728, T))
TOK_CHUNKS_BANKED = ((0, 512), (512, 1024), (1024, T))


class Progress:

    def __init__(self, sem, *steps):
        self.sem, self.steps, self.n = sem, list(steps), len(steps)
        assert len(set(steps)) == len(steps), steps
        self.next = 0

    def inc(self, step):
        assert self.steps[self.next % self.n] == step, (self.steps[self.next % self.n], step)
        self.next += 1
        return self.sem, 1

    def done(self, step, rounds=0):
        return rounds * self.n + self.steps.index(step) + 1

    def credit(self, eng):
        eng.sem_inc(self.sem, self.n)

    def now(self, step, r):
        return r * self.n + (self.n + self.steps.index(step) + 1)

    def before(self, step, r):
        return r * self.n + (self.steps.index(step) + 1)

    def back(self, n, m, r):
        return self.now(self.steps[n - m], r) if n >= m else self.before(self.steps[n - m], r)


def bc(ap, shape):
    return ap.broadcast_to(shape)


def flat(ap):
    return ap.rearrange("p a b -> p (a b)")


class Core:

    def __init__(self, nc, ctx, io):
        self.nc, self.ctx, self.io, self.sems = nc, ctx, io, []

    def sem(self, name):
        self.sems.append(self.nc.alloc_semaphore(name=name))
        return self.sems[-1]

    def recycle_semaphores(self):
        self.nc.all_engine_barrier()
        self.nc.clear_and_free_semaphores(self.sems)
        self.nc.all_engine_barrier()
        self.sems = []

    def lasting(self, name, shape, dt=F32):
        return self.ctx.enter_context(self.nc.sbuf_tensor(name, shape, dt))


ADA_FIRST = 16
ADA_STEP = (64 - ADA_FIRST) // NCH


def scale_gain(k, at, g):
    return k.nc.vector.scalar_tensor_tensor(out=k.mod[:, at:at + 8, :], in0=k.mod[:, at:at + 8, :], scalar=1.0,
                                            in1=bc(k.par[:, PCOLS[g]].unsqueeze(2), [P, 8, NCOND]),
                                            op0=ALU.add, op1=ALU.mult)


def phase_ada(k):
    nc, io = k.nc, k.io
    with ExitStack() as ctx:
        sb = lambda n, s, dt=F32: ctx.enter_context(nc.sbuf_tensor(n, s, dt))
        cT = k.cT
        ce = sb("ce", [P, KC, NCOND])
        w = [sb(f"ada_w{i}", [P, KC, 512]) for i in range(3)]
        ps = [ctx.enter_context(nc.psum_tensor(f"ada_ps{i}", [P, 512], F32)) for i in range(2)]
        s_c = k.sem("cond_loaded")
        s_par = k.sem("params_loaded")
        s_w = [k.sem(f"ada_w{i}_loaded") for i in range(3)]
        s_exp = k.sem("cond_exp_done")
        s_silu = k.sem("cond_silu_step")
        s_mm = k.sem("ada_matmul_done")
        s_mod = k.sem("ada_mod_done")
        s_const = k.sem("const_step")
        G = ADA_FIRST // 4

        with nc.Block() as block:
            @block.sync
            def _(sp):
                sp.dma_start(cT[:, :, :], io["cT"]).then_inc(s_c, 16)
                sp.dma_start(k.par[:, :], io["params"]).then_inc(s_par, 16)
                for g in range(G):
                    if g >= 3:
                        sp.wait_ge(s_mm, g - 2)
                    sp.dma_start(w[g % 3][:, :, :], io["w_ada"][g]).then_inc(s_w[g % 3], 16)

            @block.scalar
            def _(act):
                act.wait_ge(s_c, 16)
                nc.scalar.activation(ce[:, :, :], cT[:, :, :], ACT.Exp, scale=-1.0).then_inc(s_exp, 1)

            @block.gpsimd
            def _(pool):
                nc.gpsimd.memset(k.ident[:, :], 0.0).then_inc(s_const, 1)
                nc.gpsimd.memset(k.ones[:, :], 1.0).then_inc(s_const, 1)
                nc.gpsimd.memset(k.pairones[:, :], 0.0).then_inc(s_const, 1)
                nc.gpsimd.memset(k.const[:, 0:1], NORM_EPS).then_inc(s_const, 1)
                nc.gpsimd.memset(k.const[:, 1:2], LN_EPS).then_inc(s_const, 1)
                nc.gpsimd.memset(k.const[:, 2:3], 1.0).then_inc(s_const, 1)
                pool.wait_ge(s_const, 6)
                nc.gpsimd.affine_select(out=k.ident[:, :], in_=k.ident[:, :], compare_op=ALU.not_equal, fill=1.0,
                                        base=0, pattern=[[-1, P]], channel_multiplier=1).then_inc(s_const, 1)
                pool.wait_ge(s_const, 7)
                nc.gpsimd.memset(k.pairones[0:64, 0:64], 1.0).then_inc(s_const, 1)
                pool.wait_ge(s_const, 8)
                nc.gpsimd.memset(k.pairones[64:128, 64:128], 1.0).then_inc(s_const, 1)

            @block.tensor
            def _(pe):
                pe.wait_ge(s_silu, 3)
                for g in range(G):
                    pe.wait_ge(s_w[g % 3], 16 * (g // 3 + 1))
                    if g >= 2:
                        pe.wait_ge(s_mod, g - 1)
                    for m in range(4):
                        for kc in range(KC):
                            mm = nc.tensor.matmul(ps[g % 2][:, m * NCOND:(m + 1) * NCOND],
                                                  w[g % 3][:, kc, m * P:(m + 1) * P], cT[:, kc, :],
                                                  start=kc == 0, stop=kc == KC - 1)
                    mm.then_inc(s_mm, 1)

            @block.vector
            def _(dve):
                dve.wait_ge(s_exp, 1)
                nc.vector.tensor_scalar(ce[:, :, :], ce[:, :, :], 1.0, None, ALU.add).then_inc(s_silu, 1)
                dve.wait_ge(s_silu, 1)
                nc.vector.reciprocal(ce[:, :, :], ce[:, :, :]).then_inc(s_silu, 1)
                dve.wait_ge(s_silu, 2)
                nc.vector.tensor_tensor(cT[:, :, :], cT[:, :, :], ce[:, :, :], ALU.mult).then_inc(s_silu, 1)
                dve.wait_ge(s_par, 16)
                for g in range(G):
                    dve.wait_ge(s_mm, g + 1)
                    nc.vector.tensor_tensor(k.mod[:, 4 * g:4 * g + 4, :],
                                            ps[g % 2][:, 0:4 * NCOND].rearrange("p (m c) -> p m c", m=4),
                                            bc(k.par[:, 4 * g:4 * g + 4].unsqueeze(2), [P, 4, NCOND]),
                                            ALU.add).then_inc(s_mod, 1)
                dve.wait_ge(s_mod, G)
                scale_gain(k, SC1, "norm1_g").then_inc(s_mod, 1)


def rmsnorm_mod(k, tag, x, out_prompt, out_sample, scale_at, shift_at, load=None, store=None):
    nc = k.nc
    with ExitStack() as ctx:
        sb = lambda n, s, dt=F32: ctx.enter_context(nc.sbuf_tensor(f"{tag}_{n}", s, dt))
        sq = sb("sq", [P, 2, T])
        rstd = sb("rstd", [P, T])
        xr = sb("xr", [P, 2, T])
        ps = ctx.enter_context(nc.psum_tensor(f"{tag}_ps", [P, 3, 512], F32))
        pf = flat(ps[:, :, :])
        s_x = k.sem(f"{tag}_x_loaded")
        s_sq = k.sem(f"{tag}_square_done")
        s_sum = k.sem(f"{tag}_sum_step")
        s_r = k.sem(f"{tag}_rstd_step")
        s_o = k.sem(f"{tag}_out_step")
        s_st = k.sem(f"{tag}_stored")
        need = [0]
        with nc.Block() as block:
            @block.sync
            def _(sp):
                if load:
                    need[0] = load(sp, s_x)
                if store:
                    sp.wait_ge(s_o, 4 * KC)
                    n = store(sp, s_st)
                    sp.wait_ge(s_st, n)

            @block.scalar
            def _(act):
                if need[0]:
                    act.wait_ge(s_x, need[0])
                for kc in range(KC):
                    if kc >= 2:
                        act.wait_ge(s_sum, kc - 1)
                    nc.scalar.activation(sq[:, kc % 2, :], x[:, kc, :], ACT.Square).then_inc(s_sq, 1)
                act.wait_ge(s_sum, KC)
                nc.scalar.activation(rstd[:, :], pf[:, 0:T], ACT.Ln, scale=1.0 / D, bias=k.const[:, 0:1]).then_inc(s_r, 1)
                act.wait_ge(s_r, 1)
                nc.scalar.activation(rstd[:, :], rstd[:, :], ACT.Exp, scale=-0.5).then_inc(s_r, 1)

            @block.tensor
            def _(pe):
                for kc in range(KC):
                    pe.wait_ge(s_sq, kc + 1)
                    for a, b in ((0, 512), (512, 1024), (1024, T)):
                        mm = nc.tensor.matmul(pf[:, a:b], k.ones[:, :], sq[:, kc % 2, a:b], start=kc == 0, stop=kc == KC - 1)
                    mm.then_inc(s_sum, 1)

            @block.vector
            def _(dve):
                if need[0]:
                    dve.wait_ge(s_x, need[0])
                dve.wait_ge(s_r, 2)
                n = 0
                for kc in range(KC):
                    if kc >= 2:
                        dve.wait_ge(s_o, 4 * (kc - 1))
                    nc.vector.tensor_tensor(xr[:, kc % 2, :], x[:, kc, :], rstd[:, :], ALU.mult).then_inc(s_o, 1)
                    n += 1
                    dve.wait_ge(s_o, n)
                    a, b = k.mod[:, scale_at + kc, :], k.mod[:, shift_at + kc, :]
                    nc.vector.tensor_scalar(out_prompt(kc), xr[:, kc % 2, 0:SEQ], a[:, 0:1], b[:, 0:1],
                                            ALU.mult, ALU.add).then_inc(s_o, 1)
                    smp = xr[:, kc % 2, SEQ:T].rearrange("p (s t) -> p s t", s=NSEQ)
                    nc.vector.tensor_tensor(smp, smp, bc(a[:, 1:NCOND].unsqueeze(2), [P, NSEQ, DSEQ]), ALU.mult).then_inc(s_o, 1)
                    n += 2
                    dve.wait_ge(s_o, n)
                    nc.vector.tensor_tensor(out_sample(kc), smp, bc(b[:, 1:NCOND].unsqueeze(2), [P, NSEQ, DSEQ]), ALU.add).then_inc(s_o, 1)
                    n += 1


def phase_norm1(k, xe):
    nc, io = k.nc, k.io
    with nc.sbuf_tensor("x_in", [P, KC, T], F32) as x:
        smp = lambda kc: xe[:, kc, 1 + SEQ:TX].rearrange("p (s t) -> p s t", s=NSEQ)
        s_z = k.sem("xe_pad_done")
        s_sh = k.sem("xe_shift_loaded")

        def load(sp, sem):
            sp.dma_start(x[:, :, :], io["xT"]).then_inc(sem, 16)
            sp.dma_start(k.shift_sb[:, :, :], io["shiftT"]).then_inc(s_sh, 16)
            sp.wait_ge(s_sh, 16)
            return 16

        def store(sp, sem):
            with nc.allow_non_contiguous_dma(reason="last rows"):
                sp.dma_start(io["shift_out"][:, :, 0:1], xe[:, :, SEQ:SEQ + 1]).then_inc(sem, 16)
                for kc in range(KC):
                    sp.dma_start(io["shift_out"][:, kc, 1:NCOND], smp(kc)[:, :, DSEQ]).then_inc(sem, 16)
            return 16 * (KC + 1)

        rmsnorm_mod(k, "norm1", x, lambda kc: xe[:, kc, 1:1 + SEQ], lambda kc: smp(kc)[:, :, 1:1 + DSEQ],
                    SC1, SH1, load, store)
        with nc.Block() as block:
            @block.gpsimd
            def _(pool):
                nc.gpsimd.memset(xe[:, :, 0:1], 0.0).then_inc(s_z, 1)
                for kc in range(KC):
                    nc.gpsimd.tensor_copy(smp(kc)[:, :, 0], k.shift_sb[:, kc, :]).then_inc(s_z, 1)




def predecessor_views(ext):
    smp = ext[:, 1 + SEQ:TX].rearrange("p (s t) -> p s t", s=NSEQ)
    return (ext[:, 0:SEQ], ext[:, 1:1 + SEQ]), (smp[:, :, 0:DSEQ], smp[:, :, 1:1 + DSEQ])


def token_views(tok):
    return tok[:, 0:SEQ], tok[:, SEQ:T].rearrange("p (s t) -> p s t", s=NSEQ)


def token_shift(dve, out, ext, mu, sub_done, wait_sub):
    for o, e in zip(out, ext):
        for ov, (prev, cur) in zip(token_views(o), predecessor_views(e)):
            last = dve.tensor_tensor(ov, prev, cur, ALU.subtract)
    last.then_inc(*sub_done)
    wait_sub()
    for o, e, m in zip(out, ext, mu):
        for ov, (_, cur) in zip(token_views(o), predecessor_views(e)):
            last = dve.scalar_tensor_tensor(out=ov, in0=ov, scalar=m, in1=cur, op0=ALU.mult, op1=ALU.add)
    return last


PADP = CONVK - 1
CONV_IN = PADP + SEQ + NSEQ * (PADP + DSEQ)
CONV_OUT = CONV_IN - PADP


def conv_sample_view(tile):
    return tile[:, PADP + SEQ:CONV_IN].rearrange("p (s t) -> p s t", s=NSEQ)


NW = 3
LOOP_A = 6
A_TILES = XBC_TILES + RW_TILES
A_ROUNDS = A_TILES // LOOP_A
B_ROUNDS = (PROJ_TILES - A_TILES) // LOOP_A


class Slices:

    def __init__(self, whole, size):
        self.whole, self.size, self.at = whole, size, 0

    def take(self, rows, *dims):
        n = int(np.prod(dims))
        assert self.at + n <= self.size, (self.at, n, self.size)
        ap = self.whole[0:rows, self.at:self.at + n]
        self.at += n
        names = "abc"[:len(dims)]
        if len(dims) == 1:
            return ap
        return ap.rearrange(f"p ({' '.join(names)}) -> p {' '.join(names)}", **dict(zip(names[:-1], dims[:-1])))


class Projection:

    def __init__(self, k, ctx, xe):
        nc = k.nc
        self.k, self.xe = k, xe
        sb = lambda n, s: ctx.enter_context(nc.sbuf_tensor(n, s, F32))
        self.w = [sb(f"in_w{i}", [P, KC, P]) for i in range(NW)]
        self.wdt = sb("in_wdt", [P, KC, SH])
        self.out = [sb(f"in_out{i}", [P, TX]) for i in range(2)]
        self.ps = ctx.enter_context(nc.psum_tensor("in_ps", [P, 5, 512], F32))
        self.s_w = [k.sem(f"in_w{i}_loaded") for i in range(NW)]
        self.s_wdt = k.sem("in_wdt_loaded")
        self.s_mm = k.sem("in_tile_multiplied")
        self.s_ev = k.sem("in_tile_evacuated")
        self.s_st = [k.sem(f"in_stored{i}") for i in range(2)]
        self.s_dt = k.sem("in_dt_step")
        self.s_dtst = k.sem("in_dt_stored")

    def stored(self, eng, t):
        eng.wait_ge(self.s_st[t % 2], 16 * (t // 2 + 1))

    def load(self, sp, t, slot):
        sp.dma_start(self.w[slot][:, :, :], self.k.io["w_in"][t]).then_inc(self.s_w[slot], 16)

    def chunk(self, wt, cols, parity, part):
        a, b = EXT_CHUNKS[part]
        at = self.ps[0:cols, 4, 256 * parity:256 * parity + b - a] if part == 2 else self.ps[0:cols, 2 * parity + part, 0:b - a]
        return lambda kc: self.k.nc.tensor.matmul(at, wt[:, kc, :], self.xe[:, kc, a:b], start=kc == 0, stop=kc == KC - 1)

    def dt_product(self, pe):
        pe.wait_ge(self.s_wdt, 16)
        for part in range(3):
            product = self.chunk(self.wdt, SH, 1, part)
            for kc in range(KC):
                mm = product(kc)
        mm.then_inc(self.s_dt, 1)

    def tile(self, pe, t, slot, parity, loads):
        pe.wait_ge(self.s_w[slot], 16 * loads + 16)
        pe.wait_ge(self.s_ev, t + 1)
        parts = [self.chunk(self.w[slot], P, parity, i) for i in range(3)]
        for kc in range(KC):
            parts[0](kc)
            parts[1](kc)
        pe.wait_ge(self.s_ev, t + 2)
        for kc in range(KC):
            mm = parts[2](kc)
        mm.then_inc(self.s_mm, 1)

    def out_of_psum(self, cols, parity):
        ac = self.k.nc.scalar
        big = flat(self.ps[0:cols, 2 * parity:2 * parity + 2, :])
        ac.activation(self.out[parity][0:cols, 0:1024], big, ACT.Copy)
        n = TX - 1024
        return ac.activation(self.out[parity][0:cols, 1024:TX], self.ps[0:cols, 4, 256 * parity:256 * parity + n], ACT.Copy)

    def evac(self, act, t, parity, earlier):
        act.wait_ge(self.s_mm, t + 1)
        if not isinstance(earlier, int) or earlier:
            act.wait_ge(self.s_st[parity], 16 * earlier)
        self.out_of_psum(P, parity).then_inc(self.s_ev, 1)

    def store(self, pool):
        io = self.k.io
        pool.wait_ge(self.s_dt, 2)
        pool.dma_start(io["proj"][DT0, 0:SH, :], self.out[1][0:SH, :]).then_inc(self.s_dtst, 16)
        with pool.Fori(0, PROJ_TILES // 2) as r:
            for parity in range(2):
                t = 2 * r + parity
                pool.wait_ge(self.s_ev, t + 3)
                pool.dma_start(io["proj"][t], self.out[parity][:, :]).then_inc(self.s_st[parity], 16)
        for t in (PROJ_TILES - 2, PROJ_TILES - 1):
            self.stored(pool, t)


def phase_inputs(k, xe):
    nc, io = k.nc, k.io
    with ExitStack() as ctx:
        pj = Projection(k, ctx, xe)
        keep = ctx.enter_context(nc.sbuf_tensor("pre_keep", [P, T], F32))
        rp = ctx.enter_context(nc.sbuf_tensor("rwp_rp", [P, 8], F32))
        lw = ctx.enter_context(nc.sbuf_tensor("rwp_lw", [P, 2, P], F32))
        SIZE = 3 * TX + 21 * T
        arena = ctx.enter_context(nc.sbuf_tensor("pre_arena", [P, SIZE], F32))
        c_ = Slices(arena, SIZE)
        e, acc, sg = ([c_.take(P, CONV_IN) for i in range(2)] for n in range(3))
        out = [c_.take(P, T) for i in range(2)]
        state = c_.take(P, NXBC, NSEQ, PADP)
        new = c_.take(P, NXBC, NCOND, PADP)
        hp, neg_a = c_.take(SH, 2), c_.take(SH, 1)
        dx = c_.take(SH, TX)
        dkeep, dtx, ex, sq, poly, rec = (c_.take(SH, T) for n in range(6))
        rows = c_.take(SH, 3, T)
        r_ = Slices(arena, SIZE)
        x = r_.take(P, 3, TX)
        lora = r_.take(P, 2, T)
        q = r_.take(P, 3, T)
        sw, a, lam, linv, lprev, cs, kk, rn, t1, kp, gate, bonus = (r_.take(P, T) for n in range(12))
        o = r_.take(P, 4, T)
        psr = ctx.enter_context(nc.psum_tensor("rwp_ps", [P, 3, 512], F32))
        pa = flat(psr[:, :, :])

        s_in = [k.sem(f"cv_in{i}_loaded") for i in range(2)]
        s_state = k.sem("cv_state_loaded")
        s_dt = k.sem("dt_loaded")
        s_pad = k.sem("cv_pad_zeroed")
        s_out = [k.sem(f"cv_out{i}_stored") for i in range(2)]
        s_fin = k.sem("cv_states_and_dt_stored")
        s_keep = k.sem("dt_keep_step")
        s_dx = k.sem("dt_act_step")
        s_dv = k.sem("dt_dve_step")
        s_rows = k.sem("dt_rows_done")
        CA = Progress(k.sem("cv_act"), "state", "new", "sigmoid")
        CD = Progress(k.sem("cv_dve"), "tap0", "tap1", "tap2", "tap3", "silu")
        cw, cb = k.par[:, PCOLS["conv_w"]], k.par[:, PCOLS["conv_b"]]

        s_lx = k.sem("rwp_lora_loaded")
        s_x = k.sem("rwp_x_loaded")
        s_w = k.sem("rwp_weights_loaded")
        s_st = k.sem("rwp_stored")
        s_rkeep = k.sem("rwp_keep_step")
        s_lora = k.sem("rwp_lora_step")
        PE = Progress(k.sem("rwp_pe"), "zw", "za", "gate", "norm", "bonus")
        AC = Progress(k.sem("rwp_act"), "sw", "a", "gate", "lam", "linv", "lprev", "ln", "rn")
        DV = Progress(k.sem("rwp_dve"), "sub", "mix", "kkr", "sq", "cs", "csx", "norm_floor", "am", "kp", "kk",
                      "b", "rk", "outs", "bonus")
        NST = 7
        c = EXP_NEG_HALF

        with nc.Block() as block:
            @block.sync
            def _(sp):
                def conv_load(m):
                    pj.stored(sp, XBC0 + m)
                    if m >= 2:
                        sp.wait_ge(CD.sem, CD.now("silu", m - 2))
                        sp.wait_ge(CA.sem, CA.now("new", m - 2))
                    sp.dma_start(e[m % 2][:, PADP:PADP + SEQ], io["proj"][XBC0 + m, :, 1:1 + SEQ]).then_inc(s_in[m % 2], 16)
                    src = io["proj"][XBC0 + m, :, 1 + SEQ:TX].rearrange("p (s t) -> p s t", s=NSEQ)
                    sp.dma_start(conv_sample_view(e[m % 2])[:, :, PADP:], src[:, :, 1:1 + DSEQ]).then_inc(s_in[m % 2], 16)

                sp.dma_start(pj.wdt[:, :, :], io["w_dt"]).then_inc(pj.s_wdt, 16)
                for t in range(NW):
                    pj.load(sp, t, t)
                sp.dma_start(hp, io["head_params"]).then_inc(s_dt, 16)
                sp.dma_start(state, io["convT"]).then_inc(s_state, 16)
                sp.wait_ge(pj.s_dtst, 16)
                sp.dma_start(dx, io["proj"][DT0, 0:SH, :]).then_inc(s_dt, 16)
                STRAIGHT = PROJ_TILES - NW - (PROJ_TILES - NW - XBC_TILES - 1) // NW * NW
                for t in range(STRAIGHT):
                    sp.wait_ge(pj.s_mm, t + 1)
                    pj.load(sp, t + NW, t % NW)
                    if 1 <= t <= XBC_TILES:
                        conv_load(t - 1)
                with sp.Fori(0, (PROJ_TILES - NW - STRAIGHT) // NW) as r:
                    for j in range(NW):
                        t = NW * r + (STRAIGHT + j)
                        sp.wait_ge(pj.s_mm, t + 1)
                        pj.load(sp, t + NW, (STRAIGHT + j) % NW)

            @block.gpsimd
            def _(pool):
                g = nc.gpsimd
                g.memset(dkeep, 1.0).then_inc(s_keep, 1)
                for i in range(2):
                    g.memset(e[i][:, 0:PADP], 0.0).then_inc(s_pad, 1)
                g.memset(keep[:, :], 1.0).then_inc(s_rkeep, 1)
                pool.wait_ge(s_keep, 1)
                g.memset(dkeep[:, 0:SEQ].rearrange("p (c t) -> p c t", t=SL)[:, :, 0:1], 0.0).then_inc(s_keep, 1)
                g.memset(dkeep[:, SEQ:T].rearrange("p (c t) -> p c t", t=DSEQ)[:, :, 0:1], 0.0).then_inc(s_keep, 1)
                pool.wait_ge(s_rkeep, 1)
                g.memset(keep[:, 0:SEQ].rearrange("p (c t) -> p c t", t=CL)[:, :, 0:1], 0.0).then_inc(s_rkeep, 1)
                g.memset(keep[:, SEQ:T].rearrange("p (c t) -> p c t", t=DSEQ)[:, :, 0:1], 0.0).then_inc(s_rkeep, 1)
                pj.store(pool)

            @block.tensor
            def _(pe):
                PE.credit(pe)
                pj.dt_product(pe)
                pe.wait_ge(pj.s_dt, 2)

                with pe.Fori(0, A_ROUNDS) as r:
                    for j in range(LOOP_A):
                        pj.tile(pe, LOOP_A * r + j, j % NW, j % 2, (LOOP_A // NW) * r + j // NW)
                for t in range(LOOP_A * A_ROUNDS, A_TILES):
                    pj.tile(pe, t, t % NW, t % 2, t // NW)

                def product(lhsT, rhs, step):
                    for a0, b0 in TOK_CHUNKS_BANKED:
                        mm = nc.tensor.matmul(pa[:, a0:b0], lhsT, rhs[:, a0:b0], start=True, stop=True)
                    mm.then_inc(*PE.inc(step))

                with pe.Fori(0, B_ROUNDS) as r:
                    def pair_product(j):
                        if j == 0:
                            pe.wait_ge(s_lora, 4)
                            pe.wait_ge(s_w, 32 * r + 32)
                            pe.wait_ge(DV.sem, DV.before("bonus", r))
                            product(lw[0:64, 0, :], lora[0:64, 0, :], "zw")
                        elif j == 1:
                            pe.wait_ge(AC.sem, AC.now("sw", r))
                            product(lw[64:128, 0, :], lora[64:128, 0, :], "za")
                        elif j == 2:
                            pe.wait_ge(AC.sem, AC.now("a", r))
                            product(lw[:, 1, :], lora[:, 1, :], "gate")
                        elif j == 3:
                            pe.wait_ge(AC.sem, AC.now("gate", r))
                            pe.wait_ge(DV.sem, DV.now("sq", r))
                            product(k.pairones[:, :], rn, "norm")
                        elif j == 4:
                            pe.wait_ge(DV.sem, DV.now("rk", r))
                            product(k.pairones[:, :], t1, "bonus")

                    for j in range(LOOP_A):
                        t = A_TILES + j
                        pj.tile(pe, LOOP_A * r + t, t % NW, t % 2, (LOOP_A // NW) * r + t // NW)
                        pair_product(j)

            @block.scalar
            def _(act):
                ac = nc.scalar
                act.sem_inc(pj.s_ev, 2)
                act.wait_ge(pj.s_dt, 1)
                pj.out_of_psum(SH, 1).then_inc(pj.s_dt, 1)
                act.wait_ge(s_dt, 32)
                ac.activation(neg_a, hp[:, 1:2], ACT.Exp).then_inc(s_dx, 1)
                act.wait_ge(s_dv, 2)
                ac.activation(ex, dtx, ACT.Abs).then_inc(s_dx, 1)
                act.wait_ge(s_dx, 2)
                ac.activation(ex, ex, ACT.Exp, scale=-1.0).then_inc(s_dx, 1)
                CA.credit(act)
                for i in range(2):
                    act.sem_inc(s_out[i], 16)
                act.wait_ge(s_state, 16)
                pj.evac(act, 0, 0, 0)
                act.wait_ge(pj.s_dtst, 16)
                pj.evac(act, 1, 1, 0)
                with act.Fori(0, NXBC // 2) as r:
                    for h in range(2):
                        m = 2 * r + h
                        pj.evac(act, m + 2, h, r + 1)
                        smp = conv_sample_view(e[h])
                        act.wait_ge(CD.sem, CD.before("silu", 2 * r))
                        ac.activation(smp[:, :, 0:PADP], state[:, bass.ds(m, 1), :, :].rearrange("p a s t -> p (a s) t"),
                                      ACT.Copy).then_inc(*CA.inc("state"))
                        act.wait_ge(s_in[h], 32 * r + 32)
                        ac.activation(new[:, bass.ds(m, 1), 0, :].rearrange("p a t -> p (a t)"), e[h][:, SEQ:SEQ + PADP], ACT.Copy)
                        ac.activation(new[:, bass.ds(m, 1), 1:NCOND, :].rearrange("p a s t -> p (a s) t"), smp[:, :, DSEQ:],
                                      ACT.Copy).then_inc(*CA.inc("new"))
                        act.wait_ge(CD.sem, CD.now("tap3", m))
                        ac.activation(sg[h][:, 0:CONV_OUT], acc[h][:, 0:CONV_OUT], ACT.Sigmoid).then_inc(*CA.inc("sigmoid"))
                        act.wait_ge(CD.sem, CD.now("silu", m))
                        act.dma_start(io["xbc"][m], out[h]).then_inc(s_out[h], 16)
                act.wait_ge(s_rows, 2)
                act.dma_start(io["ssd_rows"], rows).then_inc(s_fin, 16)
                act.wait_ge(CA.sem, CA.now("new", NXBC - 1))
                act.dma_start(io["conv_out"], new).then_inc(s_fin, 16)
                act.wait_ge(s_fin, 32)
                for h in range(2):
                    act.wait_ge(s_out[h], 16 * (NXBC // 2) + 16)
                with act.Fori(0, (A_TILES - NXBC) // 2 - 1) as r:
                    for h in range(2):
                        pj.evac(act, 2 * r + (NXBC + 2 + h), h, r + (NXBC // 2 + 1))
                for t in range(A_TILES - 2, A_TILES):
                    pj.stored(act, t)
                for i in range(2):
                    act.dma_start(x[:, i, :], io["proj"][RW0 + 12 + i]).then_inc(s_lx, 16)

                def load(r):
                    for i in range(3):
                        act.dma_start(x[:, i, :], io["proj"][RW0 + 4 * i + r]).then_inc(s_x, 16)
                    act.dma_start(rp[:, :], io["rw_params"][r]).then_inc(s_w, 16)
                    act.dma_start(lw[:, :, :], io["lora_w"][r]).then_inc(s_w, 16)

                AC.credit(act)
                act.sem_inc(s_st, 16 * NST)
                act.wait_ge(s_lora, 2)
                ac.activation(lora[0:64, 0, :], lora[0:64, 0, :], ACT.Tanh).then_inc(s_lora, 1)
                ac.activation(lora[:, 1, :], lora[:, 1, :], ACT.Sigmoid).then_inc(s_lora, 1)
                with act.Fori(0, NPAIR) as r:
                    act.wait_ge(DV.sem, DV.before("bonus", r))
                    act.wait_ge(AC.sem, AC.before("rn", r))
                    load(r)

                    def evac(j):
                        pj.evac(act, LOOP_A * r + (A_TILES + j), j % 2, (LOOP_A // 2) * r + (A_TILES + j) // 2)

                    evac(0)
                    act.wait_ge(s_w, 32 * r + 32)
                    act.wait_ge(PE.sem, PE.now("zw", r))
                    ac.activation(sw, pa[:, 0:T], ACT.Sigmoid, bias=rp[:, RWP_W0:RWP_W0 + 1]).then_inc(*AC.inc("sw"))
                    evac(1)
                    act.wait_ge(PE.sem, PE.now("za", r))
                    ac.activation(a, pa[:, 0:T], ACT.Sigmoid, bias=rp[:, RWP_A0:RWP_A0 + 1]).then_inc(*AC.inc("a"))
                    evac(2)
                    act.wait_ge(PE.sem, PE.now("gate", r))
                    act.wait_ge(s_st, 16 * NST * r + 16 * NST)
                    ac.activation(gate, pa[:, 0:T], ACT.Copy).then_inc(*AC.inc("gate"))
                    act.wait_ge(DV.sem, DV.now("cs", r))
                    ac.activation(lam, cs, ACT.Exp, scale=-c).then_inc(*AC.inc("lam"))
                    ac.activation(linv, cs, ACT.Exp, scale=c).then_inc(*AC.inc("linv"))
                    act.wait_ge(DV.sem, DV.now("csx", r))
                    ac.activation(lprev, lprev, ACT.Exp, scale=-c).then_inc(*AC.inc("lprev"))
                    evac(3)
                    act.wait_ge(DV.sem, DV.now("norm_floor", r))
                    ac.activation(rn, rn, ACT.Ln).then_inc(*AC.inc("ln"))
                    act.wait_ge(AC.sem, AC.now("ln", r))
                    ac.activation(rn, rn, ACT.Exp, scale=-0.5).then_inc(*AC.inc("rn"))
                    evac(4)
                    act.wait_ge(DV.sem, DV.now("outs", r))
                    for n in range(4):
                        act.dma_start(io["rwc"][:, :, n, r, :].rearrange("c p t -> p c t"),
                                      o[:, n, :].rearrange("p (c t) -> p c t", t=CL)).then_inc(s_st, 16)
                    act.dma_start(io["rwc"][:, :, 4, r, :].rearrange("c p t -> p c t"),
                                  q[:, 2, :].rearrange("p (c t) -> p c t", t=CL)).then_inc(s_st, 16)
                    act.wait_ge(AC.sem, AC.now("gate", r))
                    act.dma_start(io["rw_gate"][r], gate).then_inc(s_st, 16)
                    act.wait_ge(DV.sem, DV.now("bonus", r))
                    act.dma_start(io["rw_bonus"][r], bonus).then_inc(s_st, 16)
                    evac(5)
                act.wait_ge(s_st, 16 * NST * NPAIR + 16 * NST)

            @block.vector
            def _(dve):
                v = nc.vector
                n = [0]

                def step(ins):
                    ins.then_inc(s_dv, 1)
                    n[0] += 1
                    dve.wait_ge(s_dv, n[0])

                dve.wait_ge(s_dt, 32)
                v.tensor_copy(dtx[:, 0:SEQ], dx[:, 1:1 + SEQ])
                step(v.tensor_copy(token_views(dtx)[1], predecessor_views(dx)[1][1]))
                step(v.tensor_scalar(dtx, dtx, hp[:, 0:1], None, ALU.add))
                dve.wait_ge(s_dx, 3)
                step(v.tensor_scalar(rec, ex, 2.0, None, ALU.add))
                step(v.reciprocal(rec, rec))
                step(v.tensor_tensor(ex, ex, rec, ALU.mult))
                step(v.tensor_tensor(sq, ex, ex, ALU.mult))
                step(v.tensor_scalar(poly, sq, 1.0 / 15, None, ALU.mult))
                for d in (13, 11, 9, 7, 5, 3):
                    step(v.scalar_tensor_tensor(out=poly, in0=poly, scalar=1.0 / d, in1=sq, op0=ALU.add, op1=ALU.mult))
                step(v.scalar_tensor_tensor(out=poly, in0=poly, scalar=1.0, in1=ex, op0=ALU.add, op1=ALU.mult))
                step(v.tensor_scalar(dtx, dtx, 0.0, None, ALU.max))
                step(v.scalar_tensor_tensor(out=rows[:, 0, :], in0=poly, scalar=2.0, in1=dtx, op0=ALU.mult, op1=ALU.add))
                dve.wait_ge(s_keep, 3)
                step(v.tensor_scalar(dtx, rows[:, 0, :], neg_a[:, 0:1], -1.0, ALU.mult, ALU.mult))
                step(v.tensor_tensor_scan(rows[:, 1, :], dkeep, dtx, 0.0, ALU.mult, ALU.add))
                for span, lo, hi in ((SL, 0, SEQ), (DSEQ, SEQ, T)):
                    cs_ = rows[:, 1, lo:hi].rearrange("p (c t) -> p c t", t=span)
                    v.tensor_tensor(rows[:, 2, lo:hi].rearrange("p (c t) -> p c t", t=span),
                                    bc(cs_[:, :, span - 1:span], [SH, (hi - lo) // span, span]), cs_, ALU.subtract).then_inc(s_rows, 1)
                CD.credit(dve)
                dve.wait_ge(s_pad, 2)
                with dve.Fori(0, NXBC // 2) as r:
                    for h in range(2):
                        m = 2 * r + h
                        done = lambda s_: dve.wait_ge(CD.sem, CD.now(s_, m))
                        dve.wait_ge(s_in[h], 32 * r + 32)
                        dve.wait_ge(CA.sem, CA.now("state", m))
                        wc = lambda j: cw[:, bass.ds(m + j * NXBC, 1)]
                        a_ = acc[h][:, 0:CONV_OUT]
                        v.tensor_scalar(a_, e[h][:, 0:CONV_OUT], wc(0), cb[:, bass.ds(m, 1)], ALU.mult, ALU.add).then_inc(*CD.inc("tap0"))
                        for j in range(1, CONVK):
                            done(f"tap{j - 1}")
                            v.scalar_tensor_tensor(out=a_, in0=e[h][:, j:j + CONV_OUT], scalar=wc(j), in1=a_,
                                                   op0=ALU.mult, op1=ALU.add).then_inc(*CD.inc(f"tap{j}"))
                        dve.wait_ge(CA.sem, CA.now("sigmoid", m))
                        dve.wait_ge(s_out[h], 16 * r + 16)
                        v.tensor_tensor(out[h][:, 0:SEQ], acc[h][:, 0:SEQ], sg[h][:, 0:SEQ], ALU.mult)
                        v.tensor_tensor(token_views(out[h])[1], conv_sample_view(acc[h])[:, :, 0:DSEQ],
                                        conv_sample_view(sg[h])[:, :, 0:DSEQ], ALU.mult).then_inc(*CD.inc("silu"))

                DV.credit(dve)
                dve.wait_ge(s_lx, 32)
                mu = k.par[:, PCOLS["mu_lora"]]
                token_shift(v, [lora[:, i, :] for i in range(2)], [x[:, i, :] for i in range(2)],
                            [mu[:, i:i + 1] for i in range(2)], (s_lora, 1),
                            lambda: dve.wait_ge(s_lora, 1)).then_inc(s_lora, 1)
                dve.wait_ge(s_rkeep, 3)
                with dve.Fori(0, NPAIR) as r:
                    now = lambda s: dve.wait_ge(DV.sem, DV.now(s, r))
                    col = lambda n: rp[:, n:n + 1]
                    dve.wait_ge(s_x, 48 * r + 48)
                    dve.wait_ge(s_w, 32 * r + 32)
                    dve.wait_ge(s_st, 16 * NST * r + 16 * NST)
                    token_shift(v, [q[:, i, :] for i in range(3)], [x[:, i, :] for i in range(3)],
                                [col(RWP_MU + i) for i in range(3)], DV.inc("sub"),
                                lambda: now("sub")).then_inc(*DV.inc("mix"))
                    now("mix")
                    v.tensor_scalar(kk, q[:, 1, :], col(RWP_KK), None, ALU.mult).then_inc(*DV.inc("kkr"))
                    now("kkr")
                    v.tensor_tensor(rn, kk, kk, ALU.mult).then_inc(*DV.inc("sq"))
                    dve.wait_ge(AC.sem, AC.now("sw", r))
                    v.tensor_tensor_scan(cs, keep[:, :], sw, 0.0, ALU.mult, ALU.add).then_inc(*DV.inc("cs"))
                    now("cs")
                    v.tensor_tensor(lprev, cs, sw, ALU.subtract).then_inc(*DV.inc("csx"))
                    dve.wait_ge(PE.sem, PE.now("norm", r))
                    v.tensor_scalar(rn, pa[:, 0:T], 1e-24, LN_SCALE, ALU.max, ALU.mult).then_inc(*DV.inc("norm_floor"))
                    dve.wait_ge(AC.sem, AC.now("a", r))
                    v.scalar_tensor_tensor(out=t1, in0=a, scalar=-1.0, in1=q[:, 1, :],
                                           op0=ALU.add, op1=ALU.mult).then_inc(*DV.inc("am"))
                    now("am")
                    v.scalar_tensor_tensor(out=kp, in0=t1, scalar=col(RWP_KA), in1=q[:, 1, :],
                                           op0=ALU.mult, op1=ALU.add).then_inc(*DV.inc("kp"))
                    dve.wait_ge(AC.sem, AC.now("rn", r))
                    v.scalar_tensor_tensor(out=kk, in0=kk, scalar=LN_SCALE ** 0.5, in1=rn,
                                           op0=ALU.mult, op1=ALU.mult).then_inc(*DV.inc("kk"))
                    now("kk")
                    v.tensor_tensor(rn, kk, a, ALU.mult).then_inc(*DV.inc("b"))
                    v.scalar_tensor_tensor(out=t1, in0=q[:, 0, :], scalar=col(RWP_RK), in1=kp,
                                           op0=ALU.mult, op1=ALU.mult).then_inc(*DV.inc("rk"))
                    dve.wait_ge(AC.sem, AC.now("lprev", r))
                    now("b")
                    v.tensor_tensor(o[:, 0, :], kk, lprev, ALU.mult)
                    v.tensor_tensor(o[:, 1, :], q[:, 0, :], lam, ALU.mult)
                    v.tensor_tensor(o[:, 2, :], rn, linv, ALU.mult)
                    v.tensor_tensor(o[:, 3, :], kp, linv, ALU.mult)
                    v.tensor_copy(k.lam_end[:, r, 0:NCH], lam[:, CL - 1:SEQ:CL])
                    v.tensor_copy(k.lam_end[:, r, NCH:NCH + NSEQ], lam[:, SEQ + DSEQ - 1:T:DSEQ]).then_inc(*DV.inc("outs"))
                    dve.wait_ge(PE.sem, PE.now("bonus", r))
                    v.tensor_tensor(bonus, pa[:, 0:T], q[:, 2, :], ALU.mult).then_inc(*DV.inc("bonus"))


def halves():
    return slice(0, 64), slice(64, 128)


def phase_masks(k):
    nc = k.nc
    s = k.sem("mask_step")
    with nc.Block() as block:
        @block.gpsimd
        def _(pool):
            g = nc.gpsimd
            n = [0]

            def stage(ops):
                for op in ops:
                    op().then_inc(s, 1)
                    n[0] += 1
                    pool.wait_ge(s, n[0])

            def keep(view, pattern, base, cm):
                return lambda: g.affine_select(out=view, in_=view, compare_op=ALU.is_ge, fill=0.0, base=base,
                                               pattern=pattern, channel_multiplier=cm)

            stage([lambda: g.memset(k.mt_mask[:, :, :, :], 1.0), lambda: g.memset(k.lv_mask[:, :, :, :], 0.0),
                   lambda: g.memset(k.seq_cols[:, :, :], 1.0), lambda: g.memset(k.seq_rows[:, :], 1.0)])
            for rows in halves():
                for kind in range(2):
                    for b in range(4):
                        m = k.mt_mask[rows, kind, b, :]
                        stage([keep(m, [[1, CL]], -1 if b % 2 == 0 else 0, -1)])
                blk = k.mt_mask[rows, 1, :, :].rearrange("p b (s t) -> p b s t", s=NSEQ)
                for b in range(4):
                    stage([keep(blk[:, b], [[-DSEQ, NSEQ], [0, DSEQ]], 0, 1)])
                    stage([keep(blk[:, b], [[DSEQ, NSEQ], [0, DSEQ]], DSEQ - 1, -1)])
                stage([keep(k.seq_rows[rows, :], [[-DSEQ, NSEQ]], 0, 1)])
                stage([keep(k.seq_rows[rows, :], [[DSEQ, NSEQ]], DSEQ - 1, -1)])
                for lv in range(LEVELS):
                    z = 1 << lv
                    nb = CL // (2 * z)
                    xm = k.lv_mask[rows, lv, 0, :].rearrange("p (b h w) -> p b h w", h=2, w=z)[:, :, 0, :]
                    ym = k.lv_mask[rows, lv, 1, :].rearrange("p (b h w) -> p b h w", h=2, w=z)[:, :, 1, :]
                    stage([lambda: g.memset(xm, 1.0), lambda: g.memset(ym, 1.0)])
                    stage([keep(xm, [[-2 * z, nb], [0, z]], -z, 1), keep(ym, [[-2 * z, nb], [0, z]], 0, 1)])
                    stage([keep(xm, [[2 * z, nb], [0, z]], 2 * z - 1, -1), keep(ym, [[2 * z, nb], [0, z]], z - 1, -1)])
                for i in range(2):
                    stage([lambda: g.tensor_copy(k.ident2[rows, i, :], k.ident[rows, rows])])
            stage([lambda: g.memset(k.ssd_mask[:, :], 1.0), lambda: g.memset(k.ssd_mask_smp[:, :], 1.0),
                   lambda: g.memset(k.head_sel[:, :, :], 1.0)])
            stage([keep(k.ssd_mask[:, :], [[1, SL]], 0, -1), keep(k.ssd_mask_smp[:, :], [[1, CL]], 0, -1)])
            blk = k.ssd_mask_smp[:, :].rearrange("p (s t) -> p s t", s=NSEQ)
            stage([keep(blk, [[-DSEQ, NSEQ], [0, DSEQ]], 0, 1)])
            stage([keep(k.head_sel[:, :, :], [[-1, SH], [0, P]], 0, 1)])
            stage([keep(k.head_sel[:, :, :], [[1, SH], [0, P]], 0, -1)])
            stage([keep(k.seq_cols[:, :, :], [[-DSEQ, NSEQ], [1, CL]], 0, 0)])
            stage([keep(k.seq_cols[:, :, :], [[DSEQ, NSEQ], [-1, CL]], DSEQ - 1, 0)])


KA, RB, BT, KT, VV = range(5)
BANK_MT, BANK_M, BANK_TOK, BANK_P, BANK_Q, BANK_U, BANK_Y, BANK_S = 0, 2, 3, 5, 6, 7, 2, 5


def level_steps(name, levels):
    return [f"{name}{lv}" for lv in range(1, levels)]


def rw_matrix_pe(k, b, pe, in5, levels, at, between=lambda n: None):
    nc, PE, AC, DV = k.nc, b.PE, b.AC, b.DV
    ps = b.ps
    heads = [(p_, rows) for p_ in range(NPAIR) for rows in halves()]
    mt = ps[:, BANK_MT:BANK_MT + 2, :].rearrange("p a (b m) -> p (a b) m", m=256)
    tok = ps[:, BANK_TOK:BANK_TOK + 2, :].rearrange("p a b -> p (a b)")[:, 0:768].rearrange("p (q a t) -> p q a t", q=3, a=4)
    four = lambda bank: ps[:, bank, 0:256].rearrange("p (a t) -> p a t", a=4)
    pq = ps[:, BANK_Q, :].rearrange("p (a i t) -> p a i t", a=4, i=2)
    for p_, rows in heads:
        for i, w in enumerate((BT, KT)):
            mm = nc.tensor.matmul(mt[rows, p_, 128 * i:128 * i + 128], in5[rows, w, p_, :], in5[rows, KA:RB + 1, p_, :],
                                  start=True, stop=True)
    mm.then_inc(*PE.inc("mt"))
    for p_, rows in heads:
        mm = nc.tensor.matmul(four(BANK_M)[rows, p_, :], in5[rows, KA, p_, :], in5[rows, BT, p_, :], start=True, stop=True)
    mm.then_inc(*PE.inc("m"))
    for q, w in enumerate((BT, KT, VV)):
        for p_, rows in heads:
            mm = nc.tensor.matmul(tok[rows, q, p_, :], in5[rows, w, p_, :], k.ident[rows, rows], start=True, stop=True)
    mm.then_inc(*PE.inc("tok"))
    for lv in range(1, levels):
        if lv > 1:
            between(3)
        at(DV, f"xy{lv - 1}")
        for p_, rows in heads:
            mm = nc.tensor.matmul(four(BANK_P)[rows, p_, :], b.mt[rows, p_, 0:64], b.xy[rows, p_, 0, :], start=True, stop=True)
        mm.then_inc(*PE.inc(f"mx{lv}"))
        between(2)
        at(AC, f"mx{lv}")
        for p_, rows in heads:
            nc.tensor.matmul(pq[rows, p_, 0, :], b.xy[rows, p_, 1, :], b.mx[rows, p_, :], start=True, stop=True)
            mm = nc.tensor.matmul(pq[rows, p_, 1, :], b.mx[rows, p_, :], b.xy[rows, p_, 1, :], start=True, stop=True)
        mm.then_inc(*PE.inc(f"xmx{lv}"))


def rw_matrix_act(k, b, levels, at):
    nc, PE, AC = k.nc, b.PE, b.AC
    tok = b.ps[:, BANK_TOK:BANK_TOK + 2, :].rearrange("p a b -> p (a b)")[:, 0:768]
    at(PE, "tok")
    nc.scalar.activation(b.tok[:, :, :, :].rearrange("p q a t -> p (q a t)"), tok, ACT.Copy).then_inc(*AC.inc("tok"))
    for lv in range(1, levels):
        at(PE, f"mx{lv}")
        nc.scalar.activation(b.mx[:, :, :].rearrange("p a t -> p (a t)"), b.ps[:, BANK_P, 0:256], ACT.Copy).then_inc(*AC.inc(f"mx{lv}"))


def rw_matrix_dve(k, b, kind, levels, at):
    v, PE, DV = k.nc.vector, b.PE, b.DV
    mt = b.ps[:, BANK_MT:BANK_MT + 2, :].rearrange("p a (b m) -> p (a b) m", m=256)
    m = b.ps[:, BANK_M, 0:256].rearrange("p (a t) -> p a t", a=4)
    mask = k.mt_mask[:, kind, :, :].rearrange("p b t -> p (b t)").unsqueeze(1)
    at(PE, "mt")
    v.tensor_tensor(b.mt[:, :, :], mt, bc(mask, [P, NPAIR, 256]), ALU.mult).then_inc(*DV.inc("mt"))
    at(PE, "m")
    at(DV, "mt")
    v.tensor_tensor(b.tmp[:, :, 0, :], m, bc(k.lv_mask[:, 0, 0:1, :], [P, NPAIR, CL]), ALU.mult)
    v.tensor_tensor(b.tmp[:, :, 1, :], b.mt[:, :, 0:64], bc(k.lv_mask[:, 0, 1:2, :], [P, NPAIR, CL]), ALU.mult).then_inc(*DV.inc("t0"))
    at(DV, "t0")
    xy = b.xy[:, :, :, :].rearrange("p a i t -> p a (i t)")
    tmp = b.tmp[:, :, :, :].rearrange("p a i t -> p a (i t)")
    one = bc(k.ident2[:, :, :].rearrange("p i t -> p (i t)").unsqueeze(1), [P, NPAIR, 128])
    v.tensor_tensor(xy, one, tmp, ALU.subtract).then_inc(*DV.inc("xy0"))
    pq = b.ps[:, BANK_Q, :].rearrange("p (a m) -> p a m", a=4)
    for lv in range(1, levels):
        at(PE, f"xmx{lv}")
        lm = k.lv_mask[:, lv, :, :].rearrange("p i t -> p (i t)").unsqueeze(1)
        v.tensor_tensor(tmp, pq, bc(lm, [P, NPAIR, 128]), ALU.mult).then_inc(*DV.inc(f"t{lv}"))
        at(DV, f"t{lv}")
        v.tensor_tensor(xy, xy, tmp, ALU.subtract).then_inc(*DV.inc(f"xy{lv}"))


class RwBuffers:
    def __init__(self, k, ctx, tag, levels):
        sb = lambda n, s: ctx.enter_context(k.nc.sbuf_tensor(f"{tag}_{n}", s, F32))
        self.mt = sb("mt", [P, NPAIR, 256])
        self.xy = sb("xy", [P, NPAIR, 2, CL])
        self.mx = sb("mx", [P, NPAIR, CL])
        self.tmp = sb("tmp", [P, NPAIR, 2, CL])
        self.tok = sb("tok", [P, 3, NPAIR, CL])
        self.rhs = sb("rhs", [P, NPAIR, CL])
        self.u = sb("u", [P, NPAIR, CL])
        self.ps = ctx.enter_context(k.nc.psum_tensor(f"{tag}_ps", [P, 8, 512], F32))
        prompt = tag == "rwc"
        self.PE = Progress(k.sem(f"{tag}_pe"), "mt", "m", "tok",
                           *[s for lv in range(1, levels) for s in (f"mx{lv}", f"xmx{lv}")],
                           *(["mod"] if prompt else []), "rhs", "u", "y", "s")
        self.AC = Progress(k.sem(f"{tag}_act"), "tok", *level_steps("mx", levels), "u", "y")
        self.DV = Progress(k.sem(f"{tag}_dve"), "mt", "t0", "xy0",
                           *[s for lv in range(1, levels) for s in (f"t{lv}", f"xy{lv}")],
                           *(["mod", "rhs"] if prompt else ["masked", "rhs", "umask"]), "s_add", "s")


def phase_rw_prompt(k):
    nc, io = k.nc, k.io
    with ExitStack() as ctx:
        b = RwBuffers(k, ctx, "rwc", LEVELS)
        PE, AC, DV = b.PE, b.AC, b.DV
        in5 = [ctx.enter_context(nc.sbuf_tensor(f"rwc_in{i}", [P, 5, NPAIR, CL], F32)) for i in range(2)]
        S = ctx.enter_context(nc.sbuf_tensor("rwc_state", [P, NPAIR, CL], F32))
        y = [ctx.enter_context(nc.sbuf_tensor(f"rwc_y{i}", [P, NPAIR, CL], F32)) for i in range(2)]
        wa = [ctx.enter_context(nc.sbuf_tensor(f"rwc_ada{i}", [P, KC, ADA_STEP * P], F32)) for i in range(2)]
        s_in = [k.sem(f"rwc_in{i}_loaded") for i in range(2)]
        s_wa = [k.sem(f"rwc_ada{i}_loaded") for i in range(2)]
        s_mod = k.sem("rwc_gains_scaled")
        modp = b.ps[:, BANK_M, 256:256 + ADA_STEP * NCOND].rearrange("p (m c) -> p m c", m=ADA_STEP)
        s_y = k.sem("rwc_y_stored")
        s_init = k.sem("rwc_state_zeroed")
        heads = [(p_, rows) for p_ in range(NPAIR) for rows in halves()]
        four = lambda bank: b.ps[:, bank, 0:256].rearrange("p (a t) -> p a t", a=4)

        def at_of(eng, c):
            return lambda S_, step: eng.wait_ge(S_.sem, S_.now(step, c))

        def pe_at_of(pe, c, one):
            def at(S_, step):
                pe.wait_ge(S_.sem, S_.now(step, c))
                pe.reg_alu(one, one, 1, ALU.max)
            return at

        with nc.Block() as block:
            @block.sync
            def _(sp):
                def load(c, h):
                    sp.dma_start(in5[h][:, :, :, :], io["rwc"][c]).then_inc(s_in[h], 16)
                    sp.dma_start(wa[h][:, :, :], io["w_ada_rest"][c]).then_inc(s_wa[h], 16)

                def store(c, h):
                    sp.wait_ge(AC.sem, AC.now("y", c))
                    sp.dma_start(io["rw_y"][c], y[h][:, :, :]).then_inc(s_y, 16)

                for h in range(2):
                    load(h, h)
                with sp.Fori(0, NCH // 2 - 1) as r:
                    for h in range(2):
                        store(2 * r + h, h)
                        sp.wait_ge(PE.sem, PE.now("y", 2 * r + h))
                        load(2 * r + (h + 2), h)
                for h in range(2):
                    store(NCH - 2 + h, h)
                sp.wait_ge(DV.sem, DV.now("s", NCH - 1))
                sp.dma_start(io["wkv_out"][0], S[:, :, :]).then_inc(s_y, 16)
                sp.wait_ge(s_y, 16 * NCH + 32 + 16)

            @block.tensor
            def _(pe):
                PE.credit(pe)
                one = pe.alloc_register("rwc_one")
                pe.reg_mov(one, 1)
                with pe.Fori(0, NCH // 2) as r:
                    for h in range(2):
                        c = 2 * r + h
                        at = pe_at_of(pe, c, one)
                        pe.wait_ge(s_in[h], 16 * r + 16)
                        pe.wait_ge(DV.sem, DV.before("s", c))
                        pe.wait_ge(AC.sem, AC.before("y", c))
                        pe.wait_ge(s_init, one)
                        pe.reg_alu(one, one, 1, ALU.max)

                        def modulation():
                            pe.wait_ge(s_wa[h], 16 * r + 16)
                            pe.reg_alu(one, one, 1, ALU.max)
                            for m in range(ADA_STEP):
                                for kc in range(KC):
                                    yield nc.tensor.matmul(modp[:, m, :], wa[h][:, kc, m * P:(m + 1) * P], k.cT[:, kc, :],
                                                           start=kc == 0, stop=kc == KC - 1)

                        rest = modulation()
                        rw_matrix_pe(k, b, pe, in5[h], LEVELS, at, lambda n: [next(rest, None) for _ in range(n)])
                        for mm in rest:
                            pass
                        mm.then_inc(*PE.inc("mod"))
                        at(AC, "tok")
                        for p_, rows in heads:
                            o_ = four(BANK_U)[rows, p_, :]
                            nc.tensor.matmul(o_, in5[h][rows, KA, p_, :], S[rows, p_, :], start=True, stop=False)
                            mm = nc.tensor.matmul(o_, b.mt[rows, p_, 128:192], b.tok[rows, 2, p_, :], start=False, stop=True)
                        mm.then_inc(*PE.inc("rhs"))
                        at(DV, "rhs")
                        for p_, rows in heads:
                            mm = nc.tensor.matmul(four(BANK_U)[rows, p_, :], b.xy[rows, p_, 1, :], b.rhs[rows, p_, :],
                                                  start=True, stop=True)
                        mm.then_inc(*PE.inc("u"))
                        at(AC, "u")
                        for p_, rows in heads:
                            o_ = four(BANK_Y)[rows, p_, :]
                            nc.tensor.matmul(o_, S[rows, p_, :], in5[h][rows, RB, p_, :], start=True, stop=False)
                            nc.tensor.matmul(o_, b.u[rows, p_, :], b.mt[rows, p_, 64:128], start=False, stop=False)
                            mm = nc.tensor.matmul(o_, b.tok[rows, 2, p_, :], b.mt[rows, p_, 192:256], start=False, stop=True)
                        mm.then_inc(*PE.inc("y"))
                        for p_, rows in heads:
                            o_ = four(BANK_S)[rows, p_, :]
                            nc.tensor.matmul(o_, b.tok[rows, 0, p_, :], b.u[rows, p_, :], start=True, stop=False)
                            mm = nc.tensor.matmul(o_, b.tok[rows, 1, p_, :], b.tok[rows, 2, p_, :], start=False, stop=True)
                        mm.then_inc(*PE.inc("s"))

            @block.scalar
            def _(act):
                AC.credit(act)
                act.sem_inc(s_y, 32)
                with act.Fori(0, NCH // 2) as r:
                    for h in range(2):
                        c = 2 * r + h
                        at = at_of(act, c)
                        rw_matrix_act(k, b, LEVELS, at)
                        at(PE, "u")
                        nc.scalar.activation(b.u[:, :, :].rearrange("p a t -> p (a t)"), b.ps[:, BANK_U, 0:256],
                                             ACT.Copy, scale=-1.0).then_inc(*AC.inc("u"))
                        at(PE, "y")
                        act.wait_ge(s_y, 32 * r + 32)
                        nc.scalar.activation(y[h][:, :, :].rearrange("p a t -> p (a t)"), b.ps[:, BANK_Y, 0:256],
                                             ACT.Copy).then_inc(*AC.inc("y"))

            @block.vector
            def _(dve):
                v = nc.vector
                DV.credit(dve)
                v.memset(S[:, :, :], 0.0).then_inc(s_init, 1)
                with dve.Fori(0, NCH // 2) as r:
                    for h in range(2):
                        c = 2 * r + h
                        at = at_of(dve, c)

                        def modulation():
                            at(PE, "mod")
                            tiles = bass.ds(c * ADA_STEP + ADA_FIRST, ADA_STEP)
                            v.tensor_tensor(k.mod[:, tiles, :], modp, bc(k.par[:, tiles].unsqueeze(2), [P, ADA_STEP, NCOND]),
                                            ALU.add).then_inc(*DV.inc("mod"))

                        rw_matrix_dve(k, b, 0, LEVELS, at)
                        modulation()
                        at(PE, "rhs")
                        v.tensor_copy(b.rhs[:, :, :], four(BANK_U)).then_inc(*DV.inc("rhs"))
                        at(PE, "s")
                        dve.wait_ge(s_init, 1)
                        dve.wait_ge(DV.sem, DV.before("s", c))
                        v.tensor_tensor(S[:, :, :], four(BANK_S), S[:, :, :], ALU.add).then_inc(*DV.inc("s_add"))
                        at(DV, "s_add")
                        v.tensor_tensor(S[:, :, :], S[:, :, :], bc(k.lam_end[:, :, bass.ds(c, 1)], [P, NPAIR, CL]),
                                        ALU.mult).then_inc(*DV.inc("s"))
                dve.wait_ge(DV.sem, DV.now("mod", NCH - 1))
                scale_gain(k, SC2, "norm2_g").then_inc(s_mod, 1)
                scale_gain(k, SCF, "final_g").then_inc(s_mod, 1)


def phase_rw_samples(k):
    nc, io = k.nc, k.io
    levels = DSEQ.bit_length() - 1
    with ExitStack() as ctx:
        b = RwBuffers(k, ctx, "rws", levels)
        PE, AC, DV = b.PE, b.AC, b.DV
        sb = lambda n, s: ctx.enter_context(nc.sbuf_tensor(f"rws_{n}", s, F32))
        in5 = sb("in", [P, 5, NPAIR, CL])
        S = sb("state", [P, NSEQ, NPAIR, CL])
        y = sb("y", [P, NPAIR, CL])
        kr = sb("kr", [P, 2 * NPAIR, NSEQ, CL])
        um = sb("um", [P, 2, NPAIR, NSEQ, CL])
        s_in = k.sem("rws_loaded")
        s_out = k.sem("rws_stored")
        heads = [(p_, rows) for p_ in range(NPAIR) for rows in halves()]
        four = lambda bank: b.ps[:, bank, 0:256].rearrange("p (a t) -> p a t", a=4)
        at_of = lambda eng: (lambda S_, step: eng.wait_ge(S_.sem, S_.done(step)))
        SBANK = (0, 1, 3, 4)

        with nc.Block() as block:
            @block.sync
            def _(sp):
                sp.dma_start(in5[:, :, :, :], io["rwc"][NCH]).then_inc(s_in, 16)
                sp.dma_start(S[:, :, :, :], io["wkvT"].rearrange("s p a v -> p s a v")).then_inc(s_in, 16)
                sp.wait_ge(AC.sem, AC.done("y"))
                sp.dma_start(io["rw_y"][NCH], y[:, :, :]).then_inc(s_out, 16)
                sp.wait_ge(DV.sem, DV.done("s"))
                sp.dma_start(io["wkv_out"][1:NCOND].rearrange("s p a v -> p s a v"), S[:, :, :, :]).then_inc(s_out, 16)
                sp.wait_ge(s_out, 32)

            @block.tensor
            def _(pe):
                at = at_of(pe)
                pe.wait_ge(s_in, 32)
                rw_matrix_pe(k, b, pe, in5, levels, at)
                at(AC, "tok")
                at(DV, "masked")
                for p_, rows in heads:
                    o_ = four(BANK_U)[rows, p_, :]
                    for s in range(NSEQ):
                        nc.tensor.matmul(o_, kr[rows, p_, s, :], S[rows, s, p_, :], start=s == 0, stop=False)
                    mm = nc.tensor.matmul(o_, b.mt[rows, p_, 128:192], b.tok[rows, 2, p_, :], start=False, stop=True)
                mm.then_inc(*PE.inc("rhs"))
                at(DV, "rhs")
                for p_, rows in heads:
                    mm = nc.tensor.matmul(four(BANK_U)[rows, p_, :], b.xy[rows, p_, 1, :], b.rhs[rows, p_, :],
                                          start=True, stop=True)
                mm.then_inc(*PE.inc("u"))
                at(AC, "u")
                for p_, rows in heads:
                    o_ = four(BANK_Y)[rows, p_, :]
                    for s in range(NSEQ):
                        nc.tensor.matmul(o_, S[rows, s, p_, :], kr[rows, NPAIR + p_, s, :], start=s == 0, stop=False)
                    nc.tensor.matmul(o_, b.u[rows, p_, :], b.mt[rows, p_, 64:128], start=False, stop=False)
                    mm = nc.tensor.matmul(o_, b.tok[rows, 2, p_, :], b.mt[rows, p_, 192:256], start=False, stop=True)
                mm.then_inc(*PE.inc("y"))
                at(DV, "umask")
                for p_, rows in heads:
                    o_ = b.ps[rows, SBANK[p_], :]
                    nc.tensor.matmul(o_, b.tok[rows, 0, p_, :], um[rows, 0, p_, :, :], start=True, stop=False)
                    mm = nc.tensor.matmul(o_, b.tok[rows, 1, p_, :], um[rows, 1, p_, :, :], start=False, stop=True)
                mm.then_inc(*PE.inc("s"))

            @block.scalar
            def _(act):
                at = at_of(act)
                rw_matrix_act(k, b, levels, at)
                at(PE, "u")
                nc.scalar.activation(b.u[:, :, :].rearrange("p a t -> p (a t)"), b.ps[:, BANK_U, 0:256],
                                     ACT.Copy, scale=-1.0).then_inc(*AC.inc("u"))
                at(PE, "y")
                nc.scalar.activation(y[:, :, :].rearrange("p a t -> p (a t)"), b.ps[:, BANK_Y, 0:256],
                                     ACT.Copy).then_inc(*AC.inc("y"))

            @block.vector
            def _(dve):
                v = nc.vector
                at = at_of(dve)
                rw_matrix_dve(k, b, 1, levels, at)
                dve.wait_ge(s_in, 32)
                src = in5[:, 0:2, :, :].rearrange("p q a t -> p (q a) t").unsqueeze(2)
                v.tensor_tensor(kr[:, :, :, :], bc(src, [P, 2 * NPAIR, NSEQ, CL]),
                                bc(k.seq_cols[:, :, :].unsqueeze(1), [P, 2 * NPAIR, NSEQ, CL]),
                                ALU.mult).then_inc(*DV.inc("masked"))
                at(PE, "rhs")
                v.tensor_copy(b.rhs[:, :, :], four(BANK_U)).then_inc(*DV.inc("rhs"))
                at(AC, "u")
                rows_of = bc(k.seq_rows[:, :].unsqueeze(1).unsqueeze(3), [P, NPAIR, NSEQ, CL])
                v.tensor_tensor(um[:, 0], bc(b.u[:, :, :].unsqueeze(2), [P, NPAIR, NSEQ, CL]), rows_of, ALU.mult)
                v.tensor_tensor(um[:, 1], bc(b.tok[:, 2, :, :].unsqueeze(2), [P, NPAIR, NSEQ, CL]), rows_of,
                                ALU.mult).then_inc(*DV.inc("umask"))
                at(PE, "s")
                for p_ in range(NPAIR):
                    last = v.tensor_tensor(S[:, :, p_, :], b.ps[:, SBANK[p_], :].rearrange("p (s t) -> p s t", s=NSEQ),
                                           S[:, :, p_, :], ALU.add)
                last.then_inc(*DV.inc("s_add"))
                at(DV, "s_add")
                for p_ in range(NPAIR):
                    last = v.tensor_tensor(S[:, :, p_, :], S[:, :, p_, :],
                                           bc(k.lam_end[:, p_, NCH:NCH + NSEQ].unsqueeze(2), [P, NSEQ, CL]), ALU.mult)
                last.then_inc(*DV.inc("s"))


def phase_ssd(k):
    for c in ("prompt", "samples"):
        ssd_chunks(k, c)


def ssd_chunks(k, which):
    nc, io = k.nc, k.io
    smp = which == "samples"
    L = NSEQ * DSEQ if smp else SL
    rounds = 1 if smp else NSC // 2
    slots = 1 if smp else 2
    tag = "ss" if smp else "sp"
    with ExitStack() as ctx:
        sb = lambda n, s: ctx.enter_context(nc.sbuf_tensor(f"{tag}_{n}", s, F32))
        inx = [sb(f"in{i}", [P, NXBC, L]) for i in range(slots)]
        rows = [sb(f"rows{i}", [SH, 3, L]) for i in range(slots)]
        y = [sb(f"y{i}", [P, KC, L]) for i in range(slots)]
        S = sb("state", [P, NSEQ if smp else 1, SH, SD])
        col = sb("col", [P, 3, SH])
        cb = sb("cb", [P, SG, L])
        btok = sb("btok", [P, SG, SN])
        xt = sb("xt", [P, SH, SD])
        xd = sb("xd", [P, SH, SD])
        w = sb("w", [P, SH, L])
        ce = sb("ce", [P, SH, L])
        end = sb("end", [P, NSEQ if smp else 1, SH])
        xm = [sb(f"xm{i}", [P, SH, SD]) for i in range(2)] if smp else None
        ps = ctx.enter_context(nc.psum_tensor(f"{tag}_ps", [P, 8, 512], F32))
        s_in = [k.sem(f"{tag}_in{i}_loaded") for i in range(slots)]
        s_S = k.sem(f"{tag}_state_ready")
        s_y = k.sem(f"{tag}_y_stored")
        s_out = k.sem(f"{tag}_state_stored")
        s_xm = k.sem(f"{tag}_masked_x")
        s_sm = k.sem(f"{tag}_state_matmul")
        s_sv = k.sem(f"{tag}_state_step")
        PE = Progress(k.sem(f"{tag}_pe"), "col", "bc", "x", "csb", "y", "s")
        AC = Progress(k.sem(f"{tag}_act"), "col", "btok", "excs", "dec", "y")
        DV = Progress(k.sem(f"{tag}_dve"), "cb", "x", "xd", "diff", "end", "w", "ce", "s_decay", "s")
        cview = ps[:, 0, 0:3 * SH].rearrange("p (q h) -> p q h", q=3)
        bcv = ps[:, 1, :].rearrange("p (i g m) -> p i g m", i=2, g=SG)
        xv = ps[:, 2:4, :].rearrange("p a b -> p (a b)").rearrange("p (h m) -> p h m", h=SH)
        csb = ps[:, 4:8, :].rearrange("p a b -> p (a b)")[:, 0:SH * SL].rearrange("p (h l) -> p h l", h=SH)[:, :, 0:L]
        yv = ps[:, 2:4, :].rearrange("p a b -> p (a b)").rearrange("p (a l) -> p a l", a=KC)[:, :, 0:L]
        tokens = lambda c: slice(SEQ, T) if smp else bass.ds(c * SL, SL)

        def at_of(eng, c):
            if smp:
                return lambda S_, step: eng.wait_ge(S_.sem, S_.done(step))
            return lambda S_, step: eng.wait_ge(S_.sem, S_.now(step, c))

        def chunks(eng):
            if smp:
                yield 0, 0, 0
                return
            with eng.Fori(0, rounds) as r:
                for h in range(2):
                    yield 2 * r + h, h, r

        with nc.Block() as block:
            @block.sync
            def _(sp):
                if smp:
                    sp.dma_start(S[:, :, :, :].rearrange("p s h m -> p s (h m)"), io["ssmT"].rearrange("s n m -> n s m")).then_inc(s_S, 16)
                for c, h, r in chunks(sp):
                    if not smp:
                        sp.wait_ge(PE.sem, PE.before("y", 2 * r))
                        sp.wait_ge(DV.sem, DV.before("ce", 2 * r))
                    sp.dma_start(inx[h][:, :, :], io["xbc"][:, :, tokens(c)].rearrange("a p t -> p a t")).then_inc(s_in[h], 16)
                    sp.dma_start(rows[h][:, :, :], io["ssd_rows"][:, :, tokens(c)]).then_inc(s_in[h], 16)
                if smp:
                    sp.wait_ge(s_sv, 2 * NSEQ * 2)
                    sp.dma_start(io["ssm_out"][1:NCOND].rearrange("s n m -> n s m"), S[:, :, :, :].rearrange("p s h m -> p s (h m)")).then_inc(s_S, 16)
                    sp.wait_ge(s_S, 32)
                else:
                    sp.wait_ge(DV.sem, DV.now("s", NSC - 1))
                    sp.dma_start(io["ssm_out"][0], S[:, 0, :, :].rearrange("p h m -> p (h m)")).then_inc(s_out, 16)
                    sp.wait_ge(s_out, 16)

            @block.gpsimd
            def _(pool):
                for c, h, r in chunks(pool):
                    at_of(pool, c)(AC, "y")
                    pool.dma_start(io["ssd_y"][:, :, tokens(c)].rearrange("a p t -> p a t"), y[h][:, :, :]).then_inc(s_y, 16)
                pool.wait_ge(s_y, 16 if smp else 16 * NSC)

            @block.tensor
            def _(pe):
                if not smp:
                    PE.credit(pe)
                for c, h, r in chunks(pe):
                    at = at_of(pe, c)
                    pe.wait_ge(s_in[h], 32 * r + 32)
                    if not smp:
                        pe.wait_ge(DV.sem, DV.before("s", c))
                        pe.wait_ge(AC.sem, AC.before("y", c))
                        pe.wait_ge(s_S, 1)
                    for i in range(3):
                        mm = nc.tensor.matmul(cview[0:L, i, :], rows[h][:, i, :], k.ident[0:SH, 0:SH], start=True, stop=True)
                    mm.then_inc(*PE.inc("col"))
                    for g in range(SG):
                        nc.tensor.matmul(bcv[0:L, 0, g, 0:L], inx[h][:, 8 + g, :], inx[h][:, 10 + g, :], start=True, stop=True)
                        mm = nc.tensor.transpose(bcv[0:L, 1, g, :], inx[h][:, 8 + g, :], k.ident[:, :])
                    mm.then_inc(*PE.inc("bc"))
                    for i in range(KC):
                        mm = nc.tensor.transpose(xv[0:L, 2 * i:2 * i + 2, :].rearrange("p h m -> p (h m)"), inx[h][:, i, :], k.ident[:, :])
                    mm.then_inc(*PE.inc("x"))
                    for i in range(SH):
                        mm = nc.tensor.matmul(csb[:, i, :], k.head_sel[:, i, :], rows[h][:, 1, :], start=True, stop=True)
                    mm.then_inc(*PE.inc("csb"))
                    if smp:
                        pe.wait_ge(s_S, 16)
                    at(DV, "x")
                    at(DV, "w")
                    at(DV, "ce")
                    for i in range(SH):
                        o_ = yv[64 * (i % 2):64 * (i % 2) + 64, i // 2, :]
                        nc.tensor.matmul(o_, xt[0:L, i, :], w[0:L, i, :], start=True, stop=False)
                        if smp:
                            for s in range(NSEQ):
                                t = slice(DSEQ * s, DSEQ * s + DSEQ)
                                mm = nc.tensor.matmul(o_[:, t], S[:, s, i, :], ce[:, i, t], start=False, stop=s == NSEQ - 1)
                        else:
                            mm = nc.tensor.matmul(o_, S[:, 0, i, :], ce[:, i, :], start=False, stop=True)
                    mm.then_inc(*PE.inc("y"))
                    at(AC, "col")
                    at(AC, "btok")
                    at(DV, "xd")
                    if smp:
                        for s in range(NSEQ):
                            pe.wait_ge(s_xm, s + 1)
                            for g in range(SG):
                                n = 2 * s + g
                                if n >= 2:
                                    pe.wait_ge(s_sv, 2 * (n - 1))
                                nc.tensor.matmul(ps[:, n % 2, :], btok[0:L, g, :],
                                                 xm[s % 2][0:L, 8 * g:8 * g + 8, :].rearrange("p h m -> p (h m)"),
                                                 start=True, stop=True).then_inc(s_sm, 1)
                    else:
                        for g in range(SG):
                            mm = nc.tensor.matmul(ps[:, g, :], btok[:, g, :], xd[:, 8 * g:8 * g + 8, :].rearrange("p h m -> p (h m)"),
                                                  start=True, stop=True)
                        mm.then_inc(*PE.inc("s"))

            @block.scalar
            def _(act):
                a = nc.scalar
                if not smp:
                    AC.credit(act)
                for c, h, r in chunks(act):
                    at = at_of(act, c)
                    at(PE, "col")
                    a.activation(col[0:L, 0:2, :], cview[0:L, 0:2, :], ACT.Copy)
                    a.activation(col[0:L, 2, :], cview[0:L, 2, :], ACT.Exp).then_inc(*AC.inc("col"))
                    at(PE, "bc")
                    a.activation(btok[0:L, :, :], bcv[0:L, 1, :, :], ACT.Copy).then_inc(*AC.inc("btok"))
                    at(PE, "csb")
                    a.activation(ce[:, :, :], csb, ACT.Exp).then_inc(*AC.inc("excs"))
                    at(DV, "diff")
                    a.activation(w[0:L, :, :], w[0:L, :, :], ACT.Exp).then_inc(*AC.inc("dec"))
                    at(PE, "y")
                    if not smp:
                        act.wait_ge(s_y, 32 * r)
                    a.activation(y[h][:, :, :], yv, ACT.Copy).then_inc(*AC.inc("y"))

            @block.vector
            def _(dve):
                v = nc.vector
                if not smp:
                    DV.credit(dve)
                    v.memset(S[:, 0, :, :], 0.0).then_inc(s_S, 1)
                mask = k.ssd_mask_smp if smp else k.ssd_mask
                for c, h, r in chunks(dve):
                    at = at_of(dve, c)
                    at(AC, "btok")
                    v.tensor_tensor(cb[0:L, :, :], bcv[0:L, 0, :, 0:L], bc(mask[0:L, 0:L].unsqueeze(1), [L, SG, L]),
                                    ALU.mult).then_inc(*DV.inc("cb"))
                    at(PE, "x")
                    v.tensor_tensor(xt[0:L, :, :], xv[0:L, :, :], bc(col[0:L, 0, :].unsqueeze(2), [L, SH, SD]), ALU.mult).then_inc(*DV.inc("x"))
                    at(DV, "x")
                    v.tensor_tensor(xd[0:L, :, :], xt[0:L, :, :], bc(col[0:L, 2, :].unsqueeze(2), [L, SH, SD]), ALU.mult).then_inc(*DV.inc("xd"))
                    at(AC, "excs")
                    for i in range(SH):
                        last = v.tensor_scalar(w[0:L, i, :], csb[0:L, i, :], col[0:L, 1, i:i + 1], 0.0, ALU.subtract, ALU.min)
                    last.then_inc(*DV.inc("diff"))
                    if smp:
                        v.tensor_copy(end[:, :, :], ce[:, :, DSEQ - 1:L:DSEQ].rearrange("p h s -> p s h")).then_inc(*DV.inc("end"))
                    else:
                        v.tensor_copy(end[:, 0, :], ce[:, :, L - 1]).then_inc(*DV.inc("end"))
                    at(AC, "dec")
                    for g in range(SG):
                        hh = slice(8 * g, 8 * g + 8)
                        last = v.tensor_tensor(w[0:L, hh, :], w[0:L, hh, :], bc(cb[0:L, g:g + 1, :], [L, 8, L]), ALU.mult)
                    last.then_inc(*DV.inc("w"))
                    at(DV, "end")
                    for g in range(SG):
                        hh = slice(8 * g, 8 * g + 8)
                        last = v.tensor_tensor(ce[:, hh, :], ce[:, hh, :], bc(inx[h][:, 10 + g:11 + g, :], [P, 8, L]), ALU.mult)
                    last.then_inc(*DV.inc("ce"))
                    at(PE, "y")
                    if smp:
                        for s in range(NSEQ):
                            if s >= 2:
                                dve.wait_ge(s_sm, 2 * (s - 1))
                            v.tensor_scalar(xm[s % 2][0:L, :, :], xd[0:L, :, :], k.seq_rows[0:L, s:s + 1], None, ALU.mult).then_inc(s_xm, 1)
                            for g in range(SG):
                                n = 2 * s + g
                                sv = S[:, s, 8 * g:8 * g + 8, :]
                                v.tensor_tensor(sv, sv, bc(end[:, s, 8 * g:8 * g + 8].unsqueeze(2), [P, 8, SD]), ALU.mult).then_inc(s_sv, 1)
                                dve.wait_ge(s_sv, 2 * n + 1)
                                dve.wait_ge(s_sm, n + 1)
                                v.tensor_tensor(sv, sv, ps[:, n % 2, :].rearrange("p (h m) -> p h m", h=8), ALU.add).then_inc(s_sv, 1)
                    else:
                        dve.wait_ge(s_S, 1)
                        v.tensor_tensor(S[:, 0], S[:, 0], bc(end[:, 0, :].unsqueeze(2), [P, SH, SD]), ALU.mult).then_inc(*DV.inc("s_decay"))
                        at(DV, "s_decay")
                        at(PE, "s")
                        for g in range(SG):
                            sv = S[:, 0, 8 * g:8 * g + 8, :]
                            last = v.tensor_tensor(sv, sv, ps[:, g, :].rearrange("p (h m) -> p h m", h=8), ALU.add)
                        last.then_inc(*DV.inc("s"))


def phase_rw_post(k, oa):
    nc, io = k.nc, k.io
    with ExitStack() as ctx:
        sb = lambda n, s: ctx.enter_context(nc.sbuf_tensor(f"ro_{n}", s, F32))
        y, gate, bonus = ([sb(f"{n}{i}", [P, T]) for i in range(2)] for n in ("y", "gate", "bonus"))
        sq, rs = sb("sq", [P, T]), sb("rs", [P, T])
        ps = [ctx.enter_context(nc.psum_tensor(f"ro_ps{i}", [P, 3, 512], F32)) for i in range(2)]
        pm, pv = (flat(p_[:, :, :]) for p_ in ps)
        s_in = [k.sem(f"ro_in{i}_loaded") for i in range(2)]
        PE = Progress(k.sem("ro_pe"), "mean", "var")
        AC = Progress(k.sem("ro_act"), "sq", "ln", "rstd")
        DV = Progress(k.sem("ro_dve"), "center", "norm", "affine", "bonus", "gate")
        with nc.Block() as block:
            @block.sync
            def _(sp):
                for p_ in range(NPAIR):
                    h = p_ % 2
                    if p_ >= 2:
                        sp.wait_ge(DV.sem, DV.done("gate", p_ - 2))
                    sp.dma_start(y[h][:, :].rearrange("p (c t) -> p c t", t=CL),
                                 io["rw_y"][:, :, p_, :].rearrange("c p t -> p c t")).then_inc(s_in[h], 16)
                    sp.dma_start(gate[h][:, :], io["rw_gate"][p_]).then_inc(s_in[h], 16)
                    sp.dma_start(bonus[h][:, :], io["rw_bonus"][p_]).then_inc(s_in[h], 16)

            @block.tensor
            def _(pe):
                for p_ in range(NPAIR):
                    pe.wait_ge(s_in[p_ % 2], 48 * (p_ // 2 + 1))
                    for out, src, step in ((pm, y[p_ % 2], "mean"), (pv, sq, "var")):
                        if step == "var":
                            pe.wait_ge(AC.sem, AC.done("sq", p_))
                        elif p_ >= 1:
                            pe.wait_ge(DV.sem, DV.done("center", p_ - 1))
                        for a, b in TOK_CHUNKS_BANKED:
                            mm = nc.tensor.matmul(out[:, a:b], k.pairones[:, :], src[:, a:b], start=True, stop=True)
                        mm.then_inc(*PE.inc(step))

            @block.scalar
            def _(act):
                for p_ in range(NPAIR):
                    act.wait_ge(DV.sem, DV.done("center", p_))
                    nc.scalar.activation(sq[:, :], y[p_ % 2][:, :], ACT.Square).then_inc(*AC.inc("sq"))
                    act.wait_ge(PE.sem, PE.done("var", p_))
                    nc.scalar.activation(rs[:, :], pv[:, 0:T], ACT.Ln, scale=1.0 / RD, bias=k.const[:, 1:2]).then_inc(*AC.inc("ln"))
                    act.wait_ge(AC.sem, AC.done("ln", p_))
                    nc.scalar.activation(rs[:, :], rs[:, :], ACT.Exp, scale=-0.5).then_inc(*AC.inc("rstd"))

            @block.vector
            def _(dve):
                v = nc.vector
                lnw, lnb = k.par[:, PCOLS["ln_w"]], k.par[:, PCOLS["ln_b"]]
                for p_ in range(NPAIR):
                    h = p_ % 2
                    yt = y[h][:, :]
                    now = lambda s_: dve.wait_ge(DV.sem, DV.done(s_, p_))
                    dve.wait_ge(PE.sem, PE.done("mean", p_))
                    v.scalar_tensor_tensor(out=yt, in0=pm[:, 0:T], scalar=-1.0 / RD, in1=yt, op0=ALU.mult,
                                           op1=ALU.add).then_inc(*DV.inc("center"))
                    dve.wait_ge(AC.sem, AC.done("rstd", p_))
                    v.tensor_tensor(yt, yt, rs[:, :], ALU.mult).then_inc(*DV.inc("norm"))
                    now("norm")
                    v.tensor_scalar(yt, yt, lnw[:, p_:p_ + 1], lnb[:, p_:p_ + 1], ALU.mult, ALU.add).then_inc(*DV.inc("affine"))
                    now("affine")
                    v.tensor_tensor(yt, yt, bonus[h][:, :], ALU.add).then_inc(*DV.inc("bonus"))
                    now("bonus")
                    v.tensor_tensor(oa[:, p_, :], yt, gate[h][:, :], ALU.mult).then_inc(*DV.inc("gate"))


def phase_ssd_post(k, ob):
    nc, io = k.nc, k.io
    GT = KC // SG
    with ExitStack() as ctx:
        sb = lambda n, s: ctx.enter_context(nc.sbuf_tensor(f"so_{n}", s, F32))
        y, x, z = ([sb(f"{n}{i}", [P, T]) for i in range(2)] for n in ("y", "x", "z"))
        sg, sq, rs = sb("sg", [P, T]), sb("sq", [P, T]), sb("rs", [P, T])
        d = sb("d", [P, KC])
        ps = ctx.enter_context(nc.psum_tensor("so_ps", [P, 3, 512], F32))
        pf = flat(ps[:, :, :])
        s_in = [k.sem(f"so_in{i}_loaded") for i in range(2)]
        s_d = k.sem("so_d_loaded")
        s_r = k.sem("so_rstd_step")
        s_n = k.sem("so_scaled")
        PE = Progress(k.sem("so_pe"), "sum")
        AC = Progress(k.sem("so_act"), "sigmoid", "sq")
        DV = Progress(k.sem("so_dve"), "silu", "skip", "gate")
        with nc.Block() as block:
            @block.sync
            def _(sp):
                for h, rows in enumerate(halves()):
                    sp.dma_start(d[rows, :], bc(io["ssm_D"][h:h + 1, :], [64, KC])).then_inc(s_d, 16)
                for i in range(KC):
                    if i >= 2:
                        sp.wait_ge(DV.sem, DV.done("gate", i - 2))
                    for t, src in ((y, io["ssd_y"][i]), (x, io["xbc"][i]), ):
                        sp.dma_start(t[i % 2][:, :], src).then_inc(s_in[i % 2], 16)
                    zsrc = io["proj"][Z0 + i]
                    (_, zp), (_, zs) = predecessor_views(zsrc)
                    op, os = token_views(z[i % 2])
                    sp.dma_start(op, zp).then_inc(s_in[i % 2], 16)
                    sp.dma_start(os, zs).then_inc(s_in[i % 2], 16)

            @block.tensor
            def _(pe):
                for i in range(KC):
                    pe.wait_ge(AC.sem, AC.done("sq", i))
                    if i and i % GT == 0:
                        pe.wait_ge(s_r, 2 * (i // GT))
                    for a, b in TOK_CHUNKS_BANKED:
                        mm = nc.tensor.matmul(pf[:, a:b], k.ones[:, :], sq[:, a:b], start=i % GT == 0, stop=i % GT == GT - 1)
                    mm.then_inc(*PE.inc("sum"))

            @block.scalar
            def _(act):
                for i in range(KC):
                    act.wait_ge(s_in[i % 2], 64 * (i // 2 + 1))
                    if i:
                        act.wait_ge(DV.sem, DV.done("silu", i - 1))
                    nc.scalar.activation(sg[:, :], z[i % 2][:, :], ACT.Sigmoid).then_inc(*AC.inc("sigmoid"))
                    act.wait_ge(DV.sem, DV.done("gate", i))
                    if i:
                        act.wait_ge(PE.sem, PE.done("sum", i - 1))
                    nc.scalar.activation(sq[:, :], ob[:, i, :], ACT.Square).then_inc(*AC.inc("sq"))
                    if i % GT == GT - 1:
                        act.wait_ge(PE.sem, PE.done("sum", i))
                        if i > GT:
                            act.wait_ge(s_n, GT)
                        nc.scalar.activation(rs[:, :], pf[:, 0:T], ACT.Ln, scale=1.0 / (GT * P), bias=k.const[:, 0:1]).then_inc(s_r, 1)
                        act.wait_ge(s_r, 2 * (i // GT) + 1)
                        nc.scalar.activation(rs[:, :], rs[:, :], ACT.Exp, scale=-0.5).then_inc(s_r, 1)

            @block.vector
            def _(dve):
                v = nc.vector
                nw = k.par[:, PCOLS["ssm_norm_w"]]
                dve.wait_ge(s_d, 32)
                for i in range(KC):
                    h = i % 2
                    now = lambda s_: dve.wait_ge(DV.sem, DV.done(s_, i))
                    dve.wait_ge(AC.sem, AC.done("sigmoid", i))
                    v.tensor_tensor(z[h][:, :], z[h][:, :], sg[:, :], ALU.mult).then_inc(*DV.inc("silu"))
                    v.scalar_tensor_tensor(out=y[h][:, :], in0=x[h][:, :], scalar=d[:, i:i + 1], in1=y[h][:, :],
                                           op0=ALU.mult, op1=ALU.add).then_inc(*DV.inc("skip"))
                    now("skip")
                    v.tensor_tensor(ob[:, i, :], y[h][:, :], z[h][:, :], ALU.mult).then_inc(*DV.inc("gate"))
                    if i % GT == GT - 1:
                        dve.wait_ge(s_r, 2 * (i // GT) + 2)
                        now("gate")
                        for j in range(i - GT + 1, i + 1):
                            v.scalar_tensor_tensor(out=ob[:, j, :], in0=ob[:, j, :], scalar=nw[:, j:j + 1], in1=rs[:, :],
                                                   op0=ALU.mult, op1=ALU.mult).then_inc(s_n, 1)


def phase_merge(k, oa, ob, x1):
    nc, io = k.nc, k.io
    with ExitStack() as ctx:
        sb = lambda n, s: ctx.enter_context(nc.sbuf_tensor(f"mg_{n}", s, F32))
        merged = sb("merged", [P, KC, T])
        wa = [sb(f"wa{i}", [P, NPAIR, P]) for i in range(2)]
        wb = [sb(f"wb{i}", [P, KC, P]) for i in range(2)]
        wo = [sb(f"wo{i}", [P, KC, P]) for i in range(2)]
        ga = [sb(f"ga{i}", [P, T]) for i in range(2)]
        gb = [sb(f"gb{i}", [P, T]) for i in range(2)]
        tmp = sb("tmp", [P, T])
        ps = [ctx.enter_context(nc.psum_tensor(f"mg_ps{i}", [P, 3, 512], F32)) for i in range(2)]
        pf = [flat(p_[:, :, :]) for p_ in ps]
        s_w = [k.sem(f"mg_w{i}_loaded") for i in range(2)]
        s_g = [k.sem(f"mg_gates{i}_loaded") for i in range(2)]
        s_wo = [k.sem(f"mg_wo{i}_loaded") for i in range(2)]
        s_x = k.sem("mg_x_loaded")
        s_xs = k.sem("mg_x1_stored")
        PE = Progress(k.sem("mg_pe"), "a", "b")
        AC = Progress(k.sem("mg_act"), "ga", "gb")
        DV = Progress(k.sem("mg_dve"), "a", "b", "sum")
        s_out = k.sem("mg_out_matmul")
        s_res = k.sem("mg_residual_step")

        with nc.Block() as block:
            @block.sync
            def _(sp):
                sp.dma_start(x1[:, :, :], io["xT"]).then_inc(s_x, 16)
                for m in range(KC):
                    h = m % 2
                    if m >= 2:
                        sp.wait_ge(PE.sem, PE.done("b", m - 2))
                    sp.dma_start(wa[h][:, :, :], io["w_pa"][m]).then_inc(s_w[h], 16)
                    sp.dma_start(wb[h][:, :, :], io["w_pb"][m]).then_inc(s_w[h], 16)
                    if m >= 2:
                        sp.wait_ge(DV.sem, DV.done("sum", m - 2))
                    for t, at in ((ga, 0), (gb, KC)):
                        (_, gp), (_, gs) = predecessor_views(io["proj"][GATE0 + at + m])
                        op, os = token_views(t[h])
                        sp.dma_start(op, gp).then_inc(s_g[h], 16)
                        sp.dma_start(os, gs).then_inc(s_g[h], 16)
                for m in range(KC):
                    if m >= 2:
                        sp.wait_ge(s_out, m - 1)
                    sp.dma_start(wo[m % 2][:, :, :], io["w_out"][m]).then_inc(s_wo[m % 2], 16)
                sp.wait_ge(s_res, 3 * KC)
                sp.dma_start(io["x1"], x1[:, :, :]).then_inc(s_xs, 16)
                sp.wait_ge(s_xs, 16)

            @block.tensor
            def _(pe):
                for m in range(KC):
                    h = m % 2
                    pe.wait_ge(s_w[h], 32 * (m // 2 + 1))
                    for out, w, src, n, step in ((pf[0], wa[h], oa, NPAIR, "a"), (pf[1], wb[h], ob, KC, "b")):
                        if m:
                            pe.wait_ge(DV.sem, DV.done(step, m - 1))
                        for kc in range(n):
                            for a, b in TOK_CHUNKS_BANKED:
                                mm = nc.tensor.matmul(out[:, a:b], w[:, kc, :], src[:, kc, a:b], start=kc == 0, stop=kc == n - 1)
                        mm.then_inc(*PE.inc(step))
                pe.wait_ge(DV.sem, DV.done("sum", KC - 1))
                for m in range(KC):
                    pe.wait_ge(s_wo[m % 2], 16 * (m // 2 + 1))
                    if m >= 2:
                        pe.wait_ge(s_res, 3 * (m - 1))
                    for kc in range(KC):
                        for a, b in TOK_CHUNKS_BANKED:
                            mm = nc.tensor.matmul(pf[m % 2][:, a:b], wo[m % 2][:, kc, :], merged[:, kc, a:b], start=kc == 0, stop=kc == KC - 1)
                    mm.then_inc(s_out, 1)

            @block.scalar
            def _(act):
                for m in range(KC):
                    h = m % 2
                    act.wait_ge(s_g[h], 64 * (m // 2 + 1))
                    nc.scalar.activation(ga[h][:, :], ga[h][:, :], ACT.Sigmoid).then_inc(*AC.inc("ga"))
                    nc.scalar.activation(gb[h][:, :], gb[h][:, :], ACT.Sigmoid).then_inc(*AC.inc("gb"))

            @block.vector
            def _(dve):
                v = nc.vector
                for m in range(KC):
                    h = m % 2
                    dve.wait_ge(AC.sem, AC.done("ga", m))
                    dve.wait_ge(PE.sem, PE.done("a", m))
                    v.tensor_tensor(ga[h][:, :], pf[0][:, 0:T], ga[h][:, :], ALU.mult).then_inc(*DV.inc("a"))
                    dve.wait_ge(AC.sem, AC.done("gb", m))
                    dve.wait_ge(PE.sem, PE.done("b", m))
                    v.tensor_tensor(gb[h][:, :], pf[1][:, 0:T], gb[h][:, :], ALU.mult).then_inc(*DV.inc("b"))
                    dve.wait_ge(DV.sem, DV.done("b", m))
                    v.tensor_tensor(merged[:, m, :], ga[h][:, :], gb[h][:, :], ALU.add).then_inc(*DV.inc("sum"))
                dve.wait_ge(s_x, 16)
                for m in range(KC):
                    dve.wait_ge(s_out, m + 1)
                    add_gated(k, dve, x1[:, m, :], pf[m % 2][:, 0:T], tmp, GT1 + m, s_res, 3 * m)


def add_gated(k, dve, x, y, tmp, gate_at, sem, base):
    v = k.nc.vector
    g = k.mod[:, gate_at, :]
    (xp, xs), (yp, ys), (_, ts) = token_views(x), token_views(y), token_views(tmp)
    if base:
        dve.wait_ge(sem, base)
    v.tensor_tensor(ts, ys, bc(g[:, 1:NCOND].unsqueeze(2), [P, NSEQ, DSEQ]), ALU.mult).then_inc(sem, 1)
    v.scalar_tensor_tensor(out=xp, in0=yp, scalar=g[:, 0:1], in1=xp, op0=ALU.mult, op1=ALU.add).then_inc(sem, 1)
    dve.wait_ge(sem, base + 1)
    v.tensor_tensor(xs, xs, ts, ALU.add).then_inc(sem, 1)


def phase_norm2(k, x, load=None):
    rmsnorm_mod(k, "norm2", x, lambda kc: x[:, kc, 0:SEQ], lambda kc: token_views(x[:, kc, :])[1], SC2, SH2, load)


NTILE = -(-T // P)
LAST = T - (NTILE - 1) * P
NEG = -3.0e38


def phase_scores(k, xn2, scores):
    nc, io = k.nc, k.io
    NQ = 2 * PH
    with ExitStack() as ctx:
        sb = lambda n, s: ctx.enter_context(nc.sbuf_tensor(f"sc_{n}", s, F32))
        w = [sb(f"w{i}", [P, KC, P]) for i in range(2)]
        q = [sb(f"q{i}", [P, T]) for i in range(2)]
        keys = sb("keys", [P, NQ, NK])
        psq = ctx.enter_context(nc.psum_tensor("sc_psq", [P, 3, 512], F32))
        pss = ctx.enter_context(nc.psum_tensor("sc_pss", [P, 3, 512], F32))
        pq = flat(psq[:, :, :])
        s_w = [k.sem(f"sc_w{i}_loaded") for i in range(2)]
        s_k = k.sem("sc_keys_loaded")
        s_q = k.sem("sc_query_matmul")
        s_s = k.sem("sc_score_matmul")
        s_qe = k.sem("sc_query_evac")
        s_se = k.sem("sc_score_evac")
        with nc.Block() as block:
            @block.sync
            def _(sp):
                sp.dma_start(keys[:, :, :], io["keysT"]).then_inc(s_k, 16)
                for i in range(NQ):
                    if i >= 2:
                        sp.wait_ge(s_q, i - 1)
                    sp.dma_start(w[i % 2][:, :, :], io["w_q"][i]).then_inc(s_w[i % 2], 16)

            def score(pe, i):
                pe.wait_ge(s_qe, i + 1)
                if i:
                    pe.wait_ge(s_se, i)
                for j in range(NTILE):
                    n = LAST if j == NTILE - 1 else P
                    mm = nc.tensor.matmul(flat(pss[:, :, :])[0:n, j * NK:(j + 1) * NK], q[i % 2][:, j * P:j * P + n],
                                          keys[:, i, :], start=True, stop=True)
                mm.then_inc(s_s, 1)

            @block.tensor
            def _(pe):
                pe.wait_ge(s_k, 16)
                for i in range(NQ):
                    pe.wait_ge(s_w[i % 2], 16 * (i // 2 + 1))
                    if i:
                        pe.wait_ge(s_qe, i)
                    for kc in range(KC):
                        for a, b in TOK_CHUNKS_BANKED:
                            mm = nc.tensor.matmul(pq[:, a:b], w[i % 2][:, kc, :], xn2[:, kc, a:b], start=kc == 0, stop=kc == KC - 1)
                    mm.then_inc(s_q, 1)
                    if i:
                        score(pe, i - 1)
                score(pe, NQ - 1)

            @block.scalar
            def _(act):
                for i in range(NQ):
                    act.wait_ge(s_q, i + 1)
                    if i >= 2:
                        act.wait_ge(s_s, i - 1)
                    nc.scalar.activation(q[i % 2][:, :], pq[:, 0:T], ACT.Copy).then_inc(s_qe, 1)

            @block.vector
            def _(dve):
                v = nc.vector
                full = (NTILE - 1) * NK
                for i in range(NQ):
                    dve.wait_ge(s_s, i + 1)
                    v.tensor_copy(scores[:, 0:NTILE - 1, i, :], flat(pss[:, :, :])[:, 0:full].rearrange("p (j n) -> p j n", n=NK))
                    v.tensor_copy(scores[0:LAST, NTILE - 1, i, :], flat(pss[:, :, :])[0:LAST, full:full + NK]).then_inc(s_se, 1)


def phase_topk(k, scores, selT):
    nc = k.nc
    NQ, K2 = 2 * PH, TOPK * TOPK
    HK = PH * TOPK
    with ExitStack() as ctx:
        sb = lambda n, s, dt=F32: ctx.enter_context(nc.sbuf_tensor(f"tk_{n}", s, dt))
        s1 = [sb(f"s{i}", [P, NQ, NK]) for i in range(2)]
        val = sb("val", [P, NQ, TOPK])
        idx = sb("idx", [P, NQ, TOPK], U32)
        idf = sb("idf", [P, NQ, TOPK])
        cand = sb("cand", [P, PH, K2])
        best = sb("best", [P, PH, TOPK])
        prob = sb("prob", [P, PH, TOPK])
        pos = sb("pos", [P, PH, TOPK], U32)
        ab = sb("ab", [P, 2, HK], U32)
        abf = sb("abf", [P, 2, HK])
        eq = sb("eq", [P, HK, TOPK])
        sel = [sb(f"sel{i}", [P, 3, HK]) for i in range(2)]
        ssum = sb("ssum", [P, PH])
        iota_i = sb("iota_i", [P, TOPK], I32)
        iota = sb("iota", [P, TOPK])
        ps = [ctx.enter_context(nc.psum_tensor(f"tk_ps{i}", [P, 512], F32)) for i in range(2)]
        s_io = k.sem("tk_iota_step")
        AC = Progress(k.sem("tk_act"), "stage", "exp", "sel")
        PE = Progress(k.sem("tk_pe"), "turned")
        DV = Progress(k.sem("tk_dve"), "max1", "idx1", "rep1", "max2", "idx2", "idf", "cand", "cmax1", "cidx1", "crep1",
                      "cmax2", "cidx2", "shift", "abf", "off", "eq0", "pick0", "e0", "eq1", "pick1", "e1", "sum", "rec", "gate")

        def select(dve, v, j, slot, n, done):
            r = slice(0, n)
            sc = s1[slot]
            for i in range(NQ):
                last = v.max(val[r, i, 0:8], sc[r, i, :])
            last.then_inc(*DV.inc("max1"))
            done(DV, "max1")
            for i in range(NQ):
                last = v.max_index(idx[r, i, 0:8], val[r, i, 0:8], sc[r, i, :])
            last.then_inc(*DV.inc("idx1"))
            done(DV, "idx1")
            for i in range(NQ):
                last = v.match_replace(out=sc[r, i, :], in_to_replace=val[r, i, 0:8], in_values=sc[r, i, :], imm_value=NEG)
            last.then_inc(*DV.inc("rep1"))
            done(DV, "rep1")
            for i in range(NQ):
                last = v.max(val[r, i, 8:16], sc[r, i, :])
            last.then_inc(*DV.inc("max2"))
            done(DV, "max2")
            for i in range(NQ):
                last = v.max_index(idx[r, i, 8:16], val[r, i, 8:16], sc[r, i, :])
            last.then_inc(*DV.inc("idx2"))
            done(DV, "idx2")
            v.tensor_copy(idf[r, :, :], idx[r, :, :]).then_inc(*DV.inc("idf"))
            vv = val[r, :, :].rearrange("p (h s) a -> p h s a", s=2)
            v.tensor_tensor(cand[r, :, :].rearrange("p h (a b) -> p h a b", a=TOPK),
                            bc(vv[:, :, 0, :].unsqueeze(3), [n, PH, TOPK, TOPK]),
                            bc(vv[:, :, 1, :].unsqueeze(2), [n, PH, TOPK, TOPK]), ALU.add).then_inc(*DV.inc("cand"))
            done(DV, "cand")
            for h in range(PH):
                last = v.max(best[r, h, 0:8], cand[r, h, :])
            last.then_inc(*DV.inc("cmax1"))
            done(DV, "cmax1")
            for h in range(PH):
                last = v.max_index(pos[r, h, 0:8], best[r, h, 0:8], cand[r, h, :])
            last.then_inc(*DV.inc("cidx1"))
            done(DV, "cidx1")
            for h in range(PH):
                last = v.match_replace(out=cand[r, h, :], in_to_replace=best[r, h, 0:8], in_values=cand[r, h, :], imm_value=NEG)
            last.then_inc(*DV.inc("crep1"))
            done(DV, "crep1")
            for h in range(PH):
                last = v.max(best[r, h, 8:16], cand[r, h, :])
            last.then_inc(*DV.inc("cmax2"))
            done(DV, "cmax2")
            for h in range(PH):
                last = v.max_index(pos[r, h, 8:16], best[r, h, 8:16], cand[r, h, :])
            last.then_inc(*DV.inc("cidx2"))
            done(DV, "cidx2")
            pf = pos[r, :, :].rearrange("p h a -> p (h a)")
            v.tensor_scalar(ab[r, 0, :], pf, 4, None, ALU.logical_shift_right)
            v.tensor_scalar(ab[r, 1, :], pf, TOPK - 1, None, ALU.bitwise_and).then_inc(*DV.inc("shift"))
            done(DV, "shift")
            v.tensor_copy(abf[r, :, :], ab[r, :, :]).then_inc(*DV.inc("abf"))
            v.tensor_tensor(prob[r, :, :], best[r, :, :], bc(best[r, :, 0:1], [n, PH, TOPK]), ALU.subtract).then_inc(*DV.inc("off"))
            done(DV, "abf")
            out = sel[slot]
            idh = idf[r, :, :].rearrange("p (h s) a -> p h s a", s=2)
            for side in range(2):
                v.tensor_tensor(eq[r, :, :], bc(abf[r, side, :].unsqueeze(2), [n, HK, TOPK]),
                                bc(iota[r, :].unsqueeze(1), [n, HK, TOPK]), ALU.is_equal).then_inc(*DV.inc(f"eq{side}"))
                done(DV, f"eq{side}")
                for h in range(PH):
                    e_ = eq[r, TOPK * h:TOPK * h + TOPK, :]
                    last = v.tensor_tensor(e_, e_, bc(idh[:, h, side, :].unsqueeze(1), [n, TOPK, TOPK]), ALU.mult)
                last.then_inc(*DV.inc(f"pick{side}"))
                done(DV, f"pick{side}")
                v.tensor_reduce(out[r, side, :], eq[r, :, :], AX.X, ALU.add).then_inc(*DV.inc(f"e{side}"))
                done(DV, f"e{side}")
            done(AC, "exp")
            v.tensor_reduce(ssum[r, :], prob[r, :, :], AX.X, ALU.add).then_inc(*DV.inc("sum"))
            done(DV, "sum")
            v.reciprocal(ssum[r, :], ssum[r, :]).then_inc(*DV.inc("rec"))
            done(DV, "rec")
            v.tensor_tensor(out[r, 2, :].rearrange("p (h a) -> p h a", h=PH), prob[r, :, :],
                            bc(ssum[r, :].unsqueeze(2), [n, PH, TOPK]), ALU.mult).then_inc(*DV.inc("gate"))

        FULL = NTILE - 1

        def tiles(eng, body):
            with eng.Fori(0, FULL // 2) as r:
                for h in range(2):
                    body(2 * r + h, h, P)
            body(FULL, 0, LAST)

        with nc.Block() as block:
            @block.gpsimd
            def _(pool):
                nc.gpsimd.iota(iota_i[:, :], [[1, TOPK]], base=0, channel_multiplier=0).then_inc(s_io, 1)
                pool.wait_ge(s_io, 1)
                nc.gpsimd.tensor_copy(iota[:, :], iota_i[:, :]).then_inc(s_io, 1)

            @block.scalar
            def _(act):
                AC.credit(act)

                def body(j, slot, n):
                    act.wait_ge(DV.sem, DV.before("idx2", j))
                    src = scores[0:n, bass.ds(j, 1), :, :].rearrange("p a i n -> p (a i) n")
                    nc.scalar.activation(s1[slot][0:n, :, :], src, ACT.Copy).then_inc(*AC.inc("stage"))
                    act.wait_ge(DV.sem, DV.now("off", j))
                    nc.scalar.activation(prob[0:n, :, :], prob[0:n, :, :], ACT.Exp).then_inc(*AC.inc("exp"))
                    act.wait_ge(PE.sem, PE.now("turned", j))
                    at = j * P
                    dst = selT[:, :, at:at + n] if isinstance(j, int) else selT[:, :, bass.ds(at, n)]
                    nc.scalar.activation(dst, ps[slot][:, 0:3 * P].rearrange("p (q t) -> p q t", q=3)[:, :, 0:n],
                                         ACT.Copy).then_inc(*AC.inc("sel"))
                tiles(act, body)

            @block.tensor
            def _(pe):
                PE.credit(pe)

                def body(j, slot, n):
                    pe.wait_ge(DV.sem, DV.now("gate", j))
                    pe.wait_ge(AC.sem, AC.before("sel", j))
                    for i in range(3):
                        mm = nc.tensor.transpose(ps[slot][:, i * P:i * P + n], sel[slot][0:n, i, :], k.ident[0:n, 0:n])
                    mm.then_inc(*PE.inc("turned"))
                tiles(pe, body)

            @block.vector
            def _(dve):
                DV.credit(dve)
                two = dve.alloc_register("tk_two")
                dve.reg_mov(two, 2)

                def body(j, slot, n):
                    dve.wait_ge(AC.sem, AC.now("stage", j))
                    dve.wait_ge(PE.sem, PE.before("turned", j))

                    def done(S_, step):
                        dve.wait_ge(S_.sem, S_.now(step, j))
                        dve.reg_alu(two, two, 2, ALU.max)
                    dve.wait_ge(s_io, two)
                    dve.reg_alu(two, two, 2, ALU.max)
                    select(dve, nc.vector, j, slot, n, done)
                tiles(dve, body)


TB = 64
NTB = T // TB
BATCH = 4


def phase_spread(k, selT):
    nc, io = k.nc, k.io
    RING = 4 * BATCH
    NB = TB // BATCH
    with ExitStack() as ctx:
        sb = lambda n, s, dt=F32: ctx.enter_context(nc.sbuf_tensor(f"wt_{n}", s, dt))
        iota_i = sb("iota_i", [P, NK], I32)
        iota = sb("iota", [P, NK])
        one1 = sb("one1", [P, RING, NK])
        one2 = sb("one2", [P, RING, NK])
        stage = sb("stage", [P, 2, NK, TB])
        here = sb("here", [P, 3, TB])
        ps = ctx.enter_context(nc.psum_tensor("wt_ps", [P, 8, BATCH, NK], F32))
        s_io = k.sem("wt_iota_step")
        s_here = k.sem("wt_columns_staged")
        s_st = [k.sem(f"wt_stored{i}") for i in range(2)]
        batches = [f"batch{n}" for n in range(NB)]
        OH = Progress(k.sem("wt_onehots"), *batches)
        PE = Progress(k.sem("wt_matmul"), *batches)
        EV = Progress(k.sem("wt_evac"), *batches)

        def blocks(eng, body):
            with eng.Fori(0, NTB // 2) as r:
                for h in range(2):
                    body(2 * r + h, h, r)
            body(NTB - 1, 0, NTB // 2)

        with nc.Block() as block:
            @block.gpsimd
            def _(pool):
                nc.gpsimd.iota(iota_i[:, :], [[1, NK]], base=0, channel_multiplier=0).then_inc(s_io, 1)
                pool.wait_ge(s_io, 1)
                nc.gpsimd.tensor_copy(iota[:, :], iota_i[:, :]).then_inc(s_io, 1)

            @block.sync
            def _(sp):
                def body(b, slot, r):
                    sp.wait_ge(EV.sem, EV.now(batches[-1], b))
                    sp.dma_start(io["weights"][b].rearrange("e f t -> e (f t)"),
                                 stage[:, slot, :, :].rearrange("p f t -> p (f t)")).then_inc(s_st[slot], 16)
                blocks(sp, body)
                sp.wait_ge(s_st[0], 16 * (NTB // 2 + 1))
                sp.wait_ge(s_st[1], 16 * (NTB // 2))

            @block.vector
            def _(dve):
                v = nc.vector
                OH.credit(dve)
                dve.wait_ge(s_io, 2)

                def body(b, slot, r):
                    dve.wait_ge(OH.sem, OH.before(batches[-1], b))
                    cols = selT[:, :, b * TB:b * TB + TB] if isinstance(b, int) else selT[:, :, bass.ds(b * TB, TB)]
                    v.tensor_copy(here[:, :, :], cols).then_inc(s_here, 1)
                    dve.wait_ge(s_here, b + 1)
                    for n in range(NB):
                        dve.wait_ge(PE.sem, PE.back(n, 4, b))
                        for t in range(n * BATCH, (n + 1) * BATCH):
                            at = t % RING
                            v.tensor_scalar(one1[:, at, :], iota[:, :], here[:, 0, t:t + 1], None, ALU.is_equal)
                            last = v.tensor_scalar(one2[:, at, :], iota[:, :], here[:, 1, t:t + 1], here[:, 2, t:t + 1],
                                                   ALU.is_equal, ALU.mult)
                        last.then_inc(*OH.inc(batches[n]))
                blocks(dve, body)

            @block.tensor
            def _(pe):
                PE.credit(pe)

                def body(b, slot, r):
                    for n in range(NB):
                        pe.wait_ge(OH.sem, OH.now(batches[n], b))
                        pe.wait_ge(EV.sem, EV.back(n, 8, b))
                        for t in range(n * BATCH, (n + 1) * BATCH):
                            mm = nc.tensor.matmul(ps[:, n % 8, t % BATCH, :], one2[:, t % RING, :], one1[:, t % RING, :],
                                                  start=True, stop=True)
                        mm.then_inc(*PE.inc(batches[n]))
                blocks(pe, body)

            @block.scalar
            def _(act):
                EV.credit(act)

                def body(b, slot, r):
                    act.wait_ge(s_st[slot], 16 * r)
                    for n in range(NB):
                        act.wait_ge(PE.sem, PE.now(batches[n], b))
                        dst = stage[:, slot, :, n * BATCH:(n + 1) * BATCH].rearrange("p f t -> p t f")
                        nc.scalar.activation(dst, ps[:, n % 8, :, :], ACT.Copy).then_inc(*EV.inc(batches[n]))
                blocks(act, body)


EG = 4
NG = NK // EG
NOUT = KC * len(TOK_CHUNKS)


def phase_experts(k, xn2, acc):
    nc, io = k.nc, k.io
    NC = len(TOK_CHUNKS)
    NJ = EG * NC
    with ExitStack() as ctx:
        sb = lambda n, s: ctx.enter_context(nc.sbuf_tensor(f"ex_{n}", s, F32))
        u = [sb(f"u{i}", [P, KC, P]) for i in range(EG)]
        vt = [sb(f"v{i}", [P, EG, D]) for i in range(2)]
        g = [sb(f"g{i}", [P, NTB, EG, TB]) for i in range(2)]
        w = [sb(f"w{i}", [P, EG, T]) for i in range(2)]
        psa = [ctx.enter_context(nc.psum_tensor(f"ex_psa{i}", [P, 512], F32)) for i in range(2)]
        pso = [ctx.enter_context(nc.psum_tensor(f"ex_pso{i}", [P, 512], F32)) for i in range(6)]
        s_u = [k.sem(f"ex_u{i}_loaded") for i in range(EG)]
        s_v = [k.sem(f"ex_v{i}_loaded") for i in range(2)]
        s_g = [k.sem(f"ex_g{i}_loaded") for i in range(2)]
        s_zero = k.sem("ex_acc_zeroed")
        jobs = [f"u{j}" for j in range(NJ)]
        outs = [f"v{n}" for n in range(NOUT)]
        PU = Progress(k.sem("ex_u_products"), *jobs)
        GE = Progress(k.sem("ex_gelu"), *jobs)
        MU = Progress(k.sem("ex_weighted"), *[f"e{i}" for i in range(EG)])
        PV = Progress(k.sem("ex_v_products"), *outs)
        AD = Progress(k.sem("ex_added"), *outs)
        R = NG // 2 - 1

        def schedule(eng, first, both, last):
            first((0, 0, 0))
            with eng.Fori(0, R) as r:
                both((2 * r + 1, 1, r), (2 * r, 0, r))
                both((2 * r + 2, 0, r + 1), (2 * r + 1, 1, r))
            both((NG - 1, 1, R), (NG - 2, 0, R))
            last((NG - 1, 1, R))

        with nc.Block() as block:
            @block.sync
            def _(sp):
                def load(ug, wait=True):
                    grp, _, _ = ug
                    for i in range(EG):
                        if wait:
                            sp.wait_ge(PU.sem, PU.before(jobs[NC * i + NC - 1], grp))
                        sp.dma_start(u[i][:, :, :], io["u"][grp * EG + i]).then_inc(s_u[i], 16)

                schedule(sp, lambda ug: load(ug, False), lambda ug, vg: load(ug), lambda vg: None)

            @block.gpsimd
            def _(pool):
                def load(grp, par, wait):
                    sl = slice(grp * EG, grp * EG + EG) if isinstance(grp, int) else bass.ds(grp * EG, EG)
                    if wait:
                        pool.wait_ge(MU.sem, MU.before(f"e{EG - 1}", grp - 1))
                    pool.dma_start(g[par][:, :, :, :].rearrange("p b e t -> p b (e t)"),
                                   io["weights"][:, :, sl, :].rearrange("b p e t -> p b (e t)")).then_inc(s_g[par], 16)
                    if wait:
                        pool.wait_ge(PV.sem, PV.before(outs[-1], grp - 1))
                    pool.dma_start(vt[par][:, :, :], io["v"][sl].rearrange("e p d -> p e d")).then_inc(s_v[par], 16)

                load(0, 0, False)
                load(1, 1, False)
                with pool.Fori(0, R) as r:
                    load(2 * r + 2, 0, True)
                    load(2 * r + 3, 1, True)

            @block.tensor
            def _(pe):
                def u_job(ug, j):
                    grp, _, _ = ug
                    i, c = divmod(j, NC)
                    if c == 0:
                        pe.wait_ge(s_u[i], 16 * grp + 16)
                    pe.wait_ge(GE.sem, GE.back(j, 2, grp))
                    a, b = TOK_CHUNKS[c]
                    for kc in range(KC):
                        mm = nc.tensor.matmul(psa[j % 2][:, 0:b - a], u[i][:, kc, :], xn2[:, kc, a:b],
                                              start=kc == 0, stop=kc == KC - 1)
                    mm.then_inc(*PU.inc(jobs[j]))

                def v_job(vg, n):
                    grp, par, number = vg
                    dc, c = divmod(n, NC)
                    if n == 0:
                        pe.wait_ge(s_v[par], 16 * number + 16)
                        pe.wait_ge(MU.sem, MU.now(f"e{EG - 1}", grp))
                    pe.wait_ge(AD.sem, AD.back(n, 6, grp))
                    a, b = TOK_CHUNKS[c]
                    for i in range(EG):
                        mm = nc.tensor.matmul(pso[n % 6][:, 0:b - a], vt[par][:, i, dc * P:(dc + 1) * P], w[par][:, i, a:b],
                                              start=i == 0, stop=i == EG - 1)
                    mm.then_inc(*PV.inc(outs[n]))

                def both(ug, vg):
                    for j in range(NJ):
                        u_job(ug, j)
                        v_job(vg, 2 * j)
                        v_job(vg, 2 * j + 1)

                PU.credit(pe)
                PV.credit(pe)
                schedule(pe, lambda ug: [u_job(ug, j) for j in range(NJ)], both, lambda vg: [v_job(vg, n) for n in range(NOUT)])

            @block.scalar
            def _(act):
                def gelus(ug):
                    grp, par, _ = ug
                    for j in range(NJ):
                        i, c = divmod(j, NC)
                        a, b = TOK_CHUNKS[c]
                        act.wait_ge(PU.sem, PU.now(jobs[j], grp))
                        nc.scalar.activation(w[par][:, i, a:b], psa[j % 2][:, 0:b - a], ACT.Gelu).then_inc(*GE.inc(jobs[j]))

                GE.credit(act)
                schedule(act, gelus, lambda ug, vg: gelus(ug), lambda vg: None)

            @block.vector
            def _(dve):
                v = nc.vector

                def weigh(ug, i):
                    grp, par, number = ug
                    if i == 0:
                        dve.wait_ge(s_g[par], 16 * number + 16)
                    dve.wait_ge(GE.sem, GE.now(jobs[NC * i + NC - 1], grp))
                    wv = w[par][:, i, :].rearrange("p (b t) -> p b t", t=TB)
                    v.tensor_tensor(wv, wv, g[par][:, :, i, :], ALU.mult).then_inc(*MU.inc(f"e{i}"))

                def add(vg, n):
                    grp, _, _ = vg
                    dc, c = divmod(n, NC)
                    a, b = TOK_CHUNKS[c]
                    dve.wait_ge(PV.sem, PV.now(outs[n], grp))
                    dve.wait_ge(AD.sem, AD.before(outs[n], grp))
                    v.tensor_tensor(acc[:, dc, a:b], pso[n % 6][:, 0:b - a], acc[:, dc, a:b], ALU.add).then_inc(*AD.inc(outs[n]))

                def both(ug, vg):
                    for j in range(NJ):
                        if j and j % NC == 0:
                            weigh(ug, j // NC - 1)
                        add(vg, 2 * j)
                        add(vg, 2 * j + 1)
                    weigh(ug, EG - 1)

                MU.credit(dve)
                AD.credit(dve)
                v.memset(acc[:, :, :], 0.0).then_inc(s_zero, 1)
                dve.wait_ge(s_zero, 1)
                schedule(dve, lambda ug: [weigh(ug, i) for i in range(EG)], both, lambda vg: [add(vg, n) for n in range(NOUT)])


def phase_final(k, acc):
    nc, io = k.nc, k.io
    with nc.sbuf_tensor("fin_x", [P, KC, T], F32) as x, nc.sbuf_tensor("fin_tmp", [P, T], F32) as tmp:
        s_x = k.sem("fin_x1_loaded")
        s_res = k.sem("fin_residual_step")
        with nc.Block() as block:
            @block.sync
            def _(sp):
                sp.dma_start(x[:, :, :], io["x1"]).then_inc(s_x, 16)

            @block.vector
            def _(dve):
                dve.wait_ge(s_x, 16)
                for m in range(KC):
                    add_gated(k, dve, x[:, m, :], acc[:, m, :], tmp, GT2 + m, s_res, 3 * m)

        def store(sp, sem):
            sp.dma_start(io["y_out"], acc[:, :, :]).then_inc(sem, 16)
            return 16

        rmsnorm_mod(k, "final", x, lambda kc: acc[:, kc, 0:SEQ], lambda kc: token_views(acc[:, kc, :])[1],
                    SCF, SHF, None, store)


def program(nc, io):
    with ExitStack() as ctx:
        k = Core(nc, ctx, io)
        for name, shape in (("proj", (PROJ_TILES + 1, P, TX)), ("rwc", (NCH + 1, P, 5, NPAIR, CL)),
                            ("rw_gate", (NPAIR, P, T)), ("rw_bonus", (NPAIR, P, T)), ("rw_y", (NCH + 1, P, NPAIR, CL)),
                            ("xbc", (NXBC, P, T)), ("ssd_rows", (SH, 3, T)), ("ssd_y", (KC, P, T)), ("x1", (P, KC, T)),
                            ("weights", (NTB, NK, NK, TB))):
            io[name] = nc.dram_tensor(name, shape, F32, kind="Internal").ap()
        k.par = k.lasting("par", [P, NPAR])
        k.mod = k.lasting("mod", [P, 64, NCOND])
        k.cT = k.lasting("cT", [P, KC, NCOND])
        k.ident = k.lasting("ident", [P, P])
        k.ones = k.lasting("ones", [P, P])
        k.pairones = k.lasting("pairones", [P, P])
        k.const = k.lasting("const", [P, 4])
        k.shift_sb = k.lasting("shift_sb", [P, KC, NSEQ])
        k.lam_end = k.lasting("lam_end", [P, NPAIR, NCH + NSEQ])
        k.mt_mask = k.lasting("mt_mask", [P, 2, 4, CL])
        k.lv_mask = k.lasting("lv_mask", [P, LEVELS, 2, CL])
        k.ident2 = k.lasting("ident2", [P, 2, CL])
        k.seq_cols = k.lasting("seq_cols", [P, NSEQ, CL])
        k.seq_rows = k.lasting("seq_rows", [P, NSEQ])
        k.ssd_mask = k.lasting("ssd_mask", [P, SL])
        k.ssd_mask_smp = k.lasting("ssd_mask_smp", [CL, CL])
        k.head_sel = k.lasting("head_sel", [SH, SH, P])
        phase_ada(k)
        with nc.sbuf_tensor("xe", [P, KC, TX], F32) as xe:
            phase_norm1(k, xe)
            phase_inputs(k, xe)
        phase_masks(k)
        phase_rw_prompt(k)
        phase_rw_samples(k)
        phase_ssd(k)
        k.recycle_semaphores()
        with nc.sbuf_tensor("x1_sb", [P, KC, T], F32) as xn2:
            with nc.sbuf_tensor("oa", [P, NPAIR, T], F32) as oa, nc.sbuf_tensor("ob", [P, KC, T], F32) as ob:
                phase_rw_post(k, oa)
                phase_ssd_post(k, ob)
                phase_merge(k, oa, ob, xn2)
            phase_norm2(k, xn2)
            with nc.sbuf_tensor("selT", [P, 3, T], F32) as selT:
                with nc.sbuf_tensor("scores", [P, NTILE, 2 * PH, NK], F32) as scores:
                    phase_scores(k, xn2, scores)
                    phase_topk(k, scores, selT)
                phase_spread(k, selT)
            with nc.sbuf_tensor("acc", [P, KC, T], F32) as acc:
                phase_experts(k, xn2, acc)
                phase_final(k, acc)


def _rows(a, tiles):
    return np.ascontiguousarray(a.reshape(tiles, P, -1).transpose(1, 0, 2))


def _cols(v):
    return v.reshape(-1, P).T


def _weight(a):
    kk, m = a.shape
    return np.ascontiguousarray(a.reshape(kk // P, P, m // P, P).transpose(2, 1, 0, 3))


def _arrays(x):
    f = lambda n: np.asarray(x[n])
    out = {}
    toks = np.concatenate([f("x_prompt").reshape(SEQ, D), f("x_sample").reshape(NSEQ * DSEQ, D)])
    out["xT"] = _rows(toks.T, KC)
    out["cT"] = _rows(np.concatenate([f("c_prompt"), f("c_sample")]).T, KC)
    out["shiftT"] = _rows(f("state_shift")[0].T, KC)
    wa = np.concatenate([f("w_ada")[0], f("w_ada_f")], axis=1)
    grouped = lambda w, n: np.ascontiguousarray(w.reshape(KC, P, -1, n).transpose(2, 1, 0, 3))
    out["w_ada"] = grouped(wa[:, :ADA_FIRST * P], 4 * P)
    out["w_ada_rest"] = grouped(wa[:, ADA_FIRST * P:], ADA_STEP * P)
    cw = f("ssm_conv_w")[0].reshape(CONVK, NXBC, P).transpose(2, 0, 1).reshape(P, CONVK * NXBC)
    mu = f("rw_mu")[0]
    out["params"] = np.ascontiguousarray(np.concatenate(
        [_cols(f("b_ada")[0]), _cols(f("b_ada_f")), _cols(f("norm1_g")[0]), _cols(f("norm2_g")[0]), _cols(f("final_g")),
         _cols(mu[3 * RDIM:]), cw, _cols(f("ssm_conv_b")[0]), _cols(f("ssm_norm_w")[0]),
         _cols(f("rw_ln_w")[0]), _cols(f("rw_ln_b")[0])], axis=1))
    r3 = [mu[0:RDIM], mu[RDIM:2 * RDIM], mu[2 * RDIM:3 * RDIM], f("rw_w0")[0], f("rw_a0")[0], f("rw_k_k")[0],
          f("rw_k_a")[0], f("rw_r_k")[0].reshape(-1)]
    out["rw_params"] = np.ascontiguousarray(np.stack([v.reshape(NPAIR, P) for v in r3], axis=2))
    wi = f("w_in")[0]
    ssm0 = RW_TILES * P
    dt0 = ssm0 + D + NXBC * P
    main = np.concatenate([wi[:, :dt0], wi[:, dt0 + SH:]], axis=1)
    wt = _weight(main)
    z, xbc = RW_TILES, RW_TILES + KC
    out["w_in"] = np.concatenate([wt[xbc:xbc + XBC_TILES], wt[:z], wt[z:xbc], wt[xbc + XBC_TILES:]])
    out["w_dt"] = _rows(wi[:, dt0:dt0 + SH], KC)
    out["lora_w"] = np.ascontiguousarray(np.stack(
        [np.concatenate([f("rw_w2")[0], f("rw_a2")[0]]), f("rw_g2")[0]]).reshape(2, P, NPAIR, P).transpose(2, 1, 0, 3))
    out["head_params"] = np.ascontiguousarray(np.stack([f("ssm_dt_bias")[0], f("ssm_A_log")[0]], axis=1))
    out["ssm_D"] = np.ascontiguousarray(f("ssm_D")[0].reshape(KC, 2).T)
    sw = f("state_wkv")[0].reshape(NSEQ, NPAIR, 2, RD, RD)
    out["wkvT"] = np.ascontiguousarray(sw.transpose(0, 2, 4, 1, 3).reshape(NSEQ, P, NPAIR, RD))
    out["convT"] = _rows(f("state_conv")[0].transpose(2, 0, 1).reshape(NXBC * P, -1), NXBC).reshape(P, NXBC, NSEQ, CONVK - 1)
    out["ssmT"] = np.ascontiguousarray(f("state_ssm")[0].transpose(0, 3, 1, 2).reshape(NSEQ, SN, SH * SD))
    out["w_pa"] = _weight(f("w_pa")[0])
    out["w_pb"] = _weight(f("w_pb")[0])
    out["w_out"] = _weight(f("w_out")[0])
    out["w_q"] = _weight(f("peer_wq")[0])
    out["keysT"] = np.ascontiguousarray(f("peer_keys")[0].reshape(2 * PH, NK, P).transpose(2, 0, 1))
    out["u"] = np.ascontiguousarray(f("peer_u")[0].reshape(NK, NK, KC, P).transpose(0, 3, 2, 1))
    out["v"] = np.ascontiguousarray(f("peer_v")[0].reshape(NK, NK, D))
    return out


_OUTS = {"shift_out": (P, KC, NCOND), "y_out": (P, KC, T), "wkv_out": (NCOND, P, NPAIR, RD),
         "conv_out": (P, NXBC, NCOND, CONVK - 1), "ssm_out": (NCOND, SN, SH * SD)}


def kernel(**inputs):
    import numpy as _np
    import concourse.bacc as _bacc
    from concourse import mybir as _mybir
    from concourse.bass_utils import run_bass_kernel_spmd as _run

    nc = _bacc.Bacc("TRN2", target_bir_lowering=False, num_devices=1)
    arrays, io = {}, {}
    for name, a in _arrays(inputs).items():
        arrays["in_" + name] = a
        io[name] = nc.dram_tensor("in_" + name, a.shape, _mybir.dt.from_np(a.dtype), kind="ExternalInput").ap()
    for name, shape in _OUTS.items():
        io[name] = nc.dram_tensor("out_" + name, shape, F32, kind="ExternalOutput").ap()
    program(nc, io)
    r = _run(nc, [arrays], core_ids=[0])
    got = {n: r.results[0]["out_" + n] for n in _OUTS}

    unrow = lambda a: a.transpose(1, 0, 2).reshape(-1, a.shape[2])
    y = unrow(got["y_out"]).T
    shift = unrow(got["shift_out"]).T
    wkv = got["wkv_out"].reshape(NCOND, 2, RD, NPAIR, RD).transpose(0, 3, 1, 4, 2).reshape(NCOND, RH, RD, RD)
    conv = unrow(got["conv_out"].reshape(P, NXBC, NCOND * (CONVK - 1))).reshape(-1, NCOND, CONVK - 1).transpose(1, 2, 0)
    ssm = got["ssm_out"].reshape(NCOND, SN, SH, SD).transpose(0, 2, 3, 1)
    c = _np.ascontiguousarray
    return (c(y[:SEQ].reshape(1, SEQ, D)), c(y[SEQ:].reshape(NSEQ, DSEQ, D)),
            c(shift[None, 0:1]), c(wkv[None, 0:1]), c(conv[None, 0:1]), c(ssm[None, 0:1]),
            c(shift[None, 1:]), c(wkv[None, 1:]), c(conv[None, 1:]), c(ssm[None, 1:]))
```

```python
from contextlib import ExitStack

import numpy as np
import concourse.bass as bass
from concourse import mybir

F32 = mybir.dt.float32
F32R = mybir.dt.float32r
I32 = mybir.dt.int32
U32 = mybir.dt.uint32
ALU = mybir.AluOpType
ACT = mybir.ActivationFunctionType
AX = mybir.AxisListType

P = 128
D = 1024
KC = D // P
SEQ = 1024
NSEQ, DSEQ = 8, 8
T = SEQ + NSEQ * DSEQ
TX = 1 + SEQ + NSEQ * (DSEQ + 1)
TXE = TX + TX % 2
NCOND = 1 + NSEQ
RH, RD = 8, 64
RDIM = RH * RD
NPAIR = RDIM // P
SH, SD, SG, SN = 16, 64, 2, 128
NXBC = 12
CONVK = 4
EXP_NEG_HALF = float(np.exp(-0.5))
RW_TILES = 14
PROJ_TILES = 50
XBC_TILES = 12
XBC0, RW0, Z0, GATE0, DT0 = 0, 12, 26, 34, 50
CL = 64
NCH = SEQ // CL
SL = 128
NSC = SEQ // SL
LEVELS = 6
PH, NK, TOPK = 8, 128, 16
NORM_EPS = 1e-6
LN_EPS = 64e-5
LN_SCALE = 2.0 ** 30

PCOLS = {}
_at = 0
for _name, _n in (("b_ada", 64), ("norm1_g", 8), ("norm2_g", 8), ("final_g", 8), ("mu_lora", 2),
                  ("conv_w", 48), ("conv_b", 12), ("ssm_norm_w", 8), ("ln_w", 4), ("ln_b", 4)):
    PCOLS[_name] = slice(_at, _at + _n)
    _at += _n
NPAR = _at
RWP_MU, RWP_W0, RWP_A0, RWP_KK, RWP_KA, RWP_RK = 0, 3, 4, 5, 6, 7
SH1, SC1, GT1, SH2, SC2, GT2, SHF, SCF = (8 * i for i in range(8))
EXT_CHUNKS = ((0, 512), (512, 842), (842, TXE))
BANKED_AT = 224
TOK_CHUNKS_BANKED = ((0, 512 - BANKED_AT), (512 - BANKED_AT, 1024 - BANKED_AT), (1024 - BANKED_AT, T))


class Progress:

    def __init__(self, sem, *steps):
        self.sem, self.steps, self.n = sem, list(steps), len(steps)
        assert len(set(steps)) == len(steps), steps
        self.next = 0

    def inc(self, step):
        assert self.steps[self.next % self.n] == step, (self.steps[self.next % self.n], step)
        self.next += 1
        return self.sem, 1

    def done(self, step, rounds=0):
        return rounds * self.n + self.steps.index(step) + 1

    def credit(self, eng):
        eng.sem_inc(self.sem, self.n)

    def now(self, step, r):
        return r * self.n + (self.n + self.steps.index(step) + 1)

    def before(self, step, r):
        return r * self.n + (self.steps.index(step) + 1)

    def earlier(self, step, m, r):
        return r * self.n + (self.steps.index(step) + 1 + self.n * (1 - m))

    def back(self, n, m, r):
        return self.now(self.steps[n - m], r) if n >= m else self.before(self.steps[n - m], r)


def bc(ap, shape):
    return ap.broadcast_to(shape)


def flat(ap):
    return ap.rearrange("p a b -> p (a b)")


def banked(ps):
    return flat(ps[:, :, :])[:, BANKED_AT:BANKED_AT + T]


class Core:

    def __init__(self, nc, ctx, io):
        self.nc, self.ctx, self.io, self.sems = nc, ctx, io, []

    def sem(self, name):
        self.sems.append(self.nc.alloc_semaphore(name=name))
        return self.sems[-1]

    def recycle_semaphores(self):
        self.nc.all_engine_barrier()
        self.nc.clear_and_free_semaphores(self.sems)
        self.nc.all_engine_barrier()
        self.sems = []

    def lasting(self, name, shape, dt=F32):
        return self.ctx.enter_context(self.nc.sbuf_tensor(name, shape, dt))


ADA_FIRST = 16
ADA_STEP = (64 - ADA_FIRST) // NCH


def scale_gain(k, at, g):
    return k.nc.vector.scalar_tensor_tensor(out=k.mod[:, at:at + 8, :], in0=k.mod[:, at:at + 8, :], scalar=1.0,
                                            in1=bc(k.par[:, PCOLS[g]].unsqueeze(2), [P, 8, NCOND]),
                                            op0=ALU.add, op1=ALU.mult)


def phase_ada(k):
    nc, io = k.nc, k.io
    with ExitStack() as ctx:
        sb = lambda n, s, dt=F32: ctx.enter_context(nc.sbuf_tensor(n, s, dt))
        cT = k.cT
        ce = sb("ce", [P, KC, NCOND])
        w = [sb(f"ada_w{i}", [P, KC, 512]) for i in range(3)]
        row = [sb(f"ada_row{i}", [NCOND, 512]) for i in range(2)]
        ps = [ctx.enter_context(nc.psum_tensor(f"ada_ps{i}", [P, 512], F32)) for i in range(2)]
        pst = [ctx.enter_context(nc.psum_tensor(f"ada_pst{i}", [P, 512], F32)) for i in range(2)]
        s_c = k.sem("cond_loaded")
        s_par = k.sem("params_loaded")
        s_w = [k.sem(f"ada_w{i}_loaded") for i in range(3)]
        s_exp = k.sem("cond_exp_done")
        s_silu = k.sem("cond_silu_step")
        s_mm = k.sem("ada_matmul_done")
        s_mod = k.sem("ada_mod_done")
        s_row = k.sem("ada_row_copied")
        s_turn = k.sem("ada_row_turned")
        s_const = k.sem("const_step")
        s_mask = k.sem("mask_step")
        G = ADA_FIRST // 4

        with nc.Block() as block:
            @block.sync
            def _(sp):
                sp.dma_start(cT[:, :, :], io["cT"]).then_inc(s_c, 16)
                sp.dma_start(k.par[:, :], io["params"]).then_inc(s_par, 16)
                for g in range(G):
                    if g >= 3:
                        sp.wait_ge(s_mm, g - 2)
                    sp.dma_start(w[g % 3][:, :, :], io["w_ada"][g]).then_inc(s_w[g % 3], 16)

            @block.scalar
            def _(act):
                act.wait_ge(s_c, 16)
                nc.scalar.activation(ce[:, :, :], cT[:, :, :], ACT.Exp, scale=-1.0).then_inc(s_exp, 1)
                for g in range(G):
                    act.wait_ge(s_mm, g + 1)
                    if g >= 2:
                        act.wait_ge(s_turn, g - 1)
                    nc.scalar.activation(row[g % 2][:, :], ps[g % 2][0:NCOND, :], ACT.Copy).then_inc(s_row, 1)

            @block.gpsimd
            def _(pool):
                nc.gpsimd.memset(k.ident[:, :], 0.0).then_inc(s_const, 1)
                nc.gpsimd.memset(k.ones[:, :], 1.0).then_inc(s_const, 1)
                nc.gpsimd.memset(k.pairones[:, :], 0.0).then_inc(s_const, 1)
                nc.gpsimd.memset(k.const[:, 0:1], NORM_EPS).then_inc(s_const, 1)
                nc.gpsimd.memset(k.const[:, 1:2], LN_EPS).then_inc(s_const, 1)
                nc.gpsimd.memset(k.const[:, 2:3], 1.0).then_inc(s_const, 1)
                pool.wait_ge(s_const, 6)
                nc.gpsimd.affine_select(out=k.ident[:, :], in_=k.ident[:, :], compare_op=ALU.not_equal, fill=1.0,
                                        base=0, pattern=[[-1, P]], channel_multiplier=1).then_inc(s_const, 1)
                pool.wait_ge(s_const, 7)
                nc.gpsimd.memset(k.pairones[0:64, 0:64], 1.0).then_inc(s_const, 1)
                pool.wait_ge(s_const, 8)
                nc.gpsimd.memset(k.pairones[64:128, 64:128], 1.0).then_inc(s_const, 1)
                pool.wait_ge(s_const, 9)
                make_masks(k, pool, s_mask)

            @block.tensor
            def _(pe):
                def turn(g):
                    pe.wait_ge(s_row, g + 1)
                    if g >= 2:
                        pe.wait_ge(s_mod, g - 1)
                    for m in range(4):
                        mm = nc.tensor.matmul(pst[g % 2][:, m * NCOND:(m + 1) * NCOND], row[g % 2][:, m * P:(m + 1) * P],
                                              k.ident[0:NCOND, 0:NCOND], start=True, stop=True)
                    mm.then_inc(s_turn, 1)

                pe.wait_ge(s_silu, 3)
                for g in range(G):
                    pe.wait_ge(s_w[g % 3], 16 * (g // 3 + 1))
                    if g >= 2:
                        pe.wait_ge(s_row, g - 1)
                    for kc in range(KC):
                        mm = nc.tensor.matmul(ps[g % 2][0:NCOND, :], cT[:, kc, :], w[g % 3][:, kc, :],
                                              start=kc == 0, stop=kc == KC - 1)
                    mm.then_inc(s_mm, 1)
                    if g == 0:
                        pe.wait_ge(s_const, 7)
                    else:
                        turn(g - 1)
                turn(G - 1)

            @block.vector
            def _(dve):
                dve.wait_ge(s_exp, 1)
                nc.vector.tensor_scalar(ce[:, :, :], ce[:, :, :], 1.0, None, ALU.add).then_inc(s_silu, 1)
                dve.wait_ge(s_silu, 1)
                nc.vector.reciprocal(ce[:, :, :], ce[:, :, :]).then_inc(s_silu, 1)
                dve.wait_ge(s_silu, 2)
                nc.vector.tensor_tensor(cT[:, :, :], cT[:, :, :], ce[:, :, :], ALU.mult).then_inc(s_silu, 1)
                dve.wait_ge(s_par, 16)
                for g in range(G):
                    dve.wait_ge(s_turn, g + 1)
                    nc.vector.tensor_tensor(k.mod[:, 4 * g:4 * g + 4, :],
                                            pst[g % 2][:, 0:4 * NCOND].rearrange("p (m c) -> p m c", m=4),
                                            bc(k.par[:, 4 * g:4 * g + 4].unsqueeze(2), [P, 4, NCOND]),
                                            ALU.add).then_inc(s_mod, 1)
                dve.wait_ge(s_mod, G)
                scale_gain(k, SC1, "norm1_g").then_inc(s_mod, 1)


def rmsnorm_mod(k, tag, x, out_prompt, out_sample, scale_at, shift_at, load=None, store=None):
    nc = k.nc
    with ExitStack() as ctx:
        sb = lambda n, s, dt=F32: ctx.enter_context(nc.sbuf_tensor(f"{tag}_{n}", s, dt))
        sq = sb("sq", [P, 2, T])
        rstd = sb("rstd", [P, T])
        xr = sb("xr", [P, 2, T])
        ps = ctx.enter_context(nc.psum_tensor(f"{tag}_ps", [P, 3, 512], F32))
        pf = banked(ps)
        s_x = k.sem(f"{tag}_x_loaded")
        s_sq = k.sem(f"{tag}_square_done")
        s_sum = k.sem(f"{tag}_sum_step")
        s_r = k.sem(f"{tag}_rstd_step")
        s_o = k.sem(f"{tag}_out_step")
        s_st = k.sem(f"{tag}_stored")
        need = [0]
        with nc.Block() as block:
            @block.sync
            def _(sp):
                if load:
                    need[0] = load(sp, s_x)
                if store:
                    sp.wait_ge(s_o, 4 * KC)
                    n = store(sp, s_st)
                    sp.wait_ge(s_st, n)

            @block.scalar
            def _(act):
                if need[0]:
                    act.wait_ge(s_x, need[0])
                for kc in range(KC):
                    if kc >= 2:
                        act.wait_ge(s_sum, kc - 1)
                    nc.scalar.activation(sq[:, kc % 2, :], x[:, kc, :], ACT.Square).then_inc(s_sq, 1)
                act.wait_ge(s_sum, KC)
                nc.scalar.activation(rstd[:, :], pf[:, 0:T], ACT.Ln, scale=1.0 / D, bias=k.const[:, 0:1]).then_inc(s_r, 1)
                act.wait_ge(s_r, 1)
                nc.scalar.activation(rstd[:, :], rstd[:, :], ACT.Exp, scale=-0.5).then_inc(s_r, 1)

            @block.tensor
            def _(pe):
                for kc in range(KC):
                    pe.wait_ge(s_sq, kc + 1)
                    for a, b in TOK_CHUNKS_BANKED:
                        mm = nc.tensor.matmul(pf[:, a:b], k.ones[:, :], sq[:, kc % 2, a:b], start=kc == 0, stop=kc == KC - 1)
                    mm.then_inc(s_sum, 1)

            @block.vector
            def _(dve):
                if need[0]:
                    dve.wait_ge(s_x, need[0])
                dve.wait_ge(s_r, 2)
                n = 0
                for kc in range(KC):
                    if kc >= 2:
                        dve.wait_ge(s_o, 4 * (kc - 1))
                    nc.vector.tensor_tensor(xr[:, kc % 2, :], x[:, kc, :], rstd[:, :], ALU.mult).then_inc(s_o, 1)
                    n += 1
                    dve.wait_ge(s_o, n)
                    a, b = k.mod[:, scale_at + kc, :], k.mod[:, shift_at + kc, :]
                    nc.vector.tensor_scalar(out_prompt(kc), xr[:, kc % 2, 0:SEQ], a[:, 0:1], b[:, 0:1],
                                            ALU.mult, ALU.add).then_inc(s_o, 1)
                    smp = xr[:, kc % 2, SEQ:T].rearrange("p (s t) -> p s t", s=NSEQ)
                    nc.vector.tensor_tensor(smp, smp, bc(a[:, 1:NCOND].unsqueeze(2), [P, NSEQ, DSEQ]), ALU.mult).then_inc(s_o, 1)
                    n += 2
                    dve.wait_ge(s_o, n)
                    nc.vector.tensor_tensor(out_sample(kc), smp, bc(b[:, 1:NCOND].unsqueeze(2), [P, NSEQ, DSEQ]), ALU.add).then_inc(s_o, 1)
                    n += 1


def phase_norm1(k, xh, xl):
    nc, io = k.nc, k.io
    with nc.sbuf_tensor("xe", [P, KC, TXE], F32) as xe, nc.sbuf_tensor("x_in", [P, KC, T], F32) as x:
        smp = lambda kc: xe[:, kc, 1 + SEQ:TX].rearrange("p (s t) -> p s t", s=NSEQ)
        s_z = k.sem("xe_pad_done")
        s_sh = k.sem("xe_shift_loaded")
        s_h, s_l = k.sem("xe_high_made"), k.sem("xe_low_made")

        def load(sp, sem):
            sp.dma_start(x[:, :, :], io["xT"]).then_inc(sem, 16)
            sp.dma_start(k.shift_sb[:, :, :], io["shiftT"]).then_inc(s_sh, 16)
            sp.wait_ge(s_sh, 16)
            return 16

        def store(sp, sem):
            with nc.allow_non_contiguous_dma(reason="last rows"):
                sp.dma_start(io["shift_out"][:, :, 0:1], xe[:, :, SEQ:SEQ + 1]).then_inc(sem, 16)
                for kc in range(KC):
                    sp.dma_start(io["shift_out"][:, kc, 1:NCOND], smp(kc)[:, :, DSEQ]).then_inc(sem, 16)
            return 16 * (KC + 1)

        rmsnorm_mod(k, "norm1", x, lambda kc: xe[:, kc, 1:1 + SEQ], lambda kc: smp(kc)[:, :, 1:1 + DSEQ],
                    SC1, SH1, load, store)
        with nc.Block() as block:
            @block.gpsimd
            def _(pool):
                nc.gpsimd.memset(xe[:, :, 0:1], 0.0).then_inc(s_z, 1)
                nc.gpsimd.memset(xe[:, :, TX:TXE], 0.0).then_inc(s_z, 1)
                for kc in range(KC):
                    nc.gpsimd.tensor_copy(smp(kc)[:, :, 0], k.shift_sb[:, kc, :]).then_inc(s_z, 1)

            @block.scalar
            def _(act):
                act.wait_ge(s_z, KC + 2)
                for kc in range(KC):
                    nc.scalar.activation(xh[:, kc, :], xe[:, kc, :], ACT.Copy).then_inc(s_h, 1)

            @block.vector
            def _(dve):
                for kc in range(KC):
                    dve.wait_ge(s_h, kc + 1)
                    nc.vector.tensor_tensor(xl[:, kc, :], xe[:, kc, :], xh[:, kc, :].bitcast(F32), ALU.subtract).then_inc(s_l, 1)


def predecessor_views(ext):
    smp = ext[:, 1 + SEQ:TX].rearrange("p (s t) -> p s t", s=NSEQ)
    return (ext[:, 0:SEQ], ext[:, 1:1 + SEQ]), (smp[:, :, 0:DSEQ], smp[:, :, 1:1 + DSEQ])


def token_views(tok):
    return tok[:, 0:SEQ], tok[:, SEQ:T].rearrange("p (s t) -> p s t", s=NSEQ)


def token_shift(dve, out, ext, mu, sub_done, wait_sub):
    for o, e in zip(out, ext):
        for ov, (prev, cur) in zip(token_views(o), predecessor_views(e)):
            last = dve.tensor_tensor(ov, prev, cur, ALU.subtract)
    last.then_inc(*sub_done)
    wait_sub()
    for o, e, m in zip(out, ext, mu):
        for ov, (_, cur) in zip(token_views(o), predecessor_views(e)):
            last = dve.scalar_tensor_tensor(out=ov, in0=ov, scalar=m, in1=cur, op0=ALU.mult, op1=ALU.add)
    return last


PADP = CONVK - 1
CONV_IN = PADP + SEQ + NSEQ * (PADP + DSEQ)
CONV_OUT = CONV_IN - PADP


def conv_sample_view(tile):
    return tile[:, PADP + SEQ:CONV_IN].rearrange("p (s t) -> p s t", s=NSEQ)


LOOP_A = 6
A_TILES = XBC_TILES + RW_TILES
A_ROUNDS = A_TILES // LOOP_A
B_ROUNDS = (PROJ_TILES - A_TILES) // LOOP_A


class Slices:

    def __init__(self, whole, size):
        self.whole, self.size, self.at = whole, size, 0

    def take(self, rows, *dims):
        n = int(np.prod(dims))
        assert self.at + n <= self.size, (self.at, n, self.size)
        ap = self.whole[0:rows, self.at:self.at + n]
        self.at += n
        names = "abc"[:len(dims)]
        if len(dims) == 1:
            return ap
        return ap.rearrange(f"p ({' '.join(names)}) -> p {' '.join(names)}", **dict(zip(names[:-1], dims[:-1])))


class Projection:

    def __init__(self, k, ctx, xh, xl):
        nc = k.nc
        self.k, self.xh, self.xl = k, xh, xl
        sb = lambda n, s, dt=F32: ctx.enter_context(nc.sbuf_tensor(n, s, dt))
        self.w = [sb(f"in_w{i}", [P, KC, P]) for i in range(2)]
        self.wh, self.wl = ([sb(f"in_w_{n}{i}", [P, KC, P], F32R) for i in range(2)] for n in ("high", "low"))
        self.wdt = sb("in_wdt", [P, KC, SH])
        self.wdth, self.wdtl = (sb(f"in_wdt_{n}", [P, KC, SH], F32R) for n in ("high", "low"))
        self.out = [sb(f"in_out{i}", [P, TX]) for i in range(2)]
        self.ps = ctx.enter_context(nc.psum_tensor("in_ps", [P, 5, 512], F32))
        self.s_w = [k.sem(f"in_w{i}_loaded") for i in range(2)]
        self.s_wdt = k.sem("in_wdt_loaded")
        self.s_high = k.sem("in_w_high_made")
        self.s_low = k.sem("in_w_low_made")
        self.s_mm = k.sem("in_tile_multiplied")
        self.s_ev = k.sem("in_tile_evacuated")
        self.s_st = [k.sem(f"in_stored{i}") for i in range(2)]
        self.s_dt = k.sem("in_dt_step")
        self.s_dtst = k.sem("in_dt_stored")

    def stored(self, eng, t):
        eng.wait_ge(self.s_st[t % 2], 16 * (t // 2 + 1))

    def load(self, sp, t, slot):
        sp.dma_start(self.w[slot][:, :, :], self.k.io["w_in"][t]).then_inc(self.s_w[slot], 16)

    def split(self, pool, raw, high, low, count):
        g = self.k.nc.gpsimd
        g.tensor_copy(high[:, :, :], raw[:, :, :]).then_inc(self.s_high, 1)
        pool.wait_ge(self.s_high, count + 1)
        g.tensor_tensor(low[:, :, :], raw[:, :, :], high[:, :, :].bitcast(F32), ALU.subtract).then_inc(self.s_low, 1)

    def products(self, wh, wl, cols, parity, parts):
        def at(part):
            a, b = EXT_CHUNKS[part]
            return self.ps[0:cols, 4, 256 * parity:256 * parity + b - a] if part == 2 else self.ps[0:cols, 2 * parity + part, 0:b - a]
        passes = [(w, x, kc) for kc in range(KC) for w, x in ((wh, self.xh), (wh, self.xl), (wl, self.xh))]
        for n, (w, x, kc) in enumerate(passes):
            for part in parts:
                a, b = EXT_CHUNKS[part]
                mm = self.k.nc.tensor.matmul(at(part), w[:, kc, :], x[:, kc, a:b], start=n == 0, stop=n == len(passes) - 1)
        return mm

    def dt_product(self, pe):
        pe.wait_ge(self.s_low, 1)
        self.products(self.wdth, self.wdtl, SH, 1, (0, 1, 2)).then_inc(self.s_dt, 1)

    def tile(self, pe, t, parity):
        pe.wait_ge(self.s_low, t + 2)
        pe.wait_ge(self.s_ev, t + 1)
        self.products(self.wh[parity], self.wl[parity], P, parity, (0, 1))
        pe.wait_ge(self.s_ev, t + 2)
        self.products(self.wh[parity], self.wl[parity], P, parity, (2,)).then_inc(self.s_mm, 1)

    def out_of_psum(self, cols, parity):
        ac = self.k.nc.scalar
        n = EXT_CHUNKS[1][1]
        big = flat(self.ps[0:cols, 2 * parity:2 * parity + 2, :])[:, 0:n]
        ac.activation(self.out[parity][0:cols, 0:n], big, ACT.Copy)
        rest = self.ps[0:cols, 4, 256 * parity:256 * parity + TX - n]
        return ac.activation(self.out[parity][0:cols, n:TX], rest, ACT.Copy)

    def evac(self, act, t, parity, earlier):
        act.wait_ge(self.s_mm, t + 1)
        if not isinstance(earlier, int) or earlier:
            act.wait_ge(self.s_st[parity], 16 * earlier)
        self.out_of_psum(P, parity).then_inc(self.s_ev, 1)

    def pool_side(self, pool):
        io = self.k.io

        def split(t, parity, earlier):
            pool.wait_ge(self.s_w[parity], 16 * earlier + 16)
            pool.wait_ge(self.s_high, one)
            pool.reg_alu(one, one, 1, ALU.max)
            self.split(pool, self.w[parity], self.wh[parity], self.wl[parity], t + 1)

        def store(t, parity):
            pool.wait_ge(self.s_ev, t + 3)
            pool.dma_start(io["proj"][t], self.out[parity][:, :]).then_inc(self.s_st[parity], 16)

        pool.wait_ge(self.s_wdt, 16)
        self.split(pool, self.wdt, self.wdth, self.wdtl, 0)
        one = pool.alloc_register("in_one")
        pool.reg_mov(one, 1)
        for t in range(2):
            split(t, t, 0)
        pool.wait_ge(self.s_dt, 2)
        pool.dma_start(io["proj"][DT0, 0:SH, :], self.out[1][0:SH, :]).then_inc(self.s_dtst, 16)
        with pool.Fori(0, PROJ_TILES // 2 - 1) as r:
            for parity in range(2):
                t = 2 * r + parity
                store(t, parity)
                split(t + 2, parity, r + 1)
        for t in (PROJ_TILES - 2, PROJ_TILES - 1):
            store(t, t % 2)
        for t in (PROJ_TILES - 2, PROJ_TILES - 1):
            self.stored(pool, t)


def phase_inputs(k, xh, xl):
    nc, io = k.nc, k.io
    with ExitStack() as ctx:
        pj = Projection(k, ctx, xh, xl)
        keep = ctx.enter_context(nc.sbuf_tensor("pre_keep", [P, T], F32))
        rp = ctx.enter_context(nc.sbuf_tensor("rwp_rp", [P, 8], F32))
        lw = ctx.enter_context(nc.sbuf_tensor("rwp_lw", [P, 2, P], F32))
        SIZE = 3 * TX + 13 * T
        arena = ctx.enter_context(nc.sbuf_tensor("pre_arena", [P, SIZE], F32))
        c_ = Slices(arena, SIZE)
        e, acc, sg = ([c_.take(P, CONV_IN) for i in range(2)] for n in range(3))
        state = c_.take(P, NXBC, NSEQ, PADP)
        new = c_.take(P, NXBC, NCOND, PADP)
        hp, neg_a = c_.take(SH, 2), c_.take(SH, 1)
        dx = c_.take(SH, TX)
        dkeep, dtx, ex, sq, poly = (c_.take(SH, T) for n in range(5))
        rec = dx[:, 0:T]
        rows = c_.take(SH, 3, T)
        r_ = Slices(arena, SIZE)
        x = r_.take(P, 3, TX)
        lora = r_.take(P, 2, T)
        q = r_.take(P, 3, T)
        linv, lprev, cs, kk, rn, t1, kp, gate = (r_.take(P, T) for n in range(8))
        sw, a, lam = (x[:, i, 0:T] for i in range(3))
        bonus = cs
        o = (lprev, lam, rn, kp)
        psr = ctx.enter_context(nc.psum_tensor("rwp_ps", [P, 3, 512], F32))
        pa = banked(psr)

        s_in = [k.sem(f"cv_in{i}_loaded") for i in range(2)]
        s_state = k.sem("cv_state_loaded")
        s_dt = k.sem("dt_loaded")
        s_pad = k.sem("cv_pad_zeroed")
        s_out = [k.sem(f"cv_out{i}_stored") for i in range(2)]
        s_fin = k.sem("cv_states_and_dt_stored")
        s_keep = k.sem("dt_keep_step")
        s_dx = k.sem("dt_act_step")
        s_dv = k.sem("dt_dve_step")
        s_rows = k.sem("dt_rows_done")
        CA = Progress(k.sem("cv_act"), "state", "new", "sigmoid")
        CD = Progress(k.sem("cv_dve"), "tap0", "tap1", "tap2", "tap3", "silu")
        cw, cb = k.par[:, PCOLS["conv_w"]], k.par[:, PCOLS["conv_b"]]

        s_lx = k.sem("rwp_lora_loaded")
        s_x = k.sem("rwp_x_loaded")
        s_w = k.sem("rwp_weights_loaded")
        s_st = k.sem("rwp_stored")
        s_rkeep = k.sem("rwp_keep_step")
        s_lora = k.sem("rwp_lora_step")
        PE = Progress(k.sem("rwp_pe"), "zw", "za", "gate", "norm", "bonus")
        AC = Progress(k.sem("rwp_act"), "sw", "a", "gate", "lam", "linv", "lprev", "ln", "rn")
        DV = Progress(k.sem("rwp_dve"), "sub", "mix", "kkr", "sq", "cs", "csx", "norm_floor", "am", "kp", "kk",
                      "b", "rk", "ends", "outs", "bonus")
        NST = 7
        c = EXP_NEG_HALF

        with nc.Block() as block:
            @block.sync
            def _(sp):
                def conv_load(m):
                    pj.stored(sp, XBC0 + m)
                    if m >= 2:
                        sp.wait_ge(CD.sem, CD.now("silu", m - 2))
                        sp.wait_ge(CA.sem, CA.now("new", m - 2))
                    sp.dma_start(e[m % 2][:, PADP:PADP + SEQ], io["proj"][XBC0 + m, :, 1:1 + SEQ]).then_inc(s_in[m % 2], 16)
                    src = io["proj"][XBC0 + m, :, 1 + SEQ:TX].rearrange("p (s t) -> p s t", s=NSEQ)
                    sp.dma_start(conv_sample_view(e[m % 2])[:, :, PADP:], src[:, :, 1:1 + DSEQ]).then_inc(s_in[m % 2], 16)

                sp.dma_start(pj.wdt[:, :, :], io["w_dt"]).then_inc(pj.s_wdt, 16)
                for t in range(2):
                    pj.load(sp, t, t)
                sp.dma_start(hp, io["head_params"]).then_inc(s_dt, 16)
                sp.dma_start(state, io["convT"]).then_inc(s_state, 16)
                sp.wait_ge(pj.s_dtst, 16)
                sp.dma_start(dx, io["proj"][DT0, 0:SH, :]).then_inc(s_dt, 16)
                LAG = 3
                STRAIGHT = XBC_TILES + LAG + 1
                for t in range(STRAIGHT):
                    sp.wait_ge(pj.s_low, t + 2)
                    pj.load(sp, t + 2, t % 2)
                    if LAG <= t < XBC_TILES + LAG:
                        conv_load(t - LAG)
                with sp.Fori(0, (PROJ_TILES - 2 - STRAIGHT) // 2) as r:
                    for j in range(2):
                        t = 2 * r + (STRAIGHT + j)
                        sp.wait_ge(pj.s_low, t + 2)
                        pj.load(sp, t + 2, j)

            @block.gpsimd
            def _(pool):
                g = nc.gpsimd
                g.memset(dkeep, 1.0).then_inc(s_keep, 1)
                for i in range(2):
                    g.memset(e[i][:, 0:PADP], 0.0).then_inc(s_pad, 1)
                g.memset(keep[:, :], 1.0).then_inc(s_rkeep, 1)
                pool.wait_ge(s_keep, 1)
                g.memset(dkeep[:, 0:SEQ].rearrange("p (c t) -> p c t", t=SL)[:, :, 0:1], 0.0).then_inc(s_keep, 1)
                g.memset(dkeep[:, SEQ:T].rearrange("p (c t) -> p c t", t=DSEQ)[:, :, 0:1], 0.0).then_inc(s_keep, 1)
                pool.wait_ge(s_rkeep, 1)
                g.memset(keep[:, 0:SEQ].rearrange("p (c t) -> p c t", t=CL)[:, :, 0:1], 0.0).then_inc(s_rkeep, 1)
                g.memset(keep[:, SEQ:T].rearrange("p (c t) -> p c t", t=DSEQ)[:, :, 0:1], 0.0).then_inc(s_rkeep, 1)
                pj.pool_side(pool)

            @block.tensor
            def _(pe):
                PE.credit(pe)
                pj.dt_product(pe)
                pe.wait_ge(pj.s_dt, 2)

                with pe.Fori(0, A_ROUNDS) as r:
                    for j in range(LOOP_A):
                        pj.tile(pe, LOOP_A * r + j, j % 2)
                for t in range(LOOP_A * A_ROUNDS, A_TILES):
                    pj.tile(pe, t, t % 2)

                def product(lhsT, rhs, step):
                    for a0, b0 in TOK_CHUNKS_BANKED:
                        mm = nc.tensor.matmul(pa[:, a0:b0], lhsT, rhs[:, a0:b0], start=True, stop=True)
                    mm.then_inc(*PE.inc(step))

                with pe.Fori(0, B_ROUNDS) as r:
                    def pair_product(j):
                        if j == 0:
                            pe.wait_ge(s_lora, 4)
                            pe.wait_ge(s_w, 32 * r + 32)
                            pe.wait_ge(DV.sem, DV.before("bonus", r))
                            product(lw[0:64, 0, :], lora[0:64, 0, :], "zw")
                        elif j == 1:
                            pe.wait_ge(AC.sem, AC.now("sw", r))
                            product(lw[64:128, 0, :], lora[64:128, 0, :], "za")
                        elif j == 2:
                            pe.wait_ge(AC.sem, AC.now("a", r))
                            product(lw[:, 1, :], lora[:, 1, :], "gate")
                        elif j == 3:
                            pe.wait_ge(AC.sem, AC.now("gate", r))
                            pe.wait_ge(DV.sem, DV.now("sq", r))
                            product(k.pairones[:, :], rn, "norm")
                        elif j == 4:
                            pe.wait_ge(DV.sem, DV.now("rk", r))
                            product(k.pairones[:, :], t1, "bonus")

                    for j in range(LOOP_A):
                        pj.tile(pe, LOOP_A * r + (A_TILES + j), j % 2)
                        pair_product(j)

            @block.scalar
            def _(act):
                ac = nc.scalar
                act.sem_inc(pj.s_ev, 2)
                act.wait_ge(pj.s_dt, 1)
                pj.out_of_psum(SH, 1).then_inc(pj.s_dt, 1)
                act.wait_ge(s_dt, 32)
                ac.activation(neg_a, hp[:, 1:2], ACT.Exp).then_inc(s_dx, 1)
                act.wait_ge(s_dv, 2)
                ac.activation(ex, dtx, ACT.Abs).then_inc(s_dx, 1)
                act.wait_ge(s_dx, 2)
                ac.activation(ex, ex, ACT.Exp, scale=-1.0).then_inc(s_dx, 1)
                CA.credit(act)
                for i in range(2):
                    act.sem_inc(s_out[i], 32)
                act.wait_ge(s_state, 16)
                pj.evac(act, 0, 0, 0)
                act.wait_ge(pj.s_dtst, 16)
                pj.evac(act, 1, 1, 0)
                with act.Fori(0, NXBC // 2) as r:
                    for h in range(2):
                        m = 2 * r + h
                        pj.evac(act, m + 2, h, r + 1)
                        smp = conv_sample_view(e[h])
                        act.wait_ge(CD.sem, CD.before("silu", 2 * r))
                        ac.activation(smp[:, :, 0:PADP], state[:, bass.ds(m, 1), :, :].rearrange("p a s t -> p (a s) t"),
                                      ACT.Copy).then_inc(*CA.inc("state"))
                        act.wait_ge(s_in[h], 32 * r + 32)
                        ac.activation(new[:, bass.ds(m, 1), 0, :].rearrange("p a t -> p (a t)"), e[h][:, SEQ:SEQ + PADP], ACT.Copy)
                        ac.activation(new[:, bass.ds(m, 1), 1:NCOND, :].rearrange("p a s t -> p (a s) t"), smp[:, :, DSEQ:],
                                      ACT.Copy).then_inc(*CA.inc("new"))
                        act.wait_ge(CD.sem, CD.now("tap3", m))
                        act.wait_ge(s_out[h], 32 * r + 32)
                        ac.activation(sg[h][:, 0:CONV_OUT], acc[h][:, 0:CONV_OUT], ACT.Sigmoid).then_inc(*CA.inc("sigmoid"))
                        act.wait_ge(CD.sem, CD.now("silu", m))
                        act.dma_start(io["xbc"][m][:, 0:SEQ], sg[h][:, 0:SEQ]).then_inc(s_out[h], 16)
                        act.dma_start(io["xbc"][m][:, SEQ:T].rearrange("p (s t) -> p s t", s=NSEQ),
                                      conv_sample_view(sg[h])[:, :, 0:DSEQ]).then_inc(s_out[h], 16)
                act.wait_ge(s_rows, 2)
                act.dma_start(io["ssd_rows"], rows).then_inc(s_fin, 16)
                act.wait_ge(CA.sem, CA.now("new", NXBC - 1))
                act.dma_start(io["conv_out"], new).then_inc(s_fin, 16)
                act.wait_ge(s_fin, 32)
                for h in range(2):
                    act.wait_ge(s_out[h], 32 * (NXBC // 2) + 32)
                with act.Fori(0, (A_TILES - NXBC) // 2 - 1) as r:
                    for h in range(2):
                        pj.evac(act, 2 * r + (NXBC + 2 + h), h, r + (NXBC // 2 + 1))
                for t in range(A_TILES - 2, A_TILES):
                    pj.stored(act, t)
                for i in range(2):
                    act.dma_start(x[:, i, :], io["proj"][RW0 + 12 + i]).then_inc(s_lx, 16)

                def load(r):
                    for i in range(3):
                        act.dma_start(x[:, i, :], io["proj"][RW0 + 4 * i + r]).then_inc(s_x, 16)
                    act.dma_start(rp[:, :], io["rw_params"][r]).then_inc(s_w, 16)
                    act.dma_start(lw[:, :, :], io["lora_w"][r]).then_inc(s_w, 16)

                AC.credit(act)
                act.sem_inc(s_st, 16 * NST)
                act.wait_ge(s_lora, 2)
                ac.activation(lora[0:64, 0, :], lora[0:64, 0, :], ACT.Tanh).then_inc(s_lora, 1)
                ac.activation(lora[:, 1, :], lora[:, 1, :], ACT.Sigmoid).then_inc(s_lora, 1)
                with act.Fori(0, NPAIR) as r:
                    act.wait_ge(DV.sem, DV.before("bonus", r))
                    act.wait_ge(AC.sem, AC.before("rn", r))
                    act.wait_ge(s_st, 16 * NST * r + 16 * NST)
                    load(r)

                    def evac(j):
                        pj.evac(act, LOOP_A * r + (A_TILES + j), j % 2, (LOOP_A // 2) * r + (A_TILES + j) // 2)

                    evac(0)
                    act.wait_ge(s_w, 32 * r + 32)
                    act.wait_ge(PE.sem, PE.now("zw", r))
                    act.wait_ge(DV.sem, DV.now("mix", r))
                    ac.activation(sw, pa[:, 0:T], ACT.Sigmoid, bias=rp[:, RWP_W0:RWP_W0 + 1]).then_inc(*AC.inc("sw"))
                    evac(1)
                    act.wait_ge(PE.sem, PE.now("za", r))
                    ac.activation(a, pa[:, 0:T], ACT.Sigmoid, bias=rp[:, RWP_A0:RWP_A0 + 1]).then_inc(*AC.inc("a"))
                    evac(2)
                    act.wait_ge(PE.sem, PE.now("gate", r))
                    ac.activation(gate, pa[:, 0:T], ACT.Copy).then_inc(*AC.inc("gate"))
                    act.wait_ge(DV.sem, DV.now("cs", r))
                    ac.activation(lam, cs, ACT.Exp, scale=-c).then_inc(*AC.inc("lam"))
                    ac.activation(linv, cs, ACT.Exp, scale=c).then_inc(*AC.inc("linv"))
                    act.wait_ge(DV.sem, DV.now("csx", r))
                    ac.activation(lprev, lprev, ACT.Exp, scale=-c).then_inc(*AC.inc("lprev"))
                    evac(3)
                    act.wait_ge(DV.sem, DV.now("norm_floor", r))
                    ac.activation(rn, rn, ACT.Ln).then_inc(*AC.inc("ln"))
                    act.wait_ge(AC.sem, AC.now("ln", r))
                    ac.activation(rn, rn, ACT.Exp, scale=-0.5).then_inc(*AC.inc("rn"))
                    evac(4)
                    act.wait_ge(DV.sem, DV.now("outs", r))
                    for n in range(4):
                        act.dma_start(io["rwc"][:, :, n, r, :].rearrange("c p t -> p c t"),
                                      o[n].rearrange("p (c t) -> p c t", t=CL)).then_inc(s_st, 16)
                    act.dma_start(io["rwc"][:, :, 4, r, :].rearrange("c p t -> p c t"),
                                  q[:, 2, :].rearrange("p (c t) -> p c t", t=CL)).then_inc(s_st, 16)
                    act.wait_ge(AC.sem, AC.now("gate", r))
                    act.dma_start(io["rw_gate"][r], gate).then_inc(s_st, 16)
                    act.wait_ge(DV.sem, DV.now("bonus", r))
                    act.dma_start(io["rw_bonus"][r], bonus).then_inc(s_st, 16)
                    evac(5)
                act.wait_ge(s_st, 16 * NST * NPAIR + 16 * NST)

            @block.vector
            def _(dve):
                v = nc.vector
                n = [0]

                def step(ins):
                    ins.then_inc(s_dv, 1)
                    n[0] += 1
                    dve.wait_ge(s_dv, n[0])

                dve.wait_ge(s_dt, 32)
                v.tensor_copy(dtx[:, 0:SEQ], dx[:, 1:1 + SEQ])
                step(v.tensor_copy(token_views(dtx)[1], predecessor_views(dx)[1][1]))
                step(v.tensor_scalar(dtx, dtx, hp[:, 0:1], None, ALU.add))
                dve.wait_ge(s_dx, 3)
                step(v.tensor_scalar(rec, ex, 2.0, None, ALU.add))
                step(v.reciprocal(rec, rec))
                step(v.tensor_tensor(ex, ex, rec, ALU.mult))
                step(v.tensor_tensor(sq, ex, ex, ALU.mult))
                step(v.tensor_scalar(poly, sq, 1.0 / 15, None, ALU.mult))
                for d in (13, 11, 9, 7, 5, 3):
                    step(v.scalar_tensor_tensor(out=poly, in0=poly, scalar=1.0 / d, in1=sq, op0=ALU.add, op1=ALU.mult))
                step(v.scalar_tensor_tensor(out=poly, in0=poly, scalar=1.0, in1=ex, op0=ALU.add, op1=ALU.mult))
                step(v.tensor_scalar(dtx, dtx, 0.0, None, ALU.max))
                step(v.scalar_tensor_tensor(out=rows[:, 0, :], in0=poly, scalar=2.0, in1=dtx, op0=ALU.mult, op1=ALU.add))
                dve.wait_ge(s_keep, 3)
                step(v.tensor_scalar(dtx, rows[:, 0, :], neg_a[:, 0:1], -1.0, ALU.mult, ALU.mult))
                step(v.tensor_tensor_scan(rows[:, 1, :], dkeep, dtx, 0.0, ALU.mult, ALU.add))
                for span, lo, hi in ((SL, 0, SEQ), (DSEQ, SEQ, T)):
                    cs_ = rows[:, 1, lo:hi].rearrange("p (c t) -> p c t", t=span)
                    v.tensor_tensor(rows[:, 2, lo:hi].rearrange("p (c t) -> p c t", t=span),
                                    bc(cs_[:, :, span - 1:span], [SH, (hi - lo) // span, span]), cs_, ALU.subtract).then_inc(s_rows, 1)
                CD.credit(dve)
                dve.wait_ge(s_pad, 2)
                with dve.Fori(0, NXBC // 2) as r:
                    for h in range(2):
                        m = 2 * r + h
                        done = lambda s_: dve.wait_ge(CD.sem, CD.now(s_, m))
                        dve.wait_ge(s_in[h], 32 * r + 32)
                        dve.wait_ge(CA.sem, CA.now("state", m))
                        wc = lambda j: cw[:, bass.ds(m + j * NXBC, 1)]
                        a_ = acc[h][:, 0:CONV_OUT]
                        v.tensor_scalar(a_, e[h][:, 0:CONV_OUT], wc(0), cb[:, bass.ds(m, 1)], ALU.mult, ALU.add).then_inc(*CD.inc("tap0"))
                        for j in range(1, CONVK):
                            done(f"tap{j - 1}")
                            v.scalar_tensor_tensor(out=a_, in0=e[h][:, j:j + CONV_OUT], scalar=wc(j), in1=a_,
                                                   op0=ALU.mult, op1=ALU.add).then_inc(*CD.inc(f"tap{j}"))
                        dve.wait_ge(CA.sem, CA.now("sigmoid", m))
                        s_ = sg[h][:, 0:CONV_OUT]
                        v.tensor_tensor(s_, a_, s_, ALU.mult).then_inc(*CD.inc("silu"))

                DV.credit(dve)
                dve.wait_ge(s_lx, 32)
                mu = k.par[:, PCOLS["mu_lora"]]
                token_shift(v, [lora[:, i, :] for i in range(2)], [x[:, i, :] for i in range(2)],
                            [mu[:, i:i + 1] for i in range(2)], (s_lora, 1),
                            lambda: dve.wait_ge(s_lora, 1)).then_inc(s_lora, 1)
                dve.wait_ge(s_rkeep, 3)
                with dve.Fori(0, NPAIR) as r:
                    now = lambda s: dve.wait_ge(DV.sem, DV.now(s, r))
                    col = lambda n: rp[:, n:n + 1]
                    dve.wait_ge(s_x, 48 * r + 48)
                    dve.wait_ge(s_w, 32 * r + 32)
                    dve.wait_ge(s_st, 16 * NST * r + 16 * NST)
                    token_shift(v, [q[:, i, :] for i in range(3)], [x[:, i, :] for i in range(3)],
                                [col(RWP_MU + i) for i in range(3)], DV.inc("sub"),
                                lambda: now("sub")).then_inc(*DV.inc("mix"))
                    now("mix")
                    v.tensor_scalar(kk, q[:, 1, :], col(RWP_KK), None, ALU.mult).then_inc(*DV.inc("kkr"))
                    now("kkr")
                    v.tensor_tensor(rn, kk, kk, ALU.mult).then_inc(*DV.inc("sq"))
                    dve.wait_ge(AC.sem, AC.now("sw", r))
                    v.tensor_tensor_scan(cs, keep[:, :], sw, 0.0, ALU.mult, ALU.add).then_inc(*DV.inc("cs"))
                    now("cs")
                    v.tensor_tensor(lprev, cs, sw, ALU.subtract).then_inc(*DV.inc("csx"))
                    dve.wait_ge(PE.sem, PE.now("norm", r))
                    v.tensor_scalar(rn, pa[:, 0:T], 1e-24, LN_SCALE, ALU.max, ALU.mult).then_inc(*DV.inc("norm_floor"))
                    dve.wait_ge(AC.sem, AC.now("a", r))
                    v.scalar_tensor_tensor(out=t1, in0=a, scalar=-1.0, in1=q[:, 1, :],
                                           op0=ALU.add, op1=ALU.mult).then_inc(*DV.inc("am"))
                    now("am")
                    v.scalar_tensor_tensor(out=kp, in0=t1, scalar=col(RWP_KA), in1=q[:, 1, :],
                                           op0=ALU.mult, op1=ALU.add).then_inc(*DV.inc("kp"))
                    dve.wait_ge(AC.sem, AC.now("rn", r))
                    v.scalar_tensor_tensor(out=kk, in0=kk, scalar=LN_SCALE ** 0.5, in1=rn,
                                           op0=ALU.mult, op1=ALU.mult).then_inc(*DV.inc("kk"))
                    now("kk")
                    v.tensor_tensor(rn, kk, a, ALU.mult).then_inc(*DV.inc("b"))
                    v.scalar_tensor_tensor(out=t1, in0=q[:, 0, :], scalar=col(RWP_RK), in1=kp,
                                           op0=ALU.mult, op1=ALU.mult).then_inc(*DV.inc("rk"))
                    dve.wait_ge(AC.sem, AC.now("lprev", r))
                    now("b")
                    v.tensor_copy(k.lam_end[:, r, 0:NCH], lam[:, CL - 1:SEQ:CL])
                    v.tensor_copy(k.lam_end[:, r, NCH:NCH + NSEQ], lam[:, SEQ + DSEQ - 1:T:DSEQ]).then_inc(*DV.inc("ends"))
                    now("ends")
                    v.tensor_tensor(o[0], kk, lprev, ALU.mult)
                    v.tensor_tensor(o[1], q[:, 0, :], lam, ALU.mult)
                    v.tensor_tensor(o[2], rn, linv, ALU.mult)
                    v.tensor_tensor(o[3], kp, linv, ALU.mult).then_inc(*DV.inc("outs"))
                    dve.wait_ge(PE.sem, PE.now("bonus", r))
                    v.tensor_tensor(bonus, pa[:, 0:T], q[:, 2, :], ALU.mult).then_inc(*DV.inc("bonus"))


def halves():
    return slice(0, 64), slice(64, 128)


def make_masks(k, pool, s):
    g = k.nc.gpsimd
    n = [0]

    def stage(ops):
        for op in ops:
            op().then_inc(s, 1)
            n[0] += 1
            pool.wait_ge(s, n[0])

    def keep(view, pattern, base, cm):
        return lambda: g.affine_select(out=view, in_=view, compare_op=ALU.is_ge, fill=0.0, base=base,
                                       pattern=pattern, channel_multiplier=cm)

    stage([lambda: g.memset(k.mt_mask[:, :, :, :], 1.0), lambda: g.memset(k.lv_mask[:, :, :, :], 0.0),
           lambda: g.memset(k.seq_cols[:, :, :], 1.0), lambda: g.memset(k.seq_rows[:, :], 1.0)])
    for rows in halves():
        for kind in range(2):
            for b in range(4):
                m = k.mt_mask[rows, kind, b, :]
                stage([keep(m, [[1, CL]], -1 if b % 2 == 0 else 0, -1)])
        blk = k.mt_mask[rows, 1, :, :].rearrange("p b (s t) -> p b s t", s=NSEQ)
        for b in range(4):
            stage([keep(blk[:, b], [[-DSEQ, NSEQ], [0, DSEQ]], 0, 1)])
            stage([keep(blk[:, b], [[DSEQ, NSEQ], [0, DSEQ]], DSEQ - 1, -1)])
        stage([keep(k.seq_rows[rows, :], [[-DSEQ, NSEQ]], 0, 1)])
        stage([keep(k.seq_rows[rows, :], [[DSEQ, NSEQ]], DSEQ - 1, -1)])
        for lv in range(LEVELS):
            z = 1 << lv
            nb = CL // (2 * z)
            xm = k.lv_mask[rows, lv, 0, :].rearrange("p (b h w) -> p b h w", h=2, w=z)[:, :, 0, :]
            ym = k.lv_mask[rows, lv, 1, :].rearrange("p (b h w) -> p b h w", h=2, w=z)[:, :, 1, :]
            stage([lambda: g.memset(xm, 1.0), lambda: g.memset(ym, 1.0)])
            stage([keep(xm, [[-2 * z, nb], [0, z]], -z, 1), keep(ym, [[-2 * z, nb], [0, z]], 0, 1)])
            stage([keep(xm, [[2 * z, nb], [0, z]], 2 * z - 1, -1), keep(ym, [[2 * z, nb], [0, z]], z - 1, -1)])
        for i in range(2):
            stage([lambda: g.tensor_copy(k.ident2[rows, i, :], k.ident[rows, rows])])
    stage([lambda: g.memset(k.ssd_mask[:, :], 1.0), lambda: g.memset(k.ssd_mask_smp[:, :], 1.0)])
    stage([keep(k.ssd_mask[:, :], [[1, SL]], 0, -1), keep(k.ssd_mask_smp[:, :], [[1, CL]], 0, -1)])
    blk = k.ssd_mask_smp[:, :].rearrange("p (s t) -> p s t", s=NSEQ)
    stage([keep(blk, [[-DSEQ, NSEQ], [0, DSEQ]], 0, 1)])
    stage([keep(k.seq_cols[:, :, :], [[-DSEQ, NSEQ], [1, CL]], 0, 0)])
    stage([keep(k.seq_cols[:, :, :], [[DSEQ, NSEQ], [-1, CL]], DSEQ - 1, 0)])


def make_head_sel(k, pool, s):
    g = k.nc.gpsimd
    g.memset(k.head_sel[:, :, :], 1.0).then_inc(s, 1)
    for n, sign in enumerate((1, -1)):
        pool.wait_ge(s, n + 1)
        g.affine_select(out=k.head_sel[:, :, :], in_=k.head_sel[:, :, :], compare_op=ALU.is_ge, fill=0.0, base=0,
                        pattern=[[-sign, SH], [0, P]], channel_multiplier=sign).then_inc(s, 1)


KA, RB, BT, KT, VV = range(5)
BANK_MT, BANK_M, BANK_TOK, BANK_U = 0, 2, 3, 7
BANK_P, BANK_Q = (5, 3), (6, 4)


def in_turn(parts):
    parts = list(parts)
    while parts:
        parts = [p_ for p_ in parts if next(p_, "end") != "end"]


def in_turn_steps(chunks, first, per_level, levels):
    return ([f"{s}_{h}" for h in chunks for s in first] +
            [f"{s}{lv}_{h}" for lv in range(1, levels) for piece in per_level for h in chunks for s in piece])


class RwChunk:

    def __init__(self, k, ctx, tag, h):
        sb = lambda n, s: ctx.enter_context(k.nc.sbuf_tensor(f"{tag}_{n}{h}", s, F32))
        self.h = h
        self.mt = sb("mt", [P, NPAIR, 256])
        self.xy = sb("xy", [P, NPAIR, 2, CL])
        self.mx = sb("mx", [P, NPAIR, CL])
        self.tmp = sb("tmp", [P, NPAIR, 2, CL])
        self.tok = sb("tok", [P, 3, NPAIR, CL])


def rw_matrix_pe(k, b, ch, in5, levels, at):
    nc, PE, AC, DV, h = k.nc, b.PE, b.AC, b.DV, ch.h
    ps = b.ps
    heads = [(p_, rows) for p_ in range(NPAIR) for rows in halves()]
    mt = ps[:, BANK_MT:BANK_MT + 2, :].rearrange("p a (b m) -> p (a b) m", m=256)
    tok = ps[:, BANK_TOK:BANK_TOK + 2, :].rearrange("p a b -> p (a b)")[:, 0:768].rearrange("p (q a t) -> p q a t", q=3, a=4)
    four = lambda bank: ps[:, bank, 0:256].rearrange("p (a t) -> p a t", a=4)
    pq = ps[:, BANK_Q[h], :].rearrange("p (a i t) -> p a i t", a=4, i=2)
    if h:
        at(DV, "mt_0")
    for p_, rows in heads:
        for i, w in enumerate((BT, KT)):
            mm = nc.tensor.matmul(mt[rows, p_, 128 * i:128 * i + 128], in5[rows, w, p_, :], in5[rows, KA:RB + 1, p_, :],
                                  start=True, stop=True)
    mm.then_inc(*PE.inc(f"mt_{h}"))
    if h:
        at(DV, "t0_0")
    for p_, rows in heads:
        mm = nc.tensor.matmul(four(BANK_M)[rows, p_, :], in5[rows, KA, p_, :], in5[rows, BT, p_, :], start=True, stop=True)
    mm.then_inc(*PE.inc(f"m_{h}"))
    if h:
        at(AC, "tok_0")
    for q, w in enumerate((BT, KT, VV)):
        for p_, rows in heads:
            mm = nc.tensor.matmul(tok[rows, q, p_, :], in5[rows, w, p_, :], k.ident[rows, rows], start=True, stop=True)
    mm.then_inc(*PE.inc(f"tok_{h}"))
    yield
    for lv in range(1, levels):
        at(DV, f"xy{lv - 1}_{h}")
        if h and lv == 1:
            at(AC, "tok_1")
        for p_, rows in heads:
            mm = nc.tensor.matmul(four(BANK_P[h])[rows, p_, :], ch.mt[rows, p_, 0:64], ch.xy[rows, p_, 0, :], start=True, stop=True)
        mm.then_inc(*PE.inc(f"mx{lv}_{h}"))
        yield
        at(AC, f"mx{lv}_{h}")
        for p_, rows in heads:
            nc.tensor.matmul(pq[rows, p_, 0, :], ch.xy[rows, p_, 1, :], ch.mx[rows, p_, :], start=True, stop=True)
            mm = nc.tensor.matmul(pq[rows, p_, 1, :], ch.mx[rows, p_, :], ch.xy[rows, p_, 1, :], start=True, stop=True)
        mm.then_inc(*PE.inc(f"xmx{lv}_{h}"))
        yield


def rw_matrix_act(k, b, ch, levels, at):
    nc, PE, AC, h = k.nc, b.PE, b.AC, ch.h
    tok = b.ps[:, BANK_TOK:BANK_TOK + 2, :].rearrange("p a b -> p (a b)")[:, 0:768]
    at(PE, f"tok_{h}")
    nc.scalar.activation(ch.tok[:, :, :, :].rearrange("p q a t -> p (q a t)"), tok, ACT.Copy).then_inc(*AC.inc(f"tok_{h}"))
    yield
    for lv in range(1, levels):
        at(PE, f"mx{lv}_{h}")
        nc.scalar.activation(ch.mx[:, :, :].rearrange("p a t -> p (a t)"), b.ps[:, BANK_P[h], 0:256],
                             ACT.Copy).then_inc(*AC.inc(f"mx{lv}_{h}"))
        yield


def rw_matrix_dve(k, b, ch, kind, levels, at):
    v, PE, DV, h = k.nc.vector, b.PE, b.DV, ch.h
    mt = b.ps[:, BANK_MT:BANK_MT + 2, :].rearrange("p a (b m) -> p (a b) m", m=256)
    m = b.ps[:, BANK_M, 0:256].rearrange("p (a t) -> p a t", a=4)
    mask = k.mt_mask[:, kind, :, :].rearrange("p b t -> p (b t)").unsqueeze(1)
    at(PE, f"mt_{h}")
    v.tensor_tensor(ch.mt[:, :, :], mt, bc(mask, [P, NPAIR, 256]), ALU.mult).then_inc(*DV.inc(f"mt_{h}"))
    at(PE, f"m_{h}")
    at(DV, f"mt_{h}")
    v.tensor_tensor(ch.tmp[:, :, 0, :], m, bc(k.lv_mask[:, 0, 0:1, :], [P, NPAIR, CL]), ALU.mult)
    v.tensor_tensor(ch.tmp[:, :, 1, :], ch.mt[:, :, 0:64], bc(k.lv_mask[:, 0, 1:2, :], [P, NPAIR, CL]),
                    ALU.mult).then_inc(*DV.inc(f"t0_{h}"))
    at(DV, f"t0_{h}")
    xy = ch.xy[:, :, :, :].rearrange("p a i t -> p a (i t)")
    tmp = ch.tmp[:, :, :, :].rearrange("p a i t -> p a (i t)")
    unit = bc(k.ident2[:, :, :].rearrange("p i t -> p (i t)").unsqueeze(1), [P, NPAIR, 128])
    v.tensor_tensor(xy, unit, tmp, ALU.subtract).then_inc(*DV.inc(f"xy0_{h}"))
    yield
    pq = b.ps[:, BANK_Q[h], :].rearrange("p (a m) -> p a m", a=4)
    for lv in range(1, levels):
        at(PE, f"xmx{lv}_{h}")
        lm = k.lv_mask[:, lv, :, :].rearrange("p i t -> p (i t)").unsqueeze(1)
        v.tensor_tensor(tmp, pq, bc(lm, [P, NPAIR, 128]), ALU.mult).then_inc(*DV.inc(f"t{lv}_{h}"))
        at(DV, f"t{lv}_{h}")
        v.tensor_tensor(xy, xy, tmp, ALU.subtract).then_inc(*DV.inc(f"xy{lv}_{h}"))
        yield


class RwBuffers:

    def __init__(self, k, ctx, tag, levels, chunks, after_pe, after_act, after_dve):
        sb = lambda n, s: ctx.enter_context(k.nc.sbuf_tensor(f"{tag}_{n}", s, F32))
        self.chunks = [RwChunk(k, ctx, tag, h) for h in chunks]
        self.rhs = sb("rhs", [P, NPAIR, CL])
        self.u = sb("u", [P, NPAIR, CL])
        self.ps = ctx.enter_context(k.nc.psum_tensor(f"{tag}_ps", [P, 8, 512], F32))
        each = lambda steps: [f"{s}_{h}" for h in chunks for s in steps]
        self.PE = Progress(k.sem(f"{tag}_pe"), *in_turn_steps(chunks, ["mt", "m", "tok"], [["mx"], ["xmx"]], levels), *each(after_pe))
        self.AC = Progress(k.sem(f"{tag}_act"), *in_turn_steps(chunks, ["tok"], [["mx"]], levels), *each(after_act))
        self.DV = Progress(k.sem(f"{tag}_dve"), *in_turn_steps(chunks, ["mt", "t0", "xy0"], [["t", "xy"]], levels), *each(after_dve))


def phase_rw_prompt(k):
    nc, io = k.nc, k.io
    BANK_Y, BANK_S, BANK_MOD = 0, 1, (2, 5)
    with ExitStack() as ctx:
        b = RwBuffers(k, ctx, "rwc", LEVELS, (0, 1), ["rhs", "u", "row", "y", "s", "turn"], ["u", "row", "y"],
                      ["rhs", "s_add", "s", "mod"])
        PE, AC, DV = b.PE, b.AC, b.DV
        in5 = [ctx.enter_context(nc.sbuf_tensor(f"rwc_in{i}", [P, 5, NPAIR, CL], F32)) for i in range(2)]
        S = ctx.enter_context(nc.sbuf_tensor("rwc_state", [P, NPAIR, CL], F32))
        y = [ctx.enter_context(nc.sbuf_tensor(f"rwc_y{i}", [P, NPAIR, CL], F32)) for i in range(2)]
        wa = [ctx.enter_context(nc.sbuf_tensor(f"rwc_ada{i}", [P, KC, ADA_STEP * P], F32)) for i in range(2)]
        s_in = [k.sem(f"rwc_in{i}_loaded") for i in range(2)]
        s_wa = [k.sem(f"rwc_ada{i}_loaded") for i in range(2)]
        s_mod = k.sem("rwc_gains_scaled")
        s_y = k.sem("rwc_y_stored")
        s_init = k.sem("rwc_state_zeroed")
        s_sel = k.sem("head_sel_step")
        heads = [(p_, rows) for p_ in range(NPAIR) for rows in halves()]
        four = lambda bank: b.ps[:, bank, 0:256].rearrange("p (a t) -> p a t", a=4)
        ACOLS = ADA_STEP * P
        row = ctx.enter_context(nc.sbuf_tensor("rwc_ada_row", [NCOND, ACOLS], F32))
        rowp = lambda h: b.ps[0:NCOND, BANK_MOD[h], 0:ACOLS]
        modp = lambda h: b.ps[:, BANK_MOD[h], ACOLS:ACOLS + ADA_STEP * NCOND].rearrange("p (m c) -> p m c", m=ADA_STEP)
        R = NCH // 2

        def at_of(eng, r):
            return lambda S_, step: eng.wait_ge(S_.sem, S_.now(step, r))

        def pe_at_of(pe, r, one):
            def at(S_, step):
                pe.wait_ge(S_.sem, S_.now(step, r))
                pe.reg_alu(one, one, 1, ALU.max)
            return at

        with nc.Block() as block:
            @block.sync
            def _(sp):
                def load(c, h):
                    sp.dma_start(in5[h][:, :, :, :], io["rwc"][c]).then_inc(s_in[h], 16)
                    sp.dma_start(wa[h][:, :, :], io["w_ada_rest"][c]).then_inc(s_wa[h], 16)

                def store(r, h):
                    sp.wait_ge(AC.sem, AC.now(f"y_{h}", r))
                    sp.dma_start(io["rw_y"][2 * r + h], y[h][:, :, :]).then_inc(s_y, 16)

                for h in range(2):
                    load(h, h)
                with sp.Fori(0, R - 1) as r:
                    for h in range(2):
                        store(r, h)
                        sp.wait_ge(PE.sem, PE.now(f"turn_{h}", r))
                        load(2 * r + (h + 2), h)
                for h in range(2):
                    store(R - 1, h)
                sp.wait_ge(DV.sem, DV.now("s_1", R - 1))
                sp.dma_start(io["wkv_out"][0], S[:, :, :]).then_inc(s_y, 16)
                sp.wait_ge(s_y, 16 * NCH + 32 + 16)

            @block.gpsimd
            def _(pool):
                make_head_sel(k, pool, s_sel)

            @block.tensor
            def _(pe):
                PE.credit(pe)
                one = pe.alloc_register("rwc_one")
                pe.reg_mov(one, 1)

                def state_part(at, r, h, ch):
                    def modulation():
                        pe.wait_ge(s_wa[h], 16 * r + 16)
                        pe.reg_alu(one, one, 1, ALU.max)
                        for kc in range(KC):
                            yield nc.tensor.matmul(rowp(h), k.cT[:, kc, :], wa[h][:, kc, :], start=kc == 0, stop=kc == KC - 1)

                    rest = modulation()
                    fill = lambda n: [next(rest) for _ in range(n)]
                    for p_, rows in heads:
                        nc.tensor.matmul(four(BANK_U)[rows, p_, :], ch.mt[rows, p_, 128:192], ch.tok[rows, 2, p_, :],
                                         start=True, stop=False)
                        if p_ == 0 and rows.start == 0 and h:
                            at(DV, "s_0")
                        mm = nc.tensor.matmul(four(BANK_U)[rows, p_, :], in5[h][rows, KA, p_, :], S[rows, p_, :],
                                              start=False, stop=True)
                    mm.then_inc(*PE.inc(f"rhs_{h}"))
                    fill(4)
                    at(DV, f"rhs_{h}")
                    for p_, rows in heads:
                        mm = nc.tensor.matmul(four(BANK_U)[rows, p_, :], ch.xy[rows, p_, 1, :], b.rhs[rows, p_, :],
                                              start=True, stop=True)
                    mm.then_inc(*PE.inc(f"u_{h}"))
                    for mm in rest:
                        pass
                    mm.then_inc(*PE.inc(f"row_{h}"))
                    at(AC, f"u_{h}")
                    if h:
                        at(AC, "y_0")
                    for p_, rows in heads:
                        o_ = four(BANK_Y)[rows, p_, :]
                        nc.tensor.matmul(o_, S[rows, p_, :], in5[h][rows, RB, p_, :], start=True, stop=False)
                        nc.tensor.matmul(o_, b.u[rows, p_, :], ch.mt[rows, p_, 64:128], start=False, stop=False)
                        mm = nc.tensor.matmul(o_, ch.tok[rows, 2, p_, :], ch.mt[rows, p_, 192:256], start=False, stop=True)
                    mm.then_inc(*PE.inc(f"y_{h}"))
                    for p_, rows in heads:
                        o_ = four(BANK_S)[rows, p_, :]
                        nc.tensor.matmul(o_, ch.tok[rows, 0, p_, :], b.u[rows, p_, :], start=True, stop=False)
                        mm = nc.tensor.matmul(o_, ch.tok[rows, 1, p_, :], ch.tok[rows, 2, p_, :], start=False, stop=True)
                    mm.then_inc(*PE.inc(f"s_{h}"))
                    at(AC, f"row_{h}")
                    for m in range(ADA_STEP):
                        mm = nc.tensor.matmul(modp(h)[:, m, :], row[:, m * P:(m + 1) * P], k.ident[0:NCOND, 0:NCOND],
                                              start=True, stop=True)
                    mm.then_inc(*PE.inc(f"turn_{h}"))

                with pe.Fori(0, R) as r:
                    at = pe_at_of(pe, r, one)
                    for h in range(2):
                        pe.wait_ge(s_in[h], 16 * r + 16)
                    pe.wait_ge(DV.sem, DV.before("mod_1", r))
                    pe.wait_ge(AC.sem, AC.before("y_1", r))
                    pe.wait_ge(s_init, one)
                    pe.reg_alu(one, one, 1, ALU.max)
                    in_turn(rw_matrix_pe(k, b, ch, in5[ch.h], LEVELS, at) for ch in b.chunks)
                    for ch in b.chunks:
                        state_part(at, r, ch.h, ch)

            @block.scalar
            def _(act):
                AC.credit(act)
                act.sem_inc(s_y, 32)
                with act.Fori(0, R) as r:
                    at = at_of(act, r)
                    in_turn(rw_matrix_act(k, b, ch, LEVELS, at) for ch in b.chunks)
                    for h in range(2):
                        at(PE, f"u_{h}")
                        nc.scalar.activation(b.u[:, :, :].rearrange("p a t -> p (a t)"), b.ps[:, BANK_U, 0:256],
                                             ACT.Copy, scale=-1.0).then_inc(*AC.inc(f"u_{h}"))
                        at(PE, f"row_{h}")
                        nc.scalar.activation(row[:, :], rowp(h), ACT.Copy).then_inc(*AC.inc(f"row_{h}"))
                        at(PE, f"y_{h}")
                        act.wait_ge(s_y, 32 * r + 32)
                        nc.scalar.activation(y[h][:, :, :].rearrange("p a t -> p (a t)"), b.ps[:, BANK_Y, 0:256],
                                             ACT.Copy).then_inc(*AC.inc(f"y_{h}"))

            @block.vector
            def _(dve):
                v = nc.vector
                DV.credit(dve)
                v.memset(S[:, :, :], 0.0).then_inc(s_init, 1)
                with dve.Fori(0, R) as r:
                    at = at_of(dve, r)
                    in_turn(rw_matrix_dve(k, b, ch, 0, LEVELS, at) for ch in b.chunks)
                    for h in range(2):
                        c = 2 * r + h
                        at(PE, f"rhs_{h}")
                        v.tensor_copy(b.rhs[:, :, :], four(BANK_U)).then_inc(*DV.inc(f"rhs_{h}"))
                        at(PE, f"s_{h}")
                        if h:
                            at(DV, "s_0")
                        else:
                            dve.wait_ge(s_init, 1)
                            dve.wait_ge(DV.sem, DV.before("s_1", r))
                        v.tensor_tensor(S[:, :, :], four(BANK_S), S[:, :, :], ALU.add).then_inc(*DV.inc(f"s_add_{h}"))
                        at(DV, f"s_add_{h}")
                        v.tensor_tensor(S[:, :, :], S[:, :, :], bc(k.lam_end[:, :, bass.ds(c, 1)], [P, NPAIR, CL]),
                                        ALU.mult).then_inc(*DV.inc(f"s_{h}"))
                        at(PE, f"turn_{h}")
                        tiles = bass.ds(c * ADA_STEP + ADA_FIRST, ADA_STEP)
                        v.tensor_tensor(k.mod[:, tiles, :], modp(h), bc(k.par[:, tiles].unsqueeze(2), [P, ADA_STEP, NCOND]),
                                        ALU.add).then_inc(*DV.inc(f"mod_{h}"))
                dve.wait_ge(DV.sem, DV.now("mod_1", R - 1))
                scale_gain(k, SC2, "norm2_g").then_inc(s_mod, 1)
                scale_gain(k, SCF, "final_g").then_inc(s_mod, 1)


def phase_rw_samples(k):
    nc, io = k.nc, k.io
    levels = DSEQ.bit_length() - 1
    with ExitStack() as ctx:
        BANK_Y = 2
        b = RwBuffers(k, ctx, "rws", levels, (0,), ["rhs", "u", "y", "s"], ["u", "y"], ["masked", "rhs", "umask", "s_add", "s"])
        ch = b.chunks[0]
        PE, AC, DV = b.PE, b.AC, b.DV
        sb = lambda n, s: ctx.enter_context(nc.sbuf_tensor(f"rws_{n}", s, F32))
        in5 = sb("in", [P, 5, NPAIR, CL])
        S = sb("state", [P, NSEQ, NPAIR, CL])
        y = sb("y", [P, NPAIR, CL])
        kr = sb("kr", [P, 2 * NPAIR, NSEQ, CL])
        um = sb("um", [P, 2, NPAIR, NSEQ, CL])
        s_in = k.sem("rws_loaded")
        s_out = k.sem("rws_stored")
        heads = [(p_, rows) for p_ in range(NPAIR) for rows in halves()]
        four = lambda bank: b.ps[:, bank, 0:256].rearrange("p (a t) -> p a t", a=4)
        wait_of = lambda eng: (lambda S_, step: eng.wait_ge(S_.sem, S_.done(step)))
        at_of = lambda eng: (lambda S_, step: eng.wait_ge(S_.sem, S_.done(f"{step}_0")))
        SBANK = (0, 1, 3, 4)

        with nc.Block() as block:
            @block.sync
            def _(sp):
                sp.dma_start(in5[:, :, :, :], io["rwc"][NCH]).then_inc(s_in, 16)
                sp.dma_start(S[:, :, :, :], io["wkvT"].rearrange("s p a v -> p s a v")).then_inc(s_in, 16)
                sp.wait_ge(AC.sem, AC.done("y_0"))
                sp.dma_start(io["rw_y"][NCH], y[:, :, :]).then_inc(s_out, 16)
                sp.wait_ge(DV.sem, DV.done("s_0"))
                sp.dma_start(io["wkv_out"][1:NCOND].rearrange("s p a v -> p s a v"), S[:, :, :, :]).then_inc(s_out, 16)
                sp.wait_ge(s_out, 32)

            @block.tensor
            def _(pe):
                at, wait = at_of(pe), wait_of(pe)
                pe.wait_ge(s_in, 32)
                in_turn([rw_matrix_pe(k, b, ch, in5, levels, wait)])
                at(AC, "tok")
                at(DV, "masked")
                for p_, rows in heads:
                    o_ = four(BANK_U)[rows, p_, :]
                    for s in range(NSEQ):
                        nc.tensor.matmul(o_, kr[rows, p_, s, :], S[rows, s, p_, :], start=s == 0, stop=False)
                    mm = nc.tensor.matmul(o_, ch.mt[rows, p_, 128:192], ch.tok[rows, 2, p_, :], start=False, stop=True)
                mm.then_inc(*PE.inc("rhs_0"))
                at(DV, "rhs")
                for p_, rows in heads:
                    mm = nc.tensor.matmul(four(BANK_U)[rows, p_, :], ch.xy[rows, p_, 1, :], b.rhs[rows, p_, :],
                                          start=True, stop=True)
                mm.then_inc(*PE.inc("u_0"))
                at(AC, "u")
                for p_, rows in heads:
                    o_ = four(BANK_Y)[rows, p_, :]
                    for s in range(NSEQ):
                        nc.tensor.matmul(o_, S[rows, s, p_, :], kr[rows, NPAIR + p_, s, :], start=s == 0, stop=False)
                    nc.tensor.matmul(o_, b.u[rows, p_, :], ch.mt[rows, p_, 64:128], start=False, stop=False)
                    mm = nc.tensor.matmul(o_, ch.tok[rows, 2, p_, :], ch.mt[rows, p_, 192:256], start=False, stop=True)
                mm.then_inc(*PE.inc("y_0"))
                at(DV, "umask")
                for p_, rows in heads:
                    o_ = b.ps[rows, SBANK[p_], :]
                    nc.tensor.matmul(o_, ch.tok[rows, 0, p_, :], um[rows, 0, p_, :, :], start=True, stop=False)
                    mm = nc.tensor.matmul(o_, ch.tok[rows, 1, p_, :], um[rows, 1, p_, :, :], start=False, stop=True)
                mm.then_inc(*PE.inc("s_0"))

            @block.scalar
            def _(act):
                at, wait = at_of(act), wait_of(act)
                in_turn([rw_matrix_act(k, b, ch, levels, wait)])
                at(PE, "u")
                nc.scalar.activation(b.u[:, :, :].rearrange("p a t -> p (a t)"), b.ps[:, BANK_U, 0:256],
                                     ACT.Copy, scale=-1.0).then_inc(*AC.inc("u_0"))
                at(PE, "y")
                nc.scalar.activation(y[:, :, :].rearrange("p a t -> p (a t)"), b.ps[:, BANK_Y, 0:256],
                                     ACT.Copy).then_inc(*AC.inc("y_0"))

            @block.vector
            def _(dve):
                v = nc.vector
                at, wait = at_of(dve), wait_of(dve)
                in_turn([rw_matrix_dve(k, b, ch, 1, levels, wait)])
                dve.wait_ge(s_in, 32)
                src = in5[:, 0:2, :, :].rearrange("p q a t -> p (q a) t").unsqueeze(2)
                v.tensor_tensor(kr[:, :, :, :], bc(src, [P, 2 * NPAIR, NSEQ, CL]),
                                bc(k.seq_cols[:, :, :].unsqueeze(1), [P, 2 * NPAIR, NSEQ, CL]),
                                ALU.mult).then_inc(*DV.inc("masked_0"))
                at(PE, "rhs")
                v.tensor_copy(b.rhs[:, :, :], four(BANK_U)).then_inc(*DV.inc("rhs_0"))
                at(AC, "u")
                rows_of = bc(k.seq_rows[:, :].unsqueeze(1).unsqueeze(3), [P, NPAIR, NSEQ, CL])
                v.tensor_tensor(um[:, 0], bc(b.u[:, :, :].unsqueeze(2), [P, NPAIR, NSEQ, CL]), rows_of, ALU.mult)
                v.tensor_tensor(um[:, 1], bc(ch.tok[:, 2, :, :].unsqueeze(2), [P, NPAIR, NSEQ, CL]), rows_of,
                                ALU.mult).then_inc(*DV.inc("umask_0"))
                at(PE, "s")
                for p_ in range(NPAIR):
                    last = v.tensor_tensor(S[:, :, p_, :], b.ps[:, SBANK[p_], :].rearrange("p (s t) -> p s t", s=NSEQ),
                                           S[:, :, p_, :], ALU.add)
                last.then_inc(*DV.inc("s_add_0"))
                at(DV, "s_add")
                for p_ in range(NPAIR):
                    last = v.tensor_tensor(S[:, :, p_, :], S[:, :, p_, :],
                                           bc(k.lam_end[:, p_, NCH:NCH + NSEQ].unsqueeze(2), [P, NSEQ, CL]), ALU.mult)
                last.then_inc(*DV.inc("s_0"))


def phase_ssd(k):
    for c in ("prompt", "samples"):
        ssd_chunks(k, c)


def ssd_chunks(k, which):
    nc, io = k.nc, k.io
    smp = which == "samples"
    L = NSEQ * DSEQ if smp else SL
    rounds = 1 if smp else NSC // 2
    slots = 1 if smp else 2
    tag = "ss" if smp else "sp"
    with ExitStack() as ctx:
        sb = lambda n, s: ctx.enter_context(nc.sbuf_tensor(f"{tag}_{n}", s, F32))
        inx = [sb(f"in{i}", [P, NXBC, L]) for i in range(slots)]
        rows = [sb(f"rows{i}", [SH, 3, L]) for i in range(slots)]
        y = [sb(f"y{i}", [P, KC, L]) for i in range(slots)]
        S = sb("state", [P, NSEQ if smp else 1, SH, SD])
        col = sb("col", [P, 3, SH])
        cb = sb("cb", [P, SG, L])
        btok = sb("btok", [P, SG, SN])
        xt = sb("xt", [P, SH, SD])
        xd = sb("xd", [P, SH, SD])
        w = sb("w", [P, SH, L])
        ce = sb("ce", [P, SH, L])
        end = sb("end", [P, NSEQ if smp else 1, SH])
        xm = [sb(f"xm{i}", [P, SH, SD]) for i in range(2)] if smp else None
        ps = ctx.enter_context(nc.psum_tensor(f"{tag}_ps", [P, 8, 512], F32))
        s_in = [k.sem(f"{tag}_in{i}_loaded") for i in range(slots)]
        s_S = k.sem(f"{tag}_state_ready")
        s_y = k.sem(f"{tag}_y_stored")
        s_out = k.sem(f"{tag}_state_stored")
        s_xm = k.sem(f"{tag}_masked_x")
        s_sm = k.sem(f"{tag}_state_matmul")
        s_sv = k.sem(f"{tag}_state_step")
        PE = Progress(k.sem(f"{tag}_pe"), "col", "bc", "x", "csb", "y", "s")
        AC = Progress(k.sem(f"{tag}_act"), "col", "btok", "excs", "dec", "y")
        DV = Progress(k.sem(f"{tag}_dve"), "cb", "x", "xd", "diff", "end", "w", "ce", "s_decay", "s")
        cview = ps[:, 0, 0:3 * SH].rearrange("p (q h) -> p q h", q=3)
        bcv = ps[:, 1, :].rearrange("p (i g m) -> p i g m", i=2, g=SG)
        xv = ps[:, 2:4, :].rearrange("p a b -> p (a b)").rearrange("p (h m) -> p h m", h=SH)
        csb = ps[:, 4:8, :].rearrange("p a b -> p (a b)")[:, 0:SH * SL].rearrange("p (h l) -> p h l", h=SH)[:, :, 0:L]
        yv = ps[:, 2:4, :].rearrange("p a b -> p (a b)").rearrange("p (a l) -> p a l", a=KC)[:, :, 0:L]
        tokens = lambda c: slice(SEQ, T) if smp else bass.ds(c * SL, SL)

        def at_of(eng, c):
            if smp:
                return lambda S_, step: eng.wait_ge(S_.sem, S_.done(step))
            return lambda S_, step: eng.wait_ge(S_.sem, S_.now(step, c))

        def chunks(eng):
            if smp:
                yield 0, 0, 0
                return
            with eng.Fori(0, rounds) as r:
                for h in range(2):
                    yield 2 * r + h, h, r

        with nc.Block() as block:
            @block.sync
            def _(sp):
                if smp:
                    sp.dma_start(S[:, :, :, :].rearrange("p s h m -> p s (h m)"), io["ssmT"].rearrange("s n m -> n s m")).then_inc(s_S, 16)
                for c, h, r in chunks(sp):
                    if not smp:
                        sp.wait_ge(PE.sem, PE.before("y", 2 * r))
                        sp.wait_ge(DV.sem, DV.before("ce", 2 * r))
                    sp.dma_start(inx[h][:, :, :], io["xbc"][:, :, tokens(c)].rearrange("a p t -> p a t")).then_inc(s_in[h], 16)
                    sp.dma_start(rows[h][:, :, :], io["ssd_rows"][:, :, tokens(c)]).then_inc(s_in[h], 16)
                if smp:
                    sp.wait_ge(s_sv, 2 * NSEQ * 2)
                    sp.dma_start(io["ssm_out"][1:NCOND].rearrange("s n m -> n s m"), S[:, :, :, :].rearrange("p s h m -> p s (h m)")).then_inc(s_S, 16)
                    sp.wait_ge(s_S, 32)
                else:
                    sp.wait_ge(DV.sem, DV.now("s", NSC - 1))
                    sp.dma_start(io["ssm_out"][0], S[:, 0, :, :].rearrange("p h m -> p (h m)")).then_inc(s_out, 16)
                    sp.wait_ge(s_out, 16)

            @block.gpsimd
            def _(pool):
                for c, h, r in chunks(pool):
                    at_of(pool, c)(AC, "y")
                    pool.dma_start(io["ssd_y"][:, :, tokens(c)].rearrange("a p t -> p a t"), y[h][:, :, :]).then_inc(s_y, 16)
                pool.wait_ge(s_y, 16 if smp else 16 * NSC)

            @block.tensor
            def _(pe):
                if not smp:
                    PE.credit(pe)
                for c, h, r in chunks(pe):
                    at = at_of(pe, c)
                    pe.wait_ge(s_in[h], 32 * r + 32)
                    if not smp:
                        pe.wait_ge(DV.sem, DV.before("s", c))
                        pe.wait_ge(AC.sem, AC.before("y", c))
                        pe.wait_ge(s_S, 1)
                    for i in range(3):
                        mm = nc.tensor.matmul(cview[0:L, i, :], rows[h][:, i, :], k.ident[0:SH, 0:SH], start=True, stop=True)
                    mm.then_inc(*PE.inc("col"))
                    for g in range(SG):
                        nc.tensor.matmul(bcv[0:L, 0, g, 0:L], inx[h][:, 8 + g, :], inx[h][:, 10 + g, :], start=True, stop=True)
                        mm = nc.tensor.transpose(bcv[0:L, 1, g, :], inx[h][:, 8 + g, :], k.ident[:, :])
                    mm.then_inc(*PE.inc("bc"))
                    for i in range(KC):
                        mm = nc.tensor.transpose(xv[0:L, 2 * i:2 * i + 2, :].rearrange("p h m -> p (h m)"), inx[h][:, i, :], k.ident[:, :])
                    mm.then_inc(*PE.inc("x"))
                    for i in range(SH):
                        mm = nc.tensor.matmul(csb[:, i, :], k.head_sel[:, i, :], rows[h][:, 1, :], start=True, stop=True)
                    mm.then_inc(*PE.inc("csb"))
                    if smp:
                        pe.wait_ge(s_S, 16)
                    at(DV, "x")
                    at(DV, "w")
                    at(DV, "ce")
                    for i in range(SH):
                        o_ = yv[64 * (i % 2):64 * (i % 2) + 64, i // 2, :]
                        nc.tensor.matmul(o_, xt[0:L, i, :], w[0:L, i, :], start=True, stop=False)
                        if smp:
                            for s in range(NSEQ):
                                t = slice(DSEQ * s, DSEQ * s + DSEQ)
                                mm = nc.tensor.matmul(o_[:, t], S[:, s, i, :], ce[:, i, t], start=False, stop=s == NSEQ - 1)
                        else:
                            mm = nc.tensor.matmul(o_, S[:, 0, i, :], ce[:, i, :], start=False, stop=True)
                    mm.then_inc(*PE.inc("y"))
                    at(AC, "col")
                    at(AC, "btok")
                    at(DV, "xd")
                    if smp:
                        for s in range(NSEQ):
                            pe.wait_ge(s_xm, s + 1)
                            for g in range(SG):
                                n = 2 * s + g
                                if n >= 2:
                                    pe.wait_ge(s_sv, 2 * (n - 1))
                                nc.tensor.matmul(ps[:, n % 2, :], btok[0:L, g, :],
                                                 xm[s % 2][0:L, 8 * g:8 * g + 8, :].rearrange("p h m -> p (h m)"),
                                                 start=True, stop=True).then_inc(s_sm, 1)
                    else:
                        for g in range(SG):
                            mm = nc.tensor.matmul(ps[:, g, :], btok[:, g, :], xd[:, 8 * g:8 * g + 8, :].rearrange("p h m -> p (h m)"),
                                                  start=True, stop=True)
                        mm.then_inc(*PE.inc("s"))

            @block.scalar
            def _(act):
                a = nc.scalar
                if not smp:
                    AC.credit(act)
                for c, h, r in chunks(act):
                    at = at_of(act, c)
                    at(PE, "col")
                    a.activation(col[0:L, 0:2, :], cview[0:L, 0:2, :], ACT.Copy)
                    a.activation(col[0:L, 2, :], cview[0:L, 2, :], ACT.Exp).then_inc(*AC.inc("col"))
                    at(PE, "bc")
                    a.activation(btok[0:L, :, :], bcv[0:L, 1, :, :], ACT.Copy).then_inc(*AC.inc("btok"))
                    at(PE, "csb")
                    a.activation(ce[:, :, :], csb, ACT.Exp).then_inc(*AC.inc("excs"))
                    at(DV, "diff")
                    a.activation(w[0:L, :, :], w[0:L, :, :], ACT.Exp).then_inc(*AC.inc("dec"))
                    at(PE, "y")
                    if not smp:
                        act.wait_ge(s_y, 32 * r)
                    a.activation(y[h][:, :, :], yv, ACT.Copy).then_inc(*AC.inc("y"))

            @block.vector
            def _(dve):
                v = nc.vector
                if not smp:
                    DV.credit(dve)
                    v.memset(S[:, 0, :, :], 0.0).then_inc(s_S, 1)
                mask = k.ssd_mask_smp if smp else k.ssd_mask
                for c, h, r in chunks(dve):
                    at = at_of(dve, c)
                    at(AC, "btok")
                    v.tensor_tensor(cb[0:L, :, :], bcv[0:L, 0, :, 0:L], bc(mask[0:L, 0:L].unsqueeze(1), [L, SG, L]),
                                    ALU.mult).then_inc(*DV.inc("cb"))
                    at(PE, "x")
                    v.tensor_tensor(xt[0:L, :, :], xv[0:L, :, :], bc(col[0:L, 0, :].unsqueeze(2), [L, SH, SD]), ALU.mult).then_inc(*DV.inc("x"))
                    at(DV, "x")
                    v.tensor_tensor(xd[0:L, :, :], xt[0:L, :, :], bc(col[0:L, 2, :].unsqueeze(2), [L, SH, SD]), ALU.mult).then_inc(*DV.inc("xd"))
                    at(AC, "excs")
                    for i in range(SH):
                        last = v.tensor_scalar(w[0:L, i, :], csb[0:L, i, :], col[0:L, 1, i:i + 1], 0.0, ALU.subtract, ALU.min)
                    last.then_inc(*DV.inc("diff"))
                    if smp:
                        v.tensor_copy(end[:, :, :], ce[:, :, DSEQ - 1:L:DSEQ].rearrange("p h s -> p s h")).then_inc(*DV.inc("end"))
                    else:
                        v.tensor_copy(end[:, 0, :], ce[:, :, L - 1]).then_inc(*DV.inc("end"))
                    at(AC, "dec")
                    for g in range(SG):
                        hh = slice(8 * g, 8 * g + 8)
                        last = v.tensor_tensor(w[0:L, hh, :], w[0:L, hh, :], bc(cb[0:L, g:g + 1, :], [L, 8, L]), ALU.mult)
                    last.then_inc(*DV.inc("w"))
                    at(DV, "end")
                    for g in range(SG):
                        hh = slice(8 * g, 8 * g + 8)
                        last = v.tensor_tensor(ce[:, hh, :], ce[:, hh, :], bc(inx[h][:, 10 + g:11 + g, :], [P, 8, L]), ALU.mult)
                    last.then_inc(*DV.inc("ce"))
                    at(PE, "y")
                    if smp:
                        for s in range(NSEQ):
                            if s >= 2:
                                dve.wait_ge(s_sm, 2 * (s - 1))
                            v.tensor_scalar(xm[s % 2][0:L, :, :], xd[0:L, :, :], k.seq_rows[0:L, s:s + 1], None, ALU.mult).then_inc(s_xm, 1)
                            for g in range(SG):
                                n = 2 * s + g
                                sv = S[:, s, 8 * g:8 * g + 8, :]
                                v.tensor_tensor(sv, sv, bc(end[:, s, 8 * g:8 * g + 8].unsqueeze(2), [P, 8, SD]), ALU.mult).then_inc(s_sv, 1)
                                dve.wait_ge(s_sv, 2 * n + 1)
                                dve.wait_ge(s_sm, n + 1)
                                v.tensor_tensor(sv, sv, ps[:, n % 2, :].rearrange("p (h m) -> p h m", h=8), ALU.add).then_inc(s_sv, 1)
                    else:
                        dve.wait_ge(s_S, 1)
                        v.tensor_tensor(S[:, 0], S[:, 0], bc(end[:, 0, :].unsqueeze(2), [P, SH, SD]), ALU.mult).then_inc(*DV.inc("s_decay"))
                        at(DV, "s_decay")
                        at(PE, "s")
                        for g in range(SG):
                            sv = S[:, 0, 8 * g:8 * g + 8, :]
                            last = v.tensor_tensor(sv, sv, ps[:, g, :].rearrange("p (h m) -> p h m", h=8), ALU.add)
                        last.then_inc(*DV.inc("s"))


def phase_rw_post(k, oa):
    nc, io = k.nc, k.io
    with ExitStack() as ctx:
        sb = lambda n, s: ctx.enter_context(nc.sbuf_tensor(f"ro_{n}", s, F32))
        y, gate, bonus = ([sb(f"{n}{i}", [P, T]) for i in range(2)] for n in ("y", "gate", "bonus"))
        sq, rs = sb("sq", [P, T]), sb("rs", [P, T])
        ps = [ctx.enter_context(nc.psum_tensor(f"ro_ps{i}", [P, 3, 512], F32)) for i in range(2)]
        pm, pv = (banked(p_) for p_ in ps)
        s_in = [k.sem(f"ro_in{i}_loaded") for i in range(2)]
        PE = Progress(k.sem("ro_pe"), "mean", "var")
        AC = Progress(k.sem("ro_act"), "sq", "ln", "rstd")
        DV = Progress(k.sem("ro_dve"), "center", "norm", "affine", "bonus", "gate")
        with nc.Block() as block:
            @block.sync
            def _(sp):
                for p_ in range(NPAIR):
                    h = p_ % 2
                    if p_ >= 2:
                        sp.wait_ge(DV.sem, DV.done("gate", p_ - 2))
                    sp.dma_start(y[h][:, :].rearrange("p (c t) -> p c t", t=CL),
                                 io["rw_y"][:, :, p_, :].rearrange("c p t -> p c t")).then_inc(s_in[h], 16)
                    sp.dma_start(gate[h][:, :], io["rw_gate"][p_]).then_inc(s_in[h], 16)
                    sp.dma_start(bonus[h][:, :], io["rw_bonus"][p_]).then_inc(s_in[h], 16)

            @block.tensor
            def _(pe):
                for p_ in range(NPAIR):
                    pe.wait_ge(s_in[p_ % 2], 48 * (p_ // 2 + 1))
                    for out, src, step in ((pm, y[p_ % 2], "mean"), (pv, sq, "var")):
                        if step == "var":
                            pe.wait_ge(AC.sem, AC.done("sq", p_))
                        elif p_ >= 1:
                            pe.wait_ge(DV.sem, DV.done("center", p_ - 1))
                        for a, b in TOK_CHUNKS_BANKED:
                            mm = nc.tensor.matmul(out[:, a:b], k.pairones[:, :], src[:, a:b], start=True, stop=True)
                        mm.then_inc(*PE.inc(step))

            @block.scalar
            def _(act):
                for p_ in range(NPAIR):
                    act.wait_ge(DV.sem, DV.done("center", p_))
                    nc.scalar.activation(sq[:, :], y[p_ % 2][:, :], ACT.Square).then_inc(*AC.inc("sq"))
                    act.wait_ge(PE.sem, PE.done("var", p_))
                    nc.scalar.activation(rs[:, :], pv[:, 0:T], ACT.Ln, scale=1.0 / RD, bias=k.const[:, 1:2]).then_inc(*AC.inc("ln"))
                    act.wait_ge(AC.sem, AC.done("ln", p_))
                    nc.scalar.activation(rs[:, :], rs[:, :], ACT.Exp, scale=-0.5).then_inc(*AC.inc("rstd"))

            @block.vector
            def _(dve):
                v = nc.vector
                lnw, lnb = k.par[:, PCOLS["ln_w"]], k.par[:, PCOLS["ln_b"]]
                for p_ in range(NPAIR):
                    h = p_ % 2
                    yt = y[h][:, :]
                    now = lambda s_: dve.wait_ge(DV.sem, DV.done(s_, p_))
                    dve.wait_ge(PE.sem, PE.done("mean", p_))
                    v.scalar_tensor_tensor(out=yt, in0=pm[:, 0:T], scalar=-1.0 / RD, in1=yt, op0=ALU.mult,
                                           op1=ALU.add).then_inc(*DV.inc("center"))
                    dve.wait_ge(AC.sem, AC.done("rstd", p_))
                    v.tensor_tensor(yt, yt, rs[:, :], ALU.mult).then_inc(*DV.inc("norm"))
                    now("norm")
                    v.tensor_scalar(yt, yt, lnw[:, p_:p_ + 1], lnb[:, p_:p_ + 1], ALU.mult, ALU.add).then_inc(*DV.inc("affine"))
                    now("affine")
                    v.tensor_tensor(yt, yt, bonus[h][:, :], ALU.add).then_inc(*DV.inc("bonus"))
                    now("bonus")
                    v.tensor_tensor(oa[:, p_, :], yt, gate[h][:, :], ALU.mult).then_inc(*DV.inc("gate"))


def phase_ssd_post(k, ob):
    nc, io = k.nc, k.io
    GT = KC // SG
    with ExitStack() as ctx:
        sb = lambda n, s: ctx.enter_context(nc.sbuf_tensor(f"so_{n}", s, F32))
        y, x, z = ([sb(f"{n}{i}", [P, T]) for i in range(2)] for n in ("y", "x", "z"))
        sg, sq, rs = sb("sg", [P, T]), sb("sq", [P, T]), sb("rs", [P, T])
        d = sb("d", [P, KC])
        ps = ctx.enter_context(nc.psum_tensor("so_ps", [P, 3, 512], F32))
        pf = banked(ps)
        s_in = [k.sem(f"so_in{i}_loaded") for i in range(2)]
        s_d = k.sem("so_d_loaded")
        s_r = k.sem("so_rstd_step")
        s_n = k.sem("so_scaled")
        PE = Progress(k.sem("so_pe"), "sum")
        AC = Progress(k.sem("so_act"), "sigmoid", "sq")
        DV = Progress(k.sem("so_dve"), "silu", "skip", "gate")
        with nc.Block() as block:
            @block.sync
            def _(sp):
                for h, rows in enumerate(halves()):
                    sp.dma_start(d[rows, :], bc(io["ssm_D"][h:h + 1, :], [64, KC])).then_inc(s_d, 16)
                for i in range(KC):
                    if i >= 2:
                        sp.wait_ge(DV.sem, DV.done("gate", i - 2))
                    for t, src in ((y, io["ssd_y"][i]), (x, io["xbc"][i]), ):
                        sp.dma_start(t[i % 2][:, :], src).then_inc(s_in[i % 2], 16)
                    zsrc = io["proj"][Z0 + i]
                    (_, zp), (_, zs) = predecessor_views(zsrc)
                    op, os = token_views(z[i % 2])
                    sp.dma_start(op, zp).then_inc(s_in[i % 2], 16)
                    sp.dma_start(os, zs).then_inc(s_in[i % 2], 16)

            @block.tensor
            def _(pe):
                for i in range(KC):
                    pe.wait_ge(AC.sem, AC.done("sq", i))
                    if i and i % GT == 0:
                        pe.wait_ge(s_r, 2 * (i // GT))
                    for a, b in TOK_CHUNKS_BANKED:
                        mm = nc.tensor.matmul(pf[:, a:b], k.ones[:, :], sq[:, a:b], start=i % GT == 0, stop=i % GT == GT - 1)
                    mm.then_inc(*PE.inc("sum"))

            @block.scalar
            def _(act):
                for i in range(KC):
                    act.wait_ge(s_in[i % 2], 64 * (i // 2 + 1))
                    if i:
                        act.wait_ge(DV.sem, DV.done("silu", i - 1))
                    nc.scalar.activation(sg[:, :], z[i % 2][:, :], ACT.Sigmoid).then_inc(*AC.inc("sigmoid"))
                    act.wait_ge(DV.sem, DV.done("gate", i))
                    if i:
                        act.wait_ge(PE.sem, PE.done("sum", i - 1))
                    nc.scalar.activation(sq[:, :], ob[:, i, :], ACT.Square).then_inc(*AC.inc("sq"))
                    if i % GT == GT - 1:
                        act.wait_ge(PE.sem, PE.done("sum", i))
                        if i > GT:
                            act.wait_ge(s_n, GT)
                        nc.scalar.activation(rs[:, :], pf[:, 0:T], ACT.Ln, scale=1.0 / (GT * P), bias=k.const[:, 0:1]).then_inc(s_r, 1)
                        act.wait_ge(s_r, 2 * (i // GT) + 1)
                        nc.scalar.activation(rs[:, :], rs[:, :], ACT.Exp, scale=-0.5).then_inc(s_r, 1)

            @block.vector
            def _(dve):
                v = nc.vector
                nw = k.par[:, PCOLS["ssm_norm_w"]]
                dve.wait_ge(s_d, 32)
                for i in range(KC):
                    h = i % 2
                    now = lambda s_: dve.wait_ge(DV.sem, DV.done(s_, i))
                    dve.wait_ge(AC.sem, AC.done("sigmoid", i))
                    v.tensor_tensor(z[h][:, :], z[h][:, :], sg[:, :], ALU.mult).then_inc(*DV.inc("silu"))
                    v.scalar_tensor_tensor(out=y[h][:, :], in0=x[h][:, :], scalar=d[:, i:i + 1], in1=y[h][:, :],
                                           op0=ALU.mult, op1=ALU.add).then_inc(*DV.inc("skip"))
                    now("skip")
                    v.tensor_tensor(ob[:, i, :], y[h][:, :], z[h][:, :], ALU.mult).then_inc(*DV.inc("gate"))
                    if i % GT == GT - 1:
                        dve.wait_ge(s_r, 2 * (i // GT) + 2)
                        now("gate")
                        for j in range(i - GT + 1, i + 1):
                            v.scalar_tensor_tensor(out=ob[:, j, :], in0=ob[:, j, :], scalar=nw[:, j:j + 1], in1=rs[:, :],
                                                   op0=ALU.mult, op1=ALU.mult).then_inc(s_n, 1)


def phase_merge(k, oa, ob, x1):
    nc, io = k.nc, k.io
    with ExitStack() as ctx:
        sb = lambda n, s: ctx.enter_context(nc.sbuf_tensor(f"mg_{n}", s, F32))
        merged = sb("merged", [P, KC, T])
        wa = [sb(f"wa{i}", [P, NPAIR, P]) for i in range(2)]
        wb = [sb(f"wb{i}", [P, KC, P]) for i in range(2)]
        wo = [sb(f"wo{i}", [P, KC, P]) for i in range(2)]
        ga = [sb(f"ga{i}", [P, T]) for i in range(2)]
        gb = [sb(f"gb{i}", [P, T]) for i in range(2)]
        tmp = sb("tmp", [P, T])
        ps = [ctx.enter_context(nc.psum_tensor(f"mg_ps{i}", [P, 3, 512], F32)) for i in range(2)]
        pf = [banked(p_) for p_ in ps]
        s_w = [k.sem(f"mg_w{i}_loaded") for i in range(2)]
        s_g = [k.sem(f"mg_gates{i}_loaded") for i in range(2)]
        s_wo = [k.sem(f"mg_wo{i}_loaded") for i in range(2)]
        s_x = k.sem("mg_x_loaded")
        s_xs = k.sem("mg_x1_stored")
        PE = Progress(k.sem("mg_pe"), "a", "b")
        AC = Progress(k.sem("mg_act"), "ga", "gb")
        DV = Progress(k.sem("mg_dve"), "a", "b", "sum")
        s_out = k.sem("mg_out_matmul")
        s_res = k.sem("mg_residual_step")

        with nc.Block() as block:
            @block.sync
            def _(sp):
                sp.dma_start(x1[:, :, :], io["xT"]).then_inc(s_x, 16)
                for m in range(KC):
                    h = m % 2
                    if m >= 2:
                        sp.wait_ge(PE.sem, PE.done("b", m - 2))
                    sp.dma_start(wa[h][:, :, :], io["w_pa"][m]).then_inc(s_w[h], 16)
                    sp.dma_start(wb[h][:, :, :], io["w_pb"][m]).then_inc(s_w[h], 16)
                    if m >= 2:
                        sp.wait_ge(DV.sem, DV.done("sum", m - 2))
                    for t, at in ((ga, 0), (gb, KC)):
                        (_, gp), (_, gs) = predecessor_views(io["proj"][GATE0 + at + m])
                        op, os = token_views(t[h])
                        sp.dma_start(op, gp).then_inc(s_g[h], 16)
                        sp.dma_start(os, gs).then_inc(s_g[h], 16)
                for m in range(KC):
                    if m >= 2:
                        sp.wait_ge(s_out, m - 1)
                    sp.dma_start(wo[m % 2][:, :, :], io["w_out"][m]).then_inc(s_wo[m % 2], 16)
                sp.wait_ge(s_res, 3 * KC)
                sp.dma_start(io["x1"], x1[:, :, :]).then_inc(s_xs, 16)
                sp.wait_ge(s_xs, 16)

            @block.tensor
            def _(pe):
                for m in range(KC):
                    h = m % 2
                    pe.wait_ge(s_w[h], 32 * (m // 2 + 1))
                    for out, w, src, n, step in ((pf[0], wa[h], oa, NPAIR, "a"), (pf[1], wb[h], ob, KC, "b")):
                        if m:
                            pe.wait_ge(DV.sem, DV.done(step, m - 1))
                        for kc in range(n):
                            for a, b in TOK_CHUNKS_BANKED:
                                mm = nc.tensor.matmul(out[:, a:b], w[:, kc, :], src[:, kc, a:b], start=kc == 0, stop=kc == n - 1)
                        mm.then_inc(*PE.inc(step))
                pe.wait_ge(DV.sem, DV.done("sum", KC - 1))
                for m in range(KC):
                    pe.wait_ge(s_wo[m % 2], 16 * (m // 2 + 1))
                    if m >= 2:
                        pe.wait_ge(s_res, 3 * (m - 1))
                    for kc in range(KC):
                        for a, b in TOK_CHUNKS_BANKED:
                            mm = nc.tensor.matmul(pf[m % 2][:, a:b], wo[m % 2][:, kc, :], merged[:, kc, a:b], start=kc == 0, stop=kc == KC - 1)
                    mm.then_inc(s_out, 1)

            @block.scalar
            def _(act):
                for m in range(KC):
                    h = m % 2
                    act.wait_ge(s_g[h], 64 * (m // 2 + 1))
                    nc.scalar.activation(ga[h][:, :], ga[h][:, :], ACT.Sigmoid).then_inc(*AC.inc("ga"))
                    nc.scalar.activation(gb[h][:, :], gb[h][:, :], ACT.Sigmoid).then_inc(*AC.inc("gb"))

            @block.vector
            def _(dve):
                v = nc.vector
                for m in range(KC):
                    h = m % 2
                    dve.wait_ge(AC.sem, AC.done("ga", m))
                    dve.wait_ge(PE.sem, PE.done("a", m))
                    v.tensor_tensor(ga[h][:, :], pf[0][:, 0:T], ga[h][:, :], ALU.mult).then_inc(*DV.inc("a"))
                    dve.wait_ge(AC.sem, AC.done("gb", m))
                    dve.wait_ge(PE.sem, PE.done("b", m))
                    v.tensor_tensor(gb[h][:, :], pf[1][:, 0:T], gb[h][:, :], ALU.mult).then_inc(*DV.inc("b"))
                    dve.wait_ge(DV.sem, DV.done("b", m))
                    v.tensor_tensor(merged[:, m, :], ga[h][:, :], gb[h][:, :], ALU.add).then_inc(*DV.inc("sum"))
                dve.wait_ge(s_x, 16)
                for m in range(KC):
                    dve.wait_ge(s_out, m + 1)
                    add_gated(k, dve, x1[:, m, :], pf[m % 2][:, 0:T], tmp, GT1 + m, s_res, 3 * m)


def add_gated(k, dve, x, y, tmp, gate_at, sem, base):
    v = k.nc.vector
    g = k.mod[:, gate_at, :]
    (xp, xs), (yp, ys), (_, ts) = token_views(x), token_views(y), token_views(tmp)
    if base:
        dve.wait_ge(sem, base)
    v.tensor_tensor(ts, ys, bc(g[:, 1:NCOND].unsqueeze(2), [P, NSEQ, DSEQ]), ALU.mult).then_inc(sem, 1)
    v.scalar_tensor_tensor(out=xp, in0=yp, scalar=g[:, 0:1], in1=xp, op0=ALU.mult, op1=ALU.add).then_inc(sem, 1)
    dve.wait_ge(sem, base + 1)
    v.tensor_tensor(xs, xs, ts, ALU.add).then_inc(sem, 1)


def phase_norm2(k, xh, xl):
    nc, io = k.nc, k.io
    with nc.sbuf_tensor("x1_norm", [P, KC, T], F32) as x:
        def load(sp, sem):
            sp.dma_start(x[:, :, :], io["x1"]).then_inc(sem, 16)
            return 16

        rmsnorm_mod(k, "norm2", x, lambda kc: x[:, kc, 0:SEQ], lambda kc: token_views(x[:, kc, :])[1], SC2, SH2, load)
        s_h, s_l = k.sem("x_high_made"), k.sem("x_low_made")
        with nc.Block() as block:
            @block.scalar
            def _(act):
                for kc in range(KC):
                    nc.scalar.activation(xh[:, kc, :], x[:, kc, :], ACT.Copy).then_inc(s_h, 1)

            @block.vector
            def _(dve):
                for kc in range(KC):
                    dve.wait_ge(s_h, kc + 1)
                    nc.vector.tensor_tensor(xl[:, kc, :], x[:, kc, :], xh[:, kc, :].bitcast(F32), ALU.subtract).then_inc(s_l, 1)


NTILE = -(-T // P)
LAST = T - (NTILE - 1) * P
NEG = -3.0e38


def phase_scores(k, xh, xl, val, idx):
    nc, io = k.nc, k.io
    NQ = 2 * PH
    with ExitStack() as ctx:
        sb = lambda n, s: ctx.enter_context(nc.sbuf_tensor(f"sc_{n}", s, F32))
        w = [sb(f"w{i}", [P, KC, P]) for i in range(2)]
        wh, wl = ([ctx.enter_context(nc.sbuf_tensor(f"sc_w_{n}{i}", [P, KC, P], F32R)) for i in range(2)] for n in ("high", "low"))
        q = [sb(f"q{i}", [P, T]) for i in range(2)]
        sc = [sb(f"s{i}", [P, NTILE, NK]) for i in range(2)]
        keys = sb("keys", [P, NQ, NK])
        psq = ctx.enter_context(nc.psum_tensor("sc_psq", [P, 3, 512], F32))
        pss = ctx.enter_context(nc.psum_tensor("sc_pss", [P, 3, 512], F32))
        pq = banked(psq)
        s_w = [k.sem(f"sc_w{i}_loaded") for i in range(2)]
        s_wh = k.sem("sc_w_high_made")
        s_wl = k.sem("sc_w_low_made")
        s_k = k.sem("sc_keys_loaded")
        s_q = k.sem("sc_query_matmul")
        s_s = k.sem("sc_score_matmul")
        s_qe = k.sem("sc_query_evac")
        s_se = k.sem("sc_score_evac")
        DV = Progress(k.sem("sc_dve"), "max1", "idx1", "rep1", "max2", "idx2")
        with nc.Block() as block:
            @block.sync
            def _(sp):
                sp.dma_start(keys[:, :, :], io["keysT"]).then_inc(s_k, 16)
                for i in range(NQ):
                    if i >= 2:
                        sp.wait_ge(s_wl, i - 1)
                    sp.dma_start(w[i % 2][:, :, :], io["w_q"][i]).then_inc(s_w[i % 2], 16)

            def score(pe, i):
                pe.wait_ge(s_qe, i + 1)
                if i:
                    pe.wait_ge(s_se, i)
                for j in range(NTILE):
                    n = LAST if j == NTILE - 1 else P
                    mm = nc.tensor.matmul(flat(pss[:, :, :])[0:n, j * NK:(j + 1) * NK], q[i % 2][:, j * P:j * P + n],
                                          keys[:, i, :], start=True, stop=True)
                mm.then_inc(s_s, 1)

            @block.tensor
            def _(pe):
                pe.wait_ge(s_k, 16)
                for i in range(NQ):
                    pe.wait_ge(s_wl, i + 1)
                    if i:
                        pe.wait_ge(s_qe, i)
                    passes = [(wt[i % 2], x, kc) for kc in range(KC) for wt, x in ((wh, xh), (wh, xl), (wl, xh))]
                    for n, (wt, x, kc) in enumerate(passes):
                        for a, b in TOK_CHUNKS_BANKED:
                            mm = nc.tensor.matmul(pq[:, a:b], wt[:, kc, :], x[:, kc, a:b], start=n == 0, stop=n == len(passes) - 1)
                    mm.then_inc(s_q, 1)
                    if i:
                        score(pe, i - 1)
                score(pe, NQ - 1)

            @block.scalar
            def _(act):
                def scores(i):
                    act.wait_ge(s_s, i + 1)
                    if i >= 2:
                        act.wait_ge(DV.sem, DV.done("idx2", i - 2))
                    full = (NTILE - 1) * NK
                    flat_s = flat(pss[:, :, :])
                    nc.scalar.activation(flat(sc[i % 2][:, :, :])[:, 0:full], flat_s[:, 0:full], ACT.Copy)
                    nc.scalar.activation(sc[i % 2][0:LAST, NTILE - 1, :], flat_s[0:LAST, full:full + NK], ACT.Copy).then_inc(s_se, 1)

                def split(i):
                    act.wait_ge(s_w[i % 2], 16 * (i // 2 + 1))
                    if i >= 2:
                        act.wait_ge(s_q, i - 1)
                    nc.scalar.activation(wh[i % 2][:, :, :], w[i % 2][:, :, :], ACT.Copy).then_inc(s_wh, 1)

                split(0)
                split(1)
                for i in range(NQ):
                    act.wait_ge(s_q, i + 1)
                    if i >= 2:
                        act.wait_ge(s_s, i - 1)
                    nc.scalar.activation(q[i % 2][:, :], pq[:, 0:T], ACT.Copy).then_inc(s_qe, 1)
                    if i + 2 < NQ:
                        split(i + 2)
                    if i:
                        scores(i - 1)
                scores(NQ - 1)

            @block.vector
            def _(dve):
                v = nc.vector
                tiles = [(j, slice(0, LAST if j == NTILE - 1 else P)) for j in range(NTILE)]

                def split(i):
                    dve.wait_ge(s_wh, i + 1)
                    v.tensor_tensor(wl[i % 2][:, :, :], w[i % 2][:, :, :], wh[i % 2][:, :, :].bitcast(F32), ALU.subtract).then_inc(s_wl, 1)

                split(0)
                split(1)
                for i in range(NQ):
                    s_, top, rest = sc[i % 2], slice(0, 8), slice(8, 16)

                    def done(step):
                        dve.wait_ge(DV.sem, DV.done(step, i))

                    if i + 2 < NQ:
                        split(i + 2)
                    dve.wait_ge(s_se, i + 1)
                    for j, r in tiles:
                        last = v.max(val[r, j, i, top], s_[r, j, :])
                    last.then_inc(*DV.inc("max1"))
                    done("max1")
                    for j, r in tiles:
                        last = v.max_index(idx[r, j, i, top], val[r, j, i, top], s_[r, j, :])
                    last.then_inc(*DV.inc("idx1"))
                    done("idx1")
                    for j, r in tiles:
                        last = v.match_replace(out=s_[r, j, :], in_to_replace=val[r, j, i, top], in_values=s_[r, j, :], imm_value=NEG)
                    last.then_inc(*DV.inc("rep1"))
                    done("rep1")
                    for j, r in tiles:
                        last = v.max(val[r, j, i, rest], s_[r, j, :])
                    last.then_inc(*DV.inc("max2"))
                    done("max2")
                    for j, r in tiles:
                        last = v.max_index(idx[r, j, i, rest], val[r, j, i, rest], s_[r, j, :])
                    last.then_inc(*DV.inc("idx2"))


def phase_topk(k, val, idx, selT):
    nc = k.nc
    NQ, K2 = 2 * PH, TOPK * TOPK
    HK = PH * TOPK
    with ExitStack() as ctx:
        sb = lambda n, s, dt=F32: ctx.enter_context(nc.sbuf_tensor(f"tk_{n}", s, dt))
        idf = sb("idf", [P, NQ, TOPK])
        cand = sb("cand", [P, PH, K2])
        best = sb("best", [P, PH, TOPK])
        prob = sb("prob", [P, PH, TOPK])
        pos = sb("pos", [P, PH, TOPK], U32)
        ab = sb("ab", [P, 2, HK], U32)
        abf = sb("abf", [P, 2, HK])
        eq = sb("eq", [P, HK, TOPK])
        sel = [sb(f"sel{i}", [P, 3, HK]) for i in range(2)]
        ssum = sb("ssum", [P, PH])
        iota_i = sb("iota_i", [P, TOPK], I32)
        iota = sb("iota", [P, TOPK])
        ps = [ctx.enter_context(nc.psum_tensor(f"tk_ps{i}", [P, 512], F32)) for i in range(2)]
        s_io = k.sem("tk_iota_step")
        AC = Progress(k.sem("tk_act"), "exp", "sel")
        PE = Progress(k.sem("tk_pe"), "turned")
        DV = Progress(k.sem("tk_dve"), "idf", "cand", "cmax1", "cidx1", "crep1",
                      "cmax2", "cidx2", "shift", "abf", "off", "eq0", "pick0", "e0", "eq1", "pick1", "e1", "sum", "rec", "gate")

        def select(v, j, slot, n, done):
            r = slice(0, n)
            at = bass.ds(j, 1)
            drop = lambda ap: ap.rearrange("p j i a -> p (j i) a")
            v.tensor_copy(idf[r, :, :], drop(idx[r, at, :, :])).then_inc(*DV.inc("idf"))
            vv = drop(val[r, at, :, :]).rearrange("p (h s) a -> p h s a", s=2)
            v.tensor_tensor(cand[r, :, :].rearrange("p h (a b) -> p h a b", a=TOPK),
                            bc(vv[:, :, 0, :].unsqueeze(3), [n, PH, TOPK, TOPK]),
                            bc(vv[:, :, 1, :].unsqueeze(2), [n, PH, TOPK, TOPK]), ALU.add).then_inc(*DV.inc("cand"))
            done(DV, "cand")
            for h in range(PH):
                last = v.max(best[r, h, 0:8], cand[r, h, :])
            last.then_inc(*DV.inc("cmax1"))
            done(DV, "cmax1")
            for h in range(PH):
                last = v.max_index(pos[r, h, 0:8], best[r, h, 0:8], cand[r, h, :])
            last.then_inc(*DV.inc("cidx1"))
            done(DV, "cidx1")
            for h in range(PH):
                last = v.match_replace(out=cand[r, h, :], in_to_replace=best[r, h, 0:8], in_values=cand[r, h, :], imm_value=NEG)
            last.then_inc(*DV.inc("crep1"))
            done(DV, "crep1")
            for h in range(PH):
                last = v.max(best[r, h, 8:16], cand[r, h, :])
            last.then_inc(*DV.inc("cmax2"))
            done(DV, "cmax2")
            for h in range(PH):
                last = v.max_index(pos[r, h, 8:16], best[r, h, 8:16], cand[r, h, :])
            last.then_inc(*DV.inc("cidx2"))
            done(DV, "cidx2")
            pf = pos[r, :, :].rearrange("p h a -> p (h a)")
            v.tensor_scalar(ab[r, 0, :], pf, 4, None, ALU.logical_shift_right)
            v.tensor_scalar(ab[r, 1, :], pf, TOPK - 1, None, ALU.bitwise_and).then_inc(*DV.inc("shift"))
            done(DV, "shift")
            v.tensor_copy(abf[r, :, :], ab[r, :, :]).then_inc(*DV.inc("abf"))
            v.tensor_tensor(prob[r, :, :], best[r, :, :], bc(best[r, :, 0:1], [n, PH, TOPK]), ALU.subtract).then_inc(*DV.inc("off"))
            done(DV, "abf")
            out = sel[slot]
            idh = idf[r, :, :].rearrange("p (h s) a -> p h s a", s=2)
            for side in range(2):
                v.tensor_tensor(eq[r, :, :], bc(abf[r, side, :].unsqueeze(2), [n, HK, TOPK]),
                                bc(iota[r, :].unsqueeze(1), [n, HK, TOPK]), ALU.is_equal).then_inc(*DV.inc(f"eq{side}"))
                done(DV, f"eq{side}")
                for h in range(PH):
                    e_ = eq[r, TOPK * h:TOPK * h + TOPK, :]
                    last = v.tensor_tensor(e_, e_, bc(idh[:, h, side, :].unsqueeze(1), [n, TOPK, TOPK]), ALU.mult)
                last.then_inc(*DV.inc(f"pick{side}"))
                done(DV, f"pick{side}")
                v.tensor_reduce(out[r, side, :], eq[r, :, :], AX.X, ALU.add).then_inc(*DV.inc(f"e{side}"))
                done(DV, f"e{side}")
            done(AC, "exp")
            v.tensor_reduce(ssum[r, :], prob[r, :, :], AX.X, ALU.add).then_inc(*DV.inc("sum"))
            done(DV, "sum")
            v.reciprocal(ssum[r, :], ssum[r, :]).then_inc(*DV.inc("rec"))
            done(DV, "rec")
            v.tensor_tensor(out[r, 2, :].rearrange("p (h a) -> p h a", h=PH), prob[r, :, :],
                            bc(ssum[r, :].unsqueeze(2), [n, PH, TOPK]), ALU.mult).then_inc(*DV.inc("gate"))

        FULL = NTILE - 1

        def tiles(eng, body):
            with eng.Fori(0, FULL // 2) as r:
                for h in range(2):
                    body(2 * r + h, h, P)
            body(FULL, 0, LAST)

        with nc.Block() as block:
            @block.gpsimd
            def _(pool):
                nc.gpsimd.iota(iota_i[:, :], [[1, TOPK]], base=0, channel_multiplier=0).then_inc(s_io, 1)
                pool.wait_ge(s_io, 1)
                nc.gpsimd.tensor_copy(iota[:, :], iota_i[:, :]).then_inc(s_io, 1)

            @block.scalar
            def _(act):
                AC.credit(act)

                def body(j, slot, n):
                    act.wait_ge(DV.sem, DV.now("off", j))
                    nc.scalar.activation(prob[0:n, :, :], prob[0:n, :, :], ACT.Exp).then_inc(*AC.inc("exp"))
                    act.wait_ge(PE.sem, PE.now("turned", j))
                    at = j * P
                    dst = selT[:, :, at:at + n] if isinstance(j, int) else selT[:, :, bass.ds(at, n)]
                    nc.scalar.activation(dst, ps[slot][:, 0:3 * P].rearrange("p (q t) -> p q t", q=3)[:, :, 0:n],
                                         ACT.Copy).then_inc(*AC.inc("sel"))
                tiles(act, body)

            @block.tensor
            def _(pe):
                PE.credit(pe)

                def body(j, slot, n):
                    pe.wait_ge(DV.sem, DV.now("gate", j))
                    pe.wait_ge(AC.sem, AC.before("sel", j))
                    for i in range(3):
                        mm = nc.tensor.transpose(ps[slot][:, i * P:i * P + n], sel[slot][0:n, i, :], k.ident[0:n, 0:n])
                    mm.then_inc(*PE.inc("turned"))
                tiles(pe, body)

            @block.vector
            def _(dve):
                DV.credit(dve)
                two = dve.alloc_register("tk_two")
                dve.reg_mov(two, 2)

                def body(j, slot, n):
                    dve.wait_ge(PE.sem, PE.before("turned", j))

                    def done(S_, step):
                        dve.wait_ge(S_.sem, S_.now(step, j))
                        dve.reg_alu(two, two, 2, ALU.max)
                    dve.wait_ge(s_io, two)
                    dve.reg_alu(two, two, 2, ALU.max)
                    select(nc.vector, j, slot, n, done)
                tiles(dve, body)


TB = 64
NTB = T // TB
BATCH = 8


def phase_spread(k, selT):
    nc, io = k.nc, k.io
    AHEAD = 4
    RING = AHEAD * BATCH
    NB = TB // BATCH
    HALF = BATCH // 2
    with ExitStack() as ctx:
        sb = lambda n, s, dt=F32: ctx.enter_context(nc.sbuf_tensor(f"wt_{n}", s, dt))
        iota_i = sb("iota_i", [P, NK], I32)
        iota = sb("iota", [P, NK])
        one1 = sb("one1", [P, RING, NK])
        one2 = sb("one2", [P, RING, NK])
        stage = sb("stage", [P, 2, NK, TB])
        here = [sb(f"here{i}", [P, 3, TB]) for i in range(2)]
        ps = ctx.enter_context(nc.psum_tensor("wt_ps", [P, 4, BATCH, NK], F32))
        s_io = k.sem("wt_iota_step")
        s_here = k.sem("wt_columns_staged")
        s_st = [k.sem(f"wt_stored{i}") for i in range(2)]
        batches = [f"batch{n}" for n in range(NB)]
        OH = Progress(k.sem("wt_onehots"), *batches)
        GA = Progress(k.sem("wt_gated"), *batches)
        PE = Progress(k.sem("wt_matmul"), *batches)
        EV = Progress(k.sem("wt_evac"), *batches)

        def blocks(eng, body):
            with eng.Fori(0, NTB // 2) as r:
                for h in range(2):
                    body(2 * r + h, h, r)
            body(NTB - 1, 0, NTB // 2)

        def slots(n, lo=0, hi=BATCH):
            at = n * BATCH % RING
            return slice(at + lo, at + hi)

        with nc.Block() as block:
            @block.gpsimd
            def _(pool):
                nc.gpsimd.iota(iota_i[:, :], [[1, NK]], base=0, channel_multiplier=0).then_inc(s_io, 1)
                pool.wait_ge(s_io, 1)
                nc.gpsimd.tensor_copy(iota[:, :], iota_i[:, :]).then_inc(s_io, 1)

            @block.sync
            def _(sp):
                def body(b, slot, r):
                    sp.wait_ge(EV.sem, EV.now(batches[-1], b))
                    sp.dma_start(io["weights"][b].rearrange("e f t -> e (f t)"),
                                 stage[:, slot, :, :].rearrange("p f t -> p (f t)")).then_inc(s_st[slot], 16)
                blocks(sp, body)
                sp.wait_ge(s_st[0], 16 * (NTB // 2 + 2))
                sp.wait_ge(s_st[1], 16 * (NTB // 2 + 1))

            @block.vector
            def _(dve):
                v = nc.vector
                OH.credit(dve)
                dve.wait_ge(s_io, 2)

                def body(b, slot, r):
                    for n in range(NB):
                        dve.wait_ge(PE.sem, PE.back(n, AHEAD, b))
                        if n == 0:
                            cols = selT[:, :, b * TB:b * TB + TB] if isinstance(b, int) else selT[:, :, bass.ds(b * TB, TB)]
                            v.tensor_copy(here[slot][:, :, :], cols).then_inc(s_here, 1)
                            dve.wait_ge(s_here, b + 1)
                        t0 = n * BATCH

                        def onehots(out, side, lo, hi):
                            cnt = hi - lo
                            return v.tensor_tensor(out[:, slots(n, lo, hi), :], bc(iota[:, :].unsqueeze(1), [P, cnt, NK]),
                                                   bc(here[slot][:, side, t0 + lo:t0 + hi].unsqueeze(2), [P, cnt, NK]),
                                                   ALU.is_equal)
                        onehots(one1, 0, 0, BATCH)
                        onehots(one2, 1, 0, HALF)
                        for t in range(t0 + HALF, t0 + BATCH):
                            last = v.tensor_scalar(one2[:, t % RING, :], iota[:, :], here[slot][:, 1, t:t + 1],
                                                   here[slot][:, 2, t:t + 1], ALU.is_equal, ALU.mult)
                        last.then_inc(*OH.inc(batches[n]))
                blocks(dve, body)

            @block.tensor
            def _(pe):
                PE.credit(pe)

                def body(b, slot, r):
                    for n in range(NB):
                        pe.wait_ge(OH.sem, OH.now(batches[n], b))
                        pe.wait_ge(GA.sem, GA.now(batches[n], b))
                        pe.wait_ge(EV.sem, EV.back(n, 4, b))
                        for t in range(n * BATCH, (n + 1) * BATCH):
                            mm = nc.tensor.matmul(ps[:, n % 4, t % BATCH, :], one2[:, t % RING, :], one1[:, t % RING, :],
                                                  start=True, stop=True)
                        mm.then_inc(*PE.inc(batches[n]))
                blocks(pe, body)

            @block.scalar
            def _(act):
                GA.credit(act)
                EV.credit(act)
                for i in range(2):
                    act.sem_inc(s_st[i], 16)

                def body(b, slot, r):
                    def evac(n):
                        if n == 0:
                            act.wait_ge(s_st[slot], 16 * r + 16)
                        act.wait_ge(PE.sem, PE.now(batches[n], b))
                        dst = stage[:, slot, :, n * BATCH:(n + 1) * BATCH].rearrange("p f t -> p t f")
                        nc.scalar.activation(dst, ps[:, n % 4, :, :], ACT.Copy).then_inc(*EV.inc(batches[n]))

                    for n in range(NB):
                        act.wait_ge(OH.sem, OH.now(batches[n], b))
                        for t in range(n * BATCH, n * BATCH + HALF):
                            o_ = one2[:, t % RING, :]
                            last = nc.scalar.activation(o_, o_, ACT.Copy, scale=here[slot][:, 2, t:t + 1])
                        last.then_inc(*GA.inc(batches[n]))
                        if n:
                            evac(n - 1)
                    evac(NB - 1)
                blocks(act, body)


EX_CHUNKS = ((0, 6 * TB), (6 * TB, 12 * TB), (12 * TB, T))
NOUT = KC * len(EX_CHUNKS)


def phase_experts(k, xh, xl, acc):
    nc, io = k.nc, k.io
    NC = len(EX_CHUNKS)
    with ExitStack() as ctx:
        sb = lambda n, s, dt=F32: ctx.enter_context(nc.sbuf_tensor(f"ex_{n}", s, dt))
        u = [sb(f"u{i}", [P, KC, P]) for i in range(2)]
        uh = [sb(f"u_high{i}", [P, KC, P], F32R) for i in range(2)]
        ul = [sb(f"u_low{i}", [P, KC, P], F32R) for i in range(2)]
        vt = [sb(f"v{i}", [P, D]) for i in range(2)]
        vh, vl = ([sb(f"v_{n}{i}", [P, D], F32R) for i in range(2)] for n in ("high", "low"))
        g = [sb(f"g{i}", [P, NTB, TB]) for i in range(2)]
        w = sb("w", [P, T])
        wh, wl = ([sb(f"w_{n}{i}", [P, T], F32R) for i in range(2)] for n in ("high", "low"))
        psa = [ctx.enter_context(nc.psum_tensor(f"ex_psa{i}", [P, 512], F32)) for i in range(2)]
        pso = [ctx.enter_context(nc.psum_tensor(f"ex_pso{i}", [P, 512], F32)) for i in range(6)]
        s_u = [k.sem(f"ex_u{i}_loaded") for i in range(2)]
        s_v = [k.sem(f"ex_v{i}_loaded") for i in range(2)]
        s_g = [k.sem(f"ex_g{i}_loaded") for i in range(2)]
        s_zero = k.sem("ex_acc_zeroed")
        jobs = [f"u{j}" for j in range(NC)]
        outs = [f"v{n}" for n in range(NOUT)]
        parts = [f"w{j}" for j in range(NC)]
        PU = Progress(k.sem("ex_u_products"), *jobs)
        PV = Progress(k.sem("ex_v_products"), *outs)
        GE = Progress(k.sem("ex_gelu"), *jobs)
        UH = Progress(k.sem("ex_u_high"), "all")
        VH = Progress(k.sem("ex_v_high"), "all")
        WH = Progress(k.sem("ex_w_high"), *parts)
        UL = Progress(k.sem("ex_u_low"), "all")
        VL = Progress(k.sem("ex_v_low"), "all")
        MU = Progress(k.sem("ex_weighted"), *parts)
        WL = Progress(k.sem("ex_w_low"), *parts)
        AD = Progress(k.sem("ex_added"), *outs)
        R = NK // 2 - 1

        def schedule(eng, first, both, last):
            first((0, 0, 0))
            with eng.Fori(0, R) as r:
                both((2 * r + 1, 1, r), (2 * r, 0, r))
                both((2 * r + 2, 0, r + 1), (2 * r + 1, 1, r))
            both((NK - 1, 1, R), (NK - 2, 0, R))
            last((NK - 1, 1, R))

        as_f32 = lambda ap: ap.bitcast(F32)

        with nc.Block() as block:
            @block.sync
            def _(sp):
                def load(grp, par, free):
                    if free:
                        sp.wait_ge(UL.sem, UL.earlier("all", 2, grp))
                    sp.dma_start(u[par][:, :, :], io["u"][grp]).then_inc(s_u[par], 16)
                    if free:
                        sp.wait_ge(VL.sem, VL.earlier("all", 2, grp))
                    sp.dma_start(vt[par][:, :], io["v"][grp]).then_inc(s_v[par], 16)

                load(0, 0, False)
                load(1, 1, False)
                with sp.Fori(0, R) as r:
                    load(2 * r + 2, 0, True)
                    load(2 * r + 3, 1, True)

            @block.gpsimd
            def _(pool):
                def load(grp, par, free):
                    if free:
                        pool.wait_ge(MU.sem, MU.earlier(parts[-1], 2, grp))
                    sl = slice(grp, grp + 1) if isinstance(grp, int) else bass.ds(grp, 1)
                    pool.dma_start(g[par][:, :, :], io["weights"][:, :, sl, :].rearrange("b p e t -> p b (e t)")).then_inc(s_g[par], 16)

                load(0, 0, False)
                load(1, 1, False)
                with pool.Fori(0, R) as r:
                    load(2 * r + 2, 0, True)
                    load(2 * r + 3, 1, True)

            @block.tensor
            def _(pe):
                def u_job(ug, j):
                    grp, par, _ = ug
                    if j == 0:
                        pe.wait_ge(UL.sem, UL.now("all", grp))
                    pe.wait_ge(GE.sem, GE.back(j, 2 if j else 1, grp))
                    a, b = EX_CHUNKS[j]
                    passes = [(wt, x, kc) for kc in range(KC)
                              for wt, x in ((uh[par], xh[:, kc, a:b]), (uh[par], xl[:, kc, a:b]),
                                            (ul[par], xh[:, kc, a:b]))]
                    for n, (wt, x, kc) in enumerate(passes):
                        mm = nc.tensor.matmul(psa[j % 2][:, 0:b - a], wt[:, kc, :], x, start=n == 0, stop=n == len(passes) - 1)
                    mm.then_inc(*PU.inc(jobs[j]))

                def v_job(vg, n):
                    grp, par, _ = vg
                    dc, c = divmod(n, NC)
                    if n == 0:
                        pe.wait_ge(VL.sem, VL.now("all", grp))
                        pe.wait_ge(WL.sem, WL.now(parts[-1], grp))
                    pe.wait_ge(AD.sem, AD.back(n, 6, grp))
                    a, b = EX_CHUNKS[c]
                    ch = slice(dc * P, (dc + 1) * P)
                    out = pso[n % 6][:, 0:b - a]
                    nc.tensor.matmul(out, vh[par][:, ch], wh[par][:, a:b], start=True, stop=False)
                    nc.tensor.matmul(out, vh[par][:, ch], wl[par][:, a:b], start=False, stop=False)
                    nc.tensor.matmul(out, vl[par][:, ch], wh[par][:, a:b], start=False, stop=True).then_inc(*PV.inc(outs[n]))

                def both(ug, vg):
                    for j in range(NC):
                        u_job(ug, j)
                        for n in range(j * KC, (j + 1) * KC):
                            v_job(vg, n)

                PU.credit(pe)
                PV.credit(pe)
                schedule(pe, lambda ug: [u_job(ug, j) for j in range(NC)], both, lambda vg: [v_job(vg, n) for n in range(NOUT)])

            @block.scalar
            def _(act):
                copy = lambda out, in_: nc.scalar.activation(out, in_, ACT.Copy)

                def u_high(grp, par, number):
                    act.wait_ge(s_u[par], 16 * number + 16)
                    copy(uh[par][:, :, :], u[par][:, :, :]).then_inc(*UH.inc("all"))

                def v_high(grp, par, number):
                    act.wait_ge(s_v[par], 16 * number + 16)
                    copy(vh[par][:, :], vt[par][:, :]).then_inc(*VH.inc("all"))

                def gelu(grp, par, j):
                    a, b = EX_CHUNKS[j]
                    act.wait_ge(PU.sem, PU.now(jobs[j], grp))
                    act.wait_ge(WL.sem, WL.before(parts[j], grp))
                    nc.scalar.activation(w[:, a:b], psa[j % 2][:, 0:b - a], ACT.Gelu).then_inc(*GE.inc(jobs[j]))

                def w_high(grp, par, j):
                    a, b = EX_CHUNKS[j]
                    act.wait_ge(MU.sem, MU.now(parts[j], grp))
                    copy(wh[par][:, a:b], w[:, a:b]).then_inc(*WH.inc(parts[j]))

                def group(ug, more=True):
                    grp, par, number = ug
                    if more:
                        u_high(grp + 1, 1 - par, number + par)
                    gelu(grp, par, 0)
                    v_high(grp, par, number)
                    w_high(grp, par, 0)
                    gelu(grp, par, 1)
                    w_high(grp, par, 1)
                    gelu(grp, par, 2)
                    w_high(grp, par, 2)

                for S_ in (GE, UH, VH, WH):
                    S_.credit(act)
                u_high(0, 0, 0)
                with_last = lambda ug, vg: group(ug, more=not isinstance(ug[0], int))
                schedule(act, group, with_last, lambda vg: None)

            @block.vector
            def _(dve):
                v = nc.vector
                subtract = lambda out, in0, in1: v.tensor_tensor(out, in0, in1, ALU.subtract)

                def u_low(grp, par):
                    dve.wait_ge(UH.sem, UH.now("all", grp))
                    subtract(ul[par][:, :, :], u[par][:, :, :], as_f32(uh[par][:, :, :])).then_inc(*UL.inc("all"))

                def v_low(grp, par):
                    dve.wait_ge(VH.sem, VH.now("all", grp))
                    subtract(vl[par][:, :], vt[par][:, :], as_f32(vh[par][:, :])).then_inc(*VL.inc("all"))

                def weigh(ug, j):
                    grp, par, number = ug
                    if j == 0:
                        dve.wait_ge(s_g[par], 16 * number + 16)
                    dve.wait_ge(GE.sem, GE.now(jobs[j], grp))
                    a, b = EX_CHUNKS[j]
                    wv = w[:, a:b]
                    v.tensor_tensor(wv, wv, flat(g[par][:, a // TB:b // TB, :]), ALU.mult).then_inc(*MU.inc(parts[j]))

                def w_low(ug, j):
                    grp, par, _ = ug
                    dve.wait_ge(WH.sem, WH.now(parts[j], grp))
                    a, b = EX_CHUNKS[j]
                    subtract(wl[par][:, a:b], w[:, a:b], as_f32(wh[par][:, a:b])).then_inc(*WL.inc(parts[j]))

                def add(vg, n):
                    grp, _, _ = vg
                    dc, c = divmod(n, NC)
                    a, b = EX_CHUNKS[c]
                    dve.wait_ge(PV.sem, PV.now(outs[n], grp))
                    dve.wait_ge(AD.sem, AD.before(outs[n], grp))
                    v.tensor_tensor(acc[:, dc, a:b], pso[n % 6][:, 0:b - a], acc[:, dc, a:b], ALU.add).then_inc(*AD.inc(outs[n]))

                def group(ug, vg, more=True):
                    adds = lambda lo, hi: [add(vg, n) for n in range(lo, hi) if vg is not None]
                    grp, par, _ = ug
                    if more:
                        u_low(grp + 1, 1 - par)
                    for j in range(NC):
                        at = j * KC
                        adds(at, at + 4)
                        weigh(ug, j)
                        adds(at + 4, at + 6)
                        w_low(ug, j)
                        adds(at + 6, at + KC)
                        if j == 0:
                            v_low(grp, par)

                for S_ in (UL, VL, MU, WL, AD):
                    S_.credit(dve)
                u_low(0, 0)
                v.memset(acc[:, :, :], 0.0).then_inc(s_zero, 1)
                dve.wait_ge(s_zero, 1)
                schedule(dve, lambda ug: group(ug, None), lambda ug, vg: group(ug, vg, more=not isinstance(ug[0], int)),
                         lambda vg: [add(vg, n) for n in range(NOUT)])


def phase_final(k, acc):
    nc, io = k.nc, k.io
    with nc.sbuf_tensor("fin_x", [P, KC, T], F32) as x, nc.sbuf_tensor("fin_tmp", [P, T], F32) as tmp:
        s_x = k.sem("fin_x1_loaded")
        s_res = k.sem("fin_residual_step")
        with nc.Block() as block:
            @block.sync
            def _(sp):
                sp.dma_start(x[:, :, :], io["x1"]).then_inc(s_x, 16)

            @block.vector
            def _(dve):
                dve.wait_ge(s_x, 16)
                for m in range(KC):
                    add_gated(k, dve, x[:, m, :], acc[:, m, :], tmp, GT2 + m, s_res, 3 * m)

        def store(sp, sem):
            sp.dma_start(io["y_out"], acc[:, :, :]).then_inc(sem, 16)
            return 16

        rmsnorm_mod(k, "final", x, lambda kc: acc[:, kc, 0:SEQ], lambda kc: token_views(acc[:, kc, :])[1],
                    SCF, SHF, None, store)


def program(nc, io):
    with ExitStack() as ctx:
        k = Core(nc, ctx, io)
        for name, shape in (("proj", (PROJ_TILES + 1, P, TX)), ("rwc", (NCH + 1, P, 5, NPAIR, CL)),
                            ("rw_gate", (NPAIR, P, T)), ("rw_bonus", (NPAIR, P, T)), ("rw_y", (NCH + 1, P, NPAIR, CL)),
                            ("xbc", (NXBC, P, T)), ("ssd_rows", (SH, 3, T)), ("ssd_y", (KC, P, T)), ("x1", (P, KC, T)),
                            ("weights", (NTB, NK, NK, TB))):
            io[name] = nc.dram_tensor(name, shape, F32, kind="Internal").ap()
        k.par = k.lasting("par", [P, NPAR])
        k.mod = k.lasting("mod", [P, 64, NCOND])
        k.ident = k.lasting("ident", [P, P])
        k.ones = k.lasting("ones", [P, P])
        k.pairones = k.lasting("pairones", [P, P])
        k.const = k.lasting("const", [P, 4])
        k.shift_sb = k.lasting("shift_sb", [P, KC, NSEQ])
        with ExitStack() as until_merge:
            k.ctx = until_merge
            k.cT = k.lasting("cT", [P, KC, NCOND])
            k.lam_end = k.lasting("lam_end", [P, NPAIR, NCH + NSEQ])
            k.mt_mask = k.lasting("mt_mask", [P, 2, 4, CL])
            k.lv_mask = k.lasting("lv_mask", [P, LEVELS, 2, CL])
            k.ident2 = k.lasting("ident2", [P, 2, CL])
            k.seq_cols = k.lasting("seq_cols", [P, NSEQ, CL])
            k.seq_rows = k.lasting("seq_rows", [P, NSEQ])
            k.ssd_mask = k.lasting("ssd_mask", [P, SL])
            k.ssd_mask_smp = k.lasting("ssd_mask_smp", [CL, CL])
            phase_ada(k)
            with nc.sbuf_tensor("xe_high", [P, KC, TXE], F32R) as xh, nc.sbuf_tensor("xe_low", [P, KC, TXE], F32R) as xl:
                phase_norm1(k, xh, xl)
                phase_inputs(k, xh, xl)
            k.head_sel = k.lasting("head_sel", [SH, SH, P])
            phase_rw_prompt(k)
            phase_rw_samples(k)
            phase_ssd(k)
        k.recycle_semaphores()
        with nc.sbuf_tensor("oa", [P, NPAIR, T], F32) as oa, nc.sbuf_tensor("ob", [P, KC, T], F32) as ob:
            phase_rw_post(k, oa)
            phase_ssd_post(k, ob)
            with nc.sbuf_tensor("x1_sb", [P, KC, T], F32) as x1:
                phase_merge(k, oa, ob, x1)
        with nc.sbuf_tensor("x_high", [P, KC, T], F32R) as xh, nc.sbuf_tensor("x_low", [P, KC, T], F32R) as xl:
            phase_norm2(k, xh, xl)
            with nc.sbuf_tensor("selT", [P, 3, T], F32) as selT:
                with nc.sbuf_tensor("val", [P, NTILE, 2 * PH, TOPK], F32) as val, \
                        nc.sbuf_tensor("idx", [P, NTILE, 2 * PH, TOPK], U32) as idx:
                    phase_scores(k, xh, xl, val, idx)
                    phase_topk(k, val, idx, selT)
                phase_spread(k, selT)
            k.recycle_semaphores()
            with nc.sbuf_tensor("acc", [P, KC, T], F32) as acc:
                phase_experts(k, xh, xl, acc)
                phase_final(k, acc)
def _rows(a, tiles):
    return np.ascontiguousarray(a.reshape(tiles, P, -1).transpose(1, 0, 2))


def _cols(v):
    return v.reshape(-1, P).T


def _weight(a):
    kk, m = a.shape
    return np.ascontiguousarray(a.reshape(kk // P, P, m // P, P).transpose(2, 1, 0, 3))


def _arrays(x):
    f = lambda n: np.asarray(x[n])
    out = {}
    toks = np.concatenate([f("x_prompt").reshape(SEQ, D), f("x_sample").reshape(NSEQ * DSEQ, D)])
    out["xT"] = _rows(toks.T, KC)
    out["cT"] = _rows(np.concatenate([f("c_prompt"), f("c_sample")]).T, KC)
    out["shiftT"] = _rows(f("state_shift")[0].T, KC)
    wa = np.concatenate([f("w_ada")[0], f("w_ada_f")], axis=1)
    grouped = lambda w, n: np.ascontiguousarray(w.reshape(KC, P, -1, n).transpose(2, 1, 0, 3))
    out["w_ada"] = grouped(wa[:, :ADA_FIRST * P], 4 * P)
    out["w_ada_rest"] = grouped(wa[:, ADA_FIRST * P:], ADA_STEP * P)
    cw = f("ssm_conv_w")[0].reshape(CONVK, NXBC, P).transpose(2, 0, 1).reshape(P, CONVK * NXBC)
    mu = f("rw_mu")[0]
    out["params"] = np.ascontiguousarray(np.concatenate(
        [_cols(f("b_ada")[0]), _cols(f("b_ada_f")), _cols(f("norm1_g")[0]), _cols(f("norm2_g")[0]), _cols(f("final_g")),
         _cols(mu[3 * RDIM:]), cw, _cols(f("ssm_conv_b")[0]), _cols(f("ssm_norm_w")[0]),
         _cols(f("rw_ln_w")[0]), _cols(f("rw_ln_b")[0])], axis=1))
    r3 = [mu[0:RDIM], mu[RDIM:2 * RDIM], mu[2 * RDIM:3 * RDIM], f("rw_w0")[0], f("rw_a0")[0], f("rw_k_k")[0],
          f("rw_k_a")[0], f("rw_r_k")[0].reshape(-1)]
    out["rw_params"] = np.ascontiguousarray(np.stack([v.reshape(NPAIR, P) for v in r3], axis=2))
    wi = f("w_in")[0]
    ssm0 = RW_TILES * P
    dt0 = ssm0 + D + NXBC * P
    main = np.concatenate([wi[:, :dt0], wi[:, dt0 + SH:]], axis=1)
    wt = _weight(main)
    z, xbc = RW_TILES, RW_TILES + KC
    out["w_in"] = np.concatenate([wt[xbc:xbc + XBC_TILES], wt[:z], wt[z:xbc], wt[xbc + XBC_TILES:]])
    out["w_dt"] = _rows(wi[:, dt0:dt0 + SH], KC)
    out["lora_w"] = np.ascontiguousarray(np.stack(
        [np.concatenate([f("rw_w2")[0], f("rw_a2")[0]]), f("rw_g2")[0]]).reshape(2, P, NPAIR, P).transpose(2, 1, 0, 3))
    out["head_params"] = np.ascontiguousarray(np.stack([f("ssm_dt_bias")[0], f("ssm_A_log")[0]], axis=1))
    out["ssm_D"] = np.ascontiguousarray(f("ssm_D")[0].reshape(KC, 2).T)
    sw = f("state_wkv")[0].reshape(NSEQ, NPAIR, 2, RD, RD)
    out["wkvT"] = np.ascontiguousarray(sw.transpose(0, 2, 4, 1, 3).reshape(NSEQ, P, NPAIR, RD))
    out["convT"] = _rows(f("state_conv")[0].transpose(2, 0, 1).reshape(NXBC * P, -1), NXBC).reshape(P, NXBC, NSEQ, CONVK - 1)
    out["ssmT"] = np.ascontiguousarray(f("state_ssm")[0].transpose(0, 3, 1, 2).reshape(NSEQ, SN, SH * SD))
    out["w_pa"] = _weight(f("w_pa")[0])
    out["w_pb"] = _weight(f("w_pb")[0])
    out["w_out"] = _weight(f("w_out")[0])
    out["w_q"] = _weight(f("peer_wq")[0])
    out["keysT"] = np.ascontiguousarray(f("peer_keys")[0].reshape(2 * PH, NK, P).transpose(2, 0, 1))
    out["u"] = np.ascontiguousarray(f("peer_u")[0].reshape(NK, NK, KC, P).transpose(0, 3, 2, 1))
    out["v"] = np.ascontiguousarray(f("peer_v")[0].reshape(NK, NK, D))
    return out


_OUTS = {"shift_out": (P, KC, NCOND), "y_out": (P, KC, T), "wkv_out": (NCOND, P, NPAIR, RD),
         "conv_out": (P, NXBC, NCOND, CONVK - 1), "ssm_out": (NCOND, SN, SH * SD)}


def kernel(**inputs):
    import numpy as _np
    import concourse.bacc as _bacc
    from concourse import mybir as _mybir
    from concourse.bass_utils import run_bass_kernel_spmd as _run

    nc = _bacc.Bacc("TRN2", target_bir_lowering=False, num_devices=1)
    arrays, io = {}, {}
    for name, a in _arrays(inputs).items():
        arrays["in_" + name] = a
        io[name] = nc.dram_tensor("in_" + name, a.shape, _mybir.dt.from_np(a.dtype), kind="ExternalInput").ap()
    for name, shape in _OUTS.items():
        io[name] = nc.dram_tensor("out_" + name, shape, F32, kind="ExternalOutput").ap()
    program(nc, io)
    r = _run(nc, [arrays], core_ids=[0])
    got = {n: r.results[0]["out_" + n] for n in _OUTS}

    unrow = lambda a: a.transpose(1, 0, 2).reshape(-1, a.shape[2])
    y = unrow(got["y_out"]).T
    shift = unrow(got["shift_out"]).T
    wkv = got["wkv_out"].reshape(NCOND, 2, RD, NPAIR, RD).transpose(0, 3, 1, 4, 2).reshape(NCOND, RH, RD, RD)
    conv = unrow(got["conv_out"].reshape(P, NXBC, NCOND * (CONVK - 1))).reshape(-1, NCOND, CONVK - 1).transpose(1, 2, 0)
    ssm = got["ssm_out"].reshape(NCOND, SN, SH, SD).transpose(0, 2, 3, 1)
    c = _np.ascontiguousarray
    return (c(y[:SEQ].reshape(1, SEQ, D)), c(y[SEQ:].reshape(NSEQ, DSEQ, D)),
            c(shift[None, 0:1]), c(wkv[None, 0:1]), c(conv[None, 0:1]), c(ssm[None, 0:1]),
            c(shift[None, 1:]), c(wkv[None, 1:]), c(conv[None, 1:]), c(ssm[None, 1:]))
```
